# Optimizing a Trainium2 kernel written in Bass

```python
import math
import jax, jax.numpy as jnp
from jax import lax
import numpy as np

D_MODEL = 1024
BATCH = 1
SEQ = 512
DEPTH = 2
DEC_BATCH = 8
DEC_SEQ = 1
PAST_LEN = 256
PAGE_SIZE = 128

N_EVEN = (DEPTH + 1) // 2
N_ODD = DEPTH // 2
MIX_HALF = D_MODEL // 2
EPS = 1e-6

GLA_HEADS = 4
GLA_DV = MIX_HALF // GLA_HEADS
GLA_DK = GLA_DV // 2
GLA_LR = 16
GLA_GATE_NORM = 16.0
GLA_CHUNK = 64
GLA_COLS = 2 * GLA_HEADS * GLA_DK + 2 * MIX_HALF + GLA_LR

RWKV_HEAD = 64
RWKV_HEADS = MIX_HALF // RWKV_HEAD
RWKV_W_LR = 64
RWKV_A_LR = 64
RWKV_G_LR = 128
RWKV_COLS = 3 * MIX_HALF + RWKV_W_LR + RWKV_A_LR + RWKV_G_LR
RWKV_LN_EPS = 64e-5
EVEN_COLS = GLA_COLS + RWKV_COLS

SB_HEAD = 64
SB_HEADS = MIX_HALF // SB_HEAD
SB_BLOCK = 128

DN_HEADS = 4
DN_HEAD = MIX_HALF // DN_HEADS
DN_CONV = 4
DN_CHUNK = 64
DN_CONV_CH = 3 * MIX_HALF
ODD_COLS = 3 * MIX_HALF + DN_CONV_CH + MIX_HALF + 2 * DN_HEADS

MEM_LEN = 256
X_HEADS = 4
X_HEAD = D_MODEL // X_HEADS

FF = ((8 * D_MODEL + 3 * 256 - 1) // (3 * 256)) * 256

kernel_name = 'hybrid_gla_rwkv7_stickbreak_gdn_step'

def _offsets(sizes):
    return [int(s) for s in np.cumsum(sizes)[:-1]]

def rmsnorm(x, g):
    xf = x.astype(jnp.float32)
    return xf * lax.rsqrt(jnp.mean(xf * xf, axis=-1, keepdims=True) + EPS) * g

def l2norm(x):
    return x * lax.rsqrt(jnp.sum(x * x, axis=-1, keepdims=True) + EPS)

def to_chunks(a, c):
    b, t = a.shape[:2]
    n = -(-t // c)
    a = jnp.pad(a, [(0, 0), (0, n * c - t)] + [(0, 0)] * (a.ndim - 2))
    a = a.reshape((b, n, c) + a.shape[2:])
    return jnp.moveaxis(jnp.moveaxis(a, 1, 0), 3, 2)

def from_chunks(o, t):
    n, b, h, c = o.shape[:4]
    o = jnp.swapaxes(jnp.moveaxis(o, 0, 1), 2, 3)
    return o.reshape((b, n * c, h) + o.shape[4:])[:, :t]

def gla_recurrence(q, k, v, log_f, s0):
    t = q.shape[1]
    c = min(GLA_CHUNK, t)
    qc, kc, vc, fc = (to_chunks(a, c) for a in (q, k, v, log_f))
    bc = jnp.cumsum(fc, axis=3)
    mask = jnp.tril(jnp.ones((c, c), bool))

    def step(s, xs):
        qi, ki, vi, bi = xs
        diff = jnp.where(mask[:, :, None], bi[..., :, None, :] - bi[..., None, :, :], -jnp.inf)
        p = jnp.einsum('bhtd,bhsd,bhtsd->bhts', qi, ki, jnp.exp(diff))
        o = jnp.einsum('bhtd,bhde->bhte', qi * jnp.exp(bi), s) + jnp.einsum('bhts,bhse->bhte', p, vi)
        bl = bi[..., -1:, :]
        s = jnp.exp(bl[..., 0, :])[..., None] * s + jnp.einsum('bhsd,bhse->bhde', ki * jnp.exp(bl - bi), vi)
        return s, o

    s, o = lax.scan(step, s0, (qc, kc, vc, bc))
    return from_chunks(o, t), s

def rwkv_recurrence(r, w, k, v, kk, a, s0):
    def step(s, xs):
        rt, wt, kt, vt, kkt, at = xs
        sa = jnp.einsum('bhij,bhj->bhi', s, -kkt)
        s = s * wt[:, :, None, :] + sa[..., None] * (kkt * at)[:, :, None, :] + vt[..., None] * kt[:, :, None, :]
        return s, jnp.einsum('bhij,bhj->bhi', s, rt)

    xs = tuple(jnp.moveaxis(z, 1, 0) for z in (r, w, k, v, kk, a))
    s, y = lax.scan(step, s0, xs)
    return jnp.moveaxis(y, 0, 1), s

def delta_rule(q, k, v, g, beta, s0):
    t = q.shape[1]
    c = min(DN_CHUNK, t)
    qc, kc, vc = (to_chunks(a, c) for a in (q, k, v))
    gc, bc = (to_chunks(a, c) for a in (g, beta))
    G = jnp.cumsum(gc, axis=-1)
    incl = jnp.tril(jnp.ones((c, c), bool))
    strict = jnp.tril(jnp.ones((c, c), bool), -1)
    dmat = jnp.exp(jnp.where(incl, G[..., :, None] - G[..., None, :], -jnp.inf))
    kk = jnp.einsum('nbhtd,nbhsd->nbhts', kc, kc)
    a_mat = jnp.where(strict, bc[..., :, None] * kk * dmat, 0.0)
    ia = a_mat + jnp.eye(c, dtype=a_mat.dtype)
    tv = lax.linalg.triangular_solve(ia, bc[..., None] * vc, left_side=True, lower=True, unit_diagonal=True)
    tk = lax.linalg.triangular_solve(ia, (bc * jnp.exp(G))[..., None] * kc, left_side=True, lower=True, unit_diagonal=True)
    qk = jnp.where(incl, jnp.einsum('nbhtd,nbhsd->nbhts', qc, kc) * dmat, 0.0)

    def step(s, xs):
        tvi, tki, qi, ki, qki, gi = xs
        u = tvi - jnp.einsum('bhtd,bhde->bhte', tki, s)
        o = jnp.einsum('bhtd,bhde->bhte', qi * jnp.exp(gi)[..., None], s) + jnp.einsum('bhts,bhse->bhte', qki, u)
        gl = gi[..., -1:]
        s = jnp.exp(gl)[..., None] * s + jnp.einsum('bhtd,bhte->bhde', ki * jnp.exp(gl - gi)[..., None], u)
        return s, o

    s, o = lax.scan(step, s0, (tv, tk, qc, kc, qk, G))
    return from_chunks(o, t), s

def causal_conv(x, buf, w):
    t = x.shape[1]
    xp = jnp.concatenate([buf.astype(jnp.float32), x.astype(jnp.float32)], axis=1)
    y = sum(xp[:, i:i + t] * w[i] for i in range(DN_CONV))
    return jax.nn.silu(y), xp[:, t:]

def stick_breaking(q, k, v, bias, q_offset):
    b, t, h, dh = q.shape
    tk = k.shape[1]
    qb = SB_BLOCK if t % SB_BLOCK == 0 else t
    nb = t // qb
    q_blocks = jnp.moveaxis(q.reshape(b, nb, qb, h, dh), 1, 0)
    starts = q_offset + jnp.arange(nb, dtype=jnp.int32) * qb
    kpos = jnp.arange(tk, dtype=jnp.int32)
    kf = k.astype(jnp.float32)
    vf = v.astype(jnp.float32)
    scale = dh ** -0.5

    def block(args):
        qblk, start = args
        z = jnp.einsum('bqhd,bkhd->bhqk', qblk.astype(jnp.float32), kf) * scale + bias[None, :, None, None]
        qpos = start + jnp.arange(qb, dtype=jnp.int32)
        causal = kpos[None, :] < qpos[:, None]
        log_stay = jnp.where(causal, jax.nn.log_sigmoid(-z), 0.0)
        later = lax.cumsum(log_stay, axis=3, reverse=True) - log_stay
        wts = jnp.where(causal, jnp.exp(jax.nn.log_sigmoid(z) + later), 0.0)
        return jnp.einsum('bhqk,bkhd->bqhd', wts, vf)

    o = lax.map(block, (q_blocks, starts))
    return jnp.moveaxis(o, 0, 1).reshape(b, t, h, dh)

def even_mixer(h, p, s_gla, s_rwkv, s_shift):
    f32 = jnp.float32
    b, t, _ = h.shape
    cols = h @ p['w_in']
    g_cols, r_cols = cols[..., :GLA_COLS], cols[..., GLA_COLS:]
    nk = GLA_HEADS * GLA_DK
    gq, gk, gv, gg, glr = jnp.split(g_cols, _offsets([nk, nk, MIX_HALF, MIX_HALF, GLA_LR]), axis=-1)
    q = (gq.reshape(b, t, GLA_HEADS, GLA_DK) * GLA_DK ** -0.5).astype(f32)
    k = gk.reshape(b, t, GLA_HEADS, GLA_DK).astype(f32)
    v = gv.reshape(b, t, GLA_HEADS, GLA_DV).astype(f32)
    log_f = jax.nn.log_sigmoid(glr @ p['gla_w_a2'] + p['gla_b_a']) / GLA_GATE_NORM
    log_f = log_f.reshape(b, t, GLA_HEADS, GLA_DK).astype(f32)
    o_gla, s_gla = gla_recurrence(q, k, v, log_f, s_gla.astype(f32))
    o_gla = rmsnorm(o_gla, p['gla_norm']) * jax.nn.silu(gg.reshape(b, t, GLA_HEADS, GLA_DV))
    o_gla = o_gla.reshape(b, t, MIX_HALF)
    prev = jnp.concatenate([s_shift[:, None].astype(r_cols.dtype), r_cols[:, :-1]], axis=1)
    xr = r_cols + (prev - r_cols) * p['rwkv_mu']
    new_shift = r_cols[:, -1]
    rr, rk, rv, rw, ra, rg = jnp.split(xr, _offsets([MIX_HALF] * 3 + [RWKV_W_LR, RWKV_A_LR, RWKV_G_LR]), axis=-1)
    hs = (b, t, RWKV_HEADS, RWKV_HEAD)
    w_log = -jax.nn.softplus(-(p['rwkv_w0'] + jnp.tanh(rw) @ p['rwkv_w2'])) - 0.5
    decay = jnp.exp(-jnp.exp(w_log))
    a = jax.nn.sigmoid(p['rwkv_a0'] + ra @ p['rwkv_a2'])
    g = jax.nn.sigmoid(rg) @ p['rwkv_g2']
    kk = l2norm((rk * p['rwkv_k_k']).reshape(hs)).astype(f32)
    k2 = rk * (1.0 + (a - 1.0) * p['rwkv_k_a'])
    r4 = rr.reshape(hs).astype(f32)
    k4 = k2.reshape(hs).astype(f32)
    v4 = rv.reshape(hs).astype(f32)
    y, s_rwkv = rwkv_recurrence(r4, decay.reshape(hs).astype(f32), k4, v4, kk,
                                a.reshape(hs).astype(f32), s_rwkv.astype(f32))
    mu = jnp.mean(y, axis=-1, keepdims=True)
    var = jnp.mean(jnp.square(y - mu), axis=-1, keepdims=True)
    y = ((y - mu) * lax.rsqrt(var + RWKV_LN_EPS)).reshape(b, t, MIX_HALF) * p['rwkv_ln_w'] + p['rwkv_ln_b']
    bonus = jnp.sum(r4 * k4 * p['rwkv_r_k'].reshape(RWKV_HEADS, RWKV_HEAD), axis=-1, keepdims=True) * v4
    y = (y + bonus.reshape(b, t, MIX_HALF)) * g
    out = jnp.concatenate([o_gla, y], axis=-1) @ p['w_out']
    return out, s_gla, s_rwkv, new_shift

def odd_mixer(h, p, s_dn, s_conv, k_past, v_past):
    f32 = jnp.float32
    b, t, _ = h.shape
    cols = h @ p['w_in']
    sq, sk, sv, dqkv, dz, da, db = jnp.split(
        cols, _offsets([MIX_HALF] * 3 + [DN_CONV_CH, MIX_HALF, DN_HEADS, DN_HEADS]), axis=-1)
    shs = (b, t, SB_HEADS, SB_HEAD)
    q = rmsnorm(sq.reshape(shs), p['sb_q_norm'])
    k = rmsnorm(sk.reshape(shs), p['sb_k_norm'])
    v = sv.reshape(shs).astype(f32)
    if k_past is None:
        k_all, v_all, offset = k, v, 0
    else:
        k_all = jnp.concatenate([k_past.astype(f32), k], axis=1)
        v_all = jnp.concatenate([v_past.astype(f32), v], axis=1)
        offset = k_past.shape[1]
    o_sb = stick_breaking(q, k_all, v_all, p['sb_bias'].astype(f32), offset).reshape(b, t, MIX_HALF)
    conv_out, s_conv = causal_conv(dqkv, s_conv, p['dn_conv'])
    dq, dk, dv = jnp.split(conv_out, 3, axis=-1)
    dhs = (b, t, DN_HEADS, DN_HEAD)
    dq = l2norm(dq.reshape(dhs)) * DN_HEAD ** -0.5
    dk = l2norm(dk.reshape(dhs))
    dv = dv.reshape(dhs)
    gdec = (-jnp.exp(p['dn_a_log']) * jax.nn.softplus(da + p['dn_dt_bias'])).astype(f32)
    beta = jax.nn.sigmoid(db).astype(f32)
    o_dn, s_dn = delta_rule(dq, dk, dv, gdec, beta, s_dn.astype(f32))
    o_dn = (rmsnorm(o_dn, p['dn_norm']) * jax.nn.silu(dz.reshape(dhs))).reshape(b, t, MIX_HALF)
    out = jnp.concatenate([o_sb, o_dn], axis=-1) @ p['w_out']
    return out, k, v, s_dn, s_conv

def memory_kv(mem, mem_norm, w_xkv, xk_norm):
    b, l, _ = mem.shape
    kv = rmsnorm(mem, mem_norm) @ w_xkv
    k = rmsnorm(kv[..., :D_MODEL].reshape(b, l, X_HEADS, X_HEAD), xk_norm)
    v = kv[..., D_MODEL:].reshape(b, l, X_HEADS, X_HEAD)
    return k, v

def cross_attn(h, mk, mv, w_xq, xq_norm, w_xo):
    b, t, _ = h.shape
    q = rmsnorm((h @ w_xq).reshape(b, t, X_HEADS, X_HEAD), xq_norm)
    s = jnp.einsum('bthd,bmhd->bhtm', q, mk.astype(jnp.float32)) * X_HEAD ** -0.5
    a = jax.nn.softmax(s, axis=-1)
    o = jnp.einsum('bhtm,bmhd->bthd', a, mv.astype(jnp.float32)).reshape(b, t, D_MODEL)
    return o @ w_xo

def swiglu(h, w_gu, w_down):
    gu = h @ w_gu
    return (jax.nn.silu(gu[..., :FF]) * gu[..., FF:]) @ w_down

def setup_inputs(seed: int = 0) -> dict:
    key = jax.random.key(seed)
    keys = iter(jax.random.split(key, 64))

    def nrm(shape, scale=1.0):
        return jax.random.normal(next(keys), shape, jnp.float32) * scale

    def gain(shape):
        return 1.0 + nrm(shape, 0.05)

    def unif(shape, lo, hi):
        return jax.random.uniform(next(keys), shape, jnp.float32, lo, hi)

    n_pages = PAST_LEN // PAGE_SIZE
    n_used = DEC_BATCH * n_pages
    n_phys = n_used + (n_used + 3) // 4
    page_table = jax.random.permutation(next(keys), n_phys)[:n_used].reshape(DEC_BATCH, n_pages).astype(jnp.int32)
    dt = jnp.exp(unif((N_ODD, DN_HEADS), math.log(1e-3), math.log(1e-1)))
    dn_dt_bias = jnp.log(jnp.expm1(dt))
    ds = D_MODEL ** -0.5
    return {
        'x_prompt': nrm((BATCH, SEQ, D_MODEL)),
        'x_sample': nrm((DEC_BATCH, DEC_SEQ, D_MODEL)),
        'mem_prompt': nrm((BATCH, MEM_LEN, D_MODEL)),
        'state_gla': nrm((N_EVEN, DEC_BATCH, GLA_HEADS, GLA_DK, GLA_DV), 0.3),
        'state_rwkv': nrm((N_EVEN, DEC_BATCH, RWKV_HEADS, RWKV_HEAD, RWKV_HEAD), 0.3),
        'state_rwkv_shift': nrm((N_EVEN, DEC_BATCH, RWKV_COLS)),
        'cache_sb_k': nrm((N_ODD, n_phys, PAGE_SIZE, SB_HEADS, SB_HEAD)),
        'cache_sb_v': nrm((N_ODD, n_phys, PAGE_SIZE, SB_HEADS, SB_HEAD)),
        'page_table': page_table,
        'state_delta': nrm((N_ODD, DEC_BATCH, DN_HEADS, DN_HEAD, DN_HEAD), 0.3),
        'state_delta_conv': nrm((N_ODD, DEC_BATCH, DN_CONV - 1, DN_CONV_CH)),
        'cache_mem_k': nrm((DEPTH, DEC_BATCH, MEM_LEN, X_HEADS, X_HEAD)),
        'cache_mem_v': nrm((DEPTH, DEC_BATCH, MEM_LEN, X_HEADS, X_HEAD)),
        'norm_mix': gain((DEPTH, D_MODEL)),
        'norm_cross': gain((DEPTH, D_MODEL)),
        'norm_ffn': gain((DEPTH, D_MODEL)),
        'w_in_even': nrm((N_EVEN, D_MODEL, EVEN_COLS), ds),
        'w_out_even': nrm((N_EVEN, 2 * MIX_HALF, D_MODEL), (2 * MIX_HALF) ** -0.5),
        'gla_w_a2': nrm((N_EVEN, GLA_LR, GLA_HEADS * GLA_DK), GLA_LR ** -0.5),
        'gla_b_a': nrm((N_EVEN, GLA_HEADS * GLA_DK), 0.1),
        'gla_norm': gain((N_EVEN, GLA_DV)),
        'rwkv_mu': unif((N_EVEN, RWKV_COLS), 0.0, 1.0),
        'rwkv_w0': unif((N_EVEN, MIX_HALF), -6.0, -0.5),
        'rwkv_w2': nrm((N_EVEN, RWKV_W_LR, MIX_HALF), 0.1 * RWKV_W_LR ** -0.5),
        'rwkv_a0': nrm((N_EVEN, MIX_HALF), 0.5),
        'rwkv_a2': nrm((N_EVEN, RWKV_A_LR, MIX_HALF), RWKV_A_LR ** -0.5),
        'rwkv_g2': nrm((N_EVEN, RWKV_G_LR, MIX_HALF), RWKV_G_LR ** -0.5),
        'rwkv_k_k': 0.85 + nrm((N_EVEN, MIX_HALF), 0.05),
        'rwkv_k_a': gain((N_EVEN, MIX_HALF)),
        'rwkv_r_k': nrm((N_EVEN, MIX_HALF), 0.1),
        'rwkv_ln_w': gain((N_EVEN, MIX_HALF)),
        'rwkv_ln_b': nrm((N_EVEN, MIX_HALF), 0.05),
        'w_in_odd': nrm((N_ODD, D_MODEL, ODD_COLS), ds),
        'w_out_odd': nrm((N_ODD, 2 * MIX_HALF, D_MODEL), (2 * MIX_HALF) ** -0.5),
        'sb_q_norm': gain((N_ODD, SB_HEAD)),
        'sb_k_norm': gain((N_ODD, SB_HEAD)),
        'sb_bias': unif((N_ODD, SB_HEADS), -7.0, -5.0),
        'dn_conv': nrm((N_ODD, DN_CONV, DN_CONV_CH), DN_CONV ** -0.5),
        'dn_a_log': jnp.log(unif((N_ODD, DN_HEADS), 1.0, 16.0)),
        'dn_dt_bias': dn_dt_bias,
        'dn_norm': gain((N_ODD, DN_HEAD)),
        'mem_norm': gain((DEPTH, D_MODEL)),
        'w_xq': nrm((DEPTH, D_MODEL, D_MODEL), ds),
        'w_xkv': nrm((DEPTH, D_MODEL, 2 * D_MODEL), ds),
        'w_xo': nrm((DEPTH, D_MODEL, D_MODEL), ds),
        'xq_norm': gain((DEPTH, X_HEAD)),
        'xk_norm': gain((DEPTH, X_HEAD)),
        'w_gu': nrm((DEPTH, D_MODEL, 2 * FF), ds),
        'w_down': nrm((DEPTH, FF, D_MODEL), FF ** -0.5),
    }

def reference(x_prompt, x_sample, mem_prompt,
              state_gla, state_rwkv, state_rwkv_shift,
              cache_sb_k, cache_sb_v, page_table, state_delta, state_delta_conv,
              cache_mem_k, cache_mem_v,
              norm_mix, norm_cross, norm_ffn,
              w_in_even, w_out_even, gla_w_a2, gla_b_a, gla_norm,
              rwkv_mu, rwkv_w0, rwkv_w2, rwkv_a0, rwkv_a2, rwkv_g2, rwkv_k_k, rwkv_k_a, rwkv_r_k,
              rwkv_ln_w, rwkv_ln_b,
              w_in_odd, w_out_odd, sb_q_norm, sb_k_norm, sb_bias, dn_conv, dn_a_log, dn_dt_bias, dn_norm,
              mem_norm, w_xq, w_xkv, w_xo, xq_norm, xk_norm,
              w_gu, w_down):
    f32 = jnp.float32
    b = x_prompt.shape[0]
    db = x_sample.shape[0]
    n_past = page_table.shape[1] * PAGE_SIZE
    xp, xs = x_prompt, x_sample
    p_gla, p_rwkv, p_shift, p_sbk, p_sbv, p_dn, p_conv, p_mk, p_mv = [], [], [], [], [], [], [], [], []
    s_gla, s_rwkv, s_shift, s_sbk, s_sbv, s_dn, s_conv = [], [], [], [], [], [], []
    for i in range(DEPTH):
        j = i // 2
        if i % 2 == 0:
            ep = {'w_in': w_in_even[j], 'w_out': w_out_even[j], 'gla_w_a2': gla_w_a2[j],
                  'gla_b_a': gla_b_a[j], 'gla_norm': gla_norm[j], 'rwkv_mu': rwkv_mu[j],
                  'rwkv_w0': rwkv_w0[j], 'rwkv_w2': rwkv_w2[j], 'rwkv_a0': rwkv_a0[j],
                  'rwkv_a2': rwkv_a2[j], 'rwkv_g2': rwkv_g2[j], 'rwkv_k_k': rwkv_k_k[j],
                  'rwkv_k_a': rwkv_k_a[j], 'rwkv_r_k': rwkv_r_k[j], 'rwkv_ln_w': rwkv_ln_w[j],
                  'rwkv_ln_b': rwkv_ln_b[j]}
            o, sg, sr, sh = even_mixer(rmsnorm(xp, norm_mix[i]), ep,
                                       jnp.zeros((b, GLA_HEADS, GLA_DK, GLA_DV), f32),
                                       jnp.zeros((b, RWKV_HEADS, RWKV_HEAD, RWKV_HEAD), f32),
                                       jnp.zeros((b, RWKV_COLS), f32))
            xp = xp + o
            p_gla.append(sg)
            p_rwkv.append(sr)
            p_shift.append(sh)
            o, sg, sr, sh = even_mixer(rmsnorm(xs, norm_mix[i]), ep,
                                       state_gla[j], state_rwkv[j], state_rwkv_shift[j])
            xs = xs + o
            s_gla.append(sg)
            s_rwkv.append(sr)
            s_shift.append(sh)
        else:
            op = {'w_in': w_in_odd[j], 'w_out': w_out_odd[j], 'sb_q_norm': sb_q_norm[j],
                  'sb_k_norm': sb_k_norm[j], 'sb_bias': sb_bias[j], 'dn_conv': dn_conv[j],
                  'dn_a_log': dn_a_log[j], 'dn_dt_bias': dn_dt_bias[j], 'dn_norm': dn_norm[j]}
            o, kn, vn, sd, sc = odd_mixer(rmsnorm(xp, norm_mix[i]), op,
                                          jnp.zeros((b, DN_HEADS, DN_HEAD, DN_HEAD), f32),
                                          jnp.zeros((b, DN_CONV - 1, DN_CONV_CH), f32), None, None)
            xp = xp + o
            p_sbk.append(kn)
            p_sbv.append(vn)
            p_dn.append(sd)
            p_conv.append(sc)
            k_past = cache_sb_k[j][page_table].reshape(db, n_past, SB_HEADS, SB_HEAD)
            v_past = cache_sb_v[j][page_table].reshape(db, n_past, SB_HEADS, SB_HEAD)
            o, kn, vn, sd, sc = odd_mixer(rmsnorm(xs, norm_mix[i]), op,
                                          state_delta[j], state_delta_conv[j], k_past, v_past)
            xs = xs + o
            s_sbk.append(kn)
            s_sbv.append(vn)
            s_dn.append(sd)
            s_conv.append(sc)
        mk, mv = memory_kv(mem_prompt, mem_norm[i], w_xkv[i], xk_norm[i])
        p_mk.append(mk)
        p_mv.append(mv)
        xp = xp + cross_attn(rmsnorm(xp, norm_cross[i]), mk, mv, w_xq[i], xq_norm[i], w_xo[i])
        xs = xs + cross_attn(rmsnorm(xs, norm_cross[i]), cache_mem_k[i], cache_mem_v[i],
                             w_xq[i], xq_norm[i], w_xo[i])
        xp = xp + swiglu(rmsnorm(xp, norm_ffn[i]), w_gu[i], w_down[i])
        xs = xs + swiglu(rmsnorm(xs, norm_ffn[i]), w_gu[i], w_down[i])
    return (xp, xs,
            jnp.stack(p_gla), jnp.stack(p_rwkv), jnp.stack(p_shift),
            jnp.stack(p_sbk), jnp.stack(p_sbv), jnp.stack(p_dn), jnp.stack(p_conv),
            jnp.stack(p_mk), jnp.stack(p_mv),
            jnp.stack(s_gla), jnp.stack(s_rwkv), jnp.stack(s_shift),
            jnp.stack(s_sbk), jnp.stack(s_sbv), jnp.stack(s_dn), jnp.stack(s_conv))


_drawn_inputs = setup_inputs


def setup_inputs(seed=0):
    import zlib

    import numpy as np

    out = dict(_drawn_inputs(seed))
    spreads = {}
    factors = {'norm_cross': 6.699,
     'rwkv_w2': 8.0,
     'sb_q_norm': 64.0,
     'sb_bias': 5.505,
     'dn_norm': 3.116,
     'xq_norm': 6.788,
     'cache_sb_v': 5.532}
    for name, (base, spread) in spreads.items():
        noise = np.random.default_rng([zlib.crc32(name.encode()), seed]).standard_normal(out[name].shape)
        drawn = base * np.exp(spread * noise) if base else spread * noise
        out[name] = __import__('jax').numpy.asarray(drawn.astype(out[name].dtype))
    for name, factor in factors.items():
        out[name] = (out[name] * factor).astype(out[name].dtype)
    return out
```

```python
from contextlib import ExitStack, contextmanager

import numpy as np
import concourse.bass as bass
import concourse.mybir as mybir

F32 = mybir.dt.float32
F32R = mybir.dt.float32r
U32 = mybir.dt.uint32
I32 = mybir.dt.int32
ACT = mybir.ActivationFunctionType
ALU = mybir.AluOpType
AX = mybir.AxisListType

P = 128
D = 1024
KT = D // P
T = 512
B = 8
N = T + B
HALF = N // 2
NC = T // P
MEM = 256
FT = 2816 // P
PAGE = 128
PAST = 256
PAGES = PAST // PAGE
NPHYS = 20
EPS = 1e-6
RWKV_LN_EPS = 64e-5
SLOTS = 4
SLOT_K = 11

GQ, GK, GV, GG, RR, RK, RV, RWA, RG, GLR, EVEN_TILES = 0, 2, 4, 8, 12, 16, 20, 24, 25, 26, 27
R0, R_TILES = RR, 14
SQ, SK, SV, DQ, DK, DV, DZ, DAB, ODD_TILES = 0, 4, 8, 12, 16, 20, 24, 28, 29

LEVELS = [64, 32, 16, 8, 4, 2, 1]
CONST_NAMES = (["ident", "ones", "head_ones", "key_after", "causal", "before", "causal64", "before64", "forbid"]
               + [f"level{m}" for m in LEVELS])
CONST_AT = {n: i * P for i, n in enumerate(CONST_NAMES)}
SCAN128_AT = len(CONST_NAMES) * P
SCAN64_AT = SCAN128_AT + T
SEL_AT = SCAN64_AT + T
EPS_AT = SEL_AT + B * P
CONSTS = EPS_AT + 2


def constants():
    s, t = np.arange(P)[:, None], np.arange(P)[None, :]
    m = {
        "ident": s == t, "ones": s >= 0 * t, "head_ones": s // 64 == t // 64,
        "key_after": s >= t, "causal": s <= t, "before": s < t,
        "causal64": (s <= t) & (s // 64 == t // 64), "before64": (s < t) & (s // 64 == t // 64),
    }
    for h in LEVELS:
        m[f"level{h}"] = (s // (2 * h) == t // (2 * h)) & (s % (2 * h) < h) & (t % (2 * h) >= h)
    m["forbid"] = np.where(s >= t, -1e30, 0.0)
    out = np.zeros((P, CONSTS), np.float32)
    for n, a in CONST_AT.items():
        out[:, a:a + P] = m[n]
    out[:, SCAN128_AT:SCAN128_AT + T] = np.arange(T) % 128 != 0
    out[:, SCAN64_AT:SCAN64_AT + T] = np.arange(T) % 64 != 0
    for b in range(B):
        out[b, SEL_AT + b * P:SEL_AT + (b + 1) * P] = 1
        out[32 + b, SEL_AT + b * P:SEL_AT + (b + 1) * P] = 1
    out[:, EPS_AT], out[:, EPS_AT + 1] = EPS, RWKV_LN_EPS
    return out


SCR = 13888
MAP = {}
_at = 0
for _name, _size in (("x", KT * N), ("w", SLOTS * SLOT_K * P), ("cst", CONSTS + 6), ("par0", 1368), ("par1", 112),
                     ("rstd", N), ("o", KT * N), ("c", 29 * N), ("h", KT * N), ("scr", SCR)):
    MAP[_name] = _at
    _at += _size
MAP["end"] = _at

EVEN_PARAMS = [("g_mix", 8), ("g_cross", 8), ("g_ffn", 8), ("g_mem", 8), ("xq", 2), ("xk", 2),
               ("gla_b", 2), ("gla_norm", 1), ("mu", 14), ("w0", 4), ("a0", 4), ("k_k", 4), ("k_a", 4), ("r_k", 4),
               ("ln_w", 4), ("ln_b", 4), ("gla_a2", 256), ("wa2", 512), ("g2", 512)]
ODD_PARAMS = [("g_mix", 8), ("g_cross", 8), ("g_ffn", 8), ("g_mem", 8), ("xq", 2), ("xk", 2),
              ("sbq", 1), ("sbk", 1), ("sb_bias", 8), ("dn_conv", 48), ("dn_a", 1), ("dn_dt", 1), ("dn_norm", 1)]
N_EVEN_P = sum(w for _, w in EVEN_PARAMS)
N_ODD_P = sum(w for _, w in ODD_PARAMS)


class Signal:

    def __init__(self, sem):
        self.sem, self.base, self.count = sem, 0, 0

    def at(self, k):
        return self.base + k


class Engine:

    def __init__(self, eng, done):
        self.done = done
        self.eng = eng

    def step(self, ins):
        ins.then_inc(self.done.sem, 1)
        self.done.count += 1
        self.eng.wait_ge(self.done.sem, self.done.count)

    def tell(self, ins, signal):
        ins.then_inc(signal.sem, 1)
        signal.count += 1
        self.eng.wait_ge(signal.sem, signal.count)


class Linear:

    def __init__(self, src, units, kt):
        self.src, self.units, self.kt, self.at = src, units, kt, None


class Split:

    def __init__(self, k, name, tiles, x_hi, x_lo, kt, w_hi, w_lo):
        self.x = [k.place(f"{name}_x_{p}", at, [tiles, N], F32R) for p, at in (("hi", x_hi), ("lo", x_lo))]
        self.w = [k.place(f"{name}_w_{p}", at, [2, kt * P], F32R) for p, at in (("hi", w_hi), ("lo", w_lo))]


class Kernel:

    def __init__(self, nc, dram, ctx):
        self.nc, self.d, self.ctx = nc, dram, ctx
        self.counters = []

        self.arena = ctx.enter_context(nc.sbuf_tensor("arena", [P, MAP["end"]], F32))
        self.arena_at = nc.sbuf_base - 4 * MAP["end"]

        def sb(name, *shape):
            return self.place(name, MAP[name], list(shape), F32)

        self.x = sb("x", KT, N)
        self.h = sb("h", KT, N)
        self.o = sb("o", KT, N)
        self.c = sb("c", 29, N)
        self.w = sb("w", SLOTS, SLOT_K * P)
        self.scr = sb("scr", SCR)
        self.cst = sb("cst", CONSTS)
        self.par0, self.par1 = sb("par0", N_EVEN_P), sb("par1", N_ODD_P)
        self.pages = ctx.enter_context(nc.sbuf_tensor("pages", [1, B * PAGES], I32))
        self.rstd = sb("rstd", N)
        self.std = Split(self, "std", KT, MAP["h"], MAP["scr"], KT, MAP["scr"] + 4160, MAP["scr"] + 6208)
        self.sq = self.cut(8256, KT, N)
        self.tmp = self.cut(12416, 2, N)
        hid = MAP["o"] + 2 * FT * N
        self.mlp = Split(self, "mlp", KT, hid, hid + 4160, KT, hid + 8320, hid + 10368)
        self.mlp_tmp = [self.place(f"mlp_tmp{i}", hid + 12416 + i * N, [N], F32) for i in range(3)]
        self.mlp_sq = self.place("mlp_sq", MAP["o"], [KT, N], F32)
        self.mlp_norm = self.place("mlp_norm", MAP["o"] + KT * N, [2, N], F32)
        self.hid = Split(self, "hid", FT, MAP["o"], MAP["o"] + FT * N, SLOT_K, hid, hid + 2 * SLOT_K * P)
        self.eps = self.cst[:, EPS_AT:EPS_AT + 1]
        self.ln_eps = self.cst[:, EPS_AT + 1:EPS_AT + 2]
        self.ps = ctx.enter_context(nc.psum_tensor("ps", [P, 8, 512], F32))

        self.weights_loaded = [self.new_counter(f"weights_loaded{i}") for i in range(SLOTS)]
        self.unit_done = self.new_counter("unit_done")
        self.product_read = [self.new_counter(f"product_read{i}") for i in range(2)]
        self.weights_hi = self.new_counter("weights_hi")
        self.weights_split = self.new_counter("weights_split")
        self.plain_ready = self.new_counter("plain_ready")
        self.hi_ready = self.new_counter("hi_ready")
        self.hidden_hi = self.new_counter("hidden_hi")
        self.hidden_lo = self.new_counter("hidden_lo")
        self.inputs_loaded = [self.new_counter(f"inputs_loaded{i}") for i in range(4)]
        self.stored = self.new_counter("stored")
        self.squares_ready = self.new_counter("squares_ready")
        self.sums_ready = self.new_counter("sums_ready")
        self.scale_ready = self.new_counter("scale_ready")
        self.normed = self.new_counter("normed")
        self.exp_ready = self.new_counter("exp_ready")
        self.scores_ready = self.new_counter("scores_ready")
        self.keys_used = self.new_counter("keys_used")
        self.values_used = self.new_counter("values_used")
        self.values_loaded = [self.new_counter(f"values_loaded{i}") for i in range(3)]
        self.maxima_ready = self.new_counter("maxima_ready")
        self.tensor_out = self.new_counter("tensor_out")
        self.tensor_out2 = self.new_counter("tensor_out2")
        self.product_kept = self.new_counter("product_kept")
        self.vector_out = self.new_counter("vector_out")
        self.vector_out2 = self.new_counter("vector_out2")
        self.scalar_out = self.new_counter("scalar_out")
        self.scalar_out2 = self.new_counter("scalar_out2")
        self.pool_out = self.new_counter("pool_out")
        self.dve = Engine(nc.vector, self.new_counter("vector_step"))
        self.act = Engine(nc.scalar, self.new_counter("scalar_step"))
        self.pool = Engine(nc.gpsimd, self.new_counter("pool_step"))
        self.ring = 0
        self.stores = 0

    def place(self, name, at, shape, dt):
        return self.nc.alloc_sbuf_tensor_at(name, [P, *shape], dt, offset=self.arena_at + 4 * at)

    def new_counter(self, name):
        s = Signal(self.ctx.enter_context(self.nc.semaphore(name)))
        self.counters.append(s)
        return s

    @contextmanager
    def stage(self):
        for s in self.counters:
            s.base = s.count
        with self.nc.Block() as block:
            yield block

    def const(self, name):
        a = CONST_AT[name]
        return self.cst[:, a:a + P]

    def mask(self, name):
        return self.const(name).bitcast(U32)

    def param(self, name):
        at = 0
        for n, w in self.params[0]:
            if n == name:
                return self.params[1][:, at:at + w]
            at += w
        raise KeyError(name)

    def cut(self, at, *shape):
        n = int(np.prod(shape))
        assert at + n <= SCR, (at, shape)
        flat = self.scr[:, at:at + n]
        if len(shape) == 1:
            return flat
        names = "abcd"[:len(shape)]
        return flat.rearrange(f"p ({' '.join(names)}) -> p {' '.join(names)}", **dict(zip(names, shape)))

    def store(self, eng, out, in_):
        eng.dma_start(out, in_).then_inc(self.stored.sem, 16)
        self.stored.count += 16

    def load_unit(self, sp, lin, j, slot):
        src = lin.src[j] if isinstance(j, int) else lin.src[bass.ds(j, 1)].rearrange("o p n -> p (o n)")
        sp.dma_start(self.w[:, slot, 0:lin.kt * P], src).then_inc(self.weights_loaded[slot].sem, 16)

    def prefetch(self, sp, lin):
        lin.at = self.ring
        for j in range(SLOTS):
            if lin.at + j >= SLOTS:
                sp.wait_ge(self.weights_split.sem, lin.at + j - SLOTS + 1)
            self.load_unit(sp, lin, j, (lin.at + j) % SLOTS)
        self.ring += lin.units

    def stream(self, sp, lin):
        body = lin.units // SLOTS
        if body > 1:
            with sp.Fori(1, body) as i:
                for u in range(SLOTS):
                    sp.wait_ge(self.weights_split.sem, (i - 1) * SLOTS + (lin.at + u + 1))
                    self.load_unit(sp, lin, i * SLOTS + u, (lin.at + u) % SLOTS)
        for j in range(max(SLOTS, body * SLOTS), lin.units):
            sp.wait_ge(self.weights_split.sem, lin.at + j - SLOTS + 1)
            self.load_unit(sp, lin, j, (lin.at + j) % SLOTS)

    def split_unit(self, dve, lin, site, u, i=0):
        nc = self.nc
        slot, n = (lin.at + u) % SLOTS, lin.kt * P
        raw, hi, lo = self.w[:, slot, 0:n], site.w[0][:, u % 2, 0:n], site.w[1][:, u % 2, 0:n]
        dve.wait_ge(self.weights_loaded[slot].sem, 16 * i + 16 * ((lin.at + u) // SLOTS + 1))
        if u >= 2 or not isinstance(i, int):
            dve.wait_ge(self.unit_done.sem, i * SLOTS + (lin.at + u - 1))
        nc.vector.tensor_copy(hi, raw).then_inc(self.weights_hi.sem, 1)
        dve.wait_ge(self.weights_hi.sem, i * SLOTS + (lin.at + u + 1))
        nc.vector.tensor_tensor(lo, raw, hi.bitcast(F32), ALU.subtract).then_inc(self.weights_split.sem, 1)

    def each_unit(self, dve, lin, site, read=None):
        body = (lin.units - 2) // SLOTS
        with dve.Fori(0, body) as i:
            for u in range(SLOTS):
                if read is not None:
                    read(u, i)
                self.split_unit(dve, lin, site, u + 2, i)
        for j in range(body * SLOTS, lin.units):
            if read is not None:
                read(j, 0)
            if j + 2 < lin.units:
                self.split_unit(dve, lin, site, j + 2)

    def product(self, pe, lin, site, spans, per=1):
        nc = self.nc

        def unit(u, i):
            o = u // per
            pe.wait_ge(self.weights_split.sem, i * SLOTS + (lin.at + u + 1))
            if u % per == 0:
                read = self.product_read[o % 2]
                pe.wait_ge(read.sem, read.base + i * (SLOTS // per // 2) + o // 2)
            hi, lo = (t[:, u % 2, 0:lin.kt * P].rearrange("p (k n) -> p k n", k=lin.kt) for t in site.w)
            for k in range(lin.kt):
                x = k + (u % per) * lin.kt
                if u == 0 and per == 1:
                    pe.wait_ge(self.normed.sem, self.normed.at(k + 1))
                passes = ((hi, site.x[0]), (hi, site.x[1]), (lo, site.x[0]))
                for n, (w, v) in enumerate(passes):
                    first, last = u % per == 0 and k == 0 and n == 0, u % per == per - 1 and k == lin.kt - 1 and n == 2
                    for s, (a, b) in enumerate(spans):
                        ins = nc.tensor.matmul(self.ps[:, 2 * (o % 2) + s, 0:b - a], w[:, k, :], v[:, x, a:b],
                                               start=first, stop=last)
            ins.then_inc(self.unit_done.sem, 1)

        body = lin.units // SLOTS
        with pe.Fori(0, body) as i:
            for u in range(SLOTS):
                unit(u, i)
        for j in range(body * SLOTS, lin.units):
            unit(j, 0)

    def read_tile(self, eng, lin, u, i, read, per=1):
        if u % per == per - 1:
            o = u // per
            eng.wait_ge(self.unit_done.sem, i * SLOTS + (lin.at + u + 1))
            read(i * (SLOTS // per) + o, 2 * (o % 2)).then_inc(self.product_read[o % 2].sem, 1)

    def tiles_read(self, lin, per=1):
        for q in range(2):
            self.product_read[q].count += len(range(q, lin.units // per, 2))

    def read_tiles(self, eng, lin, read, per=1):
        body = lin.units // SLOTS
        with eng.Fori(0, body) as i:
            for u in range(SLOTS):
                self.read_tile(eng, lin, u, i, read, per)
        for j in range(body * SLOTS, lin.units):
            self.read_tile(eng, lin, j, 0, read, per)
        self.tiles_read(lin, per)

    def pair(self, bank, rows=P):
        return self.ps[0:rows, bank:bank + 2, 0:HALF]

    def norm_pe(self, pe, sq, spans):
        nc = self.nc
        for k in range(KT):
            pe.wait_ge(self.squares_ready.sem, self.squares_ready.at(k + 1))
            for s, (a, b) in enumerate(spans):
                ins = nc.tensor.matmul(self.ps[:, 6 + s, 0:b - a], self.const("ones"), sq[:, k, a:b],
                                       start=k == 0, stop=k == KT - 1)
        ins.then_inc(self.sums_ready.sem, 1)
        self.sums_ready.count += 1

    def norm_act(self, act, x, site, sq, tmp, width, spans):
        nc = self.nc
        for k in range(KT):
            nc.scalar.activation(sq[:, k, 0:width], x[:, k, 0:width], ACT.Square).then_inc(self.squares_ready.sem, 1)
        self.squares_ready.count += KT
        act.wait_ge(self.sums_ready.sem, self.sums_ready.at(1))
        n = spans[0][1]
        sums = self.ps[:, 6:6 + len(spans), 0:n]
        r = self.rstd[:, 0:width].rearrange("p (s n) -> p s n", n=n)
        self.act.step(nc.scalar.activation(r, sums, ACT.Ln, bias=self.eps, scale=1.0 / D))
        self.act.tell(nc.scalar.activation(self.rstd[:, 0:width], self.rstd[:, 0:width], ACT.Exp, scale=-0.5),
                      self.scale_ready)
        for k in range(KT):
            act.wait_ge(self.plain_ready.sem, self.plain_ready.at(k + 1))
            nc.scalar.activation(site.x[0][:, k, 0:width], tmp[:, k % 2, 0:width], ACT.Copy).then_inc(self.hi_ready.sem, 1)
        self.hi_ready.count += KT

    def norm_dve(self, dve, x, site, tmp, gain, width):
        nc = self.nc
        dve.wait_ge(self.scale_ready.sem, self.scale_ready.at(1))

        def low(k):
            dve.wait_ge(self.hi_ready.sem, self.hi_ready.at(k + 1))
            self.dve.tell(nc.vector.tensor_tensor(site.x[1][:, k, 0:width], tmp[:, k % 2, 0:width],
                                                  site.x[0][:, k, 0:width].bitcast(F32), ALU.subtract), self.normed)

        for k in range(KT):
            self.dve.tell(nc.vector.scalar_tensor_tensor(tmp[:, k % 2, 0:width], x[:, k, 0:width], gain[:, k:k + 1],
                                                         self.rstd[:, 0:width], ALU.mult, ALU.mult), self.plain_ready)
            if k:
                low(k - 1)
        low(KT - 1)

    SPANS = [(0, HALF), (HALF, N)]

    def start(self):
        nc = self.nc
        with self.stage() as block:
            @block.sync
            def _(sp):
                sp.dma_start(self.cst[:], self.d["cst"]).then_inc(self.inputs_loaded[0].sem, 16)
                sp.dma_start(self.x[:], self.d["x"]).then_inc(self.inputs_loaded[0].sem, 16)
                sp.dma_start(self.par0[:], self.d["par0"]).then_inc(self.inputs_loaded[0].sem, 16)
                sp.dma_start(self.par1[:], self.d["par1"]).then_inc(self.inputs_loaded[0].sem, 16)
                sp.dma_start(self.pages[:], self.d["page_table"]).then_inc(self.inputs_loaded[0].sem, 16)
                self.prefetch(sp, self.lin["in0"])
                sp.wait_ge(self.inputs_loaded[0].sem, self.inputs_loaded[0].at(80))
                self.inputs_loaded[0].count += 80

            @block.vector
            def _(dve):
                for read in self.product_read:
                    self.dve.tell(nc.vector.memset(self.rstd[:], 0.0), read)

    def normed_product(self, lin, x, gain, width, spans, following, read, mem=None):
        with self.stage() as block:
            @block.sync
            def _(sp):
                if mem is not None:
                    sp.dma_start(x, mem).then_inc(self.inputs_loaded[0].sem, 16)
                    self.inputs_loaded[0].count += 16
                self.stream(sp, lin)
                self.prefetch(sp, following)

            @block.tensor
            def _(pe):
                self.norm_pe(pe, self.sq, spans)
                self.product(pe, lin, self.std, spans)

            @block.scalar
            def _(act):
                if mem is not None:
                    act.wait_ge(self.inputs_loaded[0].sem, self.inputs_loaded[0].at(16))
                self.norm_act(act, x, self.std, self.sq, self.tmp, width, spans)
                self.read_tiles(act, lin, read)

            @block.vector
            def _(dve):
                for u in range(2):
                    self.split_unit(dve, lin, self.std, u)
                if mem is not None:
                    dve.wait_ge(self.inputs_loaded[0].sem, self.inputs_loaded[0].at(16))
                self.norm_dve(dve, x, self.std, self.tmp, gain, width)
                self.each_unit(dve, lin, self.std)

    def projection(self, lin, gain, following):
        self.normed_product(lin, self.x, self.param(gain), N, self.SPANS, following, lambda o, bank: (
            self.nc.scalar.activation(self.tile_pair(self.c, o), self.pair(bank), ACT.Copy)))

    def tile_pair(self, t, o):
        one = t[:, bass.ds(o, 1), :] if not isinstance(o, int) else t[:, o:o + 1, :]
        return one.rearrange("p o (s n) -> p (o s) n", s=2)

    def residual(self, lin, site, following, per=1, src=None):
        nc = self.nc
        with self.stage() as block:
            @block.sync
            def _(sp):
                self.stream(sp, lin)
                if following is not None:
                    self.prefetch(sp, following)

            @block.tensor
            def _(pe):
                self.product(pe, lin, site, self.SPANS, per)

            @block.scalar
            def _(act):
                if src is not None:
                    for k in range(KT):
                        nc.scalar.activation(site.x[0][:, k], src[:, k], ACT.Copy).then_inc(self.hi_ready.sem, 1)
                    self.hi_ready.count += KT

            @block.vector
            def _(dve):
                for u in range(2):
                    self.split_unit(dve, lin, site, u)
                if src is not None:
                    for k in range(KT):
                        dve.wait_ge(self.hi_ready.sem, self.hi_ready.at(k + 1))
                        self.dve.tell(nc.vector.tensor_tensor(site.x[1][:, k], src[:, k], site.x[0][:, k].bitcast(F32),
                                                              ALU.subtract), self.normed)

                def add(o, bank):
                    return nc.vector.tensor_tensor(self.tile_pair(self.x, o), self.tile_pair(self.x, o), self.pair(bank), ALU.add)
                self.each_unit(dve, lin, site, lambda u, i: self.read_tile(dve, lin, u, i, add, per))
                self.tiles_read(lin, per)

    G_B, G_E, G_Q, G_K, G_P, G_V = 0, 1040, 2064, 4112, 6160, 8208
    G_KT, G_DK, G_S, G_DQ, G_EX = 10256, 11280, 12304, 13328, 13344

    def gla_gates(self):
        nc, c = self.nc, self.c
        z = self.cut(self.G_Q, 2, N)
        e = self.cut(self.G_K, 2, N)
        b = self.cut(self.G_B, 2, N)
        vt = self.cut(self.G_V, NC, T)
        a2 = self.param("gla_a2")
        with self.stage() as block:
            @block.tensor
            def _(pe):
                for j in range(2):
                    for s, (lo, hi) in enumerate(self.SPANS):
                        ins = nc.tensor.matmul(self.ps[:, 2 * j + s, 0:HALF], a2[0:16, j * P:(j + 1) * P],
                                               c[0:16, GLR, lo:hi], start=True, stop=True)
                ins.then_inc(self.tensor_out.sem, 1)
                self.tensor_out.count += 1
                for t in range(NC):
                    for h in range(4):
                        ins = nc.tensor.transpose(self.ps[:, 4 + t, h * P:(h + 1) * P],
                                                  c[:, GV + h, t * P:(t + 1) * P], self.const("ident"))
                ins.then_inc(self.tensor_out2.sem, 1)
                self.tensor_out2.count += 1

            @block.scalar
            def _(act):
                act.wait_ge(self.vector_out.sem, self.vector_out.at(1))
                self.act.step(nc.scalar.activation(e, e, ACT.Exp))
                self.act.tell(nc.scalar.activation(e, e, ACT.Ln, bias=1.0), self.scalar_out)
                act.wait_ge(self.tensor_out2.sem, self.tensor_out2.at(1))
                self.act.step(nc.scalar.activation(vt.rearrange("p a b -> p (a b)"), self.banks(4, 4), ACT.Copy))
                act.wait_ge(self.vector_out.sem, self.vector_out.at(2))
                self.act.step(nc.scalar.activation(self.cut(self.G_DQ, 2, B), b[:, :, T:N], ACT.Exp))

            @block.gpsimd
            def _(pool):
                self.pool.tell(nc.gpsimd.tensor_scalar(c[:, GQ:GQ + 2, :], c[:, GQ:GQ + 2, :], 0.125, None, ALU.mult),
                               self.pool_out)

            @block.vector
            def _(dve):
                dve.wait_ge(self.tensor_out.sem, self.tensor_out.at(1))
                for j in range(2):
                    self.dve.step(nc.vector.tensor_scalar(z[:, j].rearrange("p (s n) -> p s n", s=2), self.pair(2 * j),
                                                          self.param("gla_b")[:, j:j + 1], None, ALU.add))
                self.dve.tell(nc.vector.scalar_tensor_tensor(e, z, -1.0, z, ALU.mult, ALU.min), self.vector_out)
                dve.wait_ge(self.scalar_out.sem, self.scalar_out.at(1))
                self.dve.step(nc.vector.scalar_tensor_tensor(z, z, 0.0, e, ALU.min, ALU.subtract))
                self.dve.step(nc.vector.tensor_scalar(z, z, 1.0 / 16.0, None, ALU.mult))
                scan = self.cst[:, SCAN128_AT:SCAN128_AT + T]
                for j in range(2):
                    self.dve.step(nc.vector.tensor_tensor_scan(b[:, j, 0:T], scan, z[:, j, 0:T], 0.0, ALU.mult, ALU.add))
                self.dve.tell(nc.vector.tensor_copy(b[:, :, T:N], z[:, :, T:N]), self.vector_out)

    def banks(self, at, n):
        return self.ps[:, at:at + n, :].rearrange("p a b -> p (a b)")

    def gla_levels(self):
        nc, c = self.nc, self.c
        b = self.cut(self.G_B, 2, N)[:, :, 0:T]
        diff = self.cut(self.G_E, 2, T)
        q, k = c[:, GQ:GQ + 2, 0:T], c[:, GK:GK + 2, 0:T]
        qs = [self.cut(self.G_Q + i * 1024, 2, T) for i in range(2)]
        ks = [self.cut(self.G_K + i * 1024, 2, T) for i in range(2)]
        expd = self.cut(self.G_DK, 2, T)
        pt = self.cut(self.G_P, 4, T)
        with self.stage() as block:
            @block.scalar
            def _(act):
                for i in range(len(LEVELS)):
                    act.wait_ge(self.vector_out.sem, self.vector_out.at(i + 1))
                    if i:
                        act.wait_ge(self.vector_out2.sem, self.vector_out2.at(i))
                        act.wait_ge(self.pool_out.sem, self.pool_out.at(i))
                    self.act.tell(nc.scalar.activation(expd, diff, ACT.Exp), self.scalar_out)

            @block.gpsimd
            def _(pool):
                for i in range(len(LEVELS)):
                    pool.wait_ge(self.scalar_out.sem, self.scalar_out.at(i + 1))
                    if i >= 2:
                        pool.wait_ge(self.tensor_out.sem, self.tensor_out.at(i - 1))
                    self.pool.tell(nc.gpsimd.tensor_tensor(qs[i % 2], q, expd, ALU.mult), self.pool_out)

            @block.vector
            def _(dve):
                self.dve.step(nc.vector.memset(pt, 0.0))

                def keep(i, name):
                    dve.wait_ge(self.tensor_out.sem, self.tensor_out.at(i + 1))
                    m = self.mask(name).unsqueeze(1).to_broadcast([P, NC, P])
                    for j in range(4):
                        ins = nc.vector.copy_predicated(pt[:, j].rearrange("p (c t) -> p c t", c=NC), m,
                                                        self.ps[:, 4 * (i % 2) + j, :].rearrange("p (c t) -> p c t", c=NC))
                        if j < 3:
                            self.dve.step(ins)
                        else:
                            self.dve.tell(ins, self.product_kept)

                for i, m in enumerate(LEVELS):
                    if i:
                        dve.wait_ge(self.scalar_out.sem, self.scalar_out.at(i))
                    bv = b.rearrange("p j (g w) -> p j g w", w=2 * m)
                    dv = diff.rearrange("p j (g w) -> p j g w", w=2 * m)
                    for j in range(2):
                        ref = bv[:, j, :, m - 1:m].to_broadcast([P, T // (2 * m), 2 * m])
                        self.dve.step(nc.vector.tensor_tensor(dv[:, j], bv[:, j], ref, ALU.subtract))
                    self.dve.tell(nc.vector.scalar_tensor_tensor(diff, diff, -1.0, diff, ALU.mult, ALU.min),
                                  self.vector_out)
                    if i:
                        keep(i - 1, f"level{LEVELS[i - 1]}")
                    dve.wait_ge(self.scalar_out.sem, self.scalar_out.at(i + 1))
                    if i >= 2:
                        dve.wait_ge(self.tensor_out.sem, self.tensor_out.at(i - 1))
                    self.dve.tell(nc.vector.tensor_tensor(ks[i % 2], k, expd, ALU.mult), self.vector_out2)
                keep(len(LEVELS) - 1, "level1")
                keep(len(LEVELS), "ident")

            @block.tensor
            def _(pe):
                for i in range(len(LEVELS) + 1):
                    if i < len(LEVELS):
                        pe.wait_ge(self.pool_out.sem, self.pool_out.at(i + 1))
                        pe.wait_ge(self.vector_out2.sem, self.vector_out2.at(i + 1))
                    if i >= 2:
                        pe.wait_ge(self.product_kept.sem, self.product_kept.at(i - 1))
                    lq, lk = (qs[i % 2], ks[i % 2]) if i < len(LEVELS) else (q, k)
                    for par in range(2):
                        rows = slice(64 * par, 64 * par + 64)
                        for hp in range(2):
                            for t in range(NC):
                                cols = slice(t * P, (t + 1) * P)
                                ins = nc.tensor.matmul(self.ps[:, 4 * (i % 2) + 2 * par + hp, cols], lk[rows, hp, cols],
                                                       lq[rows, hp, cols], start=True, stop=True)
                    ins.then_inc(self.tensor_out.sem, 1)
                    self.tensor_out.count += 1

    def gla_states(self):
        nc, c = self.nc, self.c
        b = self.cut(self.G_B, 2, N)[:, :, 0:T]
        pt = self.cut(self.G_P, 4, T)
        vt = self.cut(self.G_V, NC, 4, P)
        qe = self.cut(self.G_Q, 2, T)
        ke = self.cut(self.G_K, 2, T)
        ex = self.cut(self.G_Q + 1024, 2, T)
        diff = self.cut(self.G_E, 2, T)
        kt = self.cut(self.G_KT, NC, 2 * P)
        st = self.cut(self.G_K + 1024, NC, 2 * P)
        dlast = self.cut(self.G_EX, 2, NC)
        fs = self.cut(self.G_DQ, 2, B)
        ss = self.h[:].rearrange("p a b -> p (a b)")[:, 0:2048].rearrange("p (b j e) -> p b j e", b=B, j=2)
        kv = self.h[:].rearrange("p a b -> p (a b)")[:, 2048:4096].rearrange("p (b j e) -> p b j e", b=B, j=2)
        vs = self.cut(self.G_EX + 8, 4, P)
        with self.stage() as block:
            @block.sync
            def _(sp):
                sp.dma_start(ss, self.d["state_gla"]).then_inc(self.inputs_loaded[0].sem, 16)
                self.inputs_loaded[0].count += 16
                sp.wait_ge(self.vector_out2.sem, self.vector_out2.at(1))
                self.store(sp, self.d["p_gla"], st[:, NC - 1])
                sp.wait_ge(self.pool_out.sem, self.pool_out.at(3))
                self.store(sp, self.d["s_gla"], ss)
                sp.wait_ge(self.stored.sem, self.stored.count)

            @block.scalar
            def _(act):
                self.act.tell(nc.scalar.activation(ex, b, ACT.Exp), self.scalar_out)
                act.wait_ge(self.vector_out.sem, self.vector_out.at(1))
                self.act.tell(nc.scalar.activation(diff, diff, ACT.Exp), self.scalar_out)
                last = b.rearrange("p j (c w) -> p j c w", c=NC)[:, :, :, P - 1]
                self.act.tell(nc.scalar.activation(dlast, last, ACT.Exp), self.scalar_out)
                act.wait_ge(self.tensor_out.sem, self.tensor_out.at(1))
                self.act.tell(nc.scalar.activation(vs[0:B].rearrange("p a b -> p (a b)"), self.ps[0:B, 4, :], ACT.Copy),
                              self.scalar_out)
                act.wait_ge(self.tensor_out.sem, self.tensor_out.at(2))
                self.act.tell(nc.scalar.activation(kt.rearrange("p a b -> p (a b)"), self.banks(2, 2), ACT.Copy),
                              self.scalar_out)
                act.wait_ge(self.tensor_out.sem, self.tensor_out.at(5))
                self.act.step(nc.scalar.activation(self.o[:, 0:4, 0:T], self.ps[:, 0:4, :], ACT.Copy))
                act.wait_ge(self.tensor_out.sem, self.tensor_out.at(6))
                for par in range(2):
                    self.act.step(nc.scalar.activation(self.o[:, par:4:2, T:N],
                                  self.ps[:, 4 + par, 0:2 * B].rearrange("p (j b) -> p j b", b=B), ACT.Copy))

            @block.vector
            def _(dve):
                for j in range(2):
                    bj = b[:, j].rearrange("p (c w) -> p c w", c=NC)
                    ref = bj[:, :, P - 1:P].to_broadcast([P, NC, P])
                    ins = nc.vector.tensor_tensor(diff[:, j].rearrange("p (c w) -> p c w", c=NC), ref, bj, ALU.subtract)
                    self.dve.step(ins) if j == 0 else self.dve.tell(ins, self.vector_out)
                dve.wait_ge(self.scalar_out.sem, self.scalar_out.at(2))
                self.dve.tell(nc.vector.tensor_tensor(ke, c[:, GK:GK + 2, 0:T], diff, ALU.mult), self.vector_out)
                self.dve.tell(nc.vector.tensor_tensor(qe, c[:, GQ:GQ + 2, 0:T], ex, ALU.mult), self.vector_out)
                dve.wait_ge(self.tensor_out.sem, self.tensor_out.at(3))
                for b0 in range(0, B, 2):
                    k2 = c[:, GK:GK + 2, T + b0:T + b0 + 2].rearrange("p j b -> p b j").unsqueeze(3)
                    self.dve.tell(nc.vector.tensor_tensor(
                        kv[:, b0:b0 + 2], self.ps[:, 4 + b0 // 2, :].rearrange("p (b j e) -> p b j e", b=2, j=2),
                        k2.to_broadcast([P, 2, 2, P]), ALU.mult), self.vector_out)
                dve.wait_ge(self.tensor_out.sem, self.tensor_out.at(4))
                for t in range(NC):
                    for j in range(2):
                        out, new = st[:, t, j * P:(j + 1) * P], self.ps[:, 2 + t // 2, (t % 2) * 256 + j * P:(t % 2) * 256 + (j + 1) * P]
                        if t == 0:
                            ins = nc.vector.tensor_copy(out, new)
                        else:
                            ins = nc.vector.scalar_tensor_tensor(out, st[:, t - 1, j * P:(j + 1) * P], dlast[:, j, t:t + 1],
                                                                 new, ALU.mult, ALU.add)
                        if t == NC - 1 and j == 1:
                            self.dve.tell(ins, self.vector_out2)
                        else:
                            self.dve.step(ins)

            @block.gpsimd
            def _(pool):
                pool.wait_ge(self.inputs_loaded[0].sem, self.inputs_loaded[0].at(16))
                for j in range(2):
                    f = fs[:, j].unsqueeze(2).to_broadcast([P, B, P])
                    self.pool.tell(nc.gpsimd.tensor_tensor(ss[:, :, j], ss[:, :, j], f, ALU.mult), self.pool_out)
                pool.wait_ge(self.vector_out.sem, self.vector_out.at(7))
                self.pool.tell(nc.gpsimd.tensor_tensor(ss, ss, kv, ALU.add), self.pool_out)

            @block.tensor
            def _(pe):
                for h in range(4):
                    ins = nc.tensor.transpose(self.ps[0:B, 4, h * P:(h + 1) * P], c[:, GV + h, T:N], self.const("ident"))
                ins.then_inc(self.tensor_out.sem, 1)
                pe.wait_ge(self.vector_out.sem, self.vector_out.at(2))
                for t in range(NC):
                    for j in range(2):
                        ins = nc.tensor.transpose(self.ps[:, 2 + t // 2, (t % 2) * 256 + j * P:(t % 2) * 256 + (j + 1) * P],
                                                  ke[:, j, t * P:(t + 1) * P], self.const("ident"))
                ins.then_inc(self.tensor_out.sem, 1)
                pe.wait_ge(self.scalar_out.sem, self.scalar_out.at(4))
                for b0 in range(B):
                    for par in range(2):
                        ins = nc.tensor.matmul(self.ps[64 * par:64 * par + 64, 4 + b0 // 2, (b0 % 2) * 256:(b0 % 2) * 256 + 256],
                                               self.cst[0:B, SEL_AT + b0 * P:SEL_AT + b0 * P + 64],
                                               vs[0:B, par:4:2, :], start=True, stop=True)
                ins.then_inc(self.tensor_out.sem, 1)
                pe.wait_ge(self.scalar_out.sem, self.scalar_out.at(5))
                for t in range(NC):
                    for h in range(4):
                        rows = slice(64 * (h % 2), 64 * (h % 2) + 64)
                        at = (t % 2) * 256 + (h // 2) * P
                        ins = nc.tensor.matmul(self.ps[rows, 2 + t // 2, at:at + P],
                                               kt[:, t, (h // 2) * P + rows.start:(h // 2) * P + rows.stop],
                                               vt[:, t, h], start=True, stop=True)
                ins.then_inc(self.tensor_out.sem, 1)
                pe.wait_ge(self.vector_out.sem, self.vector_out.at(3))
                pe.wait_ge(self.vector_out2.sem, self.vector_out2.at(1))
                for h in range(4):
                    rows = slice(64 * (h % 2), 64 * (h % 2) + 64)
                    for t in range(NC):
                        cols = slice(t * P, (t + 1) * P)
                        out = self.ps[:, h, cols]
                        if t:
                            nc.tensor.matmul(out, st[rows, t - 1, (h // 2) * P:(h // 2 + 1) * P], qe[rows, h // 2, cols],
                                             start=True, stop=False)
                        ins = nc.tensor.matmul(out, vt[:, t, h], pt[:, 2 * (h % 2) + h // 2, cols], start=t == 0, stop=True)
                ins.then_inc(self.tensor_out.sem, 1)
                pe.wait_ge(self.pool_out.sem, self.pool_out.at(3))
                for par in range(2):
                    rows = slice(64 * par, 64 * par + 64)
                    for j in range(2):
                        for b0 in range(B):
                            at = j * B + b0
                            ins = nc.tensor.matmul(self.ps[:, 4 + par, at:at + 1], ss[rows, b0, j],
                                                   c[rows, GQ + j, T + b0:T + b0 + 1], start=True, stop=True)
                ins.then_inc(self.tensor_out.sem, 1)
                self.tensor_out.count += 6

    def gated_norm(self, n, gate, gain):
        nc, c = self.nc, self.c
        o = self.o[:, n:n + 4, :]
        sq, sg = self.cut(0, 4, N), self.cut(4 * N, 4, N)
        r = self.cut(8 * N, 4, N)
        with self.stage() as block:
            @block.scalar
            def _(act):
                for h in range(4):
                    self.act.tell(nc.scalar.activation(sq[:, h], o[:, h], ACT.Square), self.squares_ready)
                self.act.tell(nc.scalar.activation(sg, c[:, gate:gate + 4, :], ACT.Sigmoid), self.scalar_out)
                act.wait_ge(self.tensor_out.sem, self.tensor_out.at(1))
                self.act.step(nc.scalar.activation(r.rearrange("p h (s n) -> p (h s) n", s=2), self.ps[:, 0:8, 0:HALF],
                                                   ACT.Ln, bias=self.eps, scale=1.0 / P))
                self.act.tell(nc.scalar.activation(r, r, ACT.Exp, scale=-0.5), self.scalar_out)

            @block.tensor
            def _(pe):
                for h in range(4):
                    pe.wait_ge(self.squares_ready.sem, self.squares_ready.at(h + 1))
                    for s, (lo, hi) in enumerate(self.SPANS):
                        ins = nc.tensor.matmul(self.ps[:, 2 * h + s, 0:HALF], self.const("ones"), sq[:, h, lo:hi],
                                               start=True, stop=True)
                ins.then_inc(self.tensor_out.sem, 1)
                self.tensor_out.count += 1

            @block.vector
            def _(dve):
                dve.wait_ge(self.scalar_out.sem, self.scalar_out.at(1))
                self.dve.step(nc.vector.tensor_tensor(sg, sg, c[:, gate:gate + 4, :], ALU.mult))
                self.dve.step(nc.vector.scalar_tensor_tensor(sg, sg, self.param(gain)[:, 0:1], o, ALU.mult, ALU.mult))
                dve.wait_ge(self.scalar_out.sem, self.scalar_out.at(2))
                self.dve.step(nc.vector.tensor_tensor(o, sg, r, ALU.mult))

    W_KK, W_A, W_B, W_C, W_BON, W_DL, W_DS, W_1KA, W_FREE = 0, 2080, 4160, 6240, 8320, 10400, 10432, 10464, 10468
    C_G, C_A, C_W = 0, 4, 8
    OUT = 4

    def token_shift(self):
        nc, c = self.nc, self.c
        d = self.cut(0, R_TILES, N)
        sh = self.cut(R_TILES * N, R_TILES, B)
        last = self.cut(R_TILES * (N + B), R_TILES, B + 1)
        r = c[:, R0:R0 + R_TILES, :]
        with self.stage() as block:
            @block.sync
            def _(sp):
                sp.dma_start(sh, self.d["state_shift"]).then_inc(self.inputs_loaded[0].sem, 16)
                self.inputs_loaded[0].count += 16
                sp.wait_ge(self.scalar_out.sem, self.scalar_out.at(1))
                self.store(sp, self.d["shift"], last)
                sp.wait_ge(self.stored.sem, self.stored.count)

            @block.scalar
            def _(act):
                self.act.tell(nc.scalar.activation(last, r[:, :, T - 1:N], ACT.Copy), self.scalar_out)

            @block.gpsimd
            def _(pool):
                self.pool.step(nc.gpsimd.tensor_tensor(d[:, 7:, 1:T], r[:, 7:, 0:T - 1], r[:, 7:, 1:T], ALU.subtract))
                self.pool.tell(nc.gpsimd.tensor_scalar(d[:, :, 0:1], r[:, :, 0:1], -1.0, None, ALU.mult), self.pool_out)

            @block.vector
            def _(dve):
                self.dve.step(nc.vector.tensor_tensor(d[:, 0:7, 1:T], r[:, 0:7, 0:T - 1], r[:, 0:7, 1:T], ALU.subtract))
                dve.wait_ge(self.inputs_loaded[0].sem, self.inputs_loaded[0].at(16))
                self.dve.step(nc.vector.tensor_tensor(d[:, :, T:N], sh, r[:, :, T:N], ALU.subtract))
                dve.wait_ge(self.scalar_out.sem, self.scalar_out.at(1))
                dve.wait_ge(self.pool_out.sem, self.pool_out.at(1))
                for j in range(R_TILES):
                    self.dve.step(nc.vector.scalar_tensor_tensor(r[:, j], d[:, j], self.param("mu")[:, j:j + 1], r[:, j],
                                                                 ALU.mult, ALU.add))

    def rwkv_low_rank(self):
        nc, c = self.nc, self.c
        wa2, g2 = self.param("wa2"), self.param("g2")
        with self.stage() as block:
            @block.scalar
            def _(act):
                self.act.step(nc.scalar.activation(c[0:64, RWA], c[0:64, RWA], ACT.Tanh))
                self.act.tell(nc.scalar.activation(c[:, RG], c[:, RG], ACT.Sigmoid), self.scalar_out)
                for n in range(8):
                    act.wait_ge(self.tensor_out.sem, self.tensor_out.at(n + 1))
                    at, bias = (self.C_W, "w0") if n < 4 else (self.C_A, "a0")
                    j = n % 4
                    nc.scalar.activation(self.tile_pair(c, at + j), self.pair(2 * (n % 4)), ACT.Sigmoid,
                                         bias=self.param(bias)[:, j:j + 1]).then_inc(self.scalar_out.sem, 1)
                self.scalar_out.count += 8

            @block.vector
            def _(dve):
                for j in range(4):
                    dve.wait_ge(self.scalar_out.sem, self.scalar_out.at(2 + j))
                    nc.vector.tensor_scalar(c[:, self.C_W + j], c[:, self.C_W + j], -float(np.exp(-0.5)), None, ALU.mult)
                for j in range(4):
                    dve.wait_ge(self.tensor_out.sem, self.tensor_out.at(9 + j))
                    self.dve.step(nc.vector.tensor_copy(self.tile_pair(c, self.C_G + j), self.pair(2 * j)))

            @block.tensor
            def _(pe):
                pe.wait_ge(self.scalar_out.sem, self.scalar_out.at(1))
                for n in range(12):
                    if n >= 4:
                        pe.wait_ge(self.scalar_out.sem, self.scalar_out.at(n - 2))
                    rows = (slice(0, 64), slice(64, P), slice(0, P))[n // 4]
                    w, src = (g2, RG) if n >= 8 else (wa2, RWA)
                    for s, (lo, hi) in enumerate(self.SPANS):
                        ins = nc.tensor.matmul(self.ps[:, 2 * (n % 4) + s, 0:HALF], w[rows, (n % 4) * P:(n % 4 + 1) * P],
                                               c[rows, src, lo:hi], start=True, stop=True)
                    ins.then_inc(self.tensor_out.sem, 1)
                self.tensor_out.count += 12

    def eight(self, t):
        return t.rearrange("p a (s n) -> p (a s) n", s=2)

    def head_sums(self, pe, src, ready, k):
        nc = self.nc
        pe.wait_ge(ready.sem, ready.at(k))
        for j in range(4):
            for s, (lo, hi) in enumerate(self.SPANS):
                ins = nc.tensor.matmul(self.ps[:, 2 * j + s, 0:HALF], self.const("head_ones"), src[:, j, lo:hi],
                                       start=True, stop=True)
        ins.then_inc(self.tensor_out.sem, 1)
        self.tensor_out.count += 1

    def rwkv_vectors(self):
        nc, c = self.nc, self.c
        kk, wa, wb, wc, bon = (self.cut(x, 4, N) for x in (self.W_KK, self.W_A, self.W_B, self.W_C, self.W_BON))
        one_ka = self.cut(self.W_1KA, 4)
        dl, ds = self.cut(self.W_DL, 4, 8), self.cut(self.W_DS, 4, B)
        r, k, v = c[:, RR:RR + 4], c[:, RK:RK + 4], c[:, RV:RV + 4]
        a, lw = c[:, self.C_A:self.C_A + 4], c[:, self.C_W:self.C_W + 4]
        banks = self.ps[:, :, 0:HALF]
        with self.stage() as block:
            @block.vector
            def _(dve):
                for j in range(4):
                    ins = nc.vector.tensor_scalar(kk[:, j], k[:, j], self.param("k_k")[:, j:j + 1], None, ALU.mult)
                    self.dve.step(ins) if j < 3 else self.dve.tell(ins, self.vector_out)
                self.dve.step(nc.vector.tensor_scalar(one_ka, self.param("k_a"), -1.0, 1.0, ALU.mult, ALU.add))
                for j in range(4):
                    self.dve.step(nc.vector.tensor_scalar(wb[:, j], a[:, j], self.param("k_a")[:, j:j + 1],
                                                          one_ka[:, j:j + 1], ALU.mult, ALU.add))
                self.dve.step(nc.vector.tensor_tensor(k, k, wb, ALU.mult))
                for j in range(4):
                    ins = nc.vector.scalar_tensor_tensor(wc[:, j], r[:, j], self.param("r_k")[:, j:j + 1], k[:, j],
                                                         ALU.mult, ALU.mult)
                    self.dve.step(ins) if j < 3 else self.dve.tell(ins, self.vector_out)
                dve.wait_ge(self.scalar_out.sem, self.scalar_out.at(2))
                self.dve.step(nc.vector.tensor_tensor(kk, kk, wa, ALU.mult))
                self.dve.step(nc.vector.tensor_tensor(a, a, kk, ALU.mult))
                cw = wa[:, :, 0:T]
                scan = self.cst[:, SCAN64_AT:SCAN64_AT + T]
                for j in range(4):
                    self.dve.step(nc.vector.tensor_tensor_scan(cw[:, j], scan, lw[:, j, 0:T], 0.0, ALU.mult, ALU.add))
                self.dve.tell(nc.vector.tensor_tensor(lw[:, :, 0:T], cw, lw[:, :, 0:T], ALU.subtract), self.vector_out)
                dve.wait_ge(self.tensor_out.sem, self.tensor_out.at(2))
                self.dve.step(nc.vector.tensor_tensor(self.eight(bon), banks, self.eight(v), ALU.mult))
                p = slice(0, T)
                dve.wait_ge(self.scalar_out.sem, self.scalar_out.at(3))
                self.dve.step(nc.vector.tensor_tensor(r[:, :, p], r[:, :, p], wb[:, :, p], ALU.mult))
                dve.wait_ge(self.scalar_out.sem, self.scalar_out.at(4))
                self.dve.step(nc.vector.tensor_tensor(a[:, :, p], a[:, :, p], wc[:, :, p], ALU.mult))
                self.dve.step(nc.vector.tensor_tensor(k[:, :, p], k[:, :, p], wc[:, :, p], ALU.mult))
                dve.wait_ge(self.scalar_out.sem, self.scalar_out.at(5))
                self.dve.step(nc.vector.scalar_tensor_tensor(kk[:, :, p], kk[:, :, p], -1.0, lw[:, :, p],
                                                             ALU.mult, ALU.mult))

            @block.scalar
            def _(act):
                act.wait_ge(self.vector_out.sem, self.vector_out.at(1))
                self.act.tell(nc.scalar.activation(wa, kk, ACT.Square), self.scalar_out)
                act.wait_ge(self.tensor_out.sem, self.tensor_out.at(1))
                self.act.step(nc.scalar.activation(self.eight(wa), banks, ACT.Ln, bias=self.eps))
                self.act.tell(nc.scalar.activation(wa, wa, ACT.Exp, scale=-0.5), self.scalar_out)
                act.wait_ge(self.vector_out.sem, self.vector_out.at(3))
                self.act.tell(nc.scalar.activation(wb[:, :, 0:T], wa[:, :, 0:T], ACT.Exp), self.scalar_out)
                act.wait_ge(self.tensor_out.sem, self.tensor_out.at(2))
                self.act.tell(nc.scalar.activation(wc[:, :, 0:T], wa[:, :, 0:T], ACT.Exp, scale=-1.0), self.scalar_out)
                self.act.tell(nc.scalar.activation(lw, lw, ACT.Exp), self.scalar_out)
                last = wa[:, :, 0:T].rearrange("p j (c w) -> p j c w", w=64)[:, :, :, 63]
                self.act.step(nc.scalar.activation(dl, last, ACT.Exp))

            @block.tensor
            def _(pe):
                self.head_sums(pe, wa, self.scalar_out, 1)
                pe.wait_ge(self.scalar_out.sem, self.scalar_out.at(2))
                self.head_sums(pe, wc, self.vector_out, 2)

    def rwkv_sample(self):
        nc, c = self.nc, self.c
        kk = self.cut(self.W_KK, 4, N)
        hf = self.h[:].rearrange("p a b -> p (a b)")
        ss, pr = (hf[:, x:x + 2048].rearrange("p (b j i) -> p b j i", b=B, j=4) for x in (0, 2048))
        t2 = self.cut(self.W_A, B, 4, 64)
        vs = self.cut(self.W_FREE, 4, P)

        def by_seq(t, lo=0):
            return t[:, :, T:N].rearrange("p j b -> p b j").unsqueeze(3).to_broadcast([P, B, 4, 64])

        with self.stage() as block:
            @block.sync
            def _(sp):
                sp.dma_start(ss, self.d["state_rwkv"]).then_inc(self.inputs_loaded[0].sem, 16)
                self.inputs_loaded[0].count += 16
                sp.wait_ge(self.pool_out.sem, self.pool_out.at(2))
                self.store(sp, self.d["s_rwkv"], ss)
                sp.wait_ge(self.stored.sem, self.stored.count)

            @block.tensor
            def _(pe):
                for j in range(4):
                    ins = nc.tensor.transpose(self.ps[0:B, 4, j * P:(j + 1) * P], c[:, RV + j, T:N], self.const("ident"))
                ins.then_inc(self.tensor_out.sem, 1)
                pe.wait_ge(self.vector_out.sem, self.vector_out.at(1))
                flat = pr.rearrange("p b j i -> p (b j i)")
                for n in range(4):
                    ins = nc.tensor.matmul(self.ps[:, n, :], self.const("head_ones"), flat[:, n * 512:(n + 1) * 512],
                                           start=True, stop=True)
                ins.then_inc(self.tensor_out.sem, 1)
                pe.wait_ge(self.scalar_out.sem, self.scalar_out.at(1))
                vh = vs[0:B].rearrange("p j (q i) -> p j q i", q=2)
                for b0 in range(B):
                    for par in range(2):
                        ins = nc.tensor.matmul(self.ps[64 * par:64 * par + 64, 4 + b0 // 2, (b0 % 2) * 256:(b0 % 2) * 256 + 256],
                                               self.cst[0:B, SEL_AT + b0 * P:SEL_AT + b0 * P + 64], vh[:, :, par, :],
                                               start=True, stop=True)
                ins.then_inc(self.tensor_out.sem, 1)
                pe.wait_ge(self.pool_out.sem, self.pool_out.at(2))
                for par in range(2):
                    rows = slice(64 * par, 64 * par + 64)
                    for j in range(4):
                        for b0 in range(B):
                            at = j * B + b0
                            ins = nc.tensor.matmul(self.ps[rows, par, at:at + 1], ss[rows, b0, j], c[rows, RR + j, T + b0:T + b0 + 1],
                                                   start=True, stop=True)
                ins.then_inc(self.tensor_out.sem, 1)
                self.tensor_out.count += 4

            @block.scalar
            def _(act):
                act.wait_ge(self.tensor_out.sem, self.tensor_out.at(1))
                self.act.tell(nc.scalar.activation(vs[0:B].rearrange("p a b -> p (a b)"), self.ps[0:B, 4, :], ACT.Copy),
                              self.scalar_out)
                act.wait_ge(self.tensor_out.sem, self.tensor_out.at(4))
                for par in range(2):
                    rows = slice(64 * par, 64 * par + 64)
                    self.act.step(nc.scalar.activation(self.o[rows, self.OUT:self.OUT + 4, T:N],
                                  self.ps[rows, par, 0:4 * B].rearrange("p (j b) -> p j b", b=B), ACT.Copy))

            @block.gpsimd
            def _(pool):
                pool.wait_ge(self.vector_out.sem, self.vector_out.at(1))
                self.pool.step(nc.gpsimd.tensor_tensor(ss, ss, by_seq(c[:, self.C_W:self.C_W + 4]), ALU.mult))
                pool.wait_ge(self.vector_out.sem, self.vector_out.at(2))
                self.pool.tell(nc.gpsimd.tensor_tensor(ss, ss, pr, ALU.subtract), self.pool_out)
                pool.wait_ge(self.vector_out.sem, self.vector_out.at(3))
                self.pool.tell(nc.gpsimd.tensor_tensor(ss, ss, t2, ALU.add), self.pool_out)

            @block.vector
            def _(dve):
                dve.wait_ge(self.inputs_loaded[0].sem, self.inputs_loaded[0].at(16))
                self.dve.tell(nc.vector.tensor_tensor(pr, ss, by_seq(kk), ALU.mult), self.vector_out)
                dve.wait_ge(self.tensor_out.sem, self.tensor_out.at(2))
                self.dve.tell(nc.vector.tensor_tensor(pr, self.banks(0, 4).rearrange("p (b j i) -> p b j i", b=B, j=4),
                                                      by_seq(c[:, self.C_A:self.C_A + 4]), ALU.mult), self.vector_out)
                dve.wait_ge(self.tensor_out.sem, self.tensor_out.at(3))
                self.dve.tell(nc.vector.tensor_tensor(t2, self.banks(4, 4).rearrange("p (b j i) -> p b j i", b=B, j=4),
                                                      by_seq(c[:, RK:RK + 4]), ALU.mult), self.vector_out)

    def unit_inverses(self, groups, streams, masks, lt_at, t_at, x_at, inv, fill):
        nc = self.nc
        lt, tt, xx = ([self.cut(at + 1024 * i, 8, P) for i in range(streams)] for at in (lt_at, t_at, x_at))
        factor, levels = masks
        ident = self.const("ident").unsqueeze(1)

        def bank(i):
            return self.ps[:, 4 * i:4 * i + 2, :], self.ps[:, 4 * i + 2:4 * i + 4, :]

        def eight(a):
            return a.rearrange("p a (b t) -> p (a b) t", t=P)

        n_level = len(levels)
        with self.stage() as block:
            @block.tensor
            def _(pe):
                made = copied = masked = 0
                for g0 in range(0, groups, streams):
                    for i in range(streams):
                        if g0:
                            pe.wait_ge(self.vector_out.sem, self.vector_out.at((g0 // streams) * streams * (n_level + 1) - streams + i + 1))
                        fill(pe, g0 + i, 4 * i + 2)
                        self.tensor_out.count += 1
                    for n in range(n_level):
                        base_v = (g0 // streams) * streams * (n_level + 1)
                        base_s = (g0 // streams) * streams * (2 * n_level - 2)
                        if n:
                            for i in range(streams):
                                pe.wait_ge(self.scalar_out.sem, self.scalar_out.at(base_s + (2 * n - 2) * streams + i + 1))
                                for h in range(8):
                                    ins = nc.tensor.matmul(self.ps[:, 4 * i + h // 4, (h % 4) * P:(h % 4 + 1) * P], lt[i][:, h],
                                                           tt[i][:, h], start=True, stop=True)
                                ins.then_inc(self.tensor_out.sem, 1)
                                self.tensor_out.count += 1
                            for i in range(streams):
                                pe.wait_ge(self.scalar_out.sem, self.scalar_out.at(base_s + (2 * n - 1) * streams + i + 1))
                                for h in range(8):
                                    ins = nc.tensor.matmul(self.ps[:, 4 * i + 2 + h // 4, (h % 4) * P:(h % 4 + 1) * P], xx[i][:, h],
                                                           inv[g0 + i][:, h], start=True, stop=True)
                                ins.then_inc(self.tensor_out.sem, 1)
                                self.tensor_out.count += 1
                        if n < n_level - 1:
                            for i in range(streams):
                                pe.wait_ge(self.vector_out.sem, self.vector_out.at(base_v + (n + 1) * streams + i + 1))
                                for h in range(8):
                                    ins = nc.tensor.transpose(self.ps[:, 4 * i + h // 4, (h % 4) * P:(h % 4 + 1) * P],
                                                              inv[g0 + i][:, h], self.const("ident"))
                                ins.then_inc(self.tensor_out.sem, 1)
                                self.tensor_out.count += 1

            per = 3 * n_level - 2

            def product_at(g0, k, i):
                return self.tensor_out.at((g0 // streams) * streams * per + k * streams + i + 1)

            @block.scalar
            def _(act):
                for g0 in range(0, groups, streams):
                    for n in range(n_level):
                        if n:
                            for i in range(streams):
                                act.wait_ge(self.tensor_out.sem, product_at(g0, 3 * n - 1, i))
                                self.act.tell(nc.scalar.activation(xx[i], eight(bank(i)[0]), ACT.Copy), self.scalar_out)
                        if n < n_level - 1:
                            for i in range(streams):
                                act.wait_ge(self.tensor_out.sem, product_at(g0, 3 * n + 1, i))
                                self.act.tell(nc.scalar.activation(tt[i], eight(bank(i)[0]), ACT.Copy), self.scalar_out)

            @block.vector
            def _(dve):
                for g0 in range(0, groups, streams):
                    for i in range(streams):
                        dve.wait_ge(self.tensor_out.sem, product_at(g0, 0, i))
                        self.dve.tell(nc.vector.tensor_tensor(lt[i], eight(bank(i)[1]), factor(g0 + i), ALU.mult),
                                      self.vector_out)
                    for n, level in enumerate(levels):
                        m = self.const(level).unsqueeze(1).to_broadcast([P, 8, P])
                        for i in range(streams):
                            if n == 0:
                                self.dve.step(nc.vector.tensor_tensor(inv[g0 + i], lt[i], m, ALU.mult))
                                self.dve.tell(nc.vector.tensor_tensor(inv[g0 + i], inv[g0 + i], ident.to_broadcast([P, 8, P]),
                                                                      ALU.add), self.vector_out)
                            else:
                                dve.wait_ge(self.tensor_out.sem, product_at(g0, 3 * n, i))
                                self.dve.tell(nc.vector.copy_predicated(
                                    inv[g0 + i], self.mask(level).unsqueeze(1).to_broadcast([P, 8, P]), eight(bank(i)[1])),
                                    self.vector_out)

    def head_slot(self, h):
        return slice(64 * (h // 4), 64 * (h // 4) + 64), h % 4

    def rwkv_inverses(self):
        nc, c = self.nc, self.c
        a, bb = self.cut(self.W_KK, 4, N), c[:, self.C_A:self.C_A + 4]

        def fill(pe, g, bank):
            cols = slice(g * P, (g + 1) * P)
            for h in range(8):
                rows, j = self.head_slot(h)
                ins = nc.tensor.matmul(self.ps[:, bank + h // 4, j * P:(j + 1) * P], bb[rows, j, cols], a[rows, j, cols],
                                       start=True, stop=True)
            ins.then_inc(self.tensor_out.sem, 1)

        hf = self.h[:].rearrange("p a b -> p (a b)")
        self.inv = [hf[:, g * 1024:(g + 1) * 1024].rearrange("p (h t) -> p h t", h=8) for g in range(NC)]
        before = self.const("before64").unsqueeze(1).to_broadcast([P, 8, P])
        self.unit_inverses(NC, 2, (lambda g: before, [f"level{m}" for m in LEVELS[:0:-1]]), self.W_A, self.W_A + 2048,
                           self.W_A + 4096, self.inv, fill)

    def rwkv_chain(self):
        nc, c = self.nc, self.c
        A = self.cut(self.W_KK, 4, N)
        Bv, K, R = c[:, self.C_A:self.C_A + 4], c[:, RK:RK + 4], c[:, RR:RR + 4]
        ak, rb, rk = (self.cut(self.W_A + 1024 * i, 8, P) for i in range(3))
        vt, bt, kt = (self.cut(self.W_A + 3072 + 512 * i, 4, 2, 64) for i in range(3))
        p1, sa = (self.cut(self.W_A + 4608 + 512 * i, 8, 64) for i in range(2))
        st = self.cut(self.W_FREE, 9, 4, 64)
        dl = self.cut(self.W_DL, 4, 8)
        with self.stage() as block:
            @block.sync
            def _(sp):
                sp.wait_ge(self.vector_out2.sem, self.vector_out2.at(8))
                self.store(sp, self.d["p_rwkv"], st[:, 8].rearrange("p a b -> p (a b)"))
                sp.wait_ge(self.stored.sem, self.stored.count)

            @block.tensor
            def _(pe):
                for t in range(NC):
                    cols = slice(t * P, (t + 1) * P)
                    if t:
                        pe.wait_ge(self.scalar_out.sem, self.scalar_out.at(6 * t))
                    for n, src in enumerate((c[:, RV:RV + 4], Bv, K)):
                        for j in range(4):
                            ins = nc.tensor.transpose(self.ps[:, n, j * P:(j + 1) * P], src[:, j, cols], self.const("ident"))
                    ins.then_inc(self.tensor_out.sem, 1)
                    pe.wait_ge(self.scalar_out.sem, self.scalar_out.at(6 * t + 1))
                    if t:
                        pe.wait_ge(self.vector_out2.sem, self.vector_out2.at(2 * t))
                    for n, (left, right) in enumerate(((K, A), (Bv, R), (K, R))):
                        for h in range(8):
                            rows, j = self.head_slot(h)
                            ins = nc.tensor.matmul(self.ps[:, 2 + 2 * n + h // 4, j * P:(j + 1) * P], left[rows, j, cols],
                                                   right[rows, j, cols], start=True, stop=True)
                        ins.then_inc(self.tensor_out.sem, 1)
                    pe.wait_ge(self.vector_out.sem, self.vector_out.at(3 * t + 3))
                    for sub in range(2):
                        n = 2 * t + sub
                        own = slice(64 * sub, 64 * sub + 64)
                        sc = slice(t * P + 64 * sub, t * P + 64 * sub + 64)
                        if n:
                            pe.wait_ge(self.vector_out2.sem, self.vector_out2.at(n))
                        for h in range(8):
                            rows, j = self.head_slot(h)
                            out = self.ps[own, h // 4, j * 64:(j + 1) * 64]
                            nc.tensor.matmul(out, A[rows, j, sc], st[rows, n, j], start=True, stop=False)
                            ins = nc.tensor.matmul(out, ak[:, h, own], vt[:, j, h // 4], start=False, stop=True)
                        ins.then_inc(self.tensor_out.sem, 1)
                        pe.wait_ge(self.scalar_out.sem, self.scalar_out.at(6 * t + 2 + 2 * sub))
                        for h in range(8):
                            ins = nc.tensor.matmul(self.ps[own, 2, h * 64:(h + 1) * 64], self.inv[t][own, h, own], p1[own, h],
                                                   start=True, stop=True)
                        ins.then_inc(self.tensor_out.sem, 1)
                        pe.wait_ge(self.scalar_out.sem, self.scalar_out.at(6 * t + 3 + 2 * sub))
                        for h in range(8):
                            rows, j = self.head_slot(h)
                            out = self.ps[rows, 3, j * 64:(j + 1) * 64]
                            nc.tensor.matmul(out, bt[own, j, h // 4], sa[own, h], start=True, stop=False)
                            ins = nc.tensor.matmul(out, kt[own, j, h // 4], vt[own, j, h // 4], start=False, stop=True)
                        ins.then_inc(self.tensor_out.sem, 1)
                    for h in range(8):
                        rows, j = self.head_slot(h)
                        out = self.ps[rows, 4 + h // 4, j * P:(j + 1) * P]
                        nc.tensor.matmul(out, vt[:, j, h // 4], rk[:, h], start=True, stop=False)
                        nc.tensor.matmul(out, sa[:, h], rb[:, h], start=False, stop=False)
                        for sub in range(2):
                            half = slice(64 * sub, 64 * sub + 64)
                            sc = slice(t * P + 64 * sub, t * P + 64 * sub + 64)
                            ins = nc.tensor.matmul(out[:, half], st[rows, 2 * t + sub, j], R[rows, j, sc],
                                                   start=False, stop=sub == 1)
                    ins.then_inc(self.tensor_out.sem, 1)
                self.tensor_out.count += NC * 11

            @block.scalar
            def _(act):
                for t in range(NC):
                    cols = slice(t * P, (t + 1) * P)
                    act.wait_ge(self.tensor_out.sem, self.tensor_out.at(11 * t + 1))
                    tok = self.cut(self.W_A + 3072, 1536)
                    self.act.tell(nc.scalar.activation(tok, self.banks(0, 3), ACT.Copy), self.scalar_out)
                    for sub in range(2):
                        own = slice(64 * sub, 64 * sub + 64)
                        act.wait_ge(self.tensor_out.sem, self.tensor_out.at(11 * t + 5 + 3 * sub))
                        self.act.tell(nc.scalar.activation(
                            p1[own].rearrange("p (q j) i -> p q (j i)", q=2), self.ps[own, 0:2, 0:256], ACT.Copy),
                            self.scalar_out)
                        act.wait_ge(self.tensor_out.sem, self.tensor_out.at(11 * t + 6 + 3 * sub))
                        self.act.tell(nc.scalar.activation(sa[own].rearrange("p h i -> p (h i)"), self.ps[own, 2, :], ACT.Copy),
                                      self.scalar_out)
                    act.wait_ge(self.tensor_out.sem, self.tensor_out.at(11 * t + 11))
                    for q in range(2):
                        rows = slice(64 * q, 64 * q + 64)
                        ins = nc.scalar.activation(self.o[rows, self.OUT:self.OUT + 4, cols],
                                                   self.ps[rows, 4 + q, :].rearrange("p (j t) -> p j t", j=4), ACT.Copy)
                        self.act.step(ins) if q == 0 else self.act.tell(ins, self.scalar_out)

            @block.vector
            def _(dve):
                self.dve.step(nc.vector.memset(sa, 0.0))
                self.dve.step(nc.vector.memset(st[:, 0], 0.0))
                for t in range(NC):
                    for n, (out, m) in enumerate(((ak, "before64"), (rb, "causal64"), (rk, "causal64"))):
                        dve.wait_ge(self.tensor_out.sem, self.tensor_out.at(11 * t + 2 + n))
                        self.dve.tell(nc.vector.tensor_tensor(
                            out, self.ps[:, 2 + 2 * n:4 + 2 * n, :].rearrange("p a (b t) -> p (a b) t", t=P),
                            self.const(m).unsqueeze(1).to_broadcast([P, 8, P]), ALU.mult), self.vector_out)
                    for sub in range(2):
                        n = 2 * t + sub
                        dve.wait_ge(self.tensor_out.sem, self.tensor_out.at(11 * t + 7 + 3 * sub))
                        new = st[:, n + 1]
                        self.dve.step(nc.vector.tensor_tensor(new, self.ps[:, 3, 0:256].rearrange("p (j i) -> p j i", j=4),
                                                              st[:, n], ALU.add))
                        self.dve.tell(nc.vector.tensor_tensor(new, new, dl[:, :, n:n + 1].to_broadcast([P, 4, 64]), ALU.mult),
                                      self.vector_out2)

    def rwkv_output(self):
        nc, c = self.nc, self.c
        y = self.o[:, self.OUT:self.OUT + 4, :]
        sq, r, bon = self.cut(self.W_A, 4, N), self.cut(self.W_B, 4, N), self.cut(self.W_BON, 4, N)
        banks = self.ps[:, :, 0:HALF]
        with self.stage() as block:
            @block.tensor
            def _(pe):
                self.head_sums(pe, y, self.tensor_out, 0)
                pe.wait_ge(self.vector_out.sem, self.vector_out.at(1))
                self.head_sums(pe, sq, self.scalar_out, 1)

            @block.scalar
            def _(act):
                act.wait_ge(self.vector_out.sem, self.vector_out.at(1))
                self.act.tell(nc.scalar.activation(sq, y, ACT.Square), self.scalar_out)
                act.wait_ge(self.tensor_out.sem, self.tensor_out.at(2))
                self.act.step(nc.scalar.activation(self.eight(r), banks, ACT.Ln, bias=self.ln_eps, scale=1.0 / 64))
                self.act.tell(nc.scalar.activation(r, r, ACT.Exp, scale=-0.5), self.scalar_out)

            @block.vector
            def _(dve):
                dve.wait_ge(self.tensor_out.sem, self.tensor_out.at(1))
                self.dve.tell(nc.vector.scalar_tensor_tensor(self.eight(y), banks, -1.0 / 64, self.eight(y), ALU.mult, ALU.add),
                              self.vector_out)
                dve.wait_ge(self.scalar_out.sem, self.scalar_out.at(2))
                for j in range(4):
                    self.dve.step(nc.vector.scalar_tensor_tensor(y[:, j], y[:, j], self.param("ln_w")[:, j:j + 1], r[:, j],
                                                                 ALU.mult, ALU.mult))
                    self.dve.step(nc.vector.scalar_tensor_tensor(y[:, j], y[:, j], self.param("ln_b")[:, j:j + 1], bon[:, j],
                                                                 ALU.add, ALU.add))
                    self.dve.step(nc.vector.tensor_tensor(y[:, j], y[:, j], c[:, self.C_G + j], ALU.mult))

    X_KV, X_VM, X_Q, X_A = 0, 8, 12, 20

    def flat(self, tile):
        return self.c[:].rearrange("p a b -> p (a b)")[:, tile * N:]

    def memory(self, i, following):
        nc = self.nc
        lin = self.lin[f"xkv{i}"]
        mem = self.o[:].rearrange("p a b -> p (a b)")[:, 0:KT * MEM].rearrange("p (k m) -> p k m", k=KT)
        kv = self.flat(self.X_KV)[:, 0:16 * MEM].rearrange("p (a m) -> p a m", a=16)

        def read(o, bank):
            out = kv[:, o] if isinstance(o, int) else kv[:, bass.ds(o, 1), :].rearrange("p o n -> p (o n)")
            return nc.scalar.activation(out, self.ps[:, bank, 0:MEM], ACT.Copy)
        self.normed_product(lin, mem, self.param("g_mem"), MEM, [(0, MEM)], following, read, self.d["mem"])

        sq, r = self.cut(0, KT, MEM), self.cut(2048, 4, MEM)
        vm = self.flat(self.X_VM)[:, 0:2 * D].rearrange("p (a b) -> p a b", a=2)
        with self.stage() as block:
            @block.scalar
            def _(act):
                self.act.tell(nc.scalar.activation(sq, kv[:, 0:KT], ACT.Square), self.scalar_out)
                act.wait_ge(self.tensor_out.sem, self.tensor_out.at(2))
                self.act.step(nc.scalar.activation(r.rearrange("p a b -> p (a b)"), self.banks(4, 2), ACT.Ln, bias=self.eps,
                                                   scale=1.0 / 256))
                self.act.tell(nc.scalar.activation(r, r, ACT.Exp, scale=-0.5), self.scalar_out)

            @block.tensor
            def _(pe):
                for m in range(2):
                    for j in range(KT):
                        ins = nc.tensor.transpose(self.ps[:, 2 * m + j // 4, (j % 4) * P:(j % 4 + 1) * P],
                                                  kv[:, KT + j, m * P:(m + 1) * P], self.const("ident"))
                ins.then_inc(self.tensor_out.sem, 1)
                pe.wait_ge(self.scalar_out.sem, self.scalar_out.at(1))
                for h in range(4):
                    for j in range(2):
                        ins = nc.tensor.matmul(self.ps[:, 4 + h // 2, (h % 2) * MEM:(h % 2 + 1) * MEM], self.const("ones"),
                                               sq[:, 2 * h + j], start=j == 0, stop=j == 1)
                ins.then_inc(self.tensor_out.sem, 1)
                self.tensor_out.count += 2

            @block.vector
            def _(dve):
                dve.wait_ge(self.tensor_out.sem, self.tensor_out.at(1))
                self.dve.step(nc.vector.tensor_copy(vm.rearrange("p a b -> p (a b)"), self.banks(0, 4)))
                dve.wait_ge(self.scalar_out.sem, self.scalar_out.at(2))
                k4 = kv[:, 0:KT].rearrange("p (h j) m -> p h j m", j=2)
                for j in range(2):
                    self.dve.tell(nc.vector.scalar_tensor_tensor(k4[:, :, j], k4[:, :, j], self.param("xk")[:, j:j + 1], r,
                                                                 ALU.mult, ALU.mult), self.vector_out)

            @block.sync
            def _(sp):
                self.store(sp, self.d[f"p_mv{i}"], kv[:, KT:])
                sp.wait_ge(self.vector_out.sem, self.vector_out.at(2))
                self.store(sp, self.d[f"p_mk{i}"], kv[:, 0:KT])
                sp.wait_ge(self.stored.sem, self.stored.count)

    def query(self, i, following):
        nc = self.nc
        lin = self.lin[f"xq{i}"]
        q = self.c[:, self.X_Q:self.X_Q + KT]
        self.normed_product(lin, self.x, self.param("g_cross"), N, self.SPANS, following, lambda o, bank: (
            nc.scalar.activation(self.tile_pair(q, o), self.pair(bank), ACT.Copy)))

        r = self.cut(0, 4, N)
        with self.stage() as block:
            @block.scalar
            def _(act):
                self.act.tell(nc.scalar.activation(self.sq[:], q, ACT.Square), self.scalar_out)
                act.wait_ge(self.tensor_out.sem, self.tensor_out.at(1))
                self.act.step(nc.scalar.activation(self.eight(r), self.ps[:, :, 0:HALF], ACT.Ln, bias=self.eps,
                                                   scale=1.0 / 256))
                self.act.tell(nc.scalar.activation(r, r, ACT.Exp, scale=-0.5), self.scalar_out)

            @block.tensor
            def _(pe):
                pe.wait_ge(self.scalar_out.sem, self.scalar_out.at(1))
                for h in range(4):
                    for s, (lo, hi) in enumerate(self.SPANS):
                        for j in range(2):
                            ins = nc.tensor.matmul(self.ps[:, 2 * h + s, 0:HALF], self.const("ones"),
                                                   self.sq[:, 2 * h + j, lo:hi], start=j == 0, stop=j == 1)
                ins.then_inc(self.tensor_out.sem, 1)
                self.tensor_out.count += 1

            @block.vector
            def _(dve):
                dve.wait_ge(self.scalar_out.sem, self.scalar_out.at(2))
                q4 = q.rearrange("p (h j) m -> p h j m", j=2)
                for j in range(2):
                    self.dve.step(nc.vector.scalar_tensor_tensor(q4[:, :, j], q4[:, :, j], self.param("xq")[:, j:j + 1], r,
                                                                 ALU.mult, ALU.mult))

    def attention(self, i):
        nc = self.nc
        q = self.c[:, self.X_Q:self.X_Q + KT]
        kv = self.flat(self.X_KV)[:, 0:16 * MEM].rearrange("p (a m) -> p a m", a=16)
        vm = self.flat(self.X_VM)[:, 0:2 * D].rearrange("p (a b) -> p a b", a=2)
        buf = self.flat(self.X_A)
        pr = [buf[:, x * 1024:(x + 1) * 1024].rearrange("p (t m) -> p t m", t=NC) for x in range(2)]
        pt = [buf[:, (x + 2) * 1024:(x + 3) * 1024].rearrange("p (a t) -> p a t", a=2) for x in range(2)]
        small = self.flat(28)
        top, total = [small[:, 8 * x:8 * x + 4] for x in range(2)], [small[:, 8 * x + 4:8 * x + 8] for x in range(2)]
        logit, weight, row = small[:, 16:80], small[:, 80:144], small[:, 144:400]
        stop, stotal = small[:, 400:401], small[:, 401:402]
        RING = 3
        kc = [self.cut(2048 * x, 8, MEM) for x in range(RING)]
        vc = [self.cut(2048 * (RING + x), 2, D) for x in range(RING)]
        scale = 1.0 / 16
        HP = 4

        with self.stage() as block:
            @block.sync
            def _(sp):
                for b0 in range(B):
                    if b0 >= RING:
                        sp.wait_ge(self.keys_used.sem, self.keys_used.at(b0 - RING + 1))
                    sp.dma_start(kc[b0 % RING], self.d[f"mem_k{i}"][b0]).then_inc(self.inputs_loaded[b0 % RING].sem, 16)
                    if b0 < RING:
                        sp.dma_start(vc[b0], self.d[f"mem_v{i}"][b0]).then_inc(self.values_loaded[b0].sem, 16)
                for b0 in range(RING, B):
                    sp.wait_ge(self.values_used.sem, self.values_used.at(b0 - RING + 1))
                    sp.dma_start(vc[b0 % RING], self.d[f"mem_v{i}"][b0]).then_inc(self.values_loaded[b0 % RING].sem, 16)
                for b0 in range(B):
                    self.inputs_loaded[b0 % RING].count += 16
                    self.values_loaded[b0 % RING].count += 16

            @block.tensor
            def _(pe):
                def scores(h):
                    for t in range(NC):
                        for j in range(2):
                            ins = nc.tensor.matmul(self.ps[:, t // 2, (t % 2) * MEM:(t % 2 + 1) * MEM],
                                                   q[:, 2 * h + j, t * P:(t + 1) * P], kv[:, 2 * h + j],
                                                   start=j == 0, stop=j == 1)
                    ins.then_inc(self.scores_ready.sem, 1)

                def sample_scores(b0):
                    own = self.inputs_loaded[b0 % RING]
                    pe.wait_ge(own.sem, own.at(16 * (b0 // RING + 1)))
                    for h in range(HP):
                        for m in range(2):
                            at = m * 32 + b0 * HP + h
                            for j in range(2):
                                ins = nc.tensor.matmul(self.ps[:, 6, at:at + 1], kc[b0 % RING][:, 2 * h + j, m * P:(m + 1) * P],
                                                       q[:, 2 * h + j, T + b0:T + b0 + 1], start=j == 0, stop=j == 1)
                    ins.then_inc(self.keys_used.sem, 1)

                scores(0)
                for h in range(HP):
                    sample_scores(2 * h)
                    sample_scores(2 * h + 1)
                    pe.wait_ge(self.vector_out.sem, self.vector_out.at(h + 1))
                    for m in range(2):
                        for t in range(NC):
                            ins = nc.tensor.transpose(self.ps[:, 2 + m, t * P:(t + 1) * P], pr[h % 2][:, t, m * P:(m + 1) * P],
                                                      self.const("ident"))
                    ins.then_inc(self.tensor_out.sem, 1)
                    if h + 1 < HP:
                        scores(h + 1)
                    pe.wait_ge(self.scalar_out.sem, self.scalar_out.at(h + 1))
                    if h:
                        pe.wait_ge(self.vector_out2.sem, self.vector_out2.at(h))
                    for e in range(2):
                        for m in range(2):
                            ins = nc.tensor.matmul(self.ps[:, 4 + e, :], vm[:, m, (2 * h + e) * P:(2 * h + e + 1) * P],
                                                   pt[h % 2][:, m], start=m == 0, stop=m == 1)
                    ins.then_inc(self.tensor_out2.sem, 1)
                pe.wait_ge(self.scalar_out.sem, self.scalar_out.at(HP + 1))
                for m in range(2):
                    ins = nc.tensor.transpose(self.ps[0:32, 7, m * P:(m + 1) * P], logit[:, m * 32:(m + 1) * 32],
                                              self.const("ident"))
                ins.then_inc(self.tensor_out.sem, 1)
                pe.wait_ge(self.vector_out.sem, self.vector_out.at(HP + 2))
                for m in range(2):
                    ins = nc.tensor.transpose(self.ps[:, 6, m * 32:(m + 1) * 32], row[0:32, m * P:(m + 1) * P],
                                              self.cst[0:32, CONST_AT["ident"]:CONST_AT["ident"] + 32])
                ins.then_inc(self.tensor_out.sem, 1)
                pe.wait_ge(self.scalar_out.sem, self.scalar_out.at(HP + 3))
                for b0 in range(B):
                    own = self.values_loaded[b0 % RING]
                    pe.wait_ge(own.sem, own.at(16 * (b0 // RING + 1)))
                    for e in range(8):
                        for m in range(2):
                            at = m * 32 + b0 * HP + e // 2
                            ins = nc.tensor.matmul(self.ps[:, 7, e * B + b0:e * B + b0 + 1], vc[b0 % RING][:, m, e * P:(e + 1) * P],
                                                   weight[:, at:at + 1], start=m == 0, stop=m == 1)
                    ins.then_inc(self.values_used.sem, 1)
                self.scores_ready.count += HP
                self.keys_used.count += B
                self.values_used.count += B
                self.tensor_out.count += HP + 2
                self.tensor_out2.count += HP

            @block.scalar
            def _(act):
                for h in range(HP):
                    p = h % 2
                    act.wait_ge(self.maxima_ready.sem, self.maxima_ready.at(h + 1))
                    for t in range(NC):
                        ins = nc.scalar.activation(pr[p][:, t], self.ps[:, t // 2, (t % 2) * MEM:(t % 2 + 1) * MEM], ACT.Exp,
                                                   bias=top[p][:, t:t + 1], scale=scale, accum_out=total[p][:, t:t + 1])
                        self.act.step(ins) if t < NC - 1 else self.act.tell(ins, self.exp_ready)
                    act.wait_ge(self.tensor_out.sem, self.tensor_out.at(h + 1))
                    self.act.tell(nc.scalar.activation(pt[p].rearrange("p a b -> p (a b)"), self.banks(2, 2), ACT.Copy),
                                  self.scalar_out)
                act.wait_ge(self.keys_used.sem, self.keys_used.at(B))
                self.act.tell(nc.scalar.activation(logit, self.ps[:, 6, 0:64], ACT.Copy), self.scalar_out)
                act.wait_ge(self.vector_out.sem, self.vector_out.at(HP + 1))
                self.act.tell(nc.scalar.activation(row[0:32], self.ps[0:32, 7, 0:256], ACT.Exp, bias=stop[0:32], scale=scale,
                                                   accum_out=stotal[0:32]), self.scalar_out)
                act.wait_ge(self.tensor_out.sem, self.tensor_out.at(HP + 2))
                self.act.tell(nc.scalar.activation(weight, self.ps[:, 6, 0:64], ACT.Copy), self.scalar_out)
                act.wait_ge(self.values_used.sem, self.values_used.at(B))
                self.act.step(nc.scalar.activation(self.o[:, :, T:N], self.ps[:, 7, 0:64].rearrange("p (e b) -> p e b", b=B),
                                                   ACT.Copy))

            @block.vector
            def _(dve):
                for h in range(HP):
                    p = h % 2
                    dve.wait_ge(self.scores_ready.sem, self.scores_ready.at(h + 1))
                    self.dve.step(nc.vector.tensor_reduce(top[p], self.banks(0, 2).rearrange("p (t m) -> p t m", t=NC), AX.X,
                                                          ALU.max))
                    self.dve.tell(nc.vector.tensor_scalar(top[p], top[p], -scale, None, ALU.mult), self.maxima_ready)
                    dve.wait_ge(self.exp_ready.sem, self.exp_ready.at(h + 1))
                    self.dve.step(nc.vector.reciprocal(total[p], total[p]))
                    self.dve.tell(nc.vector.tensor_tensor(pr[p], pr[p], total[p].unsqueeze(2).to_broadcast([P, NC, MEM]),
                                                          ALU.mult), self.vector_out)
                    dve.wait_ge(self.tensor_out2.sem, self.tensor_out2.at(h + 1))
                    self.dve.tell(nc.vector.tensor_copy(self.o[:, 2 * h:2 * h + 2, 0:T], self.ps[:, 4:6, :]), self.vector_out2)
                dve.wait_ge(self.tensor_out.sem, self.tensor_out.at(HP + 1))
                self.dve.step(nc.vector.tensor_reduce(stop[0:32], self.ps[0:32, 7, 0:256], AX.X, ALU.max))
                self.dve.tell(nc.vector.tensor_scalar(stop[0:32], stop[0:32], -scale, None, ALU.mult), self.vector_out)
                dve.wait_ge(self.scalar_out.sem, self.scalar_out.at(HP + 2))
                self.dve.step(nc.vector.reciprocal(stotal[0:32], stotal[0:32]))
                self.dve.tell(nc.vector.tensor_scalar(row[0:32], row[0:32], stotal[0:32], None, ALU.mult), self.vector_out)

    def gate_up(self, i, following):
        nc = self.nc
        lin, site = self.lin[f"gu{i}"], self.mlp
        silu, prod = self.mlp_tmp[0:2], self.mlp_tmp[2]
        with self.stage() as block:
            @block.sync
            def _(sp):
                self.stream(sp, lin)
                self.prefetch(sp, following)

            @block.tensor
            def _(pe):
                self.norm_pe(pe, self.mlp_sq, self.SPANS)
                self.product(pe, lin, site, self.SPANS)

            @block.scalar
            def _(act):
                self.norm_act(act, self.x, site, self.mlp_sq, self.mlp_norm, N, self.SPANS)
                with act.Fori(0, FT // 2) as it:
                    for u in range(2):
                        act.wait_ge(self.unit_done.sem, it * 4 + (lin.at + 2 * u + 1))
                        act.wait_ge(self.product_read[1].sem, self.product_read[1].base + it * 2 + u - 1)
                        nc.scalar.activation(silu[u][:].rearrange("p (s n) -> p s n", s=2), self.pair(0),
                                             ACT.Silu).then_inc(self.product_read[0].sem, 1)

            @block.vector
            def _(dve):
                for u in range(2):
                    self.split_unit(dve, lin, site, u)
                self.norm_dve(dve, self.x, site, self.mlp_norm, self.param("g_ffn"), N)

                def read(u, i):
                    if u % 2 == 0:
                        return
                    tile, pairs = i * 2 + u // 2, self.product_read[1].base
                    part = [t[:, bass.ds(tile, 1), :].rearrange("p o n -> p (o n)") if not isinstance(tile, int)
                            else t[:, tile] for t in self.hid.x]
                    dve.wait_ge(self.unit_done.sem, i * SLOTS + (lin.at + u + 1))
                    dve.wait_ge(self.product_read[0].sem, self.product_read[0].base + i * 2 + (u // 2 + 1))
                    nc.vector.tensor_tensor(prod[:].rearrange("p (s n) -> p s n", s=2),
                                            silu[u // 2 % 2][:].rearrange("p (s n) -> p s n", s=2), self.pair(2),
                                            ALU.mult).then_inc(self.product_read[1].sem, 1)
                    dve.wait_ge(self.product_read[1].sem, pairs + i * 2 + (u // 2 + 1))
                    nc.vector.tensor_copy(part[0], prod[:]).then_inc(self.hidden_hi.sem, 1)
                    dve.wait_ge(self.hidden_hi.sem, self.hidden_hi.base + i * 2 + (u // 2 + 1))
                    nc.vector.tensor_tensor(part[1], prod[:], part[0].bitcast(F32), ALU.subtract).then_inc(
                        self.hidden_lo.sem, 1)

                self.each_unit(dve, lin, site, read)
                self.tiles_read(lin)
                self.hidden_hi.count += FT
                self.hidden_lo.count += FT

    S_V, S_NZ, S_L = 0, 2048, 4608
    WIDTH = [T - s * P for s in range(NC)]
    START = [sum([T - s * P for s in range(n)]) for n in range(NC)]
    TRI = sum([T - s * P for s in range(NC)])

    def stick_norms(self):
        nc, c = self.nc, self.c
        q, k, v = c[:, SQ:SQ + 4], c[:, SK:SK + 4], c[:, SV:SV + 4]
        sq, r = ([self.cut(2080 * (1 + x + y), 4, N) for x in range(2)] for y in (0, 2))
        vt = self.cut(self.S_V, NC, T)
        with self.stage() as block:
            @block.scalar
            def _(act):
                self.act.tell(nc.scalar.activation(sq[0], q, ACT.Square), self.scalar_out)
                self.act.tell(nc.scalar.activation(sq[1], k, ACT.Square), self.scalar_out)
                for x in range(2):
                    act.wait_ge(self.tensor_out.sem, self.tensor_out.at(x + 1))
                    self.act.tell(nc.scalar.activation(self.eight(r[x]), self.ps[:, :, 0:HALF], ACT.Ln, bias=self.eps,
                                                       scale=1.0 / 64), self.scalar_out)
                    self.act.tell(nc.scalar.activation(r[x], r[x], ACT.Exp, scale=-0.5), self.scalar_out)
                act.wait_ge(self.tensor_out.sem, self.tensor_out.at(3))
                self.act.step(nc.scalar.activation(vt.rearrange("p a b -> p (a b)"), self.banks(0, 4), ACT.Copy))

            @block.tensor
            def _(pe):
                self.head_sums(pe, sq[0], self.scalar_out, 1)
                pe.wait_ge(self.scalar_out.sem, self.scalar_out.at(3))
                self.head_sums(pe, sq[1], self.scalar_out, 2)
                pe.wait_ge(self.scalar_out.sem, self.scalar_out.at(5))
                for t in range(NC):
                    for j in range(4):
                        ins = nc.tensor.transpose(self.ps[:, t, j * P:(j + 1) * P], v[:, j, t * P:(t + 1) * P],
                                                  self.const("ident"))
                ins.then_inc(self.tensor_out.sem, 1)
                self.tensor_out.count += 1

            @block.vector
            def _(dve):
                for x, (t, gain) in enumerate(((q, "sbq"), (k, "sbk"))):
                    dve.wait_ge(self.scalar_out.sem, self.scalar_out.at(4 + 2 * x))
                    self.dve.tell(nc.vector.scalar_tensor_tensor(t, t, self.param(gain)[:, 0:1], r[x], ALU.mult, ALU.mult),
                                  self.vector_out)
                self.dve.step(nc.vector.tensor_scalar(q, q, 0.125, None, ALU.mult))

            @block.sync
            def _(sp):
                self.store(sp, self.d["p_sbv"], v)
                sp.wait_ge(self.vector_out.sem, self.vector_out.at(2))
                self.store(sp, self.d["p_sbk"], k)
                sp.wait_ge(self.stored.sem, self.stored.count)

    def log_stay(self, nz, out):
        nc = self.nc

        def first():
            return nc.vector.scalar_tensor_tensor(out, nz, -1.0, nz, ALU.mult, ALU.min)

        def middle():
            self.act.step(nc.scalar.activation(out, out, ACT.Exp))
            self.act.tell(nc.scalar.activation(out, out, ACT.Ln, bias=1.0), self.scalar_out)

        def last():
            return nc.vector.scalar_tensor_tensor(out, nz, 0.0, out, ALU.min, ALU.subtract)
        return first, middle, last

    def stick_prompt(self):
        nc, c = self.nc, self.c
        q, k = c[:, SQ:SQ + 4], c[:, SK:SK + 4]
        vt = self.cut(self.S_V, NC, 8, 64)
        nz = [self.cut(self.S_NZ + self.TRI * x, self.TRI) for x in range(2)]
        ls = [self.cut(self.S_L + self.TRI * x, self.TRI) for x in range(2)]
        heads = 8
        blk = [slice(self.START[s], self.START[s] + self.WIDTH[s]) for s in range(NC)]

        def z(h, s, lo=None):
            return self.ps[:, 4 * (h % 2) + s, (s if lo is None else lo) * P:T]

        with self.stage() as block:
            @block.tensor
            def _(pe):
                def logits(h):
                    rows, j = slice(64 * (h % 2), 64 * (h % 2) + 64), h // 2
                    for s in range(NC):
                        ins = nc.tensor.matmul(z(h, s), k[rows, j, s * P:(s + 1) * P], q[rows, j, s * P:T],
                                               start=True, stop=True)
                    ins.then_inc(self.scores_ready.sem, 1)

                logits(0)
                for h in range(heads):
                    rows = slice(64 * (h % 2), 64 * (h % 2) + 64)
                    if h + 1 < heads:
                        if h:
                            pe.wait_ge(self.vector_out2.sem, self.vector_out2.at(h))
                        logits(h + 1)
                    pe.wait_ge(self.vector_out.sem, self.vector_out.at(2 * h + 2))
                    for s in range(NC):
                        diagonal = self.ps[:, 4 * (h % 2) + s, s * P:(s + 1) * P]
                        nc.tensor.matmul(diagonal, self.const("ident"), self.const("forbid"), start=False, stop=False,
                                         skip_group_check=True)
                        for n in range(s, NC):
                            ins = nc.tensor.matmul(z(h, s, n), self.const("key_after" if n == s else "ones"), ls[h % 2][:, blk[n]],
                                                   start=False, stop=n == NC - 1, skip_group_check=True)
                    ins.then_inc(self.tensor_out.sem, 1)
                    pe.wait_ge(self.scalar_out.sem, self.scalar_out.at(2 * h + 2))
                    for s in range(NC):
                        ins = nc.tensor.matmul(self.ps[rows, 4 * (h % 2), s * P:T], vt[:, s, h], ls[h % 2][:, blk[s]],
                                               start=s == 0, stop=s == NC - 1)
                    ins.then_inc(self.tensor_out2.sem, 1)
                self.scores_ready.count += heads
                self.tensor_out.count += heads
                self.tensor_out2.count += heads

            @block.vector
            def _(dve):
                def first(h):
                    dve.wait_ge(self.scores_ready.sem, self.scores_ready.at(h + 1))
                    for s in range(NC):
                        self.dve.step(nc.vector.tensor_scalar(nz[h % 2][:, blk[s]], z(h, s), self.param("sb_bias")[:, h:h + 1],
                                                              -1.0, ALU.add, ALU.mult))
                    if h >= 2:
                        dve.wait_ge(self.tensor_out2.sem, self.tensor_out2.at(h - 1))
                    self.dve.tell(self.log_stay(nz[h % 2], ls[h % 2])[0](), self.vector_out)

                def second(h):
                    dve.wait_ge(self.scalar_out.sem, self.scalar_out.at(2 * h + 1))
                    self.dve.step(self.log_stay(nz[h % 2], ls[h % 2])[2]())
                    for s in range(NC):
                        d = ls[h % 2][:, self.START[s]:self.START[s] + P]
                        ins = nc.vector.tensor_tensor(d, d, self.const("before"), ALU.mult)
                        self.dve.step(ins) if s < NC - 1 else self.dve.tell(ins, self.vector_out)

                for h in range(heads):
                    first(h)
                    second(h)
                    dve.wait_ge(self.tensor_out2.sem, self.tensor_out2.at(h + 1))
                    rows = slice(64 * (h % 2), 64 * (h % 2) + 64)
                    self.dve.tell(nc.vector.tensor_copy(self.o[rows, h // 2, 0:T], self.ps[rows, 4 * (h % 2), :]),
                                  self.vector_out2)

            @block.scalar
            def _(act):
                for h in range(heads):
                    act.wait_ge(self.vector_out.sem, self.vector_out.at(2 * h + 1))
                    self.log_stay(nz[h % 2], ls[h % 2])[1]()
                    act.wait_ge(self.tensor_out.sem, self.tensor_out.at(h + 1))
                    for s in range(NC):
                        ins = nc.scalar.activation(ls[h % 2][:, blk[s]], z(h, s), ACT.Exp, bias=self.param("sb_bias")[:, h:h + 1])
                        self.act.step(ins) if s < NC - 1 else self.act.tell(ins, self.scalar_out)

    def stick_sample(self):
        nc, c = self.nc, self.c
        q = c[:, SQ:SQ + 4]
        RING = 3
        kp = [self.cut(1024 * x, PAGES, 4, P) for x in range(RING)]
        vp = [self.cut(1024 * (RING + x), PAGES, 8, 64) for x in range(RING)]
        at = 1024 * 2 * RING
        nz, ls, w = (self.cut(at + 128 * x, 128) for x in range(3))
        col = lambda pg, par, b0, j: pg * 64 + par * 32 + b0 * 4 + j
        with self.stage() as block:
            @block.sync
            def _(sp):
                def load(dst, src, b0, signal):
                    for pg in range(PAGES):
                        n = b0 * PAGES + pg
                        page = sp.value_load(self.pages[0:1, n:n + 1], min_val=0, max_val=NPHYS - 1)
                        out = dst[b0 % RING][:, pg]
                        if len(out.shape) == 3:
                            out = out.rearrange("p a b -> p (a b)")
                        sp.dma_start(out, src[bass.ds(page, 1)].rearrange("o p n -> p (o n)")).then_inc(signal.sem, 16)

                for b0 in range(B):
                    if b0 >= RING:
                        sp.wait_ge(self.keys_used.sem, self.keys_used.at(b0 - RING + 1))
                    load(kp, self.d["cache_k"], b0, self.inputs_loaded[b0 % RING])
                    if b0 < RING:
                        load(vp, self.d["cache_v"], b0, self.values_loaded[b0])
                for b0 in range(RING, B):
                    sp.wait_ge(self.values_used.sem, self.values_used.at(b0 - RING + 1))
                    load(vp, self.d["cache_v"], b0, self.values_loaded[b0 % RING])
                for b0 in range(B):
                    self.inputs_loaded[b0 % RING].count += 16 * PAGES
                    self.values_loaded[b0 % RING].count += 16 * PAGES

            @block.tensor
            def _(pe):
                for b0 in range(B):
                    own = self.inputs_loaded[b0 % RING]
                    pe.wait_ge(own.sem, own.at(16 * PAGES * (b0 // RING + 1)))
                    for par in range(2):
                        rows = slice(64 * par, 64 * par + 64)
                        for pg in range(PAGES):
                            for j in range(4):
                                x = pg * 32 + b0 * 4 + j
                                ins = nc.tensor.matmul(self.ps[:, par, x:x + 1], kp[b0 % RING][rows, pg, j],
                                                       q[rows, j, T + b0:T + b0 + 1], start=True, stop=True)
                    ins.then_inc(self.keys_used.sem, 1)
                pe.wait_ge(self.vector_out.sem, self.vector_out.at(2))
                nc.tensor.matmul(self.ps[:, 2, 64:128], self.const("key_after"), ls[:, 64:128], start=True, stop=True)
                nc.tensor.matmul(self.ps[:, 2, 0:64], self.const("key_after"), ls[:, 0:64], start=True, stop=False)
                nc.tensor.matmul(self.ps[:, 2, 0:64], self.const("ones"), ls[:, 64:128], start=False, stop=True).then_inc(
                    self.tensor_out.sem, 1)
                pe.wait_ge(self.scalar_out.sem, self.scalar_out.at(2))
                for b0 in range(B):
                    own = self.values_loaded[b0 % RING]
                    pe.wait_ge(own.sem, own.at(16 * PAGES * (b0 // RING + 1)))
                    for par in range(2):
                        rows = slice(64 * par, 64 * par + 64)
                        for j in range(4):
                            for pg in range(PAGES):
                                x = col(pg, par, b0, j)
                                ins = nc.tensor.matmul(self.ps[rows, 3, j * B + b0:j * B + b0 + 1],
                                                       vp[b0 % RING][:, pg, 2 * j + par], w[:, x:x + 1],
                                                       start=pg == 0, stop=pg == PAGES - 1)
                    ins.then_inc(self.values_used.sem, 1)
                self.keys_used.count += B
                self.values_used.count += B
                self.tensor_out.count += 1

            @block.vector
            def _(dve):
                first, _, last = self.log_stay(nz, ls)
                dve.wait_ge(self.keys_used.sem, self.keys_used.at(B))
                bias = self.param("sb_bias").rearrange("p (j q) -> p q j", q=2)
                for par in range(2):
                    for pg in range(PAGES):
                        out = nz[:, col(pg, par, 0, 0):col(pg, par, 0, 0) + 32].rearrange("p (b j) -> p b j", j=4)
                        self.dve.step(nc.vector.tensor_tensor(
                            out, self.ps[:, par, pg * 32:(pg + 1) * 32].rearrange("p (b j) -> p b j", j=4),
                            bias[:, par].unsqueeze(1).to_broadcast([P, B, 4]), ALU.add))
                self.dve.step(nc.vector.tensor_scalar(nz, nz, -1.0, None, ALU.mult))
                self.dve.tell(first(), self.vector_out)
                dve.wait_ge(self.scalar_out.sem, self.scalar_out.at(1))
                self.dve.tell(last(), self.vector_out)
                dve.wait_ge(self.tensor_out.sem, self.tensor_out.at(1))
                self.dve.tell(nc.vector.tensor_tensor(w, self.ps[:, 2, 0:128], nz, ALU.subtract), self.vector_out)

            @block.scalar
            def _(act):
                act.wait_ge(self.vector_out.sem, self.vector_out.at(1))
                self.log_stay(nz, ls)[1]()
                act.wait_ge(self.vector_out.sem, self.vector_out.at(3))
                self.act.tell(nc.scalar.activation(w, w, ACT.Exp), self.scalar_out)
                act.wait_ge(self.values_used.sem, self.values_used.at(B))
                self.act.step(nc.scalar.activation(self.o[:, 0:4, T:N], self.ps[:, 3, 0:32].rearrange("p (j b) -> p j b", b=B),
                                                   ACT.Copy))

    E_EG, E_DM, E_LD = 0, 4, 8
    E_INV, E_VT, E_KT, E_QK, E_U, E_S, E_R = 6144, 0, 2048, 4096, 8192, 10240, 12800
    E_COL = 13312

    def conv(self):
        nc, c = self.nc, self.c
        x = c[:, DQ:DQ + 12]
        y = self.cut(0, 12, N)
        buf = self.cut(12 * N, 12, 3, B)
        pc, sc = self.cut(12 * N + 288, 12, 3), self.cut(12 * N + 324, 12, 3, B)
        t = self.cut(12 * N + 612, 12, B)
        w = self.param("dn_conv").rearrange("p (i a) -> p i a", i=4)
        with self.stage() as block:
            @block.sync
            def _(sp):
                sp.dma_start(buf, self.d["state_conv"]).then_inc(self.inputs_loaded[0].sem, 16)
                self.inputs_loaded[0].count += 16
                sp.wait_ge(self.pool_out.sem, self.pool_out.at(3))
                self.store(sp, self.d["p_conv"], pc)
                self.store(sp, self.d["s_conv"], sc)
                sp.wait_ge(self.stored.sem, self.stored.count)

            @block.gpsimd
            def _(pool):
                self.pool.tell(nc.gpsimd.tensor_copy(pc, x[:, :, T - 3:T]), self.pool_out)
                self.pool.tell(nc.gpsimd.tensor_copy(sc[:, :, 2], x[:, :, T:N]), self.pool_out)
                pool.wait_ge(self.inputs_loaded[0].sem, self.inputs_loaded[0].at(16))
                self.pool.tell(nc.gpsimd.tensor_copy(sc[:, :, 0:2], buf[:, :, 1:3]), self.pool_out)

            @block.scalar
            def _(act):
                for a in range(12):
                    nc.scalar.activation(y[:, a], x[:, a], ACT.Copy, scale=w[:, 3, a:a + 1]).then_inc(self.scalar_out.sem, 1)
                self.scalar_out.count += 12
                act.wait_ge(self.pool_out.sem, self.pool_out.at(3))
                for a in range(12):
                    act.wait_ge(self.vector_out.sem, self.vector_out.at(a + 1))
                    self.act.step(nc.scalar.activation(x[:, a], y[:, a], ACT.Silu))

            @block.vector
            def _(dve):
                dve.wait_ge(self.scalar_out.sem, self.scalar_out.at(12))
                dve.wait_ge(self.inputs_loaded[0].sem, self.inputs_loaded[0].at(16))
                for i in range(3):
                    wi = w[:, i].unsqueeze(2).to_broadcast([P, 12, B])
                    self.dve.step(nc.vector.tensor_tensor(t, buf[:, :, i], wi, ALU.mult))
                    self.dve.step(nc.vector.tensor_tensor(y[:, :, T:N], y[:, :, T:N], t, ALU.add))
                for a in range(12):
                    for i in range(3):
                        lag = 3 - i
                        ins = nc.vector.scalar_tensor_tensor(y[:, a, lag:T], x[:, a, 0:T - lag], w[:, i, a:a + 1], y[:, a, lag:T],
                                                             ALU.mult, ALU.add)
                        self.dve.step(ins) if i < 2 else self.dve.tell(ins, self.vector_out)

    def delta_vectors(self):
        nc, c = self.nc, self.c
        q, k = c[:, DQ:DQ + 4], c[:, DK:DK + 4]
        sq, r = ([self.cut(2080 * (x + y), 4, N) for x in range(2)] for y in (0, 2))
        g, e, a = c[0:4, DAB], self.cut(8320, N)[0:4], self.cut(8840, 1)[0:4]
        gs = self.cut(8850, N)
        eg = c[:, self.E_EG:self.E_EG + 4]
        dm = self.flat(self.E_DM)[:, 0:2048].rearrange("p (c h t) -> p c h t", c=NC, h=4)
        ld = self.flat(self.E_LD)[:, 0:2048].rearrange("p (c h t) -> p c h t", c=NC, h=4)
        col = self.cut(self.E_COL, 4, NC, 4)
        bs = self.cut(self.E_COL + 64, 4, B)
        row = lambda h, base: self.cst[base:base + 4, SEL_AT + h * P:SEL_AT + (h + 1) * P]
        heads4 = self.ps[:, :, 0:HALF].rearrange("p (h s) n -> p h s n", s=2)

        def spread(pe, base):
            for h in range(4):
                for s, (lo, hi) in enumerate(self.SPANS):
                    ins = nc.tensor.matmul(self.ps[:, 2 * h + s, 0:HALF], row(h, base), gs[base:base + 4, lo:hi],
                                           start=True, stop=True)
            ins.then_inc(self.tensor_out.sem, 1)

        with self.stage() as block:
            @block.scalar
            def _(act):
                self.act.step(nc.scalar.activation(gs[32:36], c[32:36, DAB], ACT.Sigmoid))
                act.wait_ge(self.vector_out.sem, self.vector_out.at(1))
                self.act.step(nc.scalar.activation(e, e, ACT.Exp))
                self.act.step(nc.scalar.activation(a, self.param("dn_a")[0:4], ACT.Exp))
                self.act.tell(nc.scalar.activation(e, e, ACT.Ln, bias=1.0), self.scalar_out)
                self.act.tell(nc.scalar.activation(sq[0], q, ACT.Square), self.scalar_out)
                self.act.tell(nc.scalar.activation(sq[1], k, ACT.Square), self.scalar_out)
                for x in range(2):
                    act.wait_ge(self.tensor_out.sem, self.tensor_out.at(x + 1))
                    self.act.tell(nc.scalar.activation(self.eight(r[x]), self.ps[:, :, 0:HALF], ACT.Ln, bias=self.eps),
                                  self.scalar_out)
                    self.act.tell(nc.scalar.activation(r[x], r[x], ACT.Exp, scale=-0.5), self.scalar_out)
                act.wait_ge(self.tensor_out.sem, self.tensor_out.at(4))
                self.act.tell(nc.scalar.activation(self.eight(eg), self.ps[:, :, 0:HALF], ACT.Exp), self.scalar_out)
                act.wait_ge(self.vector_out.sem, self.vector_out.at(4))
                self.act.step(nc.scalar.activation(dm, dm, ACT.Exp))
                self.act.step(nc.scalar.activation(col[:, 2], col[:, 2], ACT.Exp))
                self.act.tell(nc.scalar.activation(col[:, 3], col[:, 3], ACT.Exp), self.scalar_out)

            @block.tensor
            def _(pe):
                for x in range(2):
                    if x:
                        pe.wait_ge(self.scalar_out.sem, self.scalar_out.at(4))
                    pe.wait_ge(self.scalar_out.sem, self.scalar_out.at(2 + x))
                    for h in range(4):
                        for s, (lo, hi) in enumerate(self.SPANS):
                            ins = nc.tensor.matmul(self.ps[:, 2 * h + s, 0:HALF], self.const("ones"), sq[x][:, h, lo:hi],
                                                   start=True, stop=True)
                    ins.then_inc(self.tensor_out.sem, 1)
                pe.wait_ge(self.scalar_out.sem, self.scalar_out.at(6))
                pe.wait_ge(self.vector_out.sem, self.vector_out.at(2))
                for n, base in enumerate((0, 32)):
                    for t in range(NC):
                        ins = nc.tensor.transpose(self.ps[:, n, t * 4:t * 4 + 4], gs[base:base + 4, t * P:(t + 1) * P],
                                                  self.cst[base:base + 4, CONST_AT["ident"] + base:CONST_AT["ident"] + base + 4])
                ins.then_inc(self.tensor_out.sem, 1)
                pe.wait_ge(self.vector_out.sem, self.vector_out.at(3))
                spread(pe, 0)
                pe.wait_ge(self.scalar_out.sem, self.scalar_out.at(8))
                pe.wait_ge(self.vector_out.sem, self.vector_out.at(4))
                spread(pe, 32)
                self.tensor_out.count += 5

            @block.vector
            def _(dve):
                self.dve.step(nc.vector.tensor_scalar(g, g, self.param("dn_dt")[0:4, 0:1], None, ALU.add))
                self.dve.tell(nc.vector.scalar_tensor_tensor(e, g, -1.0, g, ALU.mult, ALU.min), self.vector_out)
                dve.wait_ge(self.scalar_out.sem, self.scalar_out.at(1))
                self.dve.step(nc.vector.scalar_tensor_tensor(g, g, 0.0, e, ALU.max, ALU.add))
                self.dve.step(nc.vector.tensor_scalar(g, g, a, -1.0, ALU.mult, ALU.mult))
                self.dve.step(nc.vector.tensor_copy(gs[0:4, T:N], g[:, T:N]))
                self.dve.tell(nc.vector.tensor_tensor_scan(gs[0:4, 0:T], self.cst[0:4, SCAN128_AT:SCAN128_AT + T], g[:, 0:T],
                                                           0.0, ALU.mult, ALU.add), self.vector_out)
                dve.wait_ge(self.scalar_out.sem, self.scalar_out.at(5))
                self.dve.step(nc.vector.scalar_tensor_tensor(q, q, P ** -0.5, r[0], ALU.mult, ALU.mult))
                dve.wait_ge(self.scalar_out.sem, self.scalar_out.at(7))
                self.dve.step(nc.vector.tensor_tensor(k, k, r[1], ALU.mult))
                dve.wait_ge(self.tensor_out.sem, self.tensor_out.at(3))
                self.dve.tell(nc.vector.tensor_copy(col[:, 0:2].rearrange("p x c h -> p x (c h)"), self.ps[:, 0:2, 0:16]),
                              self.vector_out)
                dve.wait_ge(self.scalar_out.sem, self.scalar_out.at(8))
                for t in range(NC):
                    for h in range(4):
                        for lo, hi, bank, at in self.pieces(t):
                            self.dve.step(nc.vector.tensor_scalar(
                                dm[:, t, h, lo:hi], self.ps[:, 2 * h + bank, at:at + hi - lo], col[:, 0, t, h:h + 1], 0.0,
                                ALU.subtract, ALU.min))
                    end = (t + 1) * P - 1
                    last = heads4[:, :, end // HALF, end % HALF]
                    self.dve.step(nc.vector.tensor_copy(col[:, 3, t], last))
                    self.dve.step(nc.vector.tensor_tensor(col[:, 2, t], col[:, 3, t], col[:, 0, t], ALU.subtract))
                self.dve.tell(nc.vector.memset(bs, 0.0), self.vector_out)
                dve.wait_ge(self.tensor_out.sem, self.tensor_out.at(5))
                dve.wait_ge(self.scalar_out.sem, self.scalar_out.at(9))
                self.dve.step(nc.vector.tensor_copy(bs, heads4[:, :, 1, HALF - B:HALF]))
                for t in range(NC):
                    for lo, hi, bank, at in self.pieces(t):
                        self.dve.step(nc.vector.scalar_tensor_tensor(
                            ld[:, t, :, lo:hi], dm[:, t, :, lo:hi], -1.0, heads4[:, :, bank, at:at + hi - lo],
                            ALU.mult, ALU.mult))
                flat = ld.rearrange("p c h t -> p (c h) t")
                self.dve.step(nc.vector.tensor_tensor(flat, flat, self.const("before").unsqueeze(1).to_broadcast([P, 16, P]),
                                                      ALU.mult))
                flat = dm.rearrange("p c h t -> p (c h) t")
                self.dve.step(nc.vector.tensor_tensor(flat, flat, self.const("causal").unsqueeze(1).to_broadcast([P, 16, P]),
                                                      ALU.mult))

    def pieces(self, t):
        out = []
        for s, (lo, hi) in enumerate(self.SPANS):
            a, b = max(lo, t * P), min(hi, (t + 1) * P)
            if a < b:
                out.append((a - t * P, b - t * P, s, a - lo))
        return out

    def delta_inverses(self):
        nc, c = self.nc, self.c
        k = c[:, DK:DK + 4]
        ld = self.flat(self.E_LD)[:, 0:2048].rearrange("p (g x t) -> p g x t", g=2, x=8)

        def fill(pe, g, bank):
            for x in range(8):
                t, h = 2 * g + x // 4, x % 4
                kc = k[:, h, t * P:(t + 1) * P]
                ins = nc.tensor.matmul(self.ps[:, bank + x // 4, h * P:(h + 1) * P], kc, kc, start=True, stop=True)
            ins.then_inc(self.tensor_out.sem, 1)

        self.inv = [self.cut(self.E_INV + 1024 * g, 8, P) for g in range(2)]
        self.unit_inverses(2, 2, (lambda g: ld[:, g], [f"level{m}" for m in LEVELS[::-1]]), 0, 2048, 4096, self.inv, fill)

    def delta_chain(self):
        nc, c = self.nc, self.c
        q, k, v = (c[:, x:x + 4] for x in (DQ, DK, DV))
        eg = c[:, self.E_EG:self.E_EG + 4]
        dm = self.flat(self.E_DM)[:, 0:2048].rearrange("p (c h t) -> p c h t", c=NC, h=4)
        col = self.cut(self.E_COL, 4, NC, 4)
        inv = self.cut(self.E_INV, NC, 4, P)
        vt, kt, qk, u = (self.cut(x, NC, 4, P) for x in (self.E_VT, self.E_KT, self.E_QK, self.E_U))
        st = self.cut(self.E_S, NC + 1, 4, P)
        rr = self.cut(self.E_R, 4, P)

        def wide(t):
            return t.rearrange("p c h t -> p (c h t)")

        with self.stage() as block:
            @block.tensor
            def _(pe):
                for n, src in enumerate((v, k)):
                    for t in range(NC):
                        for h in range(4):
                            ins = nc.tensor.transpose(self.ps[:, 4 * n + t, h * P:(h + 1) * P], src[:, h, t * P:(t + 1) * P],
                                                      self.const("ident"))
                    ins.then_inc(self.tensor_out.sem, 1)
                pe.wait_ge(self.scalar_out.sem, self.scalar_out.at(1))
                for t in range(NC):
                    for h in range(4):
                        cols = slice(t * P, (t + 1) * P)
                        ins = nc.tensor.matmul(self.ps[:, t, h * P:(h + 1) * P], k[:, h, cols], q[:, h, cols],
                                               start=True, stop=True)
                ins.then_inc(self.tensor_out.sem, 1)
                pe.wait_ge(self.vector_out.sem, self.vector_out.at(1))
                for t in range(NC):
                    cols = slice(t * P, (t + 1) * P)
                    if t:
                        pe.wait_ge(self.vector_out2.sem, self.vector_out2.at(2 * t))
                        for h in range(4):
                            ins = nc.tensor.matmul(self.ps[:, 4, h * P:(h + 1) * P], k[:, h, cols], st[:, t, h],
                                                   start=True, stop=True)
                        ins.then_inc(self.tensor_out2.sem, 1)
                    pe.wait_ge(self.vector_out2.sem, self.vector_out2.at(2 * t + 1))
                    for h in range(4):
                        ins = nc.tensor.matmul(self.ps[:, 5, h * P:(h + 1) * P], inv[:, t, h], rr[:, h], start=True, stop=True)
                    ins.then_inc(self.tensor_out2.sem, 1)
                    pe.wait_ge(self.scalar_out.sem, self.scalar_out.at(2 + t))
                    for h in range(4):
                        ins = nc.tensor.matmul(self.ps[:, 6, h * P:(h + 1) * P], kt[:, t, h], u[:, t, h], start=True, stop=True)
                    ins.then_inc(self.tensor_out2.sem, 1)
                pe.wait_ge(self.vector_out.sem, self.vector_out.at(3))
                for h in range(4):
                    for t in range(NC):
                        cols = slice(t * P, (t + 1) * P)
                        nc.tensor.matmul(self.ps[:, h, cols], u[:, t, h], qk[:, t, h], start=True, stop=t == 0)
                        if t:
                            ins = nc.tensor.matmul(self.ps[:, h, cols], st[:, t, h], q[:, h, cols], start=False, stop=True)
                ins.then_inc(self.tensor_out.sem, 1)
                self.tensor_out.count += 4
                self.tensor_out2.count += 3 * NC - 1

            @block.scalar
            def _(act):
                act.wait_ge(self.tensor_out.sem, self.tensor_out.at(1))
                self.act.tell(nc.scalar.activation(wide(vt), self.banks(0, 4), ACT.Copy), self.scalar_out)
                for t in range(NC):
                    act.wait_ge(self.tensor_out2.sem, self.tensor_out2.at(3 * t + 1))
                    self.act.tell(nc.scalar.activation(u[:, t].rearrange("p h e -> p (h e)"), self.ps[:, 5, :], ACT.Copy),
                                  self.scalar_out)
                act.wait_ge(self.tensor_out.sem, self.tensor_out.at(4))
                self.act.step(nc.scalar.activation(self.o[:, 4:8, 0:T], self.ps[:, 0:4, :], ACT.Copy))

            @block.gpsimd
            def _(pool):
                pool.wait_ge(self.tensor_out.sem, self.tensor_out.at(3))
                self.pool.tell(nc.gpsimd.tensor_tensor(q[:, :, 0:T], q[:, :, 0:T], eg[:, :, 0:T], ALU.mult), self.pool_out)

            @block.vector
            def _(dve):
                flat = inv.rearrange("p c h t -> p (c h) t")
                beta = col[:, 1].rearrange("p c h -> p (c h)").unsqueeze(2).to_broadcast([P, 16, P])
                self.dve.step(nc.vector.tensor_tensor(flat, flat, beta, ALU.mult))
                dve.wait_ge(self.tensor_out.sem, self.tensor_out.at(2))
                decay = col[:, 2].rearrange("p c h -> p (c h)").unsqueeze(2).to_broadcast([P, 16, P])
                self.dve.step(nc.vector.tensor_tensor(kt.rearrange("p c h t -> p (c h) t"),
                                                      self.banks(4, 4).rearrange("p (x t) -> p x t", t=P), decay, ALU.mult))
                dve.wait_ge(self.tensor_out.sem, self.tensor_out.at(3))
                self.dve.tell(nc.vector.tensor_tensor(k[:, :, 0:T], k[:, :, 0:T], eg[:, :, 0:T], ALU.mult), self.vector_out)
                dve.wait_ge(self.scalar_out.sem, self.scalar_out.at(1))
                self.dve.tell(nc.vector.tensor_copy(rr, vt[:, 0]), self.vector_out2)
                self.dve.tell(nc.vector.tensor_tensor(wide(qk), self.banks(0, 4), wide(dm), ALU.mult), self.vector_out)
                for t in range(NC):
                    if t:
                        dve.wait_ge(self.tensor_out2.sem, self.tensor_out2.at(3 * t))
                        self.dve.tell(nc.vector.tensor_tensor(rr.rearrange("p h e -> p (h e)"), vt[:, t].rearrange("p h e -> p (h e)"),
                                                              self.ps[:, 4, :], ALU.subtract), self.vector_out2)
                    dve.wait_ge(self.tensor_out2.sem, self.tensor_out2.at(3 * t + 2))
                    new = st[:, t + 1]
                    if t == 0:
                        ins = nc.vector.tensor_copy(new.rearrange("p h e -> p (h e)"), self.ps[:, 6, :])
                    else:
                        self.dve.step(nc.vector.tensor_tensor(new, st[:, t], col[:, 3, t].unsqueeze(2).to_broadcast([P, 4, P]),
                                                              ALU.mult))
                        ins = nc.vector.tensor_tensor(new.rearrange("p h e -> p (h e)"), new.rearrange("p h e -> p (h e)"),
                                                      self.ps[:, 6, :], ALU.add)
                    self.dve.tell(ins, self.vector_out2)
                dve.wait_ge(self.pool_out.sem, self.pool_out.at(1))
                self.dve.tell(nc.vector.memset(rr, 0.0), self.vector_out)

            @block.sync
            def _(sp):
                sp.wait_ge(self.vector_out2.sem, self.vector_out2.at(2 * NC))
                self.store(sp, self.d["p_delta"], st[:, NC].rearrange("p h e -> p (h e)"))
                sp.wait_ge(self.stored.sem, self.stored.count)

    def delta_sample(self):
        nc, c = self.nc, self.c
        s4 = lambda x: c[:, x:x + 4, T:N]
        ss = self.h[:].rearrange("p a b -> p (a b)")[:, 0:4096].rearrange("p (b h e) -> p b h e", b=B, h=4)
        pr = self.cut(0, B, 4, P)
        vs = self.cut(4096, 4, P)
        nk, kb = self.cut(4608, 4, B), self.cut(4640, 4, B)
        bs = self.cut(self.E_COL + 64, 4, B)

        def by_seq(t):
            return t.rearrange("p h b -> p b h").unsqueeze(3).to_broadcast([P, B, 4, P])

        with self.stage() as block:
            @block.sync
            def _(sp):
                sp.dma_start(ss, self.d["state_delta"]).then_inc(self.inputs_loaded[0].sem, 16)
                self.inputs_loaded[0].count += 16
                sp.wait_ge(self.vector_out2.sem, self.vector_out2.at(1))
                self.store(sp, self.d["s_delta"], ss)
                sp.wait_ge(self.stored.sem, self.stored.count)

            @block.tensor
            def _(pe):
                for h in range(4):
                    ins = nc.tensor.transpose(self.ps[0:B, 0, h * P:(h + 1) * P], c[:, DV + h, T:N], self.const("ident"))
                ins.then_inc(self.tensor_out.sem, 1)
                pe.wait_ge(self.scalar_out.sem, self.scalar_out.at(1))
                pe.wait_ge(self.vector_out.sem, self.vector_out.at(1))
                for b0 in range(B):
                    nc.tensor.matmul(self.ps[:, b0, :], self.cst[0:B, SEL_AT + b0 * P:SEL_AT + (b0 + 1) * P],
                                     vs[0:B].rearrange("p h e -> p (h e)"), start=True, stop=False)
                    ins = nc.tensor.matmul(self.ps[:, b0, :], self.const("ones"), pr[:, b0].rearrange("p h e -> p (h e)"),
                                           start=False, stop=True)
                ins.then_inc(self.tensor_out.sem, 1)
                pe.wait_ge(self.vector_out2.sem, self.vector_out2.at(1))
                for h in range(4):
                    for b0 in range(B):
                        at = h * B + b0
                        ins = nc.tensor.matmul(self.ps[:, 0, at:at + 1], ss[:, b0, h], c[:, DQ + h, T + b0:T + b0 + 1],
                                               start=True, stop=True)
                ins.then_inc(self.tensor_out.sem, 1)
                self.tensor_out.count += 3

            @block.scalar
            def _(act):
                act.wait_ge(self.tensor_out.sem, self.tensor_out.at(1))
                self.act.tell(nc.scalar.activation(vs[0:B].rearrange("p a b -> p (a b)"), self.ps[0:B, 0, :], ACT.Copy),
                              self.scalar_out)
                act.wait_ge(self.tensor_out.sem, self.tensor_out.at(3))
                self.act.step(nc.scalar.activation(self.o[:, 4:8, T:N], self.ps[:, 0, 0:32].rearrange("p (h b) -> p h b", b=B),
                                                   ACT.Copy))

            @block.vector
            def _(dve):
                self.dve.step(nc.vector.tensor_scalar(nk, s4(DK), -1.0, None, ALU.mult))
                self.dve.step(nc.vector.tensor_tensor(kb, s4(DK), bs, ALU.mult))
                dve.wait_ge(self.inputs_loaded[0].sem, self.inputs_loaded[0].at(16))
                self.dve.step(nc.vector.tensor_tensor(ss, ss, by_seq(c[:, self.E_EG:self.E_EG + 4, T:N]), ALU.mult))
                self.dve.tell(nc.vector.tensor_tensor(pr, ss, by_seq(nk), ALU.mult), self.vector_out)
                dve.wait_ge(self.tensor_out.sem, self.tensor_out.at(2))
                self.dve.step(nc.vector.tensor_tensor(pr, self.banks(0, 8).rearrange("p (b h e) -> p b h e", b=B, h=4),
                                                      by_seq(kb), ALU.mult))
                self.dve.tell(nc.vector.tensor_tensor(ss, ss, pr, ALU.add), self.vector_out2)

    def run(self):
        nc = self.nc
        L = self.lin
        self.start()
        self.params = EVEN_PARAMS, self.par0
        self.projection(L["in0"], "g_mix", L["out0"])
        self.gla_gates()
        self.gla_levels()
        self.gla_states()
        self.gated_norm(0, GG, "gla_norm")
        self.token_shift()
        self.rwkv_low_rank()
        self.rwkv_vectors()
        self.rwkv_sample()
        self.rwkv_inverses()
        self.rwkv_chain()
        self.rwkv_output()
        self.residual(L["out0"], self.std, L["xkv0"], src=self.o)
        self.memory(0, L["xq0"])
        self.query(0, L["xo0"])
        self.attention(0)
        self.residual(L["xo0"], self.std, L["gu0"], src=self.o)
        self.gate_up(0, L["down0"])
        self.residual(L["down0"], self.hid, L["in1"], per=2)
        self.params = ODD_PARAMS, self.par1
        self.projection(L["in1"], "g_mix", L["out1"])
        self.stick_norms()
        self.stick_prompt()
        self.stick_sample()
        self.conv()
        self.delta_vectors()
        self.delta_inverses()
        self.delta_chain()
        self.delta_sample()
        self.gated_norm(4, DZ, "dn_norm")
        self.residual(L["out1"], self.std, L["xkv1"], src=self.o)
        self.memory(1, L["xq1"])
        self.query(1, L["xo1"])
        self.attention(1)
        self.residual(L["xo1"], self.std, L["gu1"], src=self.o)
        self.gate_up(1, L["down1"])
        self.residual(L["down1"], self.hid, None, per=2)
        self.finish()

    def finish(self):
        with self.stage() as block:
            @block.sync
            def _(sp):
                self.store(sp, self.d["y"], self.x[:])
                sp.wait_ge(self.stored.sem, self.stored.count)


def units(w, kt=KT):
    k, n = w.shape
    a = w.reshape(k // (kt * P), kt, P, n // P, P).transpose(3, 0, 2, 1, 4)
    return np.ascontiguousarray(a.reshape(-1, P, kt * P))


def feature_major(a):
    return np.ascontiguousarray(a.reshape(a.shape[0], -1, P).transpose(2, 1, 0))


def column(v):
    return v.reshape(-1, P).T


def rows(v, width=1):
    v = v.reshape(-1, width) if v.ndim == 1 else v
    out = np.zeros((P, v.shape[1]), v.dtype)
    out[:v.shape[0]] = v
    return out


def lay_out(I):
    a = {"cst": constants()}
    a["x"] = np.concatenate([feature_major(I["x_prompt"][0]), feature_major(I["x_sample"][:, 0])], axis=2)
    a["mem"] = feature_major(I["mem_prompt"][0])
    we, wo = I["w_in_even"][0], I["w_in_odd"][0]
    tail0, tail1 = np.zeros((D, P), we.dtype), np.zeros((D, P), wo.dtype)
    tail0[:, 0:16] = we[:, 1536:1552]
    tail1[:, 0:4], tail1[:, 32:36] = wo[:, 3584:3588], wo[:, 3588:3592]
    a["w_in0"] = units(np.concatenate([we[:, 0:1536], we[:, 1552:], tail0], axis=1))
    a["w_in1"] = units(np.concatenate([wo[:, :3584], tail1], axis=1))
    a["w_out0"], a["w_out1"] = units(I["w_out_even"][0]), units(I["w_out_odd"][0])
    for i in range(2):
        a[f"w_xq{i}"], a[f"w_xkv{i}"], a[f"w_xo{i}"] = (units(I[n][i]) for n in ("w_xq", "w_xkv", "w_xo"))
        gu = I["w_gu"][i].reshape(D, 2, FT, P).transpose(0, 2, 1, 3).reshape(D, -1)
        a[f"w_gu{i}"], a[f"w_down{i}"] = units(gu), units(I["w_down"][i], SLOT_K)

    def common(i):
        return [column(I[n][i]) for n in ("norm_mix", "norm_cross", "norm_ffn", "mem_norm", "xq_norm", "xk_norm")]

    a["par0"] = np.concatenate(common(0) + [
        column(I["gla_b_a"][0]), column(I["gla_norm"][0])] + [column(I["rwkv_" + n][0]) for n in
        ("mu", "w0", "a0", "k_k", "k_a", "r_k", "ln_w", "ln_b")] + [
        rows(I["gla_w_a2"][0]), np.concatenate([I["rwkv_w2"][0], I["rwkv_a2"][0]]), I["rwkv_g2"][0]], axis=1)
    a["par1"] = np.concatenate(common(1) + [
        np.tile(I["sb_q_norm"][0], 2)[:, None], np.tile(I["sb_k_norm"][0], 2)[:, None],
        np.tile(I["sb_bias"][0], (P, 1)), I["dn_conv"][0].reshape(4, 12, P).transpose(2, 0, 1).reshape(P, 48),
        rows(I["dn_a_log"][0]), rows(I["dn_dt_bias"][0]), column(I["dn_norm"][0])], axis=1)
    a["state_gla"] = I["state_gla"][0].reshape(B, 2, P, P).transpose(2, 0, 1, 3)
    a["state_rwkv"] = I["state_rwkv"][0].reshape(B, 4, 2, 64, 64).transpose(2, 4, 0, 1, 3).reshape(P, B, 4, 64)
    a["state_shift"] = feature_major(I["state_rwkv_shift"][0])
    a["state_delta"] = I["state_delta"][0].transpose(2, 0, 1, 3)
    a["state_conv"] = I["state_delta_conv"][0].reshape(B, 3, 12, P).transpose(3, 2, 1, 0)
    a["cache_k"] = I["cache_sb_k"][0].reshape(NPHYS, PAGE, 4, P).transpose(0, 3, 2, 1).reshape(NPHYS, P, 512)
    a["cache_v"] = I["cache_sb_v"][0].reshape(NPHYS, PAGE, 512)
    a["page_table"] = I["page_table"].reshape(1, B * PAGES)
    for i in range(2):
        a[f"mem_k{i}"] = I["cache_mem_k"][i].reshape(B, MEM, 8, P).transpose(0, 3, 2, 1)
        a[f"mem_v{i}"] = I["cache_mem_v"][i].reshape(B, 2, P, D).transpose(0, 2, 1, 3)
    return {k: np.ascontiguousarray(v) for k, v in a.items()}


OUTPUTS = {
    "y": (P, KT, N), "p_gla": (P, 2 * P), "s_gla": (P, B, 2, P), "shift": (P, R_TILES, B + 1),
    "p_rwkv": (P, 4 * 64), "s_rwkv": (P, B, 4, 64), "p_sbk": (P, 4, N), "p_sbv": (P, 4, N),
    "p_delta": (P, 4 * P), "s_delta": (P, B, 4, P), "p_conv": (P, 12, 3), "s_conv": (P, 12, 3, B),
    "p_mk0": (P, 8, MEM), "p_mk1": (P, 8, MEM), "p_mv0": (P, 8, MEM), "p_mv1": (P, 8, MEM),
}


def build(nc, arrays):
    with ExitStack() as ctx:
        dram = {}
        for n, a in arrays.items():
            dt = I32 if a.dtype.kind == "i" else F32
            dram[n] = nc.dram_tensor("in_" + n, list(a.shape), dt, kind="ExternalInput").ap()
        for n, shape in OUTPUTS.items():
            dram[n] = nc.dram_tensor("out_" + n, list(shape), F32, kind="ExternalOutput").ap()
        k = Kernel(nc, dram, ctx)
        k.lin = {}
        for i, n_in in enumerate((EVEN_TILES, ODD_TILES)):
            for n, count, kt in (("in", n_in, KT), ("out", 8, KT), ("xkv", 16, KT), ("xq", 8, KT), ("xo", 8, KT),
                                 ("gu", 2 * FT, KT), ("down", 16, SLOT_K)):
                k.lin[f"{n}{i}"] = Linear(dram[f"w_{n}{i}"], count, kt)
        k.run()


def kernel(**inputs):
    from concourse import bacc
    from concourse.bass_utils import run_bass_kernel_spmd

    arrays = lay_out({k: np.asarray(v) for k, v in inputs.items()})
    nc = bacc.Bacc("TRN2", target_bir_lowering=False, num_devices=1)
    build(nc, arrays)
    r = run_bass_kernel_spmd(nc, [{"in_" + n: a for n, a in arrays.items()}], core_ids=[0]).results[0]
    o = {n: np.asarray(r["out_" + n]) for n in OUTPUTS}

    def token_major(t):
        return np.ascontiguousarray(t.transpose(2, 1, 0).reshape(t.shape[2], -1))

    y, k, v = token_major(o["y"]), token_major(o["p_sbk"]), token_major(o["p_sbv"])
    rwkv = lambda t: t.reshape(2, 64, -1, 4, 64).transpose(2, 3, 0, 4, 1).reshape(-1, 8, 64, 64)
    out = (
        y[None, :T], y[T:, None],
        o["p_gla"].reshape(P, 2, P).transpose(1, 0, 2).reshape(1, 1, 4, 64, P), rwkv(o["p_rwkv"])[None],
        token_major(o["shift"])[None, :1],
        k[:T].reshape(1, 1, T, 8, 64), v[:T].reshape(1, 1, T, 8, 64),
        o["p_delta"].reshape(P, 4, P).transpose(1, 0, 2)[None, None],
        o["p_conv"].transpose(2, 1, 0).reshape(1, 1, 3, 1536),
        np.stack([token_major(o[f"p_mk{i}"]).reshape(1, MEM, 4, 256) for i in range(2)]),
        np.stack([token_major(o[f"p_mv{i}"]).reshape(1, MEM, 4, 256) for i in range(2)]),
        o["s_gla"].transpose(1, 2, 0, 3).reshape(1, B, 4, 64, P), rwkv(o["s_rwkv"])[None],
        token_major(o["shift"])[None, 1:],
        k[T:].reshape(1, B, 1, 8, 64), v[T:].reshape(1, B, 1, 8, 64),
        o["s_delta"].transpose(1, 2, 0, 3)[None],
        o["s_conv"].transpose(3, 2, 1, 0).reshape(1, B, 3, 1536),
    )
    return tuple(np.ascontiguousarray(a) for a in out)
```

```python
from contextlib import ExitStack, contextmanager

import numpy as np
import concourse.bass as bass
import concourse.mybir as mybir

F32 = mybir.dt.float32
F32R = mybir.dt.float32r
U32 = mybir.dt.uint32
I32 = mybir.dt.int32
ACT = mybir.ActivationFunctionType
ALU = mybir.AluOpType
AX = mybir.AxisListType

P = 128
D = 1024
KT = D // P
T = 512
B = 8
N = T + B
HALF = N // 2
NC = T // P
MEM = 256
FT = 2816 // P
PAGE = 128
PAST = 256
PAGES = PAST // PAGE
NPHYS = 20
EPS = 1e-6
RWKV_LN_EPS = 64e-5
SLOTS = 4
SLOT_K = 11

GQ, GK, GV, GG, RR, RK, RV, RWA, RG, GLR, EVEN_TILES = 0, 2, 4, 8, 12, 16, 20, 24, 25, 26, 27
R0, R_TILES = RR, 14
SQ, SK, SV, DQ, DK, DV, DZ, DAB, ODD_TILES = 0, 4, 8, 12, 16, 20, 24, 28, 29

LEVELS = [64, 32, 16, 8, 4, 2, 1]
CONST_NAMES = (["ident", "ones", "head_ones", "key_after", "causal", "before", "causal64", "before64", "forbid"]
               + [f"level{m}" for m in LEVELS])
CONST_AT = {n: i * P for i, n in enumerate(CONST_NAMES)}
SCAN128_AT = len(CONST_NAMES) * P
SCAN64_AT = SCAN128_AT + T
SEL_AT = SCAN64_AT + T
EPS_AT = SEL_AT + B * P
CONSTS = EPS_AT + 2


def constants():
    s, t = np.arange(P)[:, None], np.arange(P)[None, :]
    m = {
        "ident": s == t, "ones": s >= 0 * t, "head_ones": s // 64 == t // 64,
        "key_after": s >= t, "causal": s <= t, "before": s < t,
        "causal64": (s <= t) & (s // 64 == t // 64), "before64": (s < t) & (s // 64 == t // 64),
    }
    for h in LEVELS:
        m[f"level{h}"] = (s // (2 * h) == t // (2 * h)) & (s % (2 * h) < h) & (t % (2 * h) >= h)
    m["forbid"] = np.where(s >= t, -1e30, 0.0)
    out = np.zeros((P, CONSTS), np.float32)
    for n, a in CONST_AT.items():
        out[:, a:a + P] = m[n]
    out[:, SCAN128_AT:SCAN128_AT + T] = np.arange(T) % 128 != 0
    out[:, SCAN64_AT:SCAN64_AT + T] = np.arange(T) % 64 != 0
    for b in range(B):
        out[b, SEL_AT + b * P:SEL_AT + (b + 1) * P] = 1
        out[32 + b, SEL_AT + b * P:SEL_AT + (b + 1) * P] = 1
    out[:, EPS_AT], out[:, EPS_AT + 1] = EPS, RWKV_LN_EPS
    return out


SCR = 13888
MAP = {}
_at = 0
for _name, _size in (("x", KT * N), ("w", SLOTS * SLOT_K * P), ("cst", CONSTS + 6), ("par0", 1368), ("par1", 112),
                     ("rstd", N), ("o", KT * N), ("c", 29 * N), ("h", KT * N), ("scr", SCR)):
    MAP[_name] = _at
    _at += _size
MAP["end"] = _at

EVEN_PARAMS = [("g_mix", 8), ("g_cross", 8), ("g_ffn", 8), ("g_mem", 8), ("xq", 2), ("xk", 2),
               ("gla_b", 2), ("gla_norm", 1), ("mu", 14), ("w0", 4), ("a0", 4), ("k_k", 4), ("k_a", 4), ("r_k", 4),
               ("ln_w", 4), ("ln_b", 4), ("gla_a2", 256), ("wa2", 512), ("g2", 512)]
ODD_PARAMS = [("g_mix", 8), ("g_cross", 8), ("g_ffn", 8), ("g_mem", 8), ("xq", 2), ("xk", 2),
              ("sbq", 1), ("sbk", 1), ("sb_bias", 8), ("dn_conv", 48), ("dn_a", 1), ("dn_dt", 1), ("dn_norm", 1)]
N_EVEN_P = sum(w for _, w in EVEN_PARAMS)
N_ODD_P = sum(w for _, w in ODD_PARAMS)


class Signal:

    def __init__(self, sem):
        self.sem, self.base, self.count = sem, 0, 0

    def at(self, k):
        return self.base + k


class Engine:

    def __init__(self, eng, done):
        self.done = done
        self.eng = eng

    def step(self, ins):
        ins.then_inc(self.done.sem, 1)
        self.done.count += 1
        self.eng.wait_ge(self.done.sem, self.done.count)

    def tell(self, ins, signal):
        ins.then_inc(signal.sem, 1)
        signal.count += 1
        self.eng.wait_ge(signal.sem, signal.count)


class Linear:

    def __init__(self, src, units, kt):
        self.src, self.units, self.kt, self.at = src, units, kt, None


class Split:

    def __init__(self, k, name, tiles, x_hi, x_lo, kt, w_hi, w_lo):
        self.x = [k.place(f"{name}_x_{p}", at, [tiles, N], F32R) for p, at in (("hi", x_hi), ("lo", x_lo))]
        self.w = [k.place(f"{name}_w_{p}", at, [2, kt * P], F32R) for p, at in (("hi", w_hi), ("lo", w_lo))]


class Kernel:

    def __init__(self, nc, dram, ctx):
        self.nc, self.d, self.ctx = nc, dram, ctx
        self.counters = []

        self.arena = ctx.enter_context(nc.sbuf_tensor("arena", [P, MAP["end"]], F32))
        self.arena_at = nc.sbuf_base - 4 * MAP["end"]

        def sb(name, *shape):
            return self.place(name, MAP[name], list(shape), F32)

        self.x = sb("x", KT, N)
        self.h = sb("h", KT, N)
        self.o = sb("o", KT, N)
        self.c = sb("c", 29, N)
        self.w = sb("w", SLOTS, SLOT_K * P)
        self.scr = sb("scr", SCR)
        self.cst = sb("cst", CONSTS)
        self.par0, self.par1 = sb("par0", N_EVEN_P), sb("par1", N_ODD_P)
        self.pages = ctx.enter_context(nc.sbuf_tensor("pages", [1, B * PAGES], I32))
        self.rstd = sb("rstd", N)
        self.std = Split(self, "std", KT, MAP["h"], MAP["scr"], KT, MAP["scr"] + 4160, MAP["scr"] + 6208)
        self.sq = self.cut(8256, KT, N)
        self.tmp = self.cut(12416, 2, N)
        hid = MAP["o"] + 2 * FT * N
        self.mlp = Split(self, "mlp", KT, hid, hid + 4160, KT, hid + 8320, hid + 10368)
        self.mlp_tmp = [self.place(f"mlp_tmp{i}", hid + 12416 + i * N, [N], F32) for i in range(3)]
        self.mlp_sq = self.place("mlp_sq", MAP["o"], [KT, N], F32)
        self.mlp_norm = self.place("mlp_norm", MAP["o"] + KT * N, [2, N], F32)
        self.hid = Split(self, "hid", FT, MAP["o"], MAP["o"] + FT * N, SLOT_K, hid, hid + 2 * SLOT_K * P)
        self.eps = self.cst[:, EPS_AT:EPS_AT + 1]
        self.ln_eps = self.cst[:, EPS_AT + 1:EPS_AT + 2]
        self.ps = ctx.enter_context(nc.psum_tensor("ps", [P, 8, 512], F32))

        self.weights_loaded = [self.new_counter(f"weights_loaded{i}") for i in range(SLOTS)]
        self.unit_done = self.new_counter("unit_done")
        self.product_read = [self.new_counter(f"product_read{i}") for i in range(2)]
        self.weights_hi = self.new_counter("weights_hi")
        self.weights_split = self.new_counter("weights_split")
        self.plain_ready = self.new_counter("plain_ready")
        self.hi_ready = self.new_counter("hi_ready")
        self.hidden_hi = self.new_counter("hidden_hi")
        self.hidden_lo = self.new_counter("hidden_lo")
        self.inputs_loaded = [self.new_counter(f"inputs_loaded{i}") for i in range(B)]
        self.stored = self.new_counter("stored")
        self.squares_ready = self.new_counter("squares_ready")
        self.sums_ready = self.new_counter("sums_ready")
        self.scale_ready = self.new_counter("scale_ready")
        self.normed = self.new_counter("normed")
        self.exp_ready = self.new_counter("exp_ready")
        self.scores_ready = self.new_counter("scores_ready")
        self.keys_used = self.new_counter("keys_used")
        self.values_used = self.new_counter("values_used")
        self.values_loaded = [self.new_counter(f"values_loaded{i}") for i in range(B)]
        self.sample_tensor = self.new_counter("sample_tensor")
        self.sample_scalar = self.new_counter("sample_scalar")
        self.sample_vector = self.new_counter("sample_vector")
        self.cache_scaled = self.new_counter("cache_scaled")
        self.cache_summed = self.new_counter("cache_summed")
        self.exponent_ready = self.new_counter("exponent_ready")
        self.weights_ready = self.new_counter("weights_ready")
        self.maxima_ready = self.new_counter("maxima_ready")
        self.tensor_out = self.new_counter("tensor_out")
        self.tensor_out2 = self.new_counter("tensor_out2")
        self.product_kept = self.new_counter("product_kept")
        self.vector_out = self.new_counter("vector_out")
        self.vector_out2 = self.new_counter("vector_out2")
        self.scalar_out = self.new_counter("scalar_out")
        self.scalar_out2 = self.new_counter("scalar_out2")
        self.pool_out = self.new_counter("pool_out")
        self.dve = Engine(nc.vector, self.new_counter("vector_step"))
        self.act = Engine(nc.scalar, self.new_counter("scalar_step"))
        self.pool = Engine(nc.gpsimd, self.new_counter("pool_step"))
        self.ring = 0
        self.stores = 0

    def place(self, name, at, shape, dt):
        return self.nc.alloc_sbuf_tensor_at(name, [P, *shape], dt, offset=self.arena_at + 4 * at)

    def new_counter(self, name):
        s = Signal(self.ctx.enter_context(self.nc.semaphore(name)))
        self.counters.append(s)
        return s

    @contextmanager
    def stage(self):
        for s in self.counters:
            s.base = s.count
        with self.nc.Block() as block:
            yield block

    def const(self, name):
        a = CONST_AT[name]
        return self.cst[:, a:a + P]

    def mask(self, name):
        return self.const(name).bitcast(U32)

    def param(self, name):
        at = 0
        for n, w in self.params[0]:
            if n == name:
                return self.params[1][:, at:at + w]
            at += w
        raise KeyError(name)

    def cut(self, at, *shape):
        n = int(np.prod(shape))
        assert at + n <= SCR, (at, shape)
        flat = self.scr[:, at:at + n]
        if len(shape) == 1:
            return flat
        names = "abcd"[:len(shape)]
        return flat.rearrange(f"p ({' '.join(names)}) -> p {' '.join(names)}", **dict(zip(names, shape)))

    def store(self, eng, out, in_):
        eng.dma_start(out, in_).then_inc(self.stored.sem, 16)
        self.stored.count += 16

    def load_unit(self, sp, lin, j, slot):
        src = lin.src[j] if isinstance(j, int) else lin.src[bass.ds(j, 1)].rearrange("o p n -> p (o n)")
        sp.dma_start(self.w[:, slot, 0:lin.kt * P], src).then_inc(self.weights_loaded[slot].sem, 16)

    def prefetch(self, sp, lin):
        lin.at = self.ring
        for j in range(SLOTS):
            if lin.at + j >= SLOTS:
                sp.wait_ge(self.weights_split.sem, lin.at + j - SLOTS + 1)
            self.load_unit(sp, lin, j, (lin.at + j) % SLOTS)
        self.ring += lin.units

    def stream(self, sp, lin):
        body = lin.units // SLOTS
        if body > 1:
            with sp.Fori(1, body) as i:
                for u in range(SLOTS):
                    sp.wait_ge(self.weights_split.sem, (i - 1) * SLOTS + (lin.at + u + 1))
                    self.load_unit(sp, lin, i * SLOTS + u, (lin.at + u) % SLOTS)
        for j in range(max(SLOTS, body * SLOTS), lin.units):
            sp.wait_ge(self.weights_split.sem, lin.at + j - SLOTS + 1)
            self.load_unit(sp, lin, j, (lin.at + j) % SLOTS)

    def split_unit(self, dve, lin, site, u, i=0):
        nc = self.nc
        slot, n = (lin.at + u) % SLOTS, lin.kt * P
        raw, hi, lo = self.w[:, slot, 0:n], site.w[0][:, u % 2, 0:n], site.w[1][:, u % 2, 0:n]
        dve.wait_ge(self.weights_loaded[slot].sem, 16 * i + 16 * ((lin.at + u) // SLOTS + 1))
        if u >= 2 or not isinstance(i, int):
            dve.wait_ge(self.unit_done.sem, i * SLOTS + (lin.at + u - 1))
        nc.vector.tensor_copy(hi, raw).then_inc(self.weights_hi.sem, 1)
        dve.wait_ge(self.weights_hi.sem, i * SLOTS + (lin.at + u + 1))
        nc.vector.tensor_tensor(lo, raw, hi.bitcast(F32), ALU.subtract).then_inc(self.weights_split.sem, 1)

    def each_unit(self, dve, lin, site, read=None):
        body = (lin.units - 2) // SLOTS
        with dve.Fori(0, body) as i:
            for u in range(SLOTS):
                if read is not None:
                    read(u, i)
                self.split_unit(dve, lin, site, u + 2, i)
        for j in range(body * SLOTS, lin.units):
            if read is not None:
                read(j, 0)
            if j + 2 < lin.units:
                self.split_unit(dve, lin, site, j + 2)

    def product(self, pe, lin, site, spans, per=1):
        nc = self.nc

        def unit(u, i):
            o = u // per
            pe.wait_ge(self.weights_split.sem, i * SLOTS + (lin.at + u + 1))
            if u % per == 0:
                read = self.product_read[o % 2]
                pe.wait_ge(read.sem, read.base + i * (SLOTS // per // 2) + o // 2)
            hi, lo = (t[:, u % 2, 0:lin.kt * P].rearrange("p (k n) -> p k n", k=lin.kt) for t in site.w)
            for k in range(lin.kt):
                x = k + (u % per) * lin.kt
                if u == 0 and per == 1:
                    pe.wait_ge(self.normed.sem, self.normed.at(k + 1))
                passes = ((hi, site.x[0]), (hi, site.x[1]), (lo, site.x[0]))
                for n, (w, v) in enumerate(passes):
                    first, last = u % per == 0 and k == 0 and n == 0, u % per == per - 1 and k == lin.kt - 1 and n == 2
                    for s, (a, b) in enumerate(spans):
                        ins = nc.tensor.matmul(self.ps[:, 2 * (o % 2) + s, 0:b - a], w[:, k, :], v[:, x, a:b],
                                               start=first, stop=last)
            ins.then_inc(self.unit_done.sem, 1)

        body = lin.units // SLOTS
        with pe.Fori(0, body) as i:
            for u in range(SLOTS):
                unit(u, i)
        for j in range(body * SLOTS, lin.units):
            unit(j, 0)

    def read_tile(self, eng, lin, u, i, read, per=1):
        if u % per == per - 1:
            o = u // per
            eng.wait_ge(self.unit_done.sem, i * SLOTS + (lin.at + u + 1))
            read(i * (SLOTS // per) + o, 2 * (o % 2)).then_inc(self.product_read[o % 2].sem, 1)

    def tiles_read(self, lin, per=1):
        for q in range(2):
            self.product_read[q].count += len(range(q, lin.units // per, 2))

    def read_tiles(self, eng, lin, read, per=1):
        body = lin.units // SLOTS
        with eng.Fori(0, body) as i:
            for u in range(SLOTS):
                self.read_tile(eng, lin, u, i, read, per)
        for j in range(body * SLOTS, lin.units):
            self.read_tile(eng, lin, j, 0, read, per)
        self.tiles_read(lin, per)

    def pair(self, bank, rows=P):
        return self.ps[0:rows, bank:bank + 2, 0:HALF]

    def norm_pe(self, pe, sq, spans):
        nc = self.nc
        for k in range(KT):
            pe.wait_ge(self.squares_ready.sem, self.squares_ready.at(k + 1))
            for s, (a, b) in enumerate(spans):
                ins = nc.tensor.matmul(self.ps[:, 6 + s, 0:b - a], self.const("ones"), sq[:, k, a:b],
                                       start=k == 0, stop=k == KT - 1)
        ins.then_inc(self.sums_ready.sem, 1)
        self.sums_ready.count += 1

    def norm_act(self, act, x, site, sq, tmp, width, spans):
        nc = self.nc
        for k in range(KT):
            nc.scalar.activation(sq[:, k, 0:width], x[:, k, 0:width], ACT.Square).then_inc(self.squares_ready.sem, 1)
        self.squares_ready.count += KT
        act.wait_ge(self.sums_ready.sem, self.sums_ready.at(1))
        n = spans[0][1]
        sums = self.ps[:, 6:6 + len(spans), 0:n]
        r = self.rstd[:, 0:width].rearrange("p (s n) -> p s n", n=n)
        self.act.step(nc.scalar.activation(r, sums, ACT.Ln, bias=self.eps, scale=1.0 / D))
        self.act.tell(nc.scalar.activation(self.rstd[:, 0:width], self.rstd[:, 0:width], ACT.Exp, scale=-0.5),
                      self.scale_ready)
        for k in range(KT):
            act.wait_ge(self.plain_ready.sem, self.plain_ready.at(k + 1))
            nc.scalar.activation(site.x[0][:, k, 0:width], tmp[:, k % 2, 0:width], ACT.Copy).then_inc(self.hi_ready.sem, 1)
        self.hi_ready.count += KT

    def norm_dve(self, dve, x, site, tmp, gain, width):
        nc = self.nc
        dve.wait_ge(self.scale_ready.sem, self.scale_ready.at(1))

        def low(k):
            dve.wait_ge(self.hi_ready.sem, self.hi_ready.at(k + 1))
            self.dve.tell(nc.vector.tensor_tensor(site.x[1][:, k, 0:width], tmp[:, k % 2, 0:width],
                                                  site.x[0][:, k, 0:width].bitcast(F32), ALU.subtract), self.normed)

        for k in range(KT):
            self.dve.tell(nc.vector.scalar_tensor_tensor(tmp[:, k % 2, 0:width], x[:, k, 0:width], gain[:, k:k + 1],
                                                         self.rstd[:, 0:width], ALU.mult, ALU.mult), self.plain_ready)
            if k:
                low(k - 1)
        low(KT - 1)

    SPANS = [(0, HALF), (HALF, N)]

    def start(self):
        nc = self.nc
        with self.stage() as block:
            @block.sync
            def _(sp):
                sp.dma_start(self.cst[:], self.d["cst"]).then_inc(self.inputs_loaded[0].sem, 16)
                sp.dma_start(self.x[:], self.d["x"]).then_inc(self.inputs_loaded[0].sem, 16)
                sp.dma_start(self.par0[:], self.d["par0"]).then_inc(self.inputs_loaded[0].sem, 16)
                sp.dma_start(self.par1[:], self.d["par1"]).then_inc(self.inputs_loaded[0].sem, 16)
                sp.dma_start(self.pages[:], self.d["page_table"]).then_inc(self.inputs_loaded[0].sem, 16)
                self.prefetch(sp, self.lin["in0"])
                sp.wait_ge(self.inputs_loaded[0].sem, self.inputs_loaded[0].at(80))
                self.inputs_loaded[0].count += 80

            @block.vector
            def _(dve):
                for read in self.product_read:
                    self.dve.tell(nc.vector.memset(self.rstd[:], 0.0), read)

    def normed_product(self, lin, x, gain, width, spans, following, read, mem=None):
        with self.stage() as block:
            @block.sync
            def _(sp):
                if mem is not None:
                    sp.dma_start(x, mem).then_inc(self.inputs_loaded[0].sem, 16)
                    self.inputs_loaded[0].count += 16
                self.stream(sp, lin)
                self.prefetch(sp, following)

            @block.tensor
            def _(pe):
                self.norm_pe(pe, self.sq, spans)
                self.product(pe, lin, self.std, spans)

            @block.scalar
            def _(act):
                if mem is not None:
                    act.wait_ge(self.inputs_loaded[0].sem, self.inputs_loaded[0].at(16))
                self.norm_act(act, x, self.std, self.sq, self.tmp, width, spans)
                self.read_tiles(act, lin, read)

            @block.vector
            def _(dve):
                for u in range(2):
                    self.split_unit(dve, lin, self.std, u)
                if mem is not None:
                    dve.wait_ge(self.inputs_loaded[0].sem, self.inputs_loaded[0].at(16))
                self.norm_dve(dve, x, self.std, self.tmp, gain, width)
                self.each_unit(dve, lin, self.std)

    def projection(self, lin, gain, following):
        self.normed_product(lin, self.x, self.param(gain), N, self.SPANS, following, lambda o, bank: (
            self.nc.scalar.activation(self.tile_pair(self.c, o), self.pair(bank), ACT.Copy)))

    def tile_pair(self, t, o):
        one = t[:, bass.ds(o, 1), :] if not isinstance(o, int) else t[:, o:o + 1, :]
        return one.rearrange("p o (s n) -> p (o s) n", s=2)

    def residual(self, lin, site, following, per=1, src=None):
        nc = self.nc
        with self.stage() as block:
            @block.sync
            def _(sp):
                self.stream(sp, lin)
                if following is not None:
                    self.prefetch(sp, following)

            @block.tensor
            def _(pe):
                self.product(pe, lin, site, self.SPANS, per)

            @block.scalar
            def _(act):
                if src is not None:
                    for k in range(KT):
                        nc.scalar.activation(site.x[0][:, k], src[:, k], ACT.Copy).then_inc(self.hi_ready.sem, 1)
                    self.hi_ready.count += KT

            @block.vector
            def _(dve):
                for u in range(2):
                    self.split_unit(dve, lin, site, u)
                if src is not None:
                    for k in range(KT):
                        dve.wait_ge(self.hi_ready.sem, self.hi_ready.at(k + 1))
                        self.dve.tell(nc.vector.tensor_tensor(site.x[1][:, k], src[:, k], site.x[0][:, k].bitcast(F32),
                                                              ALU.subtract), self.normed)

                def add(o, bank):
                    return nc.vector.tensor_tensor(self.tile_pair(self.x, o), self.tile_pair(self.x, o), self.pair(bank), ALU.add)
                self.each_unit(dve, lin, site, lambda u, i: self.read_tile(dve, lin, u, i, add, per))
                self.tiles_read(lin, per)

    G_B, G_E, G_Q, G_K, G_P, G_V = 0, 1040, 2064, 4112, 6160, 8208
    G_KT, G_DK, G_S, G_DQ, G_EX = 10256, 11280, 12304, 13328, 13344

    def gla_gates(self):
        nc, c = self.nc, self.c
        z = self.cut(self.G_Q, 2, N)
        e = self.cut(self.G_K, 2, N)
        b = self.cut(self.G_B, 2, N)
        vt = self.cut(self.G_V, NC, T)
        a2 = self.param("gla_a2")
        with self.stage() as block:
            @block.tensor
            def _(pe):
                for j in range(2):
                    for s, (lo, hi) in enumerate(self.SPANS):
                        ins = nc.tensor.matmul(self.ps[:, 2 * j + s, 0:HALF], a2[0:16, j * P:(j + 1) * P],
                                               c[0:16, GLR, lo:hi], start=True, stop=True)
                ins.then_inc(self.tensor_out.sem, 1)
                self.tensor_out.count += 1
                for t in range(NC):
                    for h in range(4):
                        ins = nc.tensor.transpose(self.ps[:, 4 + t, h * P:(h + 1) * P],
                                                  c[:, GV + h, t * P:(t + 1) * P], self.const("ident"))
                ins.then_inc(self.tensor_out2.sem, 1)
                self.tensor_out2.count += 1

            @block.scalar
            def _(act):
                act.wait_ge(self.vector_out.sem, self.vector_out.at(1))
                self.act.step(nc.scalar.activation(e, e, ACT.Exp))
                self.act.tell(nc.scalar.activation(e, e, ACT.Ln, bias=1.0), self.scalar_out)
                act.wait_ge(self.tensor_out2.sem, self.tensor_out2.at(1))
                self.act.step(nc.scalar.activation(vt.rearrange("p a b -> p (a b)"), self.banks(4, 4), ACT.Copy))
                act.wait_ge(self.vector_out.sem, self.vector_out.at(2))
                self.act.step(nc.scalar.activation(self.cut(self.G_DQ, 2, B), b[:, :, T:N], ACT.Exp))

            @block.gpsimd
            def _(pool):
                self.pool.tell(nc.gpsimd.tensor_scalar(c[:, GQ:GQ + 2, :], c[:, GQ:GQ + 2, :], 0.125, None, ALU.mult),
                               self.pool_out)

            @block.vector
            def _(dve):
                dve.wait_ge(self.tensor_out.sem, self.tensor_out.at(1))
                for j in range(2):
                    self.dve.step(nc.vector.tensor_scalar(z[:, j].rearrange("p (s n) -> p s n", s=2), self.pair(2 * j),
                                                          self.param("gla_b")[:, j:j + 1], None, ALU.add))
                self.dve.tell(nc.vector.scalar_tensor_tensor(e, z, -1.0, z, ALU.mult, ALU.min), self.vector_out)
                dve.wait_ge(self.scalar_out.sem, self.scalar_out.at(1))
                self.dve.step(nc.vector.scalar_tensor_tensor(z, z, 0.0, e, ALU.min, ALU.subtract))
                self.dve.step(nc.vector.tensor_scalar(z, z, 1.0 / 16.0, None, ALU.mult))
                scan = self.cst[:, SCAN128_AT:SCAN128_AT + T]
                for j in range(2):
                    self.dve.step(nc.vector.tensor_tensor_scan(b[:, j, 0:T], scan, z[:, j, 0:T], 0.0, ALU.mult, ALU.add))
                self.dve.tell(nc.vector.tensor_copy(b[:, :, T:N], z[:, :, T:N]), self.vector_out)

    def banks(self, at, n):
        return self.ps[:, at:at + n, :].rearrange("p a b -> p (a b)")

    def gla_levels(self):
        nc, c = self.nc, self.c
        b = self.cut(self.G_B, 2, N)[:, :, 0:T]
        diff = self.cut(self.G_E, 2, T)
        q, k = c[:, GQ:GQ + 2, 0:T], c[:, GK:GK + 2, 0:T]
        qs = [self.cut(self.G_Q + i * 1024, 2, T) for i in range(2)]
        ks = [self.cut(self.G_K + i * 1024, 2, T) for i in range(2)]
        expd = self.cut(self.G_DK, 2, T)
        pt = self.cut(self.G_P, 4, T)
        with self.stage() as block:
            @block.scalar
            def _(act):
                for i in range(len(LEVELS)):
                    act.wait_ge(self.vector_out.sem, self.vector_out.at(i + 1))
                    if i:
                        act.wait_ge(self.vector_out2.sem, self.vector_out2.at(i))
                        act.wait_ge(self.pool_out.sem, self.pool_out.at(i))
                    self.act.tell(nc.scalar.activation(expd, diff, ACT.Exp), self.scalar_out)

            @block.gpsimd
            def _(pool):
                for i in range(len(LEVELS)):
                    pool.wait_ge(self.scalar_out.sem, self.scalar_out.at(i + 1))
                    if i >= 2:
                        pool.wait_ge(self.tensor_out.sem, self.tensor_out.at(i - 1))
                    self.pool.tell(nc.gpsimd.tensor_tensor(qs[i % 2], q, expd, ALU.mult), self.pool_out)

            @block.vector
            def _(dve):
                self.dve.step(nc.vector.memset(pt, 0.0))

                def keep(i, name):
                    dve.wait_ge(self.tensor_out.sem, self.tensor_out.at(i + 1))
                    m = self.mask(name).unsqueeze(1).to_broadcast([P, NC, P])
                    for j in range(4):
                        ins = nc.vector.copy_predicated(pt[:, j].rearrange("p (c t) -> p c t", c=NC), m,
                                                        self.ps[:, 4 * (i % 2) + j, :].rearrange("p (c t) -> p c t", c=NC))
                        if j < 3:
                            self.dve.step(ins)
                        else:
                            self.dve.tell(ins, self.product_kept)

                for i, m in enumerate(LEVELS):
                    if i:
                        dve.wait_ge(self.scalar_out.sem, self.scalar_out.at(i))
                    bv = b.rearrange("p j (g w) -> p j g w", w=2 * m)
                    dv = diff.rearrange("p j (g w) -> p j g w", w=2 * m)
                    for j in range(2):
                        ref = bv[:, j, :, m - 1:m].to_broadcast([P, T // (2 * m), 2 * m])
                        self.dve.step(nc.vector.tensor_tensor(dv[:, j], bv[:, j], ref, ALU.subtract))
                    self.dve.tell(nc.vector.scalar_tensor_tensor(diff, diff, -1.0, diff, ALU.mult, ALU.min),
                                  self.vector_out)
                    dve.wait_ge(self.scalar_out.sem, self.scalar_out.at(i + 1))
                    if i >= 2:
                        dve.wait_ge(self.tensor_out.sem, self.tensor_out.at(i - 1))
                    self.dve.tell(nc.vector.tensor_tensor(ks[i % 2], k, expd, ALU.mult), self.vector_out2)
                    if i:
                        keep(i - 1, f"level{LEVELS[i - 1]}")
                keep(len(LEVELS) - 1, "level1")
                keep(len(LEVELS), "ident")

            @block.tensor
            def _(pe):
                for i in range(len(LEVELS) + 1):
                    if i < len(LEVELS):
                        pe.wait_ge(self.pool_out.sem, self.pool_out.at(i + 1))
                        pe.wait_ge(self.vector_out2.sem, self.vector_out2.at(i + 1))
                    if i >= 2:
                        pe.wait_ge(self.product_kept.sem, self.product_kept.at(i - 1))
                    lq, lk = (qs[i % 2], ks[i % 2]) if i < len(LEVELS) else (q, k)
                    for par in range(2):
                        rows = slice(64 * par, 64 * par + 64)
                        for hp in range(2):
                            for t in range(NC):
                                cols = slice(t * P, (t + 1) * P)
                                ins = nc.tensor.matmul(self.ps[:, 4 * (i % 2) + 2 * par + hp, cols], lk[rows, hp, cols],
                                                       lq[rows, hp, cols], start=True, stop=True)
                    ins.then_inc(self.tensor_out.sem, 1)
                    self.tensor_out.count += 1

    def gla_states(self):
        nc, c = self.nc, self.c
        b = self.cut(self.G_B, 2, N)[:, :, 0:T]
        pt = self.cut(self.G_P, 4, T)
        vt = self.cut(self.G_V, NC, 4, P)
        qe = self.cut(self.G_Q, 2, T)
        ke = self.cut(self.G_K, 2, T)
        ex = self.cut(self.G_Q + 1024, 2, T)
        diff = self.cut(self.G_E, 2, T)
        kt = self.cut(self.G_KT, NC, 2 * P)
        st = self.cut(self.G_K + 1024, NC, 2 * P)
        dlast = self.cut(self.G_EX, 2, NC)
        fs = self.cut(self.G_DQ, 2, B)
        ss = self.h[:].rearrange("p a b -> p (a b)")[:, 0:2048].rearrange("p (b j e) -> p b j e", b=B, j=2)
        kv = self.h[:].rearrange("p a b -> p (a b)")[:, 2048:4096].rearrange("p (b j e) -> p b j e", b=B, j=2)
        vs = self.cut(self.G_EX + 8, 4, P)
        with self.stage() as block:
            @block.sync
            def _(sp):
                sp.dma_start(ss, self.d["state_gla"]).then_inc(self.inputs_loaded[0].sem, 16)
                self.inputs_loaded[0].count += 16
                sp.wait_ge(self.vector_out2.sem, self.vector_out2.at(1))
                self.store(sp, self.d["p_gla"], st[:, NC - 1])
                sp.wait_ge(self.pool_out.sem, self.pool_out.at(3))
                self.store(sp, self.d["s_gla"], ss)
                sp.wait_ge(self.stored.sem, self.stored.count)

            @block.scalar
            def _(act):
                self.act.tell(nc.scalar.activation(ex, b, ACT.Exp), self.scalar_out)
                act.wait_ge(self.vector_out.sem, self.vector_out.at(1))
                self.act.tell(nc.scalar.activation(diff, diff, ACT.Exp), self.scalar_out)
                last = b.rearrange("p j (c w) -> p j c w", c=NC)[:, :, :, P - 1]
                self.act.tell(nc.scalar.activation(dlast, last, ACT.Exp), self.scalar_out)
                act.wait_ge(self.tensor_out.sem, self.tensor_out.at(1))
                self.act.tell(nc.scalar.activation(vs[0:B].rearrange("p a b -> p (a b)"), self.ps[0:B, 4, :], ACT.Copy),
                              self.scalar_out)
                act.wait_ge(self.tensor_out.sem, self.tensor_out.at(2))
                self.act.tell(nc.scalar.activation(kt.rearrange("p a b -> p (a b)"), self.banks(2, 2), ACT.Copy),
                              self.scalar_out)
                act.wait_ge(self.tensor_out.sem, self.tensor_out.at(5))
                self.act.step(nc.scalar.activation(self.o[:, 0:4, 0:T], self.ps[:, 0:4, :], ACT.Copy))
                act.wait_ge(self.tensor_out.sem, self.tensor_out.at(6))
                for par in range(2):
                    self.act.step(nc.scalar.activation(self.o[:, par:4:2, T:N],
                                  self.ps[:, 4 + par, 0:2 * B].rearrange("p (j b) -> p j b", b=B), ACT.Copy))

            @block.vector
            def _(dve):
                for j in range(2):
                    bj = b[:, j].rearrange("p (c w) -> p c w", c=NC)
                    ref = bj[:, :, P - 1:P].to_broadcast([P, NC, P])
                    ins = nc.vector.tensor_tensor(diff[:, j].rearrange("p (c w) -> p c w", c=NC), ref, bj, ALU.subtract)
                    self.dve.step(ins) if j == 0 else self.dve.tell(ins, self.vector_out)
                dve.wait_ge(self.scalar_out.sem, self.scalar_out.at(2))
                self.dve.tell(nc.vector.tensor_tensor(ke, c[:, GK:GK + 2, 0:T], diff, ALU.mult), self.vector_out)
                self.dve.tell(nc.vector.tensor_tensor(qe, c[:, GQ:GQ + 2, 0:T], ex, ALU.mult), self.vector_out)
                dve.wait_ge(self.tensor_out.sem, self.tensor_out.at(3))
                for b0 in range(0, B, 2):
                    k2 = c[:, GK:GK + 2, T + b0:T + b0 + 2].rearrange("p j b -> p b j").unsqueeze(3)
                    self.dve.tell(nc.vector.tensor_tensor(
                        kv[:, b0:b0 + 2], self.ps[:, 4 + b0 // 2, :].rearrange("p (b j e) -> p b j e", b=2, j=2),
                        k2.to_broadcast([P, 2, 2, P]), ALU.mult), self.vector_out)
                dve.wait_ge(self.tensor_out.sem, self.tensor_out.at(4))
                for t in range(NC):
                    for j in range(2):
                        out, new = st[:, t, j * P:(j + 1) * P], self.ps[:, 2 + t // 2, (t % 2) * 256 + j * P:(t % 2) * 256 + (j + 1) * P]
                        if t == 0:
                            ins = nc.vector.tensor_copy(out, new)
                        else:
                            ins = nc.vector.scalar_tensor_tensor(out, st[:, t - 1, j * P:(j + 1) * P], dlast[:, j, t:t + 1],
                                                                 new, ALU.mult, ALU.add)
                        if t == NC - 1 and j == 1:
                            self.dve.tell(ins, self.vector_out2)
                        else:
                            self.dve.step(ins)

            @block.gpsimd
            def _(pool):
                pool.wait_ge(self.inputs_loaded[0].sem, self.inputs_loaded[0].at(16))
                for j in range(2):
                    f = fs[:, j].unsqueeze(2).to_broadcast([P, B, P])
                    self.pool.tell(nc.gpsimd.tensor_tensor(ss[:, :, j], ss[:, :, j], f, ALU.mult), self.pool_out)
                pool.wait_ge(self.vector_out.sem, self.vector_out.at(7))
                self.pool.tell(nc.gpsimd.tensor_tensor(ss, ss, kv, ALU.add), self.pool_out)

            @block.tensor
            def _(pe):
                for h in range(4):
                    ins = nc.tensor.transpose(self.ps[0:B, 4, h * P:(h + 1) * P], c[:, GV + h, T:N], self.const("ident"))
                ins.then_inc(self.tensor_out.sem, 1)
                pe.wait_ge(self.vector_out.sem, self.vector_out.at(2))
                for t in range(NC):
                    for j in range(2):
                        ins = nc.tensor.transpose(self.ps[:, 2 + t // 2, (t % 2) * 256 + j * P:(t % 2) * 256 + (j + 1) * P],
                                                  ke[:, j, t * P:(t + 1) * P], self.const("ident"))
                ins.then_inc(self.tensor_out.sem, 1)
                pe.wait_ge(self.scalar_out.sem, self.scalar_out.at(4))
                for b0 in range(B):
                    for par in range(2):
                        ins = nc.tensor.matmul(self.ps[64 * par:64 * par + 64, 4 + b0 // 2, (b0 % 2) * 256:(b0 % 2) * 256 + 256],
                                               self.cst[0:B, SEL_AT + b0 * P:SEL_AT + b0 * P + 64],
                                               vs[0:B, par:4:2, :], start=True, stop=True)
                ins.then_inc(self.tensor_out.sem, 1)
                pe.wait_ge(self.scalar_out.sem, self.scalar_out.at(5))
                for t in range(NC):
                    for h in range(4):
                        rows = slice(64 * (h % 2), 64 * (h % 2) + 64)
                        at = (t % 2) * 256 + (h // 2) * P
                        ins = nc.tensor.matmul(self.ps[rows, 2 + t // 2, at:at + P],
                                               kt[:, t, (h // 2) * P + rows.start:(h // 2) * P + rows.stop],
                                               vt[:, t, h], start=True, stop=True)
                ins.then_inc(self.tensor_out.sem, 1)
                pe.wait_ge(self.vector_out.sem, self.vector_out.at(3))
                pe.wait_ge(self.vector_out2.sem, self.vector_out2.at(1))
                for h in range(4):
                    rows = slice(64 * (h % 2), 64 * (h % 2) + 64)
                    for t in range(NC):
                        cols = slice(t * P, (t + 1) * P)
                        out = self.ps[:, h, cols]
                        if t:
                            nc.tensor.matmul(out, st[rows, t - 1, (h // 2) * P:(h // 2 + 1) * P], qe[rows, h // 2, cols],
                                             start=True, stop=False)
                        ins = nc.tensor.matmul(out, vt[:, t, h], pt[:, 2 * (h % 2) + h // 2, cols], start=t == 0, stop=True)
                ins.then_inc(self.tensor_out.sem, 1)
                pe.wait_ge(self.pool_out.sem, self.pool_out.at(3))
                for par in range(2):
                    rows = slice(64 * par, 64 * par + 64)
                    for j in range(2):
                        for b0 in range(B):
                            at = j * B + b0
                            ins = nc.tensor.matmul(self.ps[:, 4 + par, at:at + 1], ss[rows, b0, j],
                                                   c[rows, GQ + j, T + b0:T + b0 + 1], start=True, stop=True)
                ins.then_inc(self.tensor_out.sem, 1)
                self.tensor_out.count += 6

    def gated_norm(self, n, gate, gain):
        nc, c = self.nc, self.c
        o = self.o[:, n:n + 4, :]
        sq, sg = self.cut(0, 4, N), self.cut(4 * N, 4, N)
        r = self.cut(8 * N, 4, N)
        with self.stage() as block:
            @block.scalar
            def _(act):
                for h in range(4):
                    self.act.tell(nc.scalar.activation(sq[:, h], o[:, h], ACT.Square), self.squares_ready)
                self.act.tell(nc.scalar.activation(sg, c[:, gate:gate + 4, :], ACT.Sigmoid), self.scalar_out)
                act.wait_ge(self.tensor_out.sem, self.tensor_out.at(1))
                self.act.step(nc.scalar.activation(r.rearrange("p h (s n) -> p (h s) n", s=2), self.ps[:, 0:8, 0:HALF],
                                                   ACT.Ln, bias=self.eps, scale=1.0 / P))
                self.act.tell(nc.scalar.activation(r, r, ACT.Exp, scale=-0.5), self.scalar_out)

            @block.tensor
            def _(pe):
                for h in range(4):
                    pe.wait_ge(self.squares_ready.sem, self.squares_ready.at(h + 1))
                    for s, (lo, hi) in enumerate(self.SPANS):
                        ins = nc.tensor.matmul(self.ps[:, 2 * h + s, 0:HALF], self.const("ones"), sq[:, h, lo:hi],
                                               start=True, stop=True)
                ins.then_inc(self.tensor_out.sem, 1)
                self.tensor_out.count += 1

            @block.vector
            def _(dve):
                dve.wait_ge(self.scalar_out.sem, self.scalar_out.at(1))
                self.dve.step(nc.vector.tensor_tensor(sg, sg, c[:, gate:gate + 4, :], ALU.mult))
                self.dve.step(nc.vector.scalar_tensor_tensor(sg, sg, self.param(gain)[:, 0:1], o, ALU.mult, ALU.mult))
                dve.wait_ge(self.scalar_out.sem, self.scalar_out.at(2))
                self.dve.step(nc.vector.tensor_tensor(o, sg, r, ALU.mult))

    W_KK, W_A, W_B, W_C, W_BON, W_DL, W_DS, W_1KA, W_FREE = 0, 2080, 4160, 6240, 8320, 10400, 10432, 10464, 10468
    C_G, C_A, C_W = 0, 4, 8
    OUT = 4

    def token_shift(self):
        nc, c = self.nc, self.c
        d = self.cut(0, R_TILES, N)
        sh = self.cut(R_TILES * N, R_TILES, B)
        last = self.cut(R_TILES * (N + B), R_TILES, B + 1)
        r = c[:, R0:R0 + R_TILES, :]
        with self.stage() as block:
            @block.sync
            def _(sp):
                sp.dma_start(sh, self.d["state_shift"]).then_inc(self.inputs_loaded[0].sem, 16)
                self.inputs_loaded[0].count += 16
                sp.wait_ge(self.scalar_out.sem, self.scalar_out.at(1))
                self.store(sp, self.d["shift"], last)
                sp.wait_ge(self.stored.sem, self.stored.count)

            @block.scalar
            def _(act):
                self.act.tell(nc.scalar.activation(last, r[:, :, T - 1:N], ACT.Copy), self.scalar_out)

            @block.gpsimd
            def _(pool):
                self.pool.step(nc.gpsimd.tensor_tensor(d[:, 7:, 1:T], r[:, 7:, 0:T - 1], r[:, 7:, 1:T], ALU.subtract))
                self.pool.tell(nc.gpsimd.tensor_scalar(d[:, :, 0:1], r[:, :, 0:1], -1.0, None, ALU.mult), self.pool_out)

            @block.vector
            def _(dve):
                self.dve.step(nc.vector.tensor_tensor(d[:, 0:7, 1:T], r[:, 0:7, 0:T - 1], r[:, 0:7, 1:T], ALU.subtract))
                dve.wait_ge(self.inputs_loaded[0].sem, self.inputs_loaded[0].at(16))
                self.dve.step(nc.vector.tensor_tensor(d[:, :, T:N], sh, r[:, :, T:N], ALU.subtract))
                dve.wait_ge(self.scalar_out.sem, self.scalar_out.at(1))
                dve.wait_ge(self.pool_out.sem, self.pool_out.at(1))
                for j in range(R_TILES):
                    self.dve.step(nc.vector.scalar_tensor_tensor(r[:, j], d[:, j], self.param("mu")[:, j:j + 1], r[:, j],
                                                                 ALU.mult, ALU.add))

    def rwkv_low_rank(self):
        nc, c = self.nc, self.c
        wa2, g2 = self.param("wa2"), self.param("g2")
        with self.stage() as block:
            @block.scalar
            def _(act):
                self.act.step(nc.scalar.activation(c[0:64, RWA], c[0:64, RWA], ACT.Tanh))
                self.act.tell(nc.scalar.activation(c[:, RG], c[:, RG], ACT.Sigmoid), self.scalar_out)
                for n in range(8):
                    act.wait_ge(self.tensor_out.sem, self.tensor_out.at(n + 1))
                    at, bias = (self.C_W, "w0") if n < 4 else (self.C_A, "a0")
                    j = n % 4
                    nc.scalar.activation(self.tile_pair(c, at + j), self.pair(2 * (n % 4)), ACT.Sigmoid,
                                         bias=self.param(bias)[:, j:j + 1]).then_inc(self.scalar_out.sem, 1)
                self.scalar_out.count += 8

            @block.vector
            def _(dve):
                for j in range(4):
                    dve.wait_ge(self.scalar_out.sem, self.scalar_out.at(2 + j))
                    nc.vector.tensor_scalar(c[:, self.C_W + j], c[:, self.C_W + j], -float(np.exp(-0.5)), None, ALU.mult)
                for j in range(4):
                    dve.wait_ge(self.tensor_out.sem, self.tensor_out.at(9 + j))
                    self.dve.step(nc.vector.tensor_copy(self.tile_pair(c, self.C_G + j), self.pair(2 * j)))

            @block.tensor
            def _(pe):
                pe.wait_ge(self.scalar_out.sem, self.scalar_out.at(1))
                for n in range(12):
                    if n >= 4:
                        pe.wait_ge(self.scalar_out.sem, self.scalar_out.at(n - 2))
                    rows = (slice(0, 64), slice(64, P), slice(0, P))[n // 4]
                    w, src = (g2, RG) if n >= 8 else (wa2, RWA)
                    for s, (lo, hi) in enumerate(self.SPANS):
                        ins = nc.tensor.matmul(self.ps[:, 2 * (n % 4) + s, 0:HALF], w[rows, (n % 4) * P:(n % 4 + 1) * P],
                                               c[rows, src, lo:hi], start=True, stop=True)
                    ins.then_inc(self.tensor_out.sem, 1)
                self.tensor_out.count += 12

    def eight(self, t):
        return t.rearrange("p a (s n) -> p (a s) n", s=2)

    def head_sums(self, pe, src, ready, k):
        nc = self.nc
        pe.wait_ge(ready.sem, ready.at(k))
        for j in range(4):
            for s, (lo, hi) in enumerate(self.SPANS):
                ins = nc.tensor.matmul(self.ps[:, 2 * j + s, 0:HALF], self.const("head_ones"), src[:, j, lo:hi],
                                       start=True, stop=True)
        ins.then_inc(self.tensor_out.sem, 1)
        self.tensor_out.count += 1

    def rwkv_vectors(self):
        nc, c = self.nc, self.c
        kk, wa, wb, wc, bon = (self.cut(x, 4, N) for x in (self.W_KK, self.W_A, self.W_B, self.W_C, self.W_BON))
        one_ka = self.cut(self.W_1KA, 4)
        dl, ds = self.cut(self.W_DL, 4, 8), self.cut(self.W_DS, 4, B)
        r, k, v = c[:, RR:RR + 4], c[:, RK:RK + 4], c[:, RV:RV + 4]
        a, lw = c[:, self.C_A:self.C_A + 4], c[:, self.C_W:self.C_W + 4]
        banks = self.ps[:, :, 0:HALF]
        with self.stage() as block:
            @block.vector
            def _(dve):
                for j in range(4):
                    ins = nc.vector.tensor_scalar(kk[:, j], k[:, j], self.param("k_k")[:, j:j + 1], None, ALU.mult)
                    self.dve.step(ins) if j < 3 else self.dve.tell(ins, self.vector_out)
                self.dve.step(nc.vector.tensor_scalar(one_ka, self.param("k_a"), -1.0, 1.0, ALU.mult, ALU.add))
                for j in range(4):
                    self.dve.step(nc.vector.tensor_scalar(wb[:, j], a[:, j], self.param("k_a")[:, j:j + 1],
                                                          one_ka[:, j:j + 1], ALU.mult, ALU.add))
                self.dve.step(nc.vector.tensor_tensor(k, k, wb, ALU.mult))
                for j in range(4):
                    ins = nc.vector.scalar_tensor_tensor(wc[:, j], r[:, j], self.param("r_k")[:, j:j + 1], k[:, j],
                                                         ALU.mult, ALU.mult)
                    self.dve.step(ins) if j < 3 else self.dve.tell(ins, self.vector_out)
                dve.wait_ge(self.scalar_out.sem, self.scalar_out.at(2))
                self.dve.step(nc.vector.tensor_tensor(kk, kk, wa, ALU.mult))
                self.dve.step(nc.vector.tensor_tensor(a, a, kk, ALU.mult))
                cw = wa[:, :, 0:T]
                scan = self.cst[:, SCAN64_AT:SCAN64_AT + T]
                for j in range(4):
                    self.dve.step(nc.vector.tensor_tensor_scan(cw[:, j], scan, lw[:, j, 0:T], 0.0, ALU.mult, ALU.add))
                self.dve.tell(nc.vector.tensor_tensor(lw[:, :, 0:T], cw, lw[:, :, 0:T], ALU.subtract), self.vector_out)
                dve.wait_ge(self.tensor_out.sem, self.tensor_out.at(2))
                self.dve.step(nc.vector.tensor_tensor(self.eight(bon), banks, self.eight(v), ALU.mult))
                p = slice(0, T)
                dve.wait_ge(self.scalar_out.sem, self.scalar_out.at(3))
                self.dve.step(nc.vector.tensor_tensor(r[:, :, p], r[:, :, p], wb[:, :, p], ALU.mult))
                dve.wait_ge(self.scalar_out.sem, self.scalar_out.at(4))
                self.dve.step(nc.vector.tensor_tensor(a[:, :, p], a[:, :, p], wc[:, :, p], ALU.mult))
                self.dve.step(nc.vector.tensor_tensor(k[:, :, p], k[:, :, p], wc[:, :, p], ALU.mult))
                dve.wait_ge(self.scalar_out.sem, self.scalar_out.at(5))
                self.dve.step(nc.vector.scalar_tensor_tensor(kk[:, :, p], kk[:, :, p], -1.0, lw[:, :, p],
                                                             ALU.mult, ALU.mult))

            @block.scalar
            def _(act):
                act.wait_ge(self.vector_out.sem, self.vector_out.at(1))
                self.act.tell(nc.scalar.activation(wa, kk, ACT.Square), self.scalar_out)
                act.wait_ge(self.tensor_out.sem, self.tensor_out.at(1))
                self.act.step(nc.scalar.activation(self.eight(wa), banks, ACT.Ln, bias=self.eps))
                self.act.tell(nc.scalar.activation(wa, wa, ACT.Exp, scale=-0.5), self.scalar_out)
                act.wait_ge(self.vector_out.sem, self.vector_out.at(3))
                self.act.tell(nc.scalar.activation(wb[:, :, 0:T], wa[:, :, 0:T], ACT.Exp), self.scalar_out)
                act.wait_ge(self.tensor_out.sem, self.tensor_out.at(2))
                self.act.tell(nc.scalar.activation(wc[:, :, 0:T], wa[:, :, 0:T], ACT.Exp, scale=-1.0), self.scalar_out)
                self.act.tell(nc.scalar.activation(lw, lw, ACT.Exp), self.scalar_out)
                last = wa[:, :, 0:T].rearrange("p j (c w) -> p j c w", w=64)[:, :, :, 63]
                self.act.step(nc.scalar.activation(dl, last, ACT.Exp))

            @block.tensor
            def _(pe):
                self.head_sums(pe, wa, self.scalar_out, 1)
                pe.wait_ge(self.scalar_out.sem, self.scalar_out.at(2))
                self.head_sums(pe, wc, self.vector_out, 2)

    def rwkv_sample(self):
        nc, c = self.nc, self.c
        kk = self.cut(self.W_KK, 4, N)
        hf = self.h[:].rearrange("p a b -> p (a b)")
        ss, pr = (hf[:, x:x + 2048].rearrange("p (b j i) -> p b j i", b=B, j=4) for x in (0, 2048))
        t2 = self.cut(self.W_A, B, 4, 64)
        vs = self.cut(self.W_FREE, 4, P)

        def by_seq(t, lo=0):
            return t[:, :, T:N].rearrange("p j b -> p b j").unsqueeze(3).to_broadcast([P, B, 4, 64])

        with self.stage() as block:
            @block.sync
            def _(sp):
                sp.dma_start(ss, self.d["state_rwkv"]).then_inc(self.inputs_loaded[0].sem, 16)
                self.inputs_loaded[0].count += 16
                sp.wait_ge(self.pool_out.sem, self.pool_out.at(2))
                self.store(sp, self.d["s_rwkv"], ss)
                sp.wait_ge(self.stored.sem, self.stored.count)

            @block.tensor
            def _(pe):
                for j in range(4):
                    ins = nc.tensor.transpose(self.ps[0:B, 4, j * P:(j + 1) * P], c[:, RV + j, T:N], self.const("ident"))
                ins.then_inc(self.tensor_out.sem, 1)
                pe.wait_ge(self.vector_out.sem, self.vector_out.at(1))
                flat = pr.rearrange("p b j i -> p (b j i)")
                for n in range(4):
                    ins = nc.tensor.matmul(self.ps[:, n, :], self.const("head_ones"), flat[:, n * 512:(n + 1) * 512],
                                           start=True, stop=True)
                ins.then_inc(self.tensor_out.sem, 1)
                pe.wait_ge(self.scalar_out.sem, self.scalar_out.at(1))
                vh = vs[0:B].rearrange("p j (q i) -> p j q i", q=2)
                for b0 in range(B):
                    for par in range(2):
                        ins = nc.tensor.matmul(self.ps[64 * par:64 * par + 64, 4 + b0 // 2, (b0 % 2) * 256:(b0 % 2) * 256 + 256],
                                               self.cst[0:B, SEL_AT + b0 * P:SEL_AT + b0 * P + 64], vh[:, :, par, :],
                                               start=True, stop=True)
                ins.then_inc(self.tensor_out.sem, 1)
                pe.wait_ge(self.pool_out.sem, self.pool_out.at(2))
                for par in range(2):
                    rows = slice(64 * par, 64 * par + 64)
                    for j in range(4):
                        for b0 in range(B):
                            at = j * B + b0
                            ins = nc.tensor.matmul(self.ps[rows, par, at:at + 1], ss[rows, b0, j], c[rows, RR + j, T + b0:T + b0 + 1],
                                                   start=True, stop=True)
                ins.then_inc(self.tensor_out.sem, 1)
                self.tensor_out.count += 4

            @block.scalar
            def _(act):
                act.wait_ge(self.tensor_out.sem, self.tensor_out.at(1))
                self.act.tell(nc.scalar.activation(vs[0:B].rearrange("p a b -> p (a b)"), self.ps[0:B, 4, :], ACT.Copy),
                              self.scalar_out)
                act.wait_ge(self.tensor_out.sem, self.tensor_out.at(4))
                for par in range(2):
                    rows = slice(64 * par, 64 * par + 64)
                    self.act.step(nc.scalar.activation(self.o[rows, self.OUT:self.OUT + 4, T:N],
                                  self.ps[rows, par, 0:4 * B].rearrange("p (j b) -> p j b", b=B), ACT.Copy))

            @block.gpsimd
            def _(pool):
                pool.wait_ge(self.vector_out.sem, self.vector_out.at(1))
                self.pool.step(nc.gpsimd.tensor_tensor(ss, ss, by_seq(c[:, self.C_W:self.C_W + 4]), ALU.mult))
                pool.wait_ge(self.vector_out.sem, self.vector_out.at(2))
                self.pool.tell(nc.gpsimd.tensor_tensor(ss, ss, pr, ALU.subtract), self.pool_out)
                pool.wait_ge(self.vector_out.sem, self.vector_out.at(3))
                self.pool.tell(nc.gpsimd.tensor_tensor(ss, ss, t2, ALU.add), self.pool_out)

            @block.vector
            def _(dve):
                dve.wait_ge(self.inputs_loaded[0].sem, self.inputs_loaded[0].at(16))
                self.dve.tell(nc.vector.tensor_tensor(pr, ss, by_seq(kk), ALU.mult), self.vector_out)
                dve.wait_ge(self.tensor_out.sem, self.tensor_out.at(2))
                self.dve.tell(nc.vector.tensor_tensor(pr, self.banks(0, 4).rearrange("p (b j i) -> p b j i", b=B, j=4),
                                                      by_seq(c[:, self.C_A:self.C_A + 4]), ALU.mult), self.vector_out)
                dve.wait_ge(self.tensor_out.sem, self.tensor_out.at(3))
                self.dve.tell(nc.vector.tensor_tensor(t2, self.banks(4, 4).rearrange("p (b j i) -> p b j i", b=B, j=4),
                                                      by_seq(c[:, RK:RK + 4]), ALU.mult), self.vector_out)

    def unit_inverses(self, groups, streams, masks, lt_at, t_at, x_at, inv, fill):
        nc = self.nc
        lt, tt, xx = ([self.cut(at + 1024 * i, 8, P) for i in range(streams)] for at in (lt_at, t_at, x_at))
        factor, levels = masks
        ident = self.const("ident").unsqueeze(1)

        def bank(i):
            return self.ps[:, 4 * i:4 * i + 2, :], self.ps[:, 4 * i + 2:4 * i + 4, :]

        def eight(a):
            return a.rearrange("p a (b t) -> p (a b) t", t=P)

        n_level = len(levels)
        with self.stage() as block:
            @block.tensor
            def _(pe):
                made = copied = masked = 0
                for g0 in range(0, groups, streams):
                    for i in range(streams):
                        if g0:
                            pe.wait_ge(self.vector_out.sem, self.vector_out.at((g0 // streams) * streams * (n_level + 1) - streams + i + 1))
                        fill(pe, g0 + i, 4 * i + 2)
                        self.tensor_out.count += 1
                    for n in range(n_level):
                        base_v = (g0 // streams) * streams * (n_level + 1)
                        base_s = (g0 // streams) * streams * (2 * n_level - 2)
                        if n:
                            for i in range(streams):
                                pe.wait_ge(self.scalar_out.sem, self.scalar_out.at(base_s + (2 * n - 2) * streams + i + 1))
                                for h in range(8):
                                    ins = nc.tensor.matmul(self.ps[:, 4 * i + h // 4, (h % 4) * P:(h % 4 + 1) * P], lt[i][:, h],
                                                           tt[i][:, h], start=True, stop=True)
                                ins.then_inc(self.tensor_out.sem, 1)
                                self.tensor_out.count += 1
                            for i in range(streams):
                                pe.wait_ge(self.scalar_out.sem, self.scalar_out.at(base_s + (2 * n - 1) * streams + i + 1))
                                for h in range(8):
                                    ins = nc.tensor.matmul(self.ps[:, 4 * i + 2 + h // 4, (h % 4) * P:(h % 4 + 1) * P], xx[i][:, h],
                                                           inv[g0 + i][:, h], start=True, stop=True)
                                ins.then_inc(self.tensor_out.sem, 1)
                                self.tensor_out.count += 1
                        if n < n_level - 1:
                            for i in range(streams):
                                pe.wait_ge(self.vector_out.sem, self.vector_out.at(base_v + (n + 1) * streams + i + 1))
                                for h in range(8):
                                    ins = nc.tensor.transpose(self.ps[:, 4 * i + h // 4, (h % 4) * P:(h % 4 + 1) * P],
                                                              inv[g0 + i][:, h], self.const("ident"))
                                ins.then_inc(self.tensor_out.sem, 1)
                                self.tensor_out.count += 1

            per = 3 * n_level - 2

            def product_at(g0, k, i):
                return self.tensor_out.at((g0 // streams) * streams * per + k * streams + i + 1)

            @block.scalar
            def _(act):
                for g0 in range(0, groups, streams):
                    for n in range(n_level):
                        if n:
                            for i in range(streams):
                                act.wait_ge(self.tensor_out.sem, product_at(g0, 3 * n - 1, i))
                                self.act.tell(nc.scalar.activation(xx[i], eight(bank(i)[0]), ACT.Copy), self.scalar_out)
                        if n < n_level - 1:
                            for i in range(streams):
                                act.wait_ge(self.tensor_out.sem, product_at(g0, 3 * n + 1, i))
                                self.act.tell(nc.scalar.activation(tt[i], eight(bank(i)[0]), ACT.Copy), self.scalar_out)

            @block.vector
            def _(dve):
                for g0 in range(0, groups, streams):
                    for i in range(streams):
                        dve.wait_ge(self.tensor_out.sem, product_at(g0, 0, i))
                        self.dve.tell(nc.vector.tensor_tensor(lt[i], eight(bank(i)[1]), factor(g0 + i), ALU.mult),
                                      self.vector_out)
                    for n, level in enumerate(levels):
                        m = self.const(level).unsqueeze(1).to_broadcast([P, 8, P])
                        for i in range(streams):
                            if n == 0:
                                self.dve.step(nc.vector.tensor_tensor(inv[g0 + i], lt[i], m, ALU.mult))
                                self.dve.tell(nc.vector.tensor_tensor(inv[g0 + i], inv[g0 + i], ident.to_broadcast([P, 8, P]),
                                                                      ALU.add), self.vector_out)
                            else:
                                dve.wait_ge(self.tensor_out.sem, product_at(g0, 3 * n, i))
                                self.dve.tell(nc.vector.copy_predicated(
                                    inv[g0 + i], self.mask(level).unsqueeze(1).to_broadcast([P, 8, P]), eight(bank(i)[1])),
                                    self.vector_out)

    def head_slot(self, h):
        return slice(64 * (h // 4), 64 * (h // 4) + 64), h % 4

    def rwkv_inverses(self):
        nc, c = self.nc, self.c
        a, bb = self.cut(self.W_KK, 4, N), c[:, self.C_A:self.C_A + 4]

        def fill(pe, g, bank):
            cols = slice(g * P, (g + 1) * P)
            for h in range(8):
                rows, j = self.head_slot(h)
                ins = nc.tensor.matmul(self.ps[:, bank + h // 4, j * P:(j + 1) * P], bb[rows, j, cols], a[rows, j, cols],
                                       start=True, stop=True)
            ins.then_inc(self.tensor_out.sem, 1)

        hf = self.h[:].rearrange("p a b -> p (a b)")
        self.inv = [hf[:, g * 1024:(g + 1) * 1024].rearrange("p (h t) -> p h t", h=8) for g in range(NC)]
        before = self.const("before64").unsqueeze(1).to_broadcast([P, 8, P])
        self.unit_inverses(NC, 2, (lambda g: before, [f"level{m}" for m in LEVELS[:0:-1]]), self.W_A, self.W_A + 2048,
                           self.W_A + 4096, self.inv, fill)

    def rwkv_chain(self):
        nc, c = self.nc, self.c
        A = self.cut(self.W_KK, 4, N)
        Bv, K, R = c[:, self.C_A:self.C_A + 4], c[:, RK:RK + 4], c[:, RR:RR + 4]
        low, high = self.flat(self.C_W), self.flat(RWA)
        eight = lambda t: t.rearrange("p (h t) -> p h t", h=8)
        ak, rb, rk = ([self.cut(self.W_A + 1024 * i, 8, P), eight(odd)] for i, odd in enumerate(
            (low[:, 0:1024], low[:, 1024:2048], high[:, 0:1024])))
        tok = [self.cut(self.W_A + 3072, 1536), high[:, 1024:2560]]
        vt, bt, kt = ([t[:, 512 * i:512 * (i + 1)].rearrange("p (j q f) -> p j q f", j=4, q=2) for t in tok] for i in range(3))
        p1, sa = (self.cut(self.W_A + 4608 + 512 * i, 8, 64) for i in range(2))
        st = self.cut(self.W_FREE, 9, 4, 64)
        dl = self.cut(self.W_DL, 4, 8)
        with self.stage() as block:
            @block.sync
            def _(sp):
                sp.wait_ge(self.vector_out2.sem, self.vector_out2.at(8))
                self.store(sp, self.d["p_rwkv"], st[:, 8].rearrange("p a b -> p (a b)"))
                sp.wait_ge(self.stored.sem, self.stored.count)

            @block.tensor
            def _(pe):
                def transposes(t, n):
                    src, bank = (c[:, RV:RV + 4], Bv, K)[n], 6 + n % 2
                    if n == 2:
                        pe.wait_ge(self.scalar_out2.sem, self.scalar_out2.at(3 * t + 1))
                    elif t:
                        pe.wait_ge(self.vector_out.sem, self.vector_out.at(3 * t))
                    for j in range(4):
                        ins = nc.tensor.transpose(self.ps[:, bank, j * P:(j + 1) * P], src[:, j, t * P:(t + 1) * P],
                                                  self.const("ident"))
                    ins.then_inc(self.tensor_out2.sem, 1)

                def matrix(t, n):
                    cols = slice(t * P, (t + 1) * P)
                    left, right = ((K, A), (Bv, R), (K, R))[n]
                    if n == 0:
                        pe.wait_ge(self.scalar_out2.sem, self.scalar_out2.at(3 * t + 3))
                    else:
                        pe.wait_ge(self.vector_out.sem, self.vector_out.at(3 * t + n))
                    for h in range(8):
                        rows, j = self.head_slot(h)
                        ins = nc.tensor.matmul(self.ps[:, 6 + h // 4, j * P:(j + 1) * P], left[rows, j, cols],
                                               right[rows, j, cols], start=True, stop=True)
                    ins.then_inc(self.tensor_out2.sem, 1)

                def prepare(t, parts):
                    if t < NC:
                        for n in parts:
                            transposes(t, n) if n < 3 else matrix(t, n - 3)

                prepare(0, range(6))
                for t in range(NC):
                    x = t % 2
                    pe.wait_ge(self.vector_out.sem, self.vector_out.at(3 * t + 3))
                    for sub in range(2):
                        n = 2 * t + sub
                        own = slice(64 * sub, 64 * sub + 64)
                        sc = slice(t * P + 64 * sub, t * P + 64 * sub + 64)
                        if n:
                            pe.wait_ge(self.vector_out2.sem, self.vector_out2.at(n))
                        for h in range(8):
                            rows, j = self.head_slot(h)
                            out = self.ps[own, h // 4, j * 64:(j + 1) * 64]
                            nc.tensor.matmul(out, A[rows, j, sc], st[rows, n, j], start=True, stop=False)
                            ins = nc.tensor.matmul(out, ak[x][:, h, own], vt[x][:, j, h // 4], start=False, stop=True)
                        ins.then_inc(self.tensor_out.sem, 1)
                        prepare(t + 1, (4,) if sub else (0, 1))
                        pe.wait_ge(self.scalar_out.sem, self.scalar_out.at(5 * t + 1 + 2 * sub))
                        for h in range(8):
                            ins = nc.tensor.matmul(self.ps[own, 2, h * 64:(h + 1) * 64], self.inv[t][own, h, own], p1[own, h],
                                                   start=True, stop=True)
                        ins.then_inc(self.tensor_out.sem, 1)
                        prepare(t + 1, (5,) if sub else (2,))
                        pe.wait_ge(self.scalar_out.sem, self.scalar_out.at(5 * t + 2 + 2 * sub))
                        for h in range(8):
                            rows, j = self.head_slot(h)
                            out = self.ps[rows, 3, j * 64:(j + 1) * 64]
                            nc.tensor.matmul(out, bt[x][own, j, h // 4], sa[own, h], start=True, stop=False)
                            ins = nc.tensor.matmul(out, kt[x][own, j, h // 4], vt[x][own, j, h // 4], start=False, stop=True)
                        ins.then_inc(self.tensor_out.sem, 1)
                        if sub == 0:
                            prepare(t + 1, (3,))
                    if t:
                        pe.wait_ge(self.scalar_out.sem, self.scalar_out.at(5 * t))
                    for h in range(8):
                        rows, j = self.head_slot(h)
                        out = self.ps[rows, 4 + h // 4, j * P:(j + 1) * P]
                        nc.tensor.matmul(out, vt[x][:, j, h // 4], rk[x][:, h], start=True, stop=False)
                        nc.tensor.matmul(out, sa[:, h], rb[x][:, h], start=False, stop=False)
                        for sub in range(2):
                            half = slice(64 * sub, 64 * sub + 64)
                            sc = slice(t * P + 64 * sub, t * P + 64 * sub + 64)
                            ins = nc.tensor.matmul(out[:, half], st[rows, 2 * t + sub, j], R[rows, j, sc],
                                                   start=False, stop=sub == 1)
                    ins.then_inc(self.tensor_out.sem, 1)
                self.tensor_out.count += NC * 7
                self.tensor_out2.count += NC * 6

            @block.scalar
            def _(act):
                def copy(t, n):
                    if t < NC:
                        act.wait_ge(self.tensor_out2.sem, self.tensor_out2.at(6 * t + n + 1))
                        self.act.tell(nc.scalar.activation(tok[t % 2][:, 512 * n:512 * (n + 1)], self.ps[:, 6 + n % 2, :], ACT.Copy),
                                      self.scalar_out2)

                for n in range(3):
                    copy(0, n)
                for t in range(NC):
                    cols = slice(t * P, (t + 1) * P)
                    for sub in range(2):
                        own = slice(64 * sub, 64 * sub + 64)
                        act.wait_ge(self.tensor_out.sem, self.tensor_out.at(7 * t + 1 + 3 * sub))
                        self.act.tell(nc.scalar.activation(
                            p1[own].rearrange("p (q j) i -> p q (j i)", q=2), self.ps[own, 0:2, 0:256], ACT.Copy),
                            self.scalar_out)
                        if sub == 0:
                            copy(t + 1, 0)
                            copy(t + 1, 1)
                        act.wait_ge(self.tensor_out.sem, self.tensor_out.at(7 * t + 2 + 3 * sub))
                        self.act.tell(nc.scalar.activation(sa[own].rearrange("p h i -> p (h i)"), self.ps[own, 2, :], ACT.Copy),
                                      self.scalar_out)
                        if sub == 0:
                            copy(t + 1, 2)
                    act.wait_ge(self.tensor_out.sem, self.tensor_out.at(7 * t + 7))
                    for q in range(2):
                        rows = slice(64 * q, 64 * q + 64)
                        ins = nc.scalar.activation(self.o[rows, self.OUT:self.OUT + 4, cols],
                                                   self.ps[rows, 4 + q, :].rearrange("p (j t) -> p j t", j=4), ACT.Copy)
                    self.act.tell(ins, self.scalar_out)

            @block.vector
            def _(dve):
                def masked(t, n):
                    if t < NC:
                        out, m = ((ak, "before64"), (rb, "causal64"), (rk, "causal64"))[n]
                        dve.wait_ge(self.tensor_out2.sem, self.tensor_out2.at(6 * t + 4 + n))
                        self.dve.tell(nc.vector.tensor_tensor(
                            out[t % 2], self.ps[:, 6:8, :].rearrange("p a (b t) -> p (a b) t", t=P),
                            self.const(m).unsqueeze(1).to_broadcast([P, 8, P]), ALU.mult), self.vector_out)

                self.dve.step(nc.vector.memset(sa, 0.0))
                self.dve.step(nc.vector.memset(st[:, 0], 0.0))
                for n in range(3):
                    masked(0, n)
                for t in range(NC):
                    for sub in range(2):
                        n = 2 * t + sub
                        if sub:
                            masked(t + 1, 1)
                            masked(t + 1, 2)
                        dve.wait_ge(self.tensor_out.sem, self.tensor_out.at(7 * t + 3 + 3 * sub))
                        new = st[:, n + 1]
                        self.dve.step(nc.vector.tensor_tensor(new, self.ps[:, 3, 0:256].rearrange("p (j i) -> p j i", j=4),
                                                              st[:, n], ALU.add))
                        self.dve.tell(nc.vector.tensor_tensor(new, new, dl[:, :, n:n + 1].to_broadcast([P, 4, 64]), ALU.mult),
                                      self.vector_out2)
                        if sub == 0:
                            masked(t + 1, 0)

    def rwkv_output(self):
        nc, c = self.nc, self.c
        y = self.o[:, self.OUT:self.OUT + 4, :]
        sq, r, bon = self.cut(self.W_A, 4, N), self.cut(self.W_B, 4, N), self.cut(self.W_BON, 4, N)
        banks = self.ps[:, :, 0:HALF]
        with self.stage() as block:
            @block.tensor
            def _(pe):
                self.head_sums(pe, y, self.tensor_out, 0)
                pe.wait_ge(self.vector_out.sem, self.vector_out.at(1))
                self.head_sums(pe, sq, self.scalar_out, 1)

            @block.scalar
            def _(act):
                act.wait_ge(self.vector_out.sem, self.vector_out.at(1))
                self.act.tell(nc.scalar.activation(sq, y, ACT.Square), self.scalar_out)
                act.wait_ge(self.tensor_out.sem, self.tensor_out.at(2))
                self.act.step(nc.scalar.activation(self.eight(r), banks, ACT.Ln, bias=self.ln_eps, scale=1.0 / 64))
                self.act.tell(nc.scalar.activation(r, r, ACT.Exp, scale=-0.5), self.scalar_out)

            @block.vector
            def _(dve):
                dve.wait_ge(self.tensor_out.sem, self.tensor_out.at(1))
                self.dve.tell(nc.vector.scalar_tensor_tensor(self.eight(y), banks, -1.0 / 64, self.eight(y), ALU.mult, ALU.add),
                              self.vector_out)
                dve.wait_ge(self.scalar_out.sem, self.scalar_out.at(2))
                for j in range(4):
                    self.dve.step(nc.vector.scalar_tensor_tensor(y[:, j], y[:, j], self.param("ln_w")[:, j:j + 1], r[:, j],
                                                                 ALU.mult, ALU.mult))
                    self.dve.step(nc.vector.scalar_tensor_tensor(y[:, j], y[:, j], self.param("ln_b")[:, j:j + 1], bon[:, j],
                                                                 ALU.add, ALU.add))
                    self.dve.step(nc.vector.tensor_tensor(y[:, j], y[:, j], c[:, self.C_G + j], ALU.mult))

    X_KV, X_VM, X_Q, X_A = 0, 8, 12, 20

    def flat(self, tile):
        return self.c[:].rearrange("p a b -> p (a b)")[:, tile * N:]

    def memory(self, i, following):
        nc = self.nc
        lin = self.lin[f"xkv{i}"]
        mem = self.o[:].rearrange("p a b -> p (a b)")[:, 0:KT * MEM].rearrange("p (k m) -> p k m", k=KT)
        kv = self.flat(self.X_KV)[:, 0:16 * MEM].rearrange("p (a m) -> p a m", a=16)

        def read(o, bank):
            out = kv[:, o] if isinstance(o, int) else kv[:, bass.ds(o, 1), :].rearrange("p o n -> p (o n)")
            return nc.scalar.activation(out, self.ps[:, bank, 0:MEM], ACT.Copy)
        self.normed_product(lin, mem, self.param("g_mem"), MEM, [(0, MEM)], following, read, self.d["mem"])

        sq, r = self.cut(0, KT, MEM), self.cut(2048, 4, MEM)
        vm = self.flat(self.X_VM)[:, 0:2 * D].rearrange("p (a b) -> p a b", a=2)
        with self.stage() as block:
            @block.scalar
            def _(act):
                self.act.tell(nc.scalar.activation(sq, kv[:, 0:KT], ACT.Square), self.scalar_out)
                act.wait_ge(self.tensor_out.sem, self.tensor_out.at(2))
                self.act.step(nc.scalar.activation(r.rearrange("p a b -> p (a b)"), self.banks(4, 2), ACT.Ln, bias=self.eps,
                                                   scale=1.0 / 256))
                self.act.tell(nc.scalar.activation(r, r, ACT.Exp, scale=-0.5), self.scalar_out)

            @block.tensor
            def _(pe):
                for m in range(2):
                    for j in range(KT):
                        ins = nc.tensor.transpose(self.ps[:, 2 * m + j // 4, (j % 4) * P:(j % 4 + 1) * P],
                                                  kv[:, KT + j, m * P:(m + 1) * P], self.const("ident"))
                ins.then_inc(self.tensor_out.sem, 1)
                pe.wait_ge(self.scalar_out.sem, self.scalar_out.at(1))
                for h in range(4):
                    for j in range(2):
                        ins = nc.tensor.matmul(self.ps[:, 4 + h // 2, (h % 2) * MEM:(h % 2 + 1) * MEM], self.const("ones"),
                                               sq[:, 2 * h + j], start=j == 0, stop=j == 1)
                ins.then_inc(self.tensor_out.sem, 1)
                self.tensor_out.count += 2

            @block.vector
            def _(dve):
                dve.wait_ge(self.tensor_out.sem, self.tensor_out.at(1))
                self.dve.step(nc.vector.tensor_copy(vm.rearrange("p a b -> p (a b)"), self.banks(0, 4)))
                dve.wait_ge(self.scalar_out.sem, self.scalar_out.at(2))
                k4 = kv[:, 0:KT].rearrange("p (h j) m -> p h j m", j=2)
                for j in range(2):
                    self.dve.tell(nc.vector.scalar_tensor_tensor(k4[:, :, j], k4[:, :, j], self.param("xk")[:, j:j + 1], r,
                                                                 ALU.mult, ALU.mult), self.vector_out)

            @block.sync
            def _(sp):
                self.store(sp, self.d[f"p_mv{i}"], kv[:, KT:])
                sp.wait_ge(self.vector_out.sem, self.vector_out.at(2))
                self.store(sp, self.d[f"p_mk{i}"], kv[:, 0:KT])
                sp.wait_ge(self.stored.sem, self.stored.count)

    def query(self, i, following):
        nc = self.nc
        lin = self.lin[f"xq{i}"]
        q = self.c[:, self.X_Q:self.X_Q + KT]
        self.normed_product(lin, self.x, self.param("g_cross"), N, self.SPANS, following, lambda o, bank: (
            nc.scalar.activation(self.tile_pair(q, o), self.pair(bank), ACT.Copy)))

        sq = self.h[:]
        r = self.flat(self.X_A)[:, 0:4 * N].rearrange("p (h n) -> p h n", h=4)
        half = lambda t, x: t[:, (t.shape[1] // 2) * x:(t.shape[1] // 2) * (x + 1)]
        with self.stage() as block:
            @block.sync
            def _(sp):
                for b0 in range(6):
                    self.load_keys(sp, i, b0)

            @block.scalar
            def _(act):
                for x in range(2):
                    act.wait_ge(self.tensor_out.sem, self.tensor_out.at(x + 1))
                    out = half(r, x).rearrange("p a (s n) -> p (a s) n", s=2)
                    self.act.step(nc.scalar.activation(out, self.ps[:, 4 * x:4 * x + 4, 0:HALF], ACT.Ln, bias=self.eps,
                                                       scale=1.0 / 256))
                    self.act.tell(nc.scalar.activation(out, out, ACT.Exp, scale=-0.5), self.scalar_out)

            @block.tensor
            def _(pe):
                for h in range(4):
                    if h % 2 == 0:
                        pe.wait_ge(self.vector_out.sem, self.vector_out.at(h // 2 + 1))
                    for s, (lo, hi) in enumerate(self.SPANS):
                        for j in range(2):
                            ins = nc.tensor.matmul(self.ps[:, 2 * h + s, 0:HALF], self.const("ones"),
                                                   sq[:, 2 * h + j, lo:hi], start=j == 0, stop=j == 1)
                    if h % 2:
                        ins.then_inc(self.tensor_out.sem, 1)
                self.tensor_out.count += 2

            @block.vector
            def _(dve):
                for x in range(2):
                    self.dve.tell(nc.vector.tensor_tensor(half(sq, x), half(q, x), half(q, x), ALU.mult), self.vector_out)
                for x in range(2):
                    dve.wait_ge(self.scalar_out.sem, self.scalar_out.at(x + 1))
                    q4 = half(q, x).rearrange("p (h j) m -> p h j m", j=2)
                    for j in range(2):
                        self.dve.step(nc.vector.scalar_tensor_tensor(q4[:, :, j], q4[:, :, j], self.param("xq")[:, j:j + 1],
                                                                     half(r, x), ALU.mult, ALU.mult))

    def cache_slot(self, b0):
        return self.cut(2048 * b0, 2048) if b0 < 6 else self.h[:].rearrange("p a b -> p (a b)")[:, 2048 * (b0 - 6):2048 * (b0 - 5)]

    def load_keys(self, sp, i, b0):
        sp.dma_start(self.cache_slot(b0).rearrange("p (a m) -> p a m", a=8), self.d[f"mem_k{i}"][b0]).then_inc(
            self.inputs_loaded[b0].sem, 16)

    def attention(self, i):
        nc = self.nc
        q = self.c[:, self.X_Q:self.X_Q + KT]
        kv = self.flat(self.X_KV)[:, 0:16 * MEM].rearrange("p (a m) -> p a m", a=16)
        vm = self.flat(self.X_VM)[:, 0:2 * D].rearrange("p (a b) -> p a b", a=2)
        buf = self.flat(self.X_A)
        pr = [buf[:, x * 1024:(x + 1) * 1024].rearrange("p (t m) -> p t m", t=NC) for x in range(2)]
        pt = [buf[:, (x + 2) * 1024:(x + 3) * 1024].rearrange("p (a t) -> p a t", a=2) for x in range(2)]
        small = self.flat(28)
        top, total = [small[:, 8 * x:8 * x + 4] for x in range(2)], [small[:, 8 * x + 4:8 * x + 8] for x in range(2)]
        weight, row = small[:, 80:144], small[:, 144:400]
        stop, stotal = small[:, 400:401], small[:, 401:402]
        pick = small[:, 402:402 + 63]
        kc = [self.cache_slot(b0).rearrange("p (a m) -> p a m", a=8) for b0 in range(B)]
        vc = [self.cache_slot(b0).rearrange("p (a m) -> p a m", a=2) for b0 in range(B)]
        scale = 1.0 / 16
        HP = 4
        score_bank = (0, 6)

        with self.stage() as block:
            @block.sync
            def _(sp):
                for b0 in (6, 7):
                    self.load_keys(sp, i, b0)
                for b0 in range(B):
                    sp.wait_ge(self.keys_used.sem, self.keys_used.at(b0 + 1))
                    sp.dma_start(vc[b0], self.d[f"mem_v{i}"][b0]).then_inc(self.values_loaded[b0].sem, 16)

            @block.tensor
            def _(pe):
                def scores(h):
                    if h >= 2:
                        pe.wait_ge(self.exp_ready.sem, self.exp_ready.at(h - 1))
                    for t in range(NC):
                        for j in range(2):
                            ins = nc.tensor.matmul(self.ps[:, score_bank[h % 2] + t // 2, (t % 2) * MEM:(t % 2 + 1) * MEM],
                                                   q[:, 2 * h + j, t * P:(t + 1) * P], kv[:, 2 * h + j],
                                                   start=j == 0, stop=j == 1)
                    ins.then_inc(self.scores_ready.sem, 1)

                def sample_sums(b0, bank, terms, k, used):
                    pe.wait_ge(self.cache_summed.sem, self.cache_summed.at(k + 1))
                    for h in range(HP):
                        r = b0 * HP + h
                        ins = nc.tensor.matmul(self.ps[0:32, bank, 0:256], pick[:, 31 - r:63 - r], terms(b0, h),
                                               start=r == 0, stop=r == B * HP - 1)
                    ins.then_inc(used.sem, 1)

                def sample_scores(b0):
                    sample_sums(b0, 4, lambda b, h: kc[b][:, 2 * h], b0, self.keys_used)

                def transposes(h):
                    pe.wait_ge(self.vector_out.sem, self.vector_out.at(h + 1))
                    if h:
                        pe.wait_ge(self.scalar_out.sem, self.scalar_out.at(h))
                    for m in range(2):
                        for t in range(NC):
                            ins = nc.tensor.transpose(self.ps[:, 2 + m, t * P:(t + 1) * P], pr[h % 2][:, t, m * P:(m + 1) * P],
                                                      self.const("ident"))
                    ins.then_inc(self.tensor_out.sem, 1)

                def outputs(h):
                    pe.wait_ge(self.scalar_out.sem, self.scalar_out.at(h + 1))
                    if h:
                        pe.wait_ge(self.vector_out2.sem, self.vector_out2.at(h))
                    for e in range(2):
                        for m in range(2):
                            ins = nc.tensor.matmul(self.ps[:, 4 + e, :], vm[:, m, (2 * h + e) * P:(2 * h + e + 1) * P],
                                                   pt[h % 2][:, m], start=m == 0, stop=m == 1)
                    ins.then_inc(self.tensor_out2.sem, 1)

                scores(0)
                scores(1)
                pe.wait_ge(self.pool_out.sem, self.pool_out.at(1))
                sample_scores(0)
                sample_scores(1)
                transposes(0)
                for b0 in range(2, 5):
                    sample_scores(b0)
                scores(2)
                for b0 in range(5, B):
                    sample_scores(b0)
                transposes(1)
                pe.wait_ge(self.sample_vector.sem, self.sample_vector.at(2))
                for m in range(2):
                    ins = nc.tensor.transpose(self.ps[:, 5, m * 32:(m + 1) * 32], row[0:32, m * P:(m + 1) * P],
                                              self.cst[0:32, CONST_AT["ident"]:CONST_AT["ident"] + 32])
                ins.then_inc(self.sample_tensor.sem, 1)
                pe.wait_ge(self.sample_scalar.sem, self.sample_scalar.at(2))
                outputs(0)
                scores(3)
                transposes(2)
                outputs(1)
                pe.wait_ge(self.exp_ready.sem, self.exp_ready.at(3))
                for b0 in range(B):
                    if b0 == 2:
                        transposes(3)
                    if b0 == 4:
                        outputs(2)
                    if b0 == 6:
                        outputs(3)
                    sample_sums(b0, 0, lambda b, h: vc[b][:, 0, h * 256:(h + 1) * 256], B + b0, self.values_used)
                pe.wait_ge(self.sample_scalar.sem, self.sample_scalar.at(3))
                for j in range(2):
                    ins = nc.tensor.transpose(self.ps[:, 1, j * 32:(j + 1) * 32], row[0:32, j * P:(j + 1) * P],
                                              self.cst[0:32, CONST_AT["ident"]:CONST_AT["ident"] + 32])
                ins.then_inc(self.sample_tensor.sem, 1)
                self.scores_ready.count += HP
                self.keys_used.count += B
                self.values_used.count += B
                self.tensor_out.count += HP
                self.tensor_out2.count += HP
                self.sample_tensor.count += 2
                for b0 in range(B):
                    self.inputs_loaded[b0].count += 16
                    self.values_loaded[b0].count += 16

            @block.scalar
            def _(act):
                def exp(h):
                    p = h % 2
                    act.wait_ge(self.maxima_ready.sem, self.maxima_ready.at(h + 1))
                    if h >= 2:
                        act.wait_ge(self.tensor_out.sem, self.tensor_out.at(h - 1))
                    for t in range(NC):
                        ins = nc.scalar.activation(pr[p][:, t], self.ps[:, score_bank[p] + t // 2, (t % 2) * MEM:(t % 2 + 1) * MEM],
                                                   ACT.Exp, bias=top[p][:, t:t + 1], scale=scale, accum_out=total[p][:, t:t + 1])
                        self.act.step(ins) if t < NC - 1 else self.act.tell(ins, self.exp_ready)

                def transposed(h):
                    act.wait_ge(self.tensor_out.sem, self.tensor_out.at(h + 1))
                    if h >= 2:
                        act.wait_ge(self.tensor_out2.sem, self.tensor_out2.at(h - 1))
                    self.act.tell(nc.scalar.activation(pt[h % 2].rearrange("p a b -> p (a b)"), self.banks(2, 2), ACT.Copy),
                                  self.scalar_out)

                def first_terms(b0, values):
                    own = self.values_loaded[b0] if values else self.inputs_loaded[b0]
                    act.wait_ge(own.sem, own.at(16))
                    for h in range(HP):
                        if values:
                            t, by = vc[b0][:, 0, h * 256:(h + 1) * 256], weight[:, b0 * HP + h:b0 * HP + h + 1]
                        else:
                            t, by = kc[b0][:, 2 * h], q[:, 2 * h, T + b0:T + b0 + 1]
                        ins = nc.scalar.activation(t, t, ACT.Copy, scale=by)
                    ins.then_inc(self.cache_scaled.sem, 1)

                first_terms(0, False)
                first_terms(1, False)
                exp(0)
                first_terms(2, False)
                first_terms(3, False)
                exp(1)
                first_terms(4, False)
                transposed(0)
                for b0 in range(5, B):
                    first_terms(b0, False)
                exp(2)
                transposed(1)
                act.wait_ge(self.sample_vector.sem, self.sample_vector.at(1))
                self.act.tell(nc.scalar.activation(row[0:32], self.ps[0:32, 4, 0:256], ACT.Exp, bias=stop[0:32], scale=scale,
                                                   accum_out=stotal[0:32]), self.sample_scalar)
                act.wait_ge(self.sample_tensor.sem, self.sample_tensor.at(1))
                self.act.tell(nc.scalar.activation(weight, self.ps[:, 5, 0:64], ACT.Copy), self.sample_scalar)
                first_terms(0, True)
                first_terms(1, True)
                exp(3)
                transposed(2)
                first_terms(2, True)
                first_terms(3, True)
                transposed(3)
                for b0 in range(4, B):
                    first_terms(b0, True)
                self.cache_scaled.count += 2 * B
                act.wait_ge(self.values_used.sem, self.values_used.at(B))
                self.act.tell(nc.scalar.activation(row[0:32], self.ps[0:32, 0, 0:256], ACT.Copy), self.sample_scalar)
                act.wait_ge(self.sample_tensor.sem, self.sample_tensor.at(2))
                for j in range(2):
                    ins = nc.scalar.activation(self.o[:, :, T:N].rearrange("p (h j) b -> p j b h", j=2)[:, j],
                                               self.ps[:, 1, j * 32:(j + 1) * 32].rearrange("p (b h) -> p b h", b=B), ACT.Copy)
                self.act.step(ins)

            @block.gpsimd
            def _(pool):
                self.pool.step(nc.gpsimd.memset(pick, 0.0))
                self.pool.tell(nc.gpsimd.memset(pick[:, 31:32], 1.0), self.pool_out)

            @block.vector
            def _(dve):
                def maxima(h):
                    p = h % 2
                    dve.wait_ge(self.scores_ready.sem, self.scores_ready.at(h + 1))
                    self.dve.step(nc.vector.tensor_reduce(
                        top[p], self.banks(score_bank[p], 2).rearrange("p (t m) -> p t m", t=NC), AX.X, ALU.max))
                    self.dve.tell(nc.vector.tensor_scalar(top[p], top[p], -scale, None, ALU.mult), self.maxima_ready)

                def normalised(h):
                    p = h % 2
                    dve.wait_ge(self.exp_ready.sem, self.exp_ready.at(h + 1))
                    self.dve.step(nc.vector.reciprocal(total[p], total[p]))
                    self.dve.tell(nc.vector.tensor_tensor(pr[p], pr[p], total[p].unsqueeze(2).to_broadcast([P, NC, MEM]),
                                                          ALU.mult), self.vector_out)

                def kept(h):
                    dve.wait_ge(self.tensor_out2.sem, self.tensor_out2.at(h + 1))
                    self.dve.tell(nc.vector.tensor_copy(self.o[:, 2 * h:2 * h + 2, 0:T], self.ps[:, 4:6, :]), self.vector_out2)

                def all_terms(b0, values):
                    k = b0 + B * values
                    dve.wait_ge(self.cache_scaled.sem, self.cache_scaled.base + k + 1)
                    for h in range(HP):
                        if values:
                            at = 32 + b0 * HP + h
                            one, two = (vc[b0][:, m, h * 256:(h + 1) * 256] for m in range(2))
                            by = weight[:, at:at + 1]
                        else:
                            one, two, by = kc[b0][:, 2 * h], kc[b0][:, 2 * h + 1], q[:, 2 * h + 1, T + b0:T + b0 + 1]
                        ins = nc.vector.scalar_tensor_tensor(one, two, by, one, ALU.mult, ALU.add)
                    ins.then_inc(self.cache_summed.sem, 1)

                maxima(0)
                all_terms(0, False)
                all_terms(1, False)
                maxima(1)
                normalised(0)
                all_terms(2, False)
                all_terms(3, False)
                all_terms(4, False)
                normalised(1)
                maxima(2)
                for b0 in range(5, B):
                    all_terms(b0, False)
                dve.wait_ge(self.keys_used.sem, self.keys_used.at(B))
                self.dve.step(nc.vector.tensor_reduce(stop[0:32], self.ps[0:32, 4, 0:256], AX.X, ALU.max))
                self.dve.tell(nc.vector.tensor_scalar(stop[0:32], stop[0:32], -scale, None, ALU.mult), self.sample_vector)
                dve.wait_ge(self.sample_scalar.sem, self.sample_scalar.at(1))
                self.dve.step(nc.vector.reciprocal(stotal[0:32], stotal[0:32]))
                self.dve.tell(nc.vector.tensor_scalar(row[0:32], row[0:32], stotal[0:32], None, ALU.mult), self.sample_vector)
                normalised(2)
                kept(0)
                maxima(3)
                all_terms(0, True)
                all_terms(1, True)
                kept(1)
                normalised(3)
                all_terms(2, True)
                all_terms(3, True)
                kept(2)
                all_terms(4, True)
                all_terms(5, True)
                kept(3)
                all_terms(6, True)
                all_terms(7, True)
                self.cache_summed.count += 2 * B

    def gate_up(self, i, following):
        nc = self.nc
        lin, site = self.lin[f"gu{i}"], self.mlp
        silu, prod = self.mlp_tmp[0:2], self.mlp_tmp[2]
        with self.stage() as block:
            @block.sync
            def _(sp):
                self.stream(sp, lin)
                self.prefetch(sp, following)

            @block.tensor
            def _(pe):
                self.norm_pe(pe, self.mlp_sq, self.SPANS)
                self.product(pe, lin, site, self.SPANS)

            @block.scalar
            def _(act):
                self.norm_act(act, self.x, site, self.mlp_sq, self.mlp_norm, N, self.SPANS)
                with act.Fori(0, FT // 2) as it:
                    for u in range(2):
                        act.wait_ge(self.unit_done.sem, it * 4 + (lin.at + 2 * u + 1))
                        act.wait_ge(self.product_read[1].sem, self.product_read[1].base + it * 2 + u - 1)
                        nc.scalar.activation(silu[u][:].rearrange("p (s n) -> p s n", s=2), self.pair(0),
                                             ACT.Silu).then_inc(self.product_read[0].sem, 1)

            @block.vector
            def _(dve):
                for u in range(2):
                    self.split_unit(dve, lin, site, u)
                self.norm_dve(dve, self.x, site, self.mlp_norm, self.param("g_ffn"), N)

                def read(u, i):
                    if u % 2 == 0:
                        return
                    tile, pairs = i * 2 + u // 2, self.product_read[1].base
                    part = [t[:, bass.ds(tile, 1), :].rearrange("p o n -> p (o n)") if not isinstance(tile, int)
                            else t[:, tile] for t in self.hid.x]
                    dve.wait_ge(self.unit_done.sem, i * SLOTS + (lin.at + u + 1))
                    dve.wait_ge(self.product_read[0].sem, self.product_read[0].base + i * 2 + (u // 2 + 1))
                    nc.vector.tensor_tensor(prod[:].rearrange("p (s n) -> p s n", s=2),
                                            silu[u // 2 % 2][:].rearrange("p (s n) -> p s n", s=2), self.pair(2),
                                            ALU.mult).then_inc(self.product_read[1].sem, 1)
                    dve.wait_ge(self.product_read[1].sem, pairs + i * 2 + (u // 2 + 1))
                    nc.vector.tensor_copy(part[0], prod[:]).then_inc(self.hidden_hi.sem, 1)
                    dve.wait_ge(self.hidden_hi.sem, self.hidden_hi.base + i * 2 + (u // 2 + 1))
                    nc.vector.tensor_tensor(part[1], prod[:], part[0].bitcast(F32), ALU.subtract).then_inc(
                        self.hidden_lo.sem, 1)

                self.each_unit(dve, lin, site, read)
                self.tiles_read(lin)
                self.hidden_hi.count += FT
                self.hidden_lo.count += FT

    S_V, S_NZ, S_L = 0, 2048, 4608
    WIDTH = [T - s * P for s in range(NC)]
    START = [sum([T - s * P for s in range(n)]) for n in range(NC)]
    TRI = sum([T - s * P for s in range(NC)])

    def stick_norms(self):
        nc, c = self.nc, self.c
        q, k, v = c[:, SQ:SQ + 4], c[:, SK:SK + 4], c[:, SV:SV + 4]
        sq, r = ([self.cut(2080 * (1 + x + y), 4, N) for x in range(2)] for y in (0, 2))
        vt = self.cut(self.S_V, NC, T)
        with self.stage() as block:
            @block.scalar
            def _(act):
                self.act.tell(nc.scalar.activation(sq[0], q, ACT.Square), self.scalar_out)
                self.act.tell(nc.scalar.activation(sq[1], k, ACT.Square), self.scalar_out)
                for x in range(2):
                    act.wait_ge(self.tensor_out.sem, self.tensor_out.at(x + 1))
                    self.act.tell(nc.scalar.activation(self.eight(r[x]), self.ps[:, :, 0:HALF], ACT.Ln, bias=self.eps,
                                                       scale=1.0 / 64), self.scalar_out)
                    self.act.tell(nc.scalar.activation(r[x], r[x], ACT.Exp, scale=-0.5), self.scalar_out)
                act.wait_ge(self.tensor_out.sem, self.tensor_out.at(3))
                self.act.step(nc.scalar.activation(vt.rearrange("p a b -> p (a b)"), self.banks(0, 4), ACT.Copy))

            @block.tensor
            def _(pe):
                self.head_sums(pe, sq[0], self.scalar_out, 1)
                pe.wait_ge(self.scalar_out.sem, self.scalar_out.at(3))
                self.head_sums(pe, sq[1], self.scalar_out, 2)
                pe.wait_ge(self.scalar_out.sem, self.scalar_out.at(5))
                for t in range(NC):
                    for j in range(4):
                        ins = nc.tensor.transpose(self.ps[:, t, j * P:(j + 1) * P], v[:, j, t * P:(t + 1) * P],
                                                  self.const("ident"))
                ins.then_inc(self.tensor_out.sem, 1)
                self.tensor_out.count += 1

            @block.vector
            def _(dve):
                for x, (t, gain) in enumerate(((q, "sbq"), (k, "sbk"))):
                    dve.wait_ge(self.scalar_out.sem, self.scalar_out.at(4 + 2 * x))
                    self.dve.tell(nc.vector.scalar_tensor_tensor(t, t, self.param(gain)[:, 0:1], r[x], ALU.mult, ALU.mult),
                                  self.vector_out)
                self.dve.step(nc.vector.tensor_scalar(q, q, 0.125, None, ALU.mult))

            @block.sync
            def _(sp):
                self.store(sp, self.d["p_sbv"], v)
                sp.wait_ge(self.vector_out.sem, self.vector_out.at(2))
                self.store(sp, self.d["p_sbk"], k)
                sp.wait_ge(self.stored.sem, self.stored.count)

    def log_stay(self, nz, out):
        nc = self.nc

        def first():
            return nc.vector.scalar_tensor_tensor(out, nz, -1.0, nz, ALU.mult, ALU.min)

        def middle():
            self.act.step(nc.scalar.activation(out, out, ACT.Exp))
            self.act.tell(nc.scalar.activation(out, out, ACT.Ln, bias=1.0), self.scalar_out)

        def last():
            return nc.vector.scalar_tensor_tensor(out, nz, 0.0, out, ALU.min, ALU.subtract)
        return first, middle, last

    def stick_prompt(self):
        nc, c = self.nc, self.c
        q, k = c[:, SQ:SQ + 4], c[:, SK:SK + 4]
        vt = self.cut(self.S_V, NC, 8, 64)
        nz = [self.cut(self.S_NZ + self.TRI * x, self.TRI) for x in range(2)]
        ls = [self.cut(self.S_L + self.TRI * x, self.TRI) for x in range(2)]
        wt = self.cut(self.S_L + self.TRI * 2, self.TRI)
        heads = 8
        blk = [slice(self.START[s], self.START[s] + self.WIDTH[s]) for s in range(NC)]

        def z(h, s, lo=None):
            return self.ps[:, 4 * (h % 2) + s, (s if lo is None else lo) * P:T]

        with self.stage() as block:
            @block.sync
            def _(sp):
                for b0 in range(B):
                    self.load_pages(sp, "cache_k", b0, self.inputs_loaded[b0])
                for b0 in range(self.EARLY_V):
                    self.load_pages(sp, "cache_v", b0, self.values_loaded[b0])

            @block.tensor
            def _(pe):
                def logits(h):
                    rows, j = slice(64 * (h % 2), 64 * (h % 2) + 64), h // 2
                    for s in (1, 2, 3, 0):
                        if s == 0 and h >= 2:
                            pe.wait_ge(self.vector_out2.sem, self.vector_out2.at(h - 1))
                        ins = nc.tensor.matmul(z(h, s), k[rows, j, s * P:(s + 1) * P], q[rows, j, s * P:T],
                                               start=True, stop=True)
                    ins.then_inc(self.scores_ready.sem, 1)

                def sums(h):
                    pe.wait_ge(self.vector_out.sem, self.vector_out.at(h + 1))
                    for s in range(NC):
                        diagonal = self.ps[:, 4 * (h % 2) + s, s * P:(s + 1) * P]
                        nc.tensor.matmul(diagonal, self.const("ident"), self.const("forbid"), start=False, stop=False,
                                         skip_group_check=True)
                        for n in range(s, NC):
                            ins = nc.tensor.matmul(z(h, s, n), self.const("key_after" if n == s else "ones"), ls[h % 2][:, blk[n]],
                                                   start=False, stop=n == NC - 1, skip_group_check=True)
                        ins.then_inc(self.tensor_out.sem, 1)

                def output(h):
                    rows = slice(64 * (h % 2), 64 * (h % 2) + 64)
                    for s in range(NC):
                        pe.wait_ge(self.weights_ready.sem, self.weights_ready.at(NC * h + s + 1))
                        ins = nc.tensor.matmul(self.ps[rows, 4 * (h % 2), s * P:T], vt[:, s, h], wt[:, blk[s]],
                                               start=s == 0, stop=s == NC - 1)
                    ins.then_inc(self.tensor_out2.sem, 1)

                logits(0)
                for h in range(heads):
                    if h:
                        output(h - 1)
                    if h + 1 < heads:
                        logits(h + 1)
                    sums(h)
                output(heads - 1)
                self.scores_ready.count += heads
                self.tensor_out.count += NC * heads
                self.tensor_out2.count += heads

            @block.vector
            def _(dve):
                def first(h):
                    dve.wait_ge(self.scores_ready.sem, self.scores_ready.at(h + 1))
                    for s in range(NC):
                        ins = nc.vector.tensor_scalar(nz[h % 2][:, blk[s]], z(h, s), self.param("sb_bias")[:, h:h + 1],
                                                      -1.0, ALU.add, ALU.mult)
                    self.dve.step(ins)
                    self.dve.tell(self.log_stay(nz[h % 2], ls[h % 2])[0](), self.exponent_ready)

                def second(h):
                    dve.wait_ge(self.scalar_out.sem, self.scalar_out.at(h + 1))
                    self.dve.step(self.log_stay(nz[h % 2], ls[h % 2])[2]())
                    for s in range(NC):
                        d = ls[h % 2][:, self.START[s]:self.START[s] + P]
                        ins = nc.vector.tensor_tensor(d, d, self.const("before"), ALU.mult)
                    self.dve.tell(ins, self.vector_out)

                def keep(h):
                    dve.wait_ge(self.tensor_out2.sem, self.tensor_out2.at(h + 1))
                    rows = slice(64 * (h % 2), 64 * (h % 2) + 64)
                    self.dve.tell(nc.vector.tensor_copy(self.o[rows, h // 2, 0:T], self.ps[rows, 4 * (h % 2), :]),
                                  self.vector_out2)

                first(0)
                second(0)
                for h in range(heads):
                    if h + 1 < heads:
                        first(h + 1)
                    keep(h)
                    if h + 1 < heads:
                        second(h + 1)

            @block.scalar
            def _(act):
                def middle(h):
                    act.wait_ge(self.exponent_ready.sem, self.exponent_ready.at(h + 1))
                    self.log_stay(nz[h % 2], ls[h % 2])[1]()

                def weights(h):
                    if h:
                        act.wait_ge(self.tensor_out2.sem, self.tensor_out2.at(h))
                    for s in range(NC):
                        act.wait_ge(self.tensor_out.sem, self.tensor_out.at(NC * h + s + 1))
                        self.act.tell(nc.scalar.activation(wt[:, blk[s]], z(h, s), ACT.Exp, bias=self.param("sb_bias")[:, h:h + 1]),
                                      self.weights_ready)

                middle(0)
                for h in range(heads):
                    weights(h)
                    if h + 1 < heads:
                        middle(h + 1)

    def page_slot(self, n):
        o = self.o[:, 4:8].rearrange("p a b -> p (a b)")
        v = self.c[:, SV:SV + 4].rearrange("p a b -> p (a b)")
        h = self.h[:].rearrange("p a b -> p (a b)")
        spots = [self.cut(self.S_L + self.TRI * 3 + 1024 * x, 1024) for x in range(5)] + [h[:, 1024 * x:1024 * (x + 1)] for x in range(4)]
        spots += [t[:, 1024 * x:1024 * (x + 1)] for t in (o, v) for x in range(2)]
        spots += [self.cut(1024 * x, 1024) for x in range(3)]
        return spots[n]

    def load_pages(self, sp, name, b0, signal):
        slot = self.page_slot(b0 + (B if name == "cache_v" else 0))
        for pg in range(PAGES):
            n = b0 * PAGES + pg
            page = sp.value_load(self.pages[0:1, n:n + 1], min_val=0, max_val=NPHYS - 1)
            sp.dma_start(slot[:, pg * 512:(pg + 1) * 512], self.d[name][bass.ds(page, 1)].rearrange("o p n -> p (o n)")).then_inc(
                signal.sem, 16)

    EARLY_V = 5

    def stick_sample(self):
        nc, c = self.nc, self.c
        q = c[:, SQ:SQ + 4]
        kp = [self.page_slot(b0).rearrange("p (g j t) -> p g j t", g=PAGES, j=4) for b0 in range(B)]
        vp = [self.page_slot(B + b0).rearrange("p (g n) -> p g n", g=PAGES) for b0 in range(B)]
        R = B * 8
        at = 3072
        nz, ls, w = (self.cut(at + 128 * x, 128) for x in range(3))
        qz, wz = self.cut(3584, B, 4, R), self.cut(5632, B, PAGES, R)
        row, out = self.cut(6656, 256), self.cut(6912, 512)
        ident = self.cst[0:R, CONST_AT["ident"]:CONST_AT["ident"] + R]
        with self.stage() as block:
            @block.sync
            def _(sp):
                for b0 in range(self.EARLY_V, B):
                    self.load_pages(sp, "cache_v", b0, self.values_loaded[b0])

            @block.gpsimd
            def _(pool):
                self.pool.tell(nc.gpsimd.memset(wz, 0.0), self.pool_out)

            @block.tensor
            def _(pe):
                pe.wait_ge(self.vector_out.sem, self.vector_out.at(1))
                for b0 in range(B):
                    pe.wait_ge(self.inputs_loaded[b0].sem, self.inputs_loaded[b0].at(16 * PAGES))
                    for j in range(4):
                        ins = nc.tensor.matmul(self.ps[0:R, 0, 0:256].rearrange("r (g t) -> r g t", g=PAGES), qz[:, b0, j],
                                               kp[b0][:, :, j], start=b0 + j == 0, stop=b0 == B - 1 and j == 3)
                ins.then_inc(self.keys_used.sem, 1)
                pe.wait_ge(self.scalar_out.sem, self.scalar_out.at(1))
                for pg in range(PAGES):
                    ins = nc.tensor.transpose(self.ps[:, 1, pg * R:(pg + 1) * R], row[0:R, pg * P:(pg + 1) * P], ident)
                ins.then_inc(self.tensor_out.sem, 1)
                pe.wait_ge(self.vector_out.sem, self.vector_out.at(3))
                nc.tensor.matmul(self.ps[:, 2, 64:128], self.const("key_after"), ls[:, 64:128], start=True, stop=True)
                nc.tensor.matmul(self.ps[:, 2, 0:64], self.const("key_after"), ls[:, 0:64], start=True, stop=False)
                nc.tensor.matmul(self.ps[:, 2, 0:64], self.const("ones"), ls[:, 64:128], start=False, stop=True).then_inc(
                    self.tensor_out.sem, 1)
                pe.wait_ge(self.vector_out.sem, self.vector_out.at(5))
                for b0 in range(B):
                    pe.wait_ge(self.values_loaded[b0].sem, self.values_loaded[b0].at(16 * PAGES))
                    for pg in range(PAGES):
                        ins = nc.tensor.matmul(self.ps[0:R, 3, :], wz[:, b0, pg], vp[b0][:, pg],
                                               start=b0 + pg == 0, stop=b0 == B - 1 and pg == PAGES - 1)
                ins.then_inc(self.values_used.sem, 1)
                pe.wait_ge(self.scalar_out.sem, self.scalar_out.at(4))
                for j in range(4):
                    ins = nc.tensor.transpose(self.ps[:, 4, j * R:(j + 1) * R], out[0:R, j * P:(j + 1) * P], ident)
                ins.then_inc(self.tensor_out.sem, 1)
                self.keys_used.count += 1
                self.values_used.count += 1
                self.tensor_out.count += 3
                for b0 in range(B):
                    self.inputs_loaded[b0].count += 16 * PAGES
                    self.values_loaded[b0].count += 16 * PAGES

            @block.vector
            def _(dve):
                first, _, last = self.log_stay(nz, ls)
                self.dve.step(nc.vector.memset(qz, 0.0))
                flat = qz.rearrange("p b j r -> p (b j r)")
                for par in range(2):
                    rows = slice(64 * par, 64 * par + 64)
                    ins = nc.vector.tensor_copy(flat[rows, par:32 * R:R + 2].rearrange("p (b j) -> p b j", b=B),
                                                q[rows, :, T:N].rearrange("p j b -> p b j"))
                self.dve.tell(ins, self.vector_out)
                dve.wait_ge(self.tensor_out.sem, self.tensor_out.at(1))
                by_head = lambda t: t.rearrange("p (a h) -> p a h", h=8)
                self.dve.step(nc.vector.tensor_tensor(by_head(nz), by_head(self.ps[:, 1, 0:128]),
                                                      self.param("sb_bias").unsqueeze(1).to_broadcast([P, 16, 8]), ALU.add))
                self.dve.step(nc.vector.tensor_scalar(nz, nz, -1.0, None, ALU.mult))
                self.dve.tell(first(), self.vector_out)
                dve.wait_ge(self.scalar_out.sem, self.scalar_out.at(2))
                self.dve.tell(last(), self.vector_out)
                dve.wait_ge(self.tensor_out.sem, self.tensor_out.at(2))
                self.dve.tell(nc.vector.tensor_tensor(w, self.ps[:, 2, 0:128], nz, ALU.subtract), self.vector_out)
                dve.wait_ge(self.scalar_out.sem, self.scalar_out.at(3))
                dve.wait_ge(self.pool_out.sem, self.pool_out.at(1))
                for b0 in range(B):
                    ins = nc.vector.tensor_copy(wz[:, b0, :, 8 * b0:8 * b0 + 8],
                                                w.rearrange("p (g b h) -> p g b h", g=PAGES, b=B)[:, :, b0])
                self.dve.tell(ins, self.vector_out)

            @block.scalar
            def _(act):
                act.wait_ge(self.keys_used.sem, self.keys_used.at(1))
                self.act.tell(nc.scalar.activation(row[0:R], self.ps[0:R, 0, 0:256], ACT.Copy), self.scalar_out)
                act.wait_ge(self.vector_out.sem, self.vector_out.at(2))
                self.log_stay(nz, ls)[1]()
                act.wait_ge(self.vector_out.sem, self.vector_out.at(4))
                self.act.tell(nc.scalar.activation(w, w, ACT.Exp), self.scalar_out)
                act.wait_ge(self.values_used.sem, self.values_used.at(1))
                self.act.tell(nc.scalar.activation(out[0:R], self.ps[0:R, 3, :], ACT.Copy), self.scalar_out)
                act.wait_ge(self.tensor_out.sem, self.tensor_out.at(3))
                for par in range(2):
                    rows = slice(64 * par, 64 * par + 64)
                    for j in range(4):
                        own = self.ps[rows, 4, j * R:(j + 1) * R].rearrange("p (b h) -> p b h", h=8)[:, :, 2 * j + par]
                        ins = nc.scalar.activation(self.o[rows, j, T:N], own, ACT.Copy)
                self.act.step(ins)

    E_EG, E_DM, E_LD = 0, 4, 8
    E_INV, E_VT, E_KT, E_QK, E_U, E_S, E_R = 6144, 0, 2048, 4096, 8192, 10240, 12800
    E_COL = 13312

    def conv(self):
        nc, c = self.nc, self.c
        x = c[:, DQ:DQ + 12]
        y = self.cut(0, 12, N)
        buf = self.cut(12 * N, 12, 3, B)
        pc, sc = self.cut(12 * N + 288, 12, 3), self.cut(12 * N + 324, 12, 3, B)
        t = self.cut(12 * N + 612, 12, B)
        w = self.param("dn_conv").rearrange("p (i a) -> p i a", i=4)
        with self.stage() as block:
            @block.sync
            def _(sp):
                sp.dma_start(buf, self.d["state_conv"]).then_inc(self.inputs_loaded[0].sem, 16)
                self.inputs_loaded[0].count += 16
                sp.wait_ge(self.pool_out.sem, self.pool_out.at(3))
                self.store(sp, self.d["p_conv"], pc)
                self.store(sp, self.d["s_conv"], sc)
                sp.wait_ge(self.stored.sem, self.stored.count)

            @block.gpsimd
            def _(pool):
                self.pool.tell(nc.gpsimd.tensor_copy(pc, x[:, :, T - 3:T]), self.pool_out)
                self.pool.tell(nc.gpsimd.tensor_copy(sc[:, :, 2], x[:, :, T:N]), self.pool_out)
                pool.wait_ge(self.inputs_loaded[0].sem, self.inputs_loaded[0].at(16))
                self.pool.tell(nc.gpsimd.tensor_copy(sc[:, :, 0:2], buf[:, :, 1:3]), self.pool_out)

            @block.scalar
            def _(act):
                for a in range(12):
                    nc.scalar.activation(y[:, a], x[:, a], ACT.Copy, scale=w[:, 3, a:a + 1]).then_inc(self.scalar_out.sem, 1)
                self.scalar_out.count += 12
                act.wait_ge(self.pool_out.sem, self.pool_out.at(3))
                for a in range(12):
                    act.wait_ge(self.vector_out.sem, self.vector_out.at(a + 1))
                    self.act.step(nc.scalar.activation(x[:, a], y[:, a], ACT.Silu))

            @block.vector
            def _(dve):
                dve.wait_ge(self.scalar_out.sem, self.scalar_out.at(12))
                dve.wait_ge(self.inputs_loaded[0].sem, self.inputs_loaded[0].at(16))
                for i in range(3):
                    wi = w[:, i].unsqueeze(2).to_broadcast([P, 12, B])
                    self.dve.step(nc.vector.tensor_tensor(t, buf[:, :, i], wi, ALU.mult))
                    self.dve.step(nc.vector.tensor_tensor(y[:, :, T:N], y[:, :, T:N], t, ALU.add))
                for a in range(12):
                    for i in range(3):
                        lag = 3 - i
                        ins = nc.vector.scalar_tensor_tensor(y[:, a, lag:T], x[:, a, 0:T - lag], w[:, i, a:a + 1], y[:, a, lag:T],
                                                             ALU.mult, ALU.add)
                        self.dve.step(ins) if i < 2 else self.dve.tell(ins, self.vector_out)

    def delta_vectors(self):
        nc, c = self.nc, self.c
        q, k = c[:, DQ:DQ + 4], c[:, DK:DK + 4]
        sq, r = ([self.cut(2080 * (x + y), 4, N) for x in range(2)] for y in (0, 2))
        g, e, a = c[0:4, DAB], self.cut(8320, N)[0:4], self.cut(8840, 1)[0:4]
        gs = self.cut(8850, N)
        eg = c[:, self.E_EG:self.E_EG + 4]
        dm = self.flat(self.E_DM)[:, 0:2048].rearrange("p (c h t) -> p c h t", c=NC, h=4)
        ld = self.flat(self.E_LD)[:, 0:2048].rearrange("p (c h t) -> p c h t", c=NC, h=4)
        col = self.cut(self.E_COL, 4, NC, 4)
        bs = self.cut(self.E_COL + 64, 4, B)
        row = lambda h, base: self.cst[base:base + 4, SEL_AT + h * P:SEL_AT + (h + 1) * P]
        heads4 = self.ps[:, :, 0:HALF].rearrange("p (h s) n -> p h s n", s=2)

        def spread(pe, base):
            for h in range(4):
                for s, (lo, hi) in enumerate(self.SPANS):
                    ins = nc.tensor.matmul(self.ps[:, 2 * h + s, 0:HALF], row(h, base), gs[base:base + 4, lo:hi],
                                           start=True, stop=True)
            ins.then_inc(self.tensor_out.sem, 1)

        with self.stage() as block:
            @block.scalar
            def _(act):
                self.act.step(nc.scalar.activation(gs[32:36], c[32:36, DAB], ACT.Sigmoid))
                act.wait_ge(self.vector_out.sem, self.vector_out.at(1))
                self.act.step(nc.scalar.activation(e, e, ACT.Exp))
                self.act.step(nc.scalar.activation(a, self.param("dn_a")[0:4], ACT.Exp))
                self.act.tell(nc.scalar.activation(e, e, ACT.Ln, bias=1.0), self.scalar_out)
                self.act.tell(nc.scalar.activation(sq[0], q, ACT.Square), self.scalar_out)
                self.act.tell(nc.scalar.activation(sq[1], k, ACT.Square), self.scalar_out)
                for x in range(2):
                    act.wait_ge(self.tensor_out.sem, self.tensor_out.at(x + 1))
                    self.act.tell(nc.scalar.activation(self.eight(r[x]), self.ps[:, :, 0:HALF], ACT.Ln, bias=self.eps),
                                  self.scalar_out)
                    self.act.tell(nc.scalar.activation(r[x], r[x], ACT.Exp, scale=-0.5), self.scalar_out)
                act.wait_ge(self.tensor_out.sem, self.tensor_out.at(4))
                self.act.tell(nc.scalar.activation(self.eight(eg), self.ps[:, :, 0:HALF], ACT.Exp), self.scalar_out)
                act.wait_ge(self.vector_out.sem, self.vector_out.at(4))
                self.act.step(nc.scalar.activation(dm, dm, ACT.Exp))
                self.act.step(nc.scalar.activation(col[:, 2], col[:, 2], ACT.Exp))
                self.act.tell(nc.scalar.activation(col[:, 3], col[:, 3], ACT.Exp), self.scalar_out)

            @block.tensor
            def _(pe):
                for x in range(2):
                    if x:
                        pe.wait_ge(self.scalar_out.sem, self.scalar_out.at(4))
                    pe.wait_ge(self.scalar_out.sem, self.scalar_out.at(2 + x))
                    for h in range(4):
                        for s, (lo, hi) in enumerate(self.SPANS):
                            ins = nc.tensor.matmul(self.ps[:, 2 * h + s, 0:HALF], self.const("ones"), sq[x][:, h, lo:hi],
                                                   start=True, stop=True)
                    ins.then_inc(self.tensor_out.sem, 1)
                pe.wait_ge(self.scalar_out.sem, self.scalar_out.at(6))
                pe.wait_ge(self.vector_out.sem, self.vector_out.at(2))
                for n, base in enumerate((0, 32)):
                    for t in range(NC):
                        ins = nc.tensor.transpose(self.ps[:, n, t * 4:t * 4 + 4], gs[base:base + 4, t * P:(t + 1) * P],
                                                  self.cst[base:base + 4, CONST_AT["ident"] + base:CONST_AT["ident"] + base + 4])
                ins.then_inc(self.tensor_out.sem, 1)
                pe.wait_ge(self.vector_out.sem, self.vector_out.at(3))
                spread(pe, 0)
                pe.wait_ge(self.scalar_out.sem, self.scalar_out.at(8))
                pe.wait_ge(self.vector_out.sem, self.vector_out.at(4))
                spread(pe, 32)
                self.tensor_out.count += 5

            @block.vector
            def _(dve):
                self.dve.step(nc.vector.tensor_scalar(g, g, self.param("dn_dt")[0:4, 0:1], None, ALU.add))
                self.dve.tell(nc.vector.scalar_tensor_tensor(e, g, -1.0, g, ALU.mult, ALU.min), self.vector_out)
                dve.wait_ge(self.scalar_out.sem, self.scalar_out.at(1))
                self.dve.step(nc.vector.scalar_tensor_tensor(g, g, 0.0, e, ALU.max, ALU.add))
                self.dve.step(nc.vector.tensor_scalar(g, g, a, -1.0, ALU.mult, ALU.mult))
                self.dve.step(nc.vector.tensor_copy(gs[0:4, T:N], g[:, T:N]))
                self.dve.tell(nc.vector.tensor_tensor_scan(gs[0:4, 0:T], self.cst[0:4, SCAN128_AT:SCAN128_AT + T], g[:, 0:T],
                                                           0.0, ALU.mult, ALU.add), self.vector_out)
                dve.wait_ge(self.scalar_out.sem, self.scalar_out.at(5))
                self.dve.step(nc.vector.scalar_tensor_tensor(q, q, P ** -0.5, r[0], ALU.mult, ALU.mult))
                dve.wait_ge(self.scalar_out.sem, self.scalar_out.at(7))
                self.dve.step(nc.vector.tensor_tensor(k, k, r[1], ALU.mult))
                dve.wait_ge(self.tensor_out.sem, self.tensor_out.at(3))
                self.dve.tell(nc.vector.tensor_copy(col[:, 0:2].rearrange("p x c h -> p x (c h)"), self.ps[:, 0:2, 0:16]),
                              self.vector_out)
                dve.wait_ge(self.scalar_out.sem, self.scalar_out.at(8))
                for t in range(NC):
                    for h in range(4):
                        for lo, hi, bank, at in self.pieces(t):
                            self.dve.step(nc.vector.tensor_scalar(
                                dm[:, t, h, lo:hi], self.ps[:, 2 * h + bank, at:at + hi - lo], col[:, 0, t, h:h + 1], 0.0,
                                ALU.subtract, ALU.min))
                    end = (t + 1) * P - 1
                    last = heads4[:, :, end // HALF, end % HALF]
                    self.dve.step(nc.vector.tensor_copy(col[:, 3, t], last))
                    self.dve.step(nc.vector.tensor_tensor(col[:, 2, t], col[:, 3, t], col[:, 0, t], ALU.subtract))
                self.dve.tell(nc.vector.memset(bs, 0.0), self.vector_out)
                dve.wait_ge(self.tensor_out.sem, self.tensor_out.at(5))
                dve.wait_ge(self.scalar_out.sem, self.scalar_out.at(9))
                self.dve.step(nc.vector.tensor_copy(bs, heads4[:, :, 1, HALF - B:HALF]))
                for t in range(NC):
                    for lo, hi, bank, at in self.pieces(t):
                        self.dve.step(nc.vector.scalar_tensor_tensor(
                            ld[:, t, :, lo:hi], dm[:, t, :, lo:hi], -1.0, heads4[:, :, bank, at:at + hi - lo],
                            ALU.mult, ALU.mult))
                flat = ld.rearrange("p c h t -> p (c h) t")
                self.dve.step(nc.vector.tensor_tensor(flat, flat, self.const("before").unsqueeze(1).to_broadcast([P, 16, P]),
                                                      ALU.mult))
                flat = dm.rearrange("p c h t -> p (c h) t")
                self.dve.step(nc.vector.tensor_tensor(flat, flat, self.const("causal").unsqueeze(1).to_broadcast([P, 16, P]),
                                                      ALU.mult))

    def pieces(self, t):
        out = []
        for s, (lo, hi) in enumerate(self.SPANS):
            a, b = max(lo, t * P), min(hi, (t + 1) * P)
            if a < b:
                out.append((a - t * P, b - t * P, s, a - lo))
        return out

    def delta_inverses(self):
        nc, c = self.nc, self.c
        k = c[:, DK:DK + 4]
        ld = self.flat(self.E_LD)[:, 0:2048].rearrange("p (g x t) -> p g x t", g=2, x=8)

        def fill(pe, g, bank):
            for x in range(8):
                t, h = 2 * g + x // 4, x % 4
                kc = k[:, h, t * P:(t + 1) * P]
                ins = nc.tensor.matmul(self.ps[:, bank + x // 4, h * P:(h + 1) * P], kc, kc, start=True, stop=True)
            ins.then_inc(self.tensor_out.sem, 1)

        self.inv = [self.cut(self.E_INV + 1024 * g, 8, P) for g in range(2)]
        self.unit_inverses(2, 2, (lambda g: ld[:, g], [f"level{m}" for m in LEVELS[::-1]]), 0, 2048, 4096, self.inv, fill)

    def delta_chain(self):
        nc, c = self.nc, self.c
        q, k, v = (c[:, x:x + 4] for x in (DQ, DK, DV))
        eg = c[:, self.E_EG:self.E_EG + 4]
        dm = self.flat(self.E_DM)[:, 0:2048].rearrange("p (c h t) -> p c h t", c=NC, h=4)
        col = self.cut(self.E_COL, 4, NC, 4)
        inv = self.cut(self.E_INV, NC, 4, P)
        vt, kt, qk, u = (self.cut(x, NC, 4, P) for x in (self.E_VT, self.E_KT, self.E_QK, self.E_U))
        st = self.cut(self.E_S, NC + 1, 4, P)
        rr = self.cut(self.E_R, 4, P)

        def wide(t):
            return t.rearrange("p c h t -> p (c h t)")

        with self.stage() as block:
            @block.tensor
            def _(pe):
                for n, src in enumerate((v, k)):
                    for t in range(NC):
                        for h in range(4):
                            ins = nc.tensor.transpose(self.ps[:, 4 * n + t, h * P:(h + 1) * P], src[:, h, t * P:(t + 1) * P],
                                                      self.const("ident"))
                    ins.then_inc(self.tensor_out.sem, 1)
                pe.wait_ge(self.scalar_out.sem, self.scalar_out.at(1))
                for t in range(NC):
                    for h in range(4):
                        cols = slice(t * P, (t + 1) * P)
                        ins = nc.tensor.matmul(self.ps[:, t, h * P:(h + 1) * P], k[:, h, cols], q[:, h, cols],
                                               start=True, stop=True)
                ins.then_inc(self.tensor_out.sem, 1)
                pe.wait_ge(self.vector_out.sem, self.vector_out.at(1))
                for t in range(NC):
                    cols = slice(t * P, (t + 1) * P)
                    if t:
                        pe.wait_ge(self.vector_out2.sem, self.vector_out2.at(2 * t))
                        for h in range(4):
                            ins = nc.tensor.matmul(self.ps[:, 4, h * P:(h + 1) * P], k[:, h, cols], st[:, t, h],
                                                   start=True, stop=True)
                        ins.then_inc(self.tensor_out2.sem, 1)
                    pe.wait_ge(self.vector_out2.sem, self.vector_out2.at(2 * t + 1))
                    for h in range(4):
                        ins = nc.tensor.matmul(self.ps[:, 5, h * P:(h + 1) * P], inv[:, t, h], rr[:, h], start=True, stop=True)
                    ins.then_inc(self.tensor_out2.sem, 1)
                    pe.wait_ge(self.scalar_out.sem, self.scalar_out.at(2 + t))
                    for h in range(4):
                        ins = nc.tensor.matmul(self.ps[:, 6, h * P:(h + 1) * P], kt[:, t, h], u[:, t, h], start=True, stop=True)
                    ins.then_inc(self.tensor_out2.sem, 1)
                pe.wait_ge(self.vector_out.sem, self.vector_out.at(3))
                for h in range(4):
                    for t in range(NC):
                        cols = slice(t * P, (t + 1) * P)
                        nc.tensor.matmul(self.ps[:, h, cols], u[:, t, h], qk[:, t, h], start=True, stop=t == 0)
                        if t:
                            ins = nc.tensor.matmul(self.ps[:, h, cols], st[:, t, h], q[:, h, cols], start=False, stop=True)
                ins.then_inc(self.tensor_out.sem, 1)
                self.tensor_out.count += 4
                self.tensor_out2.count += 3 * NC - 1

            @block.scalar
            def _(act):
                act.wait_ge(self.tensor_out.sem, self.tensor_out.at(1))
                self.act.tell(nc.scalar.activation(wide(vt), self.banks(0, 4), ACT.Copy), self.scalar_out)
                for t in range(NC):
                    act.wait_ge(self.tensor_out2.sem, self.tensor_out2.at(3 * t + 1))
                    self.act.tell(nc.scalar.activation(u[:, t].rearrange("p h e -> p (h e)"), self.ps[:, 5, :], ACT.Copy),
                                  self.scalar_out)
                act.wait_ge(self.tensor_out.sem, self.tensor_out.at(4))
                self.act.step(nc.scalar.activation(self.o[:, 4:8, 0:T], self.ps[:, 0:4, :], ACT.Copy))

            @block.gpsimd
            def _(pool):
                pool.wait_ge(self.tensor_out.sem, self.tensor_out.at(3))
                self.pool.tell(nc.gpsimd.tensor_tensor(q[:, :, 0:T], q[:, :, 0:T], eg[:, :, 0:T], ALU.mult), self.pool_out)

            @block.vector
            def _(dve):
                flat = inv.rearrange("p c h t -> p (c h) t")
                beta = col[:, 1].rearrange("p c h -> p (c h)").unsqueeze(2).to_broadcast([P, 16, P])
                self.dve.step(nc.vector.tensor_tensor(flat, flat, beta, ALU.mult))
                dve.wait_ge(self.tensor_out.sem, self.tensor_out.at(2))
                decay = col[:, 2].rearrange("p c h -> p (c h)").unsqueeze(2).to_broadcast([P, 16, P])
                self.dve.step(nc.vector.tensor_tensor(kt.rearrange("p c h t -> p (c h) t"),
                                                      self.banks(4, 4).rearrange("p (x t) -> p x t", t=P), decay, ALU.mult))
                dve.wait_ge(self.tensor_out.sem, self.tensor_out.at(3))
                self.dve.tell(nc.vector.tensor_tensor(k[:, :, 0:T], k[:, :, 0:T], eg[:, :, 0:T], ALU.mult), self.vector_out)
                dve.wait_ge(self.scalar_out.sem, self.scalar_out.at(1))
                self.dve.tell(nc.vector.tensor_copy(rr, vt[:, 0]), self.vector_out2)
                self.dve.tell(nc.vector.tensor_tensor(wide(qk), self.banks(0, 4), wide(dm), ALU.mult), self.vector_out)
                for t in range(NC):
                    if t:
                        dve.wait_ge(self.tensor_out2.sem, self.tensor_out2.at(3 * t))
                        self.dve.tell(nc.vector.tensor_tensor(rr.rearrange("p h e -> p (h e)"), vt[:, t].rearrange("p h e -> p (h e)"),
                                                              self.ps[:, 4, :], ALU.subtract), self.vector_out2)
                    dve.wait_ge(self.tensor_out2.sem, self.tensor_out2.at(3 * t + 2))
                    new = st[:, t + 1]
                    if t == 0:
                        ins = nc.vector.tensor_copy(new.rearrange("p h e -> p (h e)"), self.ps[:, 6, :])
                    else:
                        self.dve.step(nc.vector.tensor_tensor(new, st[:, t], col[:, 3, t].unsqueeze(2).to_broadcast([P, 4, P]),
                                                              ALU.mult))
                        ins = nc.vector.tensor_tensor(new.rearrange("p h e -> p (h e)"), new.rearrange("p h e -> p (h e)"),
                                                      self.ps[:, 6, :], ALU.add)
                    self.dve.tell(ins, self.vector_out2)
                dve.wait_ge(self.pool_out.sem, self.pool_out.at(1))
                self.dve.tell(nc.vector.memset(rr, 0.0), self.vector_out)

            @block.sync
            def _(sp):
                sp.wait_ge(self.vector_out2.sem, self.vector_out2.at(2 * NC))
                self.store(sp, self.d["p_delta"], st[:, NC].rearrange("p h e -> p (h e)"))
                sp.wait_ge(self.stored.sem, self.stored.count)

    def delta_sample(self):
        nc, c = self.nc, self.c
        s4 = lambda x: c[:, x:x + 4, T:N]
        ss = self.h[:].rearrange("p a b -> p (a b)")[:, 0:4096].rearrange("p (b h e) -> p b h e", b=B, h=4)
        pr = self.cut(0, B, 4, P)
        vs = self.cut(4096, 4, P)
        nk, kb = self.cut(4608, 4, B), self.cut(4640, 4, B)
        bs = self.cut(self.E_COL + 64, 4, B)

        def by_seq(t):
            return t.rearrange("p h b -> p b h").unsqueeze(3).to_broadcast([P, B, 4, P])

        with self.stage() as block:
            @block.sync
            def _(sp):
                sp.dma_start(ss, self.d["state_delta"]).then_inc(self.inputs_loaded[0].sem, 16)
                self.inputs_loaded[0].count += 16
                sp.wait_ge(self.vector_out2.sem, self.vector_out2.at(1))
                self.store(sp, self.d["s_delta"], ss)
                sp.wait_ge(self.stored.sem, self.stored.count)

            @block.tensor
            def _(pe):
                for h in range(4):
                    ins = nc.tensor.transpose(self.ps[0:B, 0, h * P:(h + 1) * P], c[:, DV + h, T:N], self.const("ident"))
                ins.then_inc(self.tensor_out.sem, 1)
                pe.wait_ge(self.scalar_out.sem, self.scalar_out.at(1))
                pe.wait_ge(self.vector_out.sem, self.vector_out.at(1))
                for b0 in range(B):
                    nc.tensor.matmul(self.ps[:, b0, :], self.cst[0:B, SEL_AT + b0 * P:SEL_AT + (b0 + 1) * P],
                                     vs[0:B].rearrange("p h e -> p (h e)"), start=True, stop=False)
                    ins = nc.tensor.matmul(self.ps[:, b0, :], self.const("ones"), pr[:, b0].rearrange("p h e -> p (h e)"),
                                           start=False, stop=True)
                ins.then_inc(self.tensor_out.sem, 1)
                pe.wait_ge(self.vector_out2.sem, self.vector_out2.at(1))
                for h in range(4):
                    for b0 in range(B):
                        at = h * B + b0
                        ins = nc.tensor.matmul(self.ps[:, 0, at:at + 1], ss[:, b0, h], c[:, DQ + h, T + b0:T + b0 + 1],
                                               start=True, stop=True)
                ins.then_inc(self.tensor_out.sem, 1)
                self.tensor_out.count += 3

            @block.scalar
            def _(act):
                act.wait_ge(self.tensor_out.sem, self.tensor_out.at(1))
                self.act.tell(nc.scalar.activation(vs[0:B].rearrange("p a b -> p (a b)"), self.ps[0:B, 0, :], ACT.Copy),
                              self.scalar_out)
                act.wait_ge(self.tensor_out.sem, self.tensor_out.at(3))
                self.act.step(nc.scalar.activation(self.o[:, 4:8, T:N], self.ps[:, 0, 0:32].rearrange("p (h b) -> p h b", b=B),
                                                   ACT.Copy))

            @block.vector
            def _(dve):
                self.dve.step(nc.vector.tensor_scalar(nk, s4(DK), -1.0, None, ALU.mult))
                self.dve.step(nc.vector.tensor_tensor(kb, s4(DK), bs, ALU.mult))
                dve.wait_ge(self.inputs_loaded[0].sem, self.inputs_loaded[0].at(16))
                self.dve.step(nc.vector.tensor_tensor(ss, ss, by_seq(c[:, self.E_EG:self.E_EG + 4, T:N]), ALU.mult))
                self.dve.tell(nc.vector.tensor_tensor(pr, ss, by_seq(nk), ALU.mult), self.vector_out)
                dve.wait_ge(self.tensor_out.sem, self.tensor_out.at(2))
                self.dve.step(nc.vector.tensor_tensor(pr, self.banks(0, 8).rearrange("p (b h e) -> p b h e", b=B, h=4),
                                                      by_seq(kb), ALU.mult))
                self.dve.tell(nc.vector.tensor_tensor(ss, ss, pr, ALU.add), self.vector_out2)

    def run(self):
        nc = self.nc
        L = self.lin
        self.start()
        self.params = EVEN_PARAMS, self.par0
        self.projection(L["in0"], "g_mix", L["out0"])
        self.gla_gates()
        self.gla_levels()
        self.gla_states()
        self.gated_norm(0, GG, "gla_norm")
        self.token_shift()
        self.rwkv_low_rank()
        self.rwkv_vectors()
        self.rwkv_sample()
        self.rwkv_inverses()
        self.rwkv_chain()
        self.rwkv_output()
        self.residual(L["out0"], self.std, L["xkv0"], src=self.o)
        self.memory(0, L["xq0"])
        self.query(0, L["xo0"])
        self.attention(0)
        self.residual(L["xo0"], self.std, L["gu0"], src=self.o)
        self.gate_up(0, L["down0"])
        self.residual(L["down0"], self.hid, L["in1"], per=2)
        self.params = ODD_PARAMS, self.par1
        self.projection(L["in1"], "g_mix", L["out1"])
        self.stick_norms()
        self.stick_prompt()
        self.stick_sample()
        self.conv()
        self.delta_vectors()
        self.delta_inverses()
        self.delta_chain()
        self.delta_sample()
        self.gated_norm(4, DZ, "dn_norm")
        self.residual(L["out1"], self.std, L["xkv1"], src=self.o)
        self.memory(1, L["xq1"])
        self.query(1, L["xo1"])
        self.attention(1)
        self.residual(L["xo1"], self.std, L["gu1"], src=self.o)
        self.gate_up(1, L["down1"])
        self.residual(L["down1"], self.hid, None, per=2)
        self.finish()

    def finish(self):
        with self.stage() as block:
            @block.sync
            def _(sp):
                self.store(sp, self.d["y"], self.x[:])
                sp.wait_ge(self.stored.sem, self.stored.count)


def units(w, kt=KT):
    k, n = w.shape
    a = w.reshape(k // (kt * P), kt, P, n // P, P).transpose(3, 0, 2, 1, 4)
    return np.ascontiguousarray(a.reshape(-1, P, kt * P))


def feature_major(a):
    return np.ascontiguousarray(a.reshape(a.shape[0], -1, P).transpose(2, 1, 0))


def column(v):
    return v.reshape(-1, P).T


def rows(v, width=1):
    v = v.reshape(-1, width) if v.ndim == 1 else v
    out = np.zeros((P, v.shape[1]), v.dtype)
    out[:v.shape[0]] = v
    return out


def lay_out(I):
    a = {"cst": constants()}
    a["x"] = np.concatenate([feature_major(I["x_prompt"][0]), feature_major(I["x_sample"][:, 0])], axis=2)
    a["mem"] = feature_major(I["mem_prompt"][0])
    we, wo = I["w_in_even"][0], I["w_in_odd"][0]
    tail0, tail1 = np.zeros((D, P), we.dtype), np.zeros((D, P), wo.dtype)
    tail0[:, 0:16] = we[:, 1536:1552]
    tail1[:, 0:4], tail1[:, 32:36] = wo[:, 3584:3588], wo[:, 3588:3592]
    a["w_in0"] = units(np.concatenate([we[:, 0:1536], we[:, 1552:], tail0], axis=1))
    a["w_in1"] = units(np.concatenate([wo[:, :3584], tail1], axis=1))
    a["w_out0"], a["w_out1"] = units(I["w_out_even"][0]), units(I["w_out_odd"][0])
    for i in range(2):
        a[f"w_xq{i}"], a[f"w_xkv{i}"], a[f"w_xo{i}"] = (units(I[n][i]) for n in ("w_xq", "w_xkv", "w_xo"))
        gu = I["w_gu"][i].reshape(D, 2, FT, P).transpose(0, 2, 1, 3).reshape(D, -1)
        a[f"w_gu{i}"], a[f"w_down{i}"] = units(gu), units(I["w_down"][i], SLOT_K)

    def common(i):
        return [column(I[n][i]) for n in ("norm_mix", "norm_cross", "norm_ffn", "mem_norm", "xq_norm", "xk_norm")]

    a["par0"] = np.concatenate(common(0) + [
        column(I["gla_b_a"][0]), column(I["gla_norm"][0])] + [column(I["rwkv_" + n][0]) for n in
        ("mu", "w0", "a0", "k_k", "k_a", "r_k", "ln_w", "ln_b")] + [
        rows(I["gla_w_a2"][0]), np.concatenate([I["rwkv_w2"][0], I["rwkv_a2"][0]]), I["rwkv_g2"][0]], axis=1)
    a["par1"] = np.concatenate(common(1) + [
        np.tile(I["sb_q_norm"][0], 2)[:, None], np.tile(I["sb_k_norm"][0], 2)[:, None],
        np.tile(I["sb_bias"][0], (P, 1)), I["dn_conv"][0].reshape(4, 12, P).transpose(2, 0, 1).reshape(P, 48),
        rows(I["dn_a_log"][0]), rows(I["dn_dt_bias"][0]), column(I["dn_norm"][0])], axis=1)
    a["state_gla"] = I["state_gla"][0].reshape(B, 2, P, P).transpose(2, 0, 1, 3)
    a["state_rwkv"] = I["state_rwkv"][0].reshape(B, 4, 2, 64, 64).transpose(2, 4, 0, 1, 3).reshape(P, B, 4, 64)
    a["state_shift"] = feature_major(I["state_rwkv_shift"][0])
    a["state_delta"] = I["state_delta"][0].transpose(2, 0, 1, 3)
    a["state_conv"] = I["state_delta_conv"][0].reshape(B, 3, 12, P).transpose(3, 2, 1, 0)
    a["cache_k"] = I["cache_sb_k"][0].reshape(NPHYS, PAGE, 4, P).transpose(0, 3, 2, 1).reshape(NPHYS, P, 512)
    a["cache_v"] = I["cache_sb_v"][0].reshape(NPHYS, PAGE, 512)
    a["page_table"] = I["page_table"].reshape(1, B * PAGES)
    for i in range(2):
        a[f"mem_k{i}"] = I["cache_mem_k"][i].reshape(B, MEM, 8, P).transpose(0, 3, 2, 1)
        a[f"mem_v{i}"] = I["cache_mem_v"][i].reshape(B, 2, P, D).transpose(0, 2, 1, 3)
    return {k: np.ascontiguousarray(v) for k, v in a.items()}


OUTPUTS = {
    "y": (P, KT, N), "p_gla": (P, 2 * P), "s_gla": (P, B, 2, P), "shift": (P, R_TILES, B + 1),
    "p_rwkv": (P, 4 * 64), "s_rwkv": (P, B, 4, 64), "p_sbk": (P, 4, N), "p_sbv": (P, 4, N),
    "p_delta": (P, 4 * P), "s_delta": (P, B, 4, P), "p_conv": (P, 12, 3), "s_conv": (P, 12, 3, B),
    "p_mk0": (P, 8, MEM), "p_mk1": (P, 8, MEM), "p_mv0": (P, 8, MEM), "p_mv1": (P, 8, MEM),
}


def build(nc, arrays):
    with ExitStack() as ctx:
        dram = {}
        for n, a in arrays.items():
            dt = I32 if a.dtype.kind == "i" else F32
            dram[n] = nc.dram_tensor("in_" + n, list(a.shape), dt, kind="ExternalInput").ap()
        for n, shape in OUTPUTS.items():
            dram[n] = nc.dram_tensor("out_" + n, list(shape), F32, kind="ExternalOutput").ap()
        k = Kernel(nc, dram, ctx)
        k.lin = {}
        for i, n_in in enumerate((EVEN_TILES, ODD_TILES)):
            for n, count, kt in (("in", n_in, KT), ("out", 8, KT), ("xkv", 16, KT), ("xq", 8, KT), ("xo", 8, KT),
                                 ("gu", 2 * FT, KT), ("down", 16, SLOT_K)):
                k.lin[f"{n}{i}"] = Linear(dram[f"w_{n}{i}"], count, kt)
        k.run()


def kernel(**inputs):
    from concourse import bacc
    from concourse.bass_utils import run_bass_kernel_spmd

    arrays = lay_out({k: np.asarray(v) for k, v in inputs.items()})
    nc = bacc.Bacc("TRN2", target_bir_lowering=False, num_devices=1)
    build(nc, arrays)
    r = run_bass_kernel_spmd(nc, [{"in_" + n: a for n, a in arrays.items()}], core_ids=[0]).results[0]
    o = {n: np.asarray(r["out_" + n]) for n in OUTPUTS}

    def token_major(t):
        return np.ascontiguousarray(t.transpose(2, 1, 0).reshape(t.shape[2], -1))

    y, k, v = token_major(o["y"]), token_major(o["p_sbk"]), token_major(o["p_sbv"])
    rwkv = lambda t: t.reshape(2, 64, -1, 4, 64).transpose(2, 3, 0, 4, 1).reshape(-1, 8, 64, 64)
    out = (
        y[None, :T], y[T:, None],
        o["p_gla"].reshape(P, 2, P).transpose(1, 0, 2).reshape(1, 1, 4, 64, P), rwkv(o["p_rwkv"])[None],
        token_major(o["shift"])[None, :1],
        k[:T].reshape(1, 1, T, 8, 64), v[:T].reshape(1, 1, T, 8, 64),
        o["p_delta"].reshape(P, 4, P).transpose(1, 0, 2)[None, None],
        o["p_conv"].transpose(2, 1, 0).reshape(1, 1, 3, 1536),
        np.stack([token_major(o[f"p_mk{i}"]).reshape(1, MEM, 4, 256) for i in range(2)]),
        np.stack([token_major(o[f"p_mv{i}"]).reshape(1, MEM, 4, 256) for i in range(2)]),
        o["s_gla"].transpose(1, 2, 0, 3).reshape(1, B, 4, 64, P), rwkv(o["s_rwkv"])[None],
        token_major(o["shift"])[None, 1:],
        k[T:].reshape(1, B, 1, 8, 64), v[T:].reshape(1, B, 1, 8, 64),
        o["s_delta"].transpose(1, 2, 0, 3)[None],
        o["s_conv"].transpose(3, 2, 1, 0).reshape(1, B, 3, 1536),
    )
    return tuple(np.ascontiguousarray(a) for a in out)
```

```python
from contextlib import ExitStack, contextmanager

import numpy as np
import concourse.bass as bass
import concourse.mybir as mybir

F32 = mybir.dt.float32
F32R = mybir.dt.float32r
U32 = mybir.dt.uint32
I32 = mybir.dt.int32
ACT = mybir.ActivationFunctionType
ALU = mybir.AluOpType
AX = mybir.AxisListType

P = 128
D = 1024
KT = D // P
T = 512
B = 8
N = T + B
HALF = N // 2
NC = T // P
MEM = 256
FT = 2816 // P
PAGE = 128
PAST = 256
PAGES = PAST // PAGE
NPHYS = 20
EPS = 1e-6
RWKV_LN_EPS = 64e-5
SLOTS = 4
SLOT_K = 11

GQ, GK, GV, GG, RR, RK, RV, RWA, RG, GLR, EVEN_TILES = 0, 2, 4, 8, 12, 16, 20, 24, 25, 26, 27
R0, R_TILES = RR, 14
SQ, SK, SV, DQ, DK, DV, DZ, DAB, ODD_TILES = 0, 4, 8, 12, 16, 20, 24, 28, 29

LEVELS = [64, 32, 16, 8, 4, 2, 1]
CONST_NAMES = (["ones", "ident", "head_ones", "key_after", "causal", "before", "causal64", "before64", "forbid"]
               + [f"level{m}" for m in LEVELS])
EPS_AT = 0
FIRST_CONSTS = 4 + P
CONST_AT = {n: 4 + i * P for i, n in enumerate(CONST_NAMES)}
SCAN128_AT = 4 + len(CONST_NAMES) * P
SCAN64_AT = SCAN128_AT + T
SEL_AT = SCAN64_AT + T
CONSTS = SEL_AT + B * P


def constants():
    s, t = np.arange(P)[:, None], np.arange(P)[None, :]
    m = {
        "ident": s == t, "ones": s >= 0 * t, "head_ones": s // 64 == t // 64,
        "key_after": s >= t, "causal": s <= t, "before": s < t,
        "causal64": (s <= t) & (s // 64 == t // 64), "before64": (s < t) & (s // 64 == t // 64),
    }
    for h in LEVELS:
        m[f"level{h}"] = (s // (2 * h) == t // (2 * h)) & (s % (2 * h) < h) & (t % (2 * h) >= h)
    m["forbid"] = np.where(s >= t, -1e30, 0.0)
    out = np.zeros((P, CONSTS), np.float32)
    for n, a in CONST_AT.items():
        out[:, a:a + P] = m[n]
    out[:, SCAN128_AT:SCAN128_AT + T] = np.arange(T) % 128 != 0
    out[:, SCAN64_AT:SCAN64_AT + T] = np.arange(T) % 64 != 0
    for b in range(B):
        out[b, SEL_AT + b * P:SEL_AT + (b + 1) * P] = 1
        out[32 + b, SEL_AT + b * P:SEL_AT + (b + 1) * P] = 1
    out[:, EPS_AT], out[:, EPS_AT + 1] = EPS, RWKV_LN_EPS
    return out


SCR = 13888
MAP = {}
_at = 0
for _name, _size in (("x", KT * N), ("w", SLOTS * SLOT_K * P), ("cst", CONSTS + 4), ("par0", 1368), ("par1", 112),
                     ("rstd", N), ("o", KT * N), ("c", 29 * N), ("h", KT * N), ("scr", SCR)):
    MAP[_name] = _at
    _at += _size
MAP["end"] = _at

EVEN_PARAMS = [("g_mix", 8), ("g_cross", 8), ("g_ffn", 8), ("g_mem", 8), ("xq", 2), ("xk", 2),
               ("gla_b", 2), ("gla_norm", 1), ("mu", 14), ("w0", 4), ("a0", 4), ("k_k", 4), ("k_a", 4), ("r_k", 4),
               ("ln_w", 4), ("ln_b", 4), ("gla_a2", 256), ("wa2", 512), ("g2", 512)]
ODD_PARAMS = [("g_mix", 8), ("g_cross", 8), ("g_ffn", 8), ("g_mem", 8), ("xq", 2), ("xk", 2),
              ("sbq", 1), ("sbk", 1), ("sb_bias", 8), ("dn_conv", 48), ("dn_a", 1), ("dn_dt", 1), ("dn_norm", 1)]
N_EVEN_P = sum(w for _, w in EVEN_PARAMS)
N_ODD_P = sum(w for _, w in ODD_PARAMS)


class Signal:

    def __init__(self, sem):
        self.sem, self.base, self.count = sem, 0, 0

    def at(self, k):
        return self.base + k


class Engine:

    def __init__(self, eng, done):
        self.done = done
        self.eng = eng

    def step(self, ins):
        ins.then_inc(self.done.sem, 1)
        self.done.count += 1
        self.eng.wait_ge(self.done.sem, self.done.count)

    def tell(self, ins, signal):
        ins.then_inc(signal.sem, 1)
        signal.count += 1
        self.eng.wait_ge(signal.sem, signal.count)


class Linear:

    def __init__(self, src, units, kt):
        self.src, self.units, self.kt, self.at = src, units, kt, None


class Split:

    def __init__(self, k, name, tiles, x_hi, x_lo, kt, w_hi, w_lo):
        self.x = [k.place(f"{name}_x_{p}", at, [tiles, N], F32R) for p, at in (("hi", x_hi), ("lo", x_lo))]
        self.w = [k.place(f"{name}_w_{p}", at, [2, kt * P], F32R) for p, at in (("hi", w_hi), ("lo", w_lo))]


class Kernel:

    def __init__(self, nc, dram, ctx):
        self.nc, self.d, self.ctx = nc, dram, ctx
        self.counters = []

        self.arena = ctx.enter_context(nc.sbuf_tensor("arena", [P, MAP["end"]], F32))
        self.arena_at = nc.sbuf_base - 4 * MAP["end"]

        def sb(name, *shape):
            return self.place(name, MAP[name], list(shape), F32)

        self.x = sb("x", KT, N)
        self.h = sb("h", KT, N)
        self.o = sb("o", KT, N)
        self.c = sb("c", 29, N)
        self.w = sb("w", SLOTS, SLOT_K * P)
        self.scr = sb("scr", SCR)
        self.cst = sb("cst", CONSTS)
        self.par0, self.par1 = sb("par0", N_EVEN_P), sb("par1", N_ODD_P)
        self.pages = ctx.enter_context(nc.sbuf_tensor("pages", [1, B * PAGES], I32))
        self.rstd = sb("rstd", N)
        self.std = Split(self, "std", KT, MAP["h"], MAP["scr"], KT, MAP["scr"] + 4160, MAP["scr"] + 6208)
        self.sq = self.cut(8256, KT, N)
        self.tmp = self.cut(12416, 2, N)
        hid = MAP["o"] + 2 * FT * N
        self.mlp = Split(self, "mlp", KT, hid, hid + 4160, KT, hid + 8320, hid + 10368)
        self.mlp_tmp = [self.place(f"mlp_tmp{i}", hid + 12416 + i * N, [N], F32) for i in range(3)]
        self.mlp_norm = self.place("mlp_norm", MAP["o"] + KT * N, [2, N], F32)
        self.hid = Split(self, "hid", FT, MAP["o"], MAP["o"] + FT * N, SLOT_K, hid, hid + 2 * SLOT_K * P)
        self.eps = self.cst[:, EPS_AT:EPS_AT + 1]
        self.ln_eps = self.cst[:, EPS_AT + 1:EPS_AT + 2]
        self.ps = ctx.enter_context(nc.psum_tensor("ps", [P, 8, 512], F32))

        self.weights_loaded = [self.new_counter(f"weights_loaded{i}") for i in range(SLOTS)]
        self.unit_done = self.new_counter("unit_done")
        self.product_read = [self.new_counter(f"product_read{i}") for i in range(2)]
        self.weights_hi = self.new_counter("weights_hi")
        self.weights_split = self.new_counter("weights_split")
        self.plain_ready = self.new_counter("plain_ready")
        self.hi_ready = self.new_counter("hi_ready")
        self.hidden_hi = self.new_counter("hidden_hi")
        self.hidden_lo = self.new_counter("hidden_lo")
        self.inputs_loaded = [self.new_counter(f"inputs_loaded{i}") for i in range(B)]
        self.stored = self.new_counter("stored")
        self.squares_ready = self.new_counter("squares_ready")
        self.squares_odd = self.new_counter("squares_odd")
        self.sums_ready = self.new_counter("sums_ready")
        self.scale_ready = self.new_counter("scale_ready")
        self.normed = self.new_counter("normed")
        self.exp_ready = self.new_counter("exp_ready")
        self.scores_ready = self.new_counter("scores_ready")
        self.keys_used = self.new_counter("keys_used")
        self.values_used = self.new_counter("values_used")
        self.values_loaded = [self.new_counter(f"values_loaded{i}") for i in range(B)]
        self.sample_tensor = self.new_counter("sample_tensor")
        self.sample_scalar = self.new_counter("sample_scalar")
        self.sample_vector = self.new_counter("sample_vector")
        self.cache_scaled = self.new_counter("cache_scaled")
        self.cache_summed = self.new_counter("cache_summed")
        self.delta_loaded = self.new_counter("delta_loaded")
        self.conv_loaded = self.new_counter("conv_loaded")
        self.conv_scaled = self.new_counter("conv_scaled")
        self.conv_summed = self.new_counter("conv_summed")
        self.gate_vector = self.new_counter("gate_vector")
        self.gate_scalar = self.new_counter("gate_scalar")
        self.exponent_ready = self.new_counter("exponent_ready")
        self.weights_ready = self.new_counter("weights_ready")
        self.maxima_ready = self.new_counter("maxima_ready")
        self.tensor_out = self.new_counter("tensor_out")
        self.tensor_out2 = self.new_counter("tensor_out2")
        self.product_kept = self.new_counter("product_kept")
        self.vector_out = self.new_counter("vector_out")
        self.vector_out2 = self.new_counter("vector_out2")
        self.scalar_out = self.new_counter("scalar_out")
        self.scalar_out2 = self.new_counter("scalar_out2")
        self.pool_out = self.new_counter("pool_out")
        self.dve = Engine(nc.vector, self.new_counter("vector_step"))
        self.act = Engine(nc.scalar, self.new_counter("scalar_step"))
        self.pool = Engine(nc.gpsimd, self.new_counter("pool_step"))
        self.ring = 0
        self.stores = 0

    def place(self, name, at, shape, dt):
        return self.nc.alloc_sbuf_tensor_at(name, [P, *shape], dt, offset=self.arena_at + 4 * at)

    def new_counter(self, name):
        s = Signal(self.ctx.enter_context(self.nc.semaphore(name)))
        self.counters.append(s)
        return s

    @contextmanager
    def stage(self):
        for s in self.counters:
            s.base = s.count
        with self.nc.Block() as block:
            yield block

    def const(self, name):
        a = CONST_AT[name]
        return self.cst[:, a:a + P]

    def mask(self, name):
        return self.const(name).bitcast(U32)

    def param(self, name):
        at = 0
        for n, w in self.params[0]:
            if n == name:
                return self.params[1][:, at:at + w]
            at += w
        raise KeyError(name)

    def cut(self, at, *shape):
        n = int(np.prod(shape))
        assert at + n <= SCR, (at, shape)
        flat = self.scr[:, at:at + n]
        if len(shape) == 1:
            return flat
        names = "abcd"[:len(shape)]
        return flat.rearrange(f"p ({' '.join(names)}) -> p {' '.join(names)}", **dict(zip(names, shape)))

    def ln_exp(self):
        self.nc.scalar.preload_act_table_set("natural_log_exp_and_others")

    def store(self, eng, out, in_):
        eng.dma_start(out, in_).then_inc(self.stored.sem, 16)
        self.stored.count += 16

    def load_unit(self, sp, lin, j, slot):
        src = lin.src[j] if isinstance(j, int) else lin.src[bass.ds(j, 1)].rearrange("o p n -> p (o n)")
        sp.dma_start(self.w[:, slot, 0:lin.kt * P], src).then_inc(self.weights_loaded[slot].sem, 16)

    def prefetch(self, sp, lin):
        lin.at = self.ring
        for j in range(SLOTS):
            if lin.at + j >= SLOTS:
                sp.wait_ge(self.weights_split.sem, lin.at + j - SLOTS + 1)
            self.load_unit(sp, lin, j, (lin.at + j) % SLOTS)
        self.ring += lin.units

    def stream(self, sp, lin):
        body = lin.units // SLOTS
        if body > 1:
            with sp.Fori(1, body) as i:
                for u in range(SLOTS):
                    sp.wait_ge(self.weights_split.sem, (i - 1) * SLOTS + (lin.at + u + 1))
                    self.load_unit(sp, lin, i * SLOTS + u, (lin.at + u) % SLOTS)
        for j in range(max(SLOTS, body * SLOTS), lin.units):
            sp.wait_ge(self.weights_split.sem, lin.at + j - SLOTS + 1)
            self.load_unit(sp, lin, j, (lin.at + j) % SLOTS)

    def split_unit(self, dve, lin, site, u, i=0):
        nc = self.nc
        slot, n = (lin.at + u) % SLOTS, lin.kt * P
        raw, hi, lo = self.w[:, slot, 0:n], site.w[0][:, u % 2, 0:n], site.w[1][:, u % 2, 0:n]
        dve.wait_ge(self.weights_loaded[slot].sem, 16 * i + 16 * ((lin.at + u) // SLOTS + 1))
        if u >= 2 or not isinstance(i, int):
            dve.wait_ge(self.unit_done.sem, i * SLOTS + (lin.at + u - 1))
        nc.vector.tensor_copy(hi, raw).then_inc(self.weights_hi.sem, 1)
        dve.wait_ge(self.weights_hi.sem, i * SLOTS + (lin.at + u + 1))
        nc.vector.tensor_tensor(lo, raw, hi.bitcast(F32), ALU.subtract).then_inc(self.weights_split.sem, 1)

    def each_unit(self, dve, lin, site, read=None):
        body = (lin.units - 2) // SLOTS
        with dve.Fori(0, body) as i:
            for u in range(SLOTS):
                if read is not None:
                    read(u, i)
                self.split_unit(dve, lin, site, u + 2, i)
        for j in range(body * SLOTS, lin.units):
            if read is not None:
                read(j, 0)
            if j + 2 < lin.units:
                self.split_unit(dve, lin, site, j + 2)

    def product(self, pe, lin, site, spans, per=1):
        nc = self.nc

        def unit(u, i):
            o = u // per
            pe.wait_ge(self.weights_split.sem, i * SLOTS + (lin.at + u + 1))
            if u % per == 0:
                read = self.product_read[o % 2]
                pe.wait_ge(read.sem, read.base + i * (SLOTS // per // 2) + o // 2)
            hi, lo = (t[:, u % 2, 0:lin.kt * P].rearrange("p (k n) -> p k n", k=lin.kt) for t in site.w)
            for k in range(lin.kt):
                x = k + (u % per) * lin.kt
                if u == 0 and per == 1:
                    pe.wait_ge(self.normed.sem, self.normed.at(k + 1))
                passes = ((hi, site.x[0]), (hi, site.x[1]), (lo, site.x[0]))
                for n, (w, v) in enumerate(passes):
                    first, last = u % per == 0 and k == 0 and n == 0, u % per == per - 1 and k == lin.kt - 1 and n == 2
                    for s, (a, b) in enumerate(spans):
                        ins = nc.tensor.matmul(self.ps[:, 2 * (o % 2) + s, 0:b - a], w[:, k, :], v[:, x, a:b],
                                               start=first, stop=last)
            ins.then_inc(self.unit_done.sem, 1)

        body = lin.units // SLOTS
        with pe.Fori(0, body) as i:
            for u in range(SLOTS):
                unit(u, i)
        for j in range(body * SLOTS, lin.units):
            unit(j, 0)

    def read_tile(self, eng, lin, u, i, read, per=1):
        if u % per == per - 1:
            o = u // per
            eng.wait_ge(self.unit_done.sem, i * SLOTS + (lin.at + u + 1))
            read(i * (SLOTS // per) + o, 2 * (o % 2)).then_inc(self.product_read[o % 2].sem, 1)

    def tiles_read(self, lin, per=1):
        for q in range(2):
            self.product_read[q].count += len(range(q, lin.units // per, 2))

    def read_tiles(self, eng, lin, read, per=1):
        body = lin.units // SLOTS
        with eng.Fori(0, body) as i:
            for u in range(SLOTS):
                self.read_tile(eng, lin, u, i, read, per)
        for j in range(body * SLOTS, lin.units):
            self.read_tile(eng, lin, j, 0, read, per)
        self.tiles_read(lin, per)

    def pair(self, bank, rows=P):
        return self.ps[0:rows, bank:bank + 2, 0:HALF]

    def norm_pe(self, pe, sq, spans):
        nc = self.nc
        for k in range(KT):
            own = self.squares_odd if k % 2 else self.squares_ready
            pe.wait_ge(own.sem, own.at(k // 2 + 1))
            for s, (a, b) in enumerate(spans):
                ins = nc.tensor.matmul(self.ps[:, 6 + s, 0:b - a], self.const("ones"), sq[:, k, a:b],
                                       start=k == 0, stop=k == KT - 1)
        ins.then_inc(self.sums_ready.sem, 1)
        self.sums_ready.count += 1

    def squares(self, x, sq, width):
        for k in range(0, KT, 2):
            self.nc.scalar.activation(sq[:, k, 0:width], x[:, k, 0:width], ACT.Square).then_inc(self.squares_ready.sem, 1)
        self.squares_ready.count += KT // 2

    def norm_act(self, act, x, site, tmp, width, spans, summed):
        nc = self.nc
        if summed is None:
            self.ln_exp()
            act.wait_ge(self.sums_ready.sem, self.sums_ready.at(1))
        n, bank = spans[0][1], 6 if summed is None else summed
        sums = self.ps[:, bank:bank + len(spans), 0:n]
        r = self.rstd[:, 0:width].rearrange("p (s n) -> p s n", n=n)
        self.act.step(nc.scalar.activation(r, sums, ACT.Ln, bias=self.eps, scale=1.0 / D))
        self.act.tell(nc.scalar.activation(self.rstd[:, 0:width], self.rstd[:, 0:width], ACT.Exp, scale=-0.5),
                      self.scale_ready)
        for k in range(KT):
            act.wait_ge(self.plain_ready.sem, self.plain_ready.at(k + 1))
            nc.scalar.activation(site.x[0][:, k, 0:width], tmp[:, k % 2, 0:width], ACT.Copy).then_inc(self.hi_ready.sem, 1)
        self.hi_ready.count += KT

    def norm_pool(self, x, sq, width):
        for k in range(1, KT, 2):
            self.nc.gpsimd.tensor_tensor(sq[:, k, 0:width], x[:, k, 0:width], x[:, k, 0:width], ALU.mult).then_inc(
                self.squares_odd.sem, 1)
        self.squares_odd.count += KT // 2

    def norm_dve(self, dve, x, site, tmp, gain, width):
        nc = self.nc
        dve.wait_ge(self.scale_ready.sem, self.scale_ready.at(1))

        def low(k):
            dve.wait_ge(self.hi_ready.sem, self.hi_ready.at(k + 1))
            self.dve.tell(nc.vector.tensor_tensor(site.x[1][:, k, 0:width], tmp[:, k % 2, 0:width],
                                                  site.x[0][:, k, 0:width].bitcast(F32), ALU.subtract), self.normed)

        for k in range(KT):
            self.dve.tell(nc.vector.scalar_tensor_tensor(tmp[:, k % 2, 0:width], x[:, k, 0:width], gain[:, k:k + 1],
                                                         self.rstd[:, 0:width], ALU.mult, ALU.mult), self.plain_ready)
            if k:
                low(k - 1)
        low(KT - 1)

    SPANS = [(0, HALF), (HALF, N)]

    def start(self):
        nc = self.nc
        with self.stage() as block:
            @block.sync
            def _(sp):
                sp.dma_start(self.x[:], self.d["x"]).then_inc(self.inputs_loaded[0].sem, 16)
                sp.dma_start(self.cst[:, 0:FIRST_CONSTS], self.d["cst"][:, 0:FIRST_CONSTS]).then_inc(self.inputs_loaded[0].sem, 16)
                sp.dma_start(self.par0[:], self.d["par0"]).then_inc(self.inputs_loaded[0].sem, 16)
                self.prefetch(sp, self.lin["in0"])
                sp.dma_start(self.cst[:, FIRST_CONSTS:], self.d["cst"][:, FIRST_CONSTS:]).then_inc(self.inputs_loaded[1].sem, 16)
                sp.dma_start(self.par1[:], self.d["par1"]).then_inc(self.inputs_loaded[1].sem, 16)
                sp.dma_start(self.pages[:], self.d["page_table"]).then_inc(self.inputs_loaded[1].sem, 16)
                sp.wait_ge(self.inputs_loaded[0].sem, self.inputs_loaded[0].at(48))
                self.inputs_loaded[0].count += 48

            @block.vector
            def _(dve):
                for read in self.product_read:
                    self.dve.tell(nc.vector.memset(self.rstd[:], 0.0), read)

    def normed_product(self, lin, x, gain, width, spans, following, read, mem=False, first=False, summed=None):
        with self.stage() as block:
            @block.sync
            def _(sp):
                self.stream(sp, lin)
                self.prefetch(sp, following)
                if first:
                    self.rest_loaded(sp)

            @block.tensor
            def _(pe):
                if summed is None:
                    self.norm_pe(pe, self.sq, spans)
                self.product(pe, lin, self.std, spans)

            @block.scalar
            def _(act):
                if mem:
                    act.wait_ge(self.inputs_loaded[0].sem, self.inputs_loaded[0].at(16))
                if summed is None:
                    self.squares(x, self.sq, width)
                self.norm_act(act, x, self.std, self.tmp, width, spans, summed)
                self.read_tiles(act, lin, read)

            @block.gpsimd
            def _(pool):
                if mem:
                    pool.wait_ge(self.inputs_loaded[0].sem, self.inputs_loaded[0].at(16))
                if summed is None:
                    self.norm_pool(x, self.sq, width)

            @block.vector
            def _(dve):
                for u in range(2):
                    self.split_unit(dve, lin, self.std, u)
                if mem:
                    dve.wait_ge(self.inputs_loaded[0].sem, self.inputs_loaded[0].at(16))
                    self.inputs_loaded[0].count += 16
                self.norm_dve(dve, x, self.std, self.tmp, gain, width)
                self.each_unit(dve, lin, self.std)

    def projection(self, lin, gain, following, first=False):
        self.normed_product(lin, self.x, self.param(gain), N, self.SPANS, following, lambda o, bank: (
            self.nc.scalar.activation(self.tile_pair(self.c, o), self.pair(bank), ACT.Copy)),
                            first=first, summed=None if first else 6)

    def tile_pair(self, t, o):
        one = t[:, bass.ds(o, 1), :] if not isinstance(o, int) else t[:, o:o + 1, :]
        return one.rearrange("p o (s n) -> p (o s) n", s=2)

    def memory_rows(self):
        return self.flat(self.X_A)[:, 0:KT * MEM].rearrange("p (k m) -> p k m", k=KT)

    def residual(self, lin, site, following, per=1, src=None, load_memory=False, summed=6):
        nc = self.nc
        with self.stage() as block:
            @block.sync
            def _(sp):
                if load_memory:
                    sp.dma_start(self.memory_rows(), self.d["mem"]).then_inc(self.inputs_loaded[0].sem, 16)
                self.stream(sp, lin)
                sp.wait_ge(self.stored.sem, self.stored.count)
                if following is not None:
                    self.prefetch(sp, following)

            @block.tensor
            def _(pe):
                self.product(pe, lin, site, self.SPANS, per)
                if summed is not None:
                    for k, ready in ((0, self.pool_out), (KT - 1, self.squares_ready)):
                        pe.wait_ge(ready.sem, ready.at(KT - 2 if k == 0 else KT))
                        for s, (a, b) in enumerate(self.SPANS):
                            nc.tensor.matmul(self.ps[:, summed + s, 0:b - a], self.const("ones"), self.sq[:, k, a:b],
                                             start=k == 0, stop=k == KT - 1)

            @block.scalar
            def _(act):
                if summed is not None:
                    self.ln_exp()
                if src is not None:
                    for k in range(KT):
                        nc.scalar.activation(site.x[0][:, k], src[:, k], ACT.Copy).then_inc(self.hi_ready.sem, 1)
                    self.hi_ready.count += KT
                if summed is not None:
                    for o in range(KT):
                        added = self.product_read[o % 2]
                        act.wait_ge(added.sem, added.at(o // 2 + 1))
                        nc.scalar.activation(self.sq[:, o], self.x[:, o], ACT.Square).then_inc(self.squares_ready.sem, 1)
                    self.squares_ready.count += KT

            @block.gpsimd
            def _(pool):
                if summed is not None:
                    for o in range(1, KT - 1):
                        pool.wait_ge(self.squares_ready.sem, self.squares_ready.at(o + 1))
                        self.pool.tell(nc.gpsimd.tensor_tensor(self.sq[:, 0], self.sq[:, 0], self.sq[:, o], ALU.add),
                                       self.pool_out)

            @block.vector
            def _(dve):
                self.split_unit(dve, lin, site, 0)
                if src is None:
                    self.split_unit(dve, lin, site, 1)
                if src is not None:
                    for k in range(KT):
                        dve.wait_ge(self.hi_ready.sem, self.hi_ready.at(k + 1))
                        self.dve.tell(nc.vector.tensor_tensor(site.x[1][:, k], src[:, k], site.x[0][:, k].bitcast(F32),
                                                              ALU.subtract), self.normed)
                    self.split_unit(dve, lin, site, 1)

                def add(o, bank):
                    return nc.vector.tensor_tensor(self.tile_pair(self.x, o), self.tile_pair(self.x, o), self.pair(bank), ALU.add)
                self.each_unit(dve, lin, site, lambda u, i: self.read_tile(dve, lin, u, i, add, per))
                self.tiles_read(lin, per)

    G_B, G_E, G_Q, G_K, G_P, G_V = 0, 1040, 2064, 4112, 6160, 8208
    G_KT, G_DK, G_S, G_DQ, G_EX = 10256, 11280, 12304, 13328, 13344

    def rest_loaded(self, sp):
        sp.wait_ge(self.inputs_loaded[1].sem, self.inputs_loaded[1].base + 48)
        self.inputs_loaded[1].count += 48

    def gla_gates(self):
        nc, c = self.nc, self.c
        z = self.cut(self.G_Q, 2, N)
        e = self.cut(self.G_K, 2, N)
        b = self.cut(self.G_B, 2, N)
        vt = self.cut(self.G_V, NC, T)
        a2 = self.param("gla_a2")
        with self.stage() as block:
            @block.tensor
            def _(pe):
                for j in range(2):
                    for s, (lo, hi) in enumerate(self.SPANS):
                        ins = nc.tensor.matmul(self.ps[:, 2 * j + s, 0:HALF], a2[0:16, j * P:(j + 1) * P],
                                               c[0:16, GLR, lo:hi], start=True, stop=True)
                ins.then_inc(self.tensor_out.sem, 1)
                self.tensor_out.count += 1
                for t in range(NC):
                    for h in range(4):
                        ins = nc.tensor.transpose(self.ps[:, 4 + t, h * P:(h + 1) * P],
                                                  c[:, GV + h, t * P:(t + 1) * P], self.const("ident"))
                ins.then_inc(self.tensor_out2.sem, 1)
                self.tensor_out2.count += 1

            @block.scalar
            def _(act):
                act.wait_ge(self.vector_out.sem, self.vector_out.at(1))
                self.act.step(nc.scalar.activation(e, e, ACT.Exp))
                self.act.tell(nc.scalar.activation(e, e, ACT.Ln, bias=1.0), self.scalar_out)
                act.wait_ge(self.tensor_out2.sem, self.tensor_out2.at(1))
                self.act.step(nc.scalar.activation(vt.rearrange("p a b -> p (a b)"), self.banks(4, 4), ACT.Copy))
                act.wait_ge(self.vector_out.sem, self.vector_out.at(2))
                self.act.step(nc.scalar.activation(self.cut(self.G_DQ, 2, B), b[:, :, T:N], ACT.Exp))

            @block.gpsimd
            def _(pool):
                self.pool.tell(nc.gpsimd.tensor_scalar(c[:, GQ:GQ + 2, :], c[:, GQ:GQ + 2, :], 0.125, None, ALU.mult),
                               self.pool_out)

            @block.vector
            def _(dve):
                dve.wait_ge(self.tensor_out.sem, self.tensor_out.at(1))
                for j in range(2):
                    self.dve.step(nc.vector.tensor_scalar(z[:, j].rearrange("p (s n) -> p s n", s=2), self.pair(2 * j),
                                                          self.param("gla_b")[:, j:j + 1], None, ALU.add))
                self.dve.tell(nc.vector.scalar_tensor_tensor(e, z, -1.0, z, ALU.mult, ALU.min), self.vector_out)
                dve.wait_ge(self.scalar_out.sem, self.scalar_out.at(1))
                self.dve.step(nc.vector.scalar_tensor_tensor(z, z, 0.0, e, ALU.min, ALU.subtract))
                self.dve.step(nc.vector.tensor_scalar(z, z, 1.0 / 16.0, None, ALU.mult))
                scan = self.cst[:, SCAN128_AT:SCAN128_AT + T]
                for j in range(2):
                    self.dve.step(nc.vector.tensor_tensor_scan(b[:, j, 0:T], scan, z[:, j, 0:T], 0.0, ALU.mult, ALU.add))
                self.dve.tell(nc.vector.tensor_copy(b[:, :, T:N], z[:, :, T:N]), self.vector_out)

    def banks(self, at, n):
        return self.ps[:, at:at + n, :].rearrange("p a b -> p (a b)")

    def gla_levels(self):
        nc, c = self.nc, self.c
        b = self.cut(self.G_B, 2, N)[:, :, 0:T]
        diff = self.cut(self.G_E, 2, T)
        q, k = c[:, GQ:GQ + 2, 0:T], c[:, GK:GK + 2, 0:T]
        qs = [self.cut(self.G_Q + i * 1024, 2, T) for i in range(2)]
        ks = [self.cut(self.G_K + i * 1024, 2, T) for i in range(2)]
        expd = self.cut(self.G_DK, 2, T)
        pt = self.cut(self.G_P, 4, T)
        with self.stage() as block:
            @block.sync
            def _(sp):
                states = self.h[:].rearrange("p a b -> p (a b)")[:, 0:2048].rearrange("p (b j e) -> p b j e", b=B, j=2)
                sp.dma_start(states, self.d["state_gla"]).then_inc(self.inputs_loaded[1].sem, 16)

            @block.scalar
            def _(act):
                for i in range(len(LEVELS)):
                    act.wait_ge(self.vector_out.sem, self.vector_out.at(i + 1))
                    if i:
                        act.wait_ge(self.vector_out2.sem, self.vector_out2.at(i))
                        act.wait_ge(self.pool_out.sem, self.pool_out.at(i))
                    self.act.tell(nc.scalar.activation(expd, diff, ACT.Exp), self.scalar_out)

            @block.gpsimd
            def _(pool):
                for i in range(len(LEVELS)):
                    pool.wait_ge(self.scalar_out.sem, self.scalar_out.at(i + 1))
                    if i >= 2:
                        pool.wait_ge(self.tensor_out.sem, self.tensor_out.at(i - 1))
                    self.pool.tell(nc.gpsimd.tensor_tensor(qs[i % 2], q, expd, ALU.mult), self.pool_out)

            @block.vector
            def _(dve):
                self.dve.step(nc.vector.memset(pt, 0.0))

                def keep(i, name):
                    dve.wait_ge(self.tensor_out.sem, self.tensor_out.at(i + 1))
                    m = self.mask(name).unsqueeze(1).to_broadcast([P, NC, P])
                    for j in range(4):
                        ins = nc.vector.copy_predicated(pt[:, j].rearrange("p (c t) -> p c t", c=NC), m,
                                                        self.ps[:, 4 * (i % 2) + j, :].rearrange("p (c t) -> p c t", c=NC))
                        if j < 3:
                            self.dve.step(ins)
                        else:
                            self.dve.tell(ins, self.product_kept)

                for i, m in enumerate(LEVELS):
                    if i:
                        dve.wait_ge(self.scalar_out.sem, self.scalar_out.at(i))
                    bv = b.rearrange("p j (g w) -> p j g w", w=2 * m)
                    dv = diff.rearrange("p j (g w) -> p j g w", w=2 * m)
                    for j in range(2):
                        ref = bv[:, j, :, m - 1:m].to_broadcast([P, T // (2 * m), 2 * m])
                        self.dve.step(nc.vector.tensor_tensor(dv[:, j], bv[:, j], ref, ALU.subtract))
                    self.dve.tell(nc.vector.scalar_tensor_tensor(diff, diff, -1.0, diff, ALU.mult, ALU.min),
                                  self.vector_out)
                    dve.wait_ge(self.scalar_out.sem, self.scalar_out.at(i + 1))
                    if i >= 2:
                        dve.wait_ge(self.tensor_out.sem, self.tensor_out.at(i - 1))
                    self.dve.tell(nc.vector.tensor_tensor(ks[i % 2], k, expd, ALU.mult), self.vector_out2)
                    if i:
                        keep(i - 1, f"level{LEVELS[i - 1]}")
                keep(len(LEVELS) - 1, "level1")
                keep(len(LEVELS), "ident")

            @block.tensor
            def _(pe):
                for i in range(len(LEVELS) + 1):
                    if i < len(LEVELS):
                        pe.wait_ge(self.pool_out.sem, self.pool_out.at(i + 1))
                        pe.wait_ge(self.vector_out2.sem, self.vector_out2.at(i + 1))
                    if i >= 2:
                        pe.wait_ge(self.product_kept.sem, self.product_kept.at(i - 1))
                    lq, lk = (qs[i % 2], ks[i % 2]) if i < len(LEVELS) else (q, k)
                    for par in range(2):
                        rows = slice(64 * par, 64 * par + 64)
                        for hp in range(2):
                            for t in range(NC):
                                cols = slice(t * P, (t + 1) * P)
                                ins = nc.tensor.matmul(self.ps[:, 4 * (i % 2) + 2 * par + hp, cols], lk[rows, hp, cols],
                                                       lq[rows, hp, cols], start=True, stop=True)
                    ins.then_inc(self.tensor_out.sem, 1)
                    self.tensor_out.count += 1

    def shift_parts(self):
        nc = self.nc
        d = self.cut(self.G_DK, T)
        sh, ds = self.cut(self.G_DK + T, R_TILES, B), self.cut(self.G_DK + T + 112, R_TILES, B)
        last = self.cut(self.G_DK + T + 224, R_TILES, B + 1)
        r = self.c[:, R0:R0 + R_TILES, :]

        def first(dve):
            dve.wait_ge(self.inputs_loaded[0].sem, self.inputs_loaded[0].at(16))
            self.inputs_loaded[0].count += 16
            dve.wait_ge(self.squares_ready.sem, self.squares_ready.at(1))
            self.dve.step(nc.vector.tensor_tensor(ds, sh, r[:, :, T:N], ALU.subtract))

        def tiles(lo, hi):
            for j in range(lo, hi):
                mu = self.param("mu")[:, j:j + 1]
                nc.vector.tensor_scalar(d[:, 0:1], r[:, j, 0:1], -1.0, None, ALU.mult)
                self.dve.step(nc.vector.tensor_tensor(d[:, 1:T], r[:, j, 0:T - 1], r[:, j, 1:T], ALU.subtract))
                nc.vector.scalar_tensor_tensor(r[:, j, T:N], ds[:, j], mu, r[:, j, T:N], ALU.mult, ALU.add)
                self.dve.step(nc.vector.scalar_tensor_tensor(r[:, j, 0:T], d, mu, r[:, j, 0:T], ALU.mult, ALU.add))
        return sh, last, r, first, tiles

    def gla_states(self):
        nc, c = self.nc, self.c
        b = self.cut(self.G_B, 2, N)[:, :, 0:T]
        pt = self.cut(self.G_P, 4, T)
        vt = self.cut(self.G_V, NC, 4, P)
        qe = self.cut(self.G_Q, 2, T)
        ke = self.cut(self.G_K, 2, T)
        ex = self.cut(self.G_Q + 1024, 2, T)
        diff = self.cut(self.G_E, 2, T)
        kt = self.cut(self.G_KT, NC, 2 * P)
        st = self.cut(self.G_K + 1024, NC, 2 * P)
        dlast = self.cut(self.G_EX, 2, NC)
        fs = self.cut(self.G_DQ, 2, B)
        ss = self.h[:].rearrange("p a b -> p (a b)")[:, 0:2048].rearrange("p (b j e) -> p b j e", b=B, j=2)
        kv = self.h[:].rearrange("p a b -> p (a b)")[:, 2048:4096].rearrange("p (b j e) -> p b j e", b=B, j=2)
        vs = self.cut(self.G_EX + 8, 4, P)
        sh, last_rows, rows_r, shift_first, shift_tiles = self.shift_parts()
        with self.stage() as block:
            @block.sync
            def _(sp):
                sp.dma_start(sh, self.d["state_shift"]).then_inc(self.inputs_loaded[0].sem, 16)
                sp.wait_ge(self.squares_ready.sem, self.squares_ready.at(1))
                self.store(sp, self.d["shift"], last_rows)
                sp.wait_ge(self.vector_out2.sem, self.vector_out2.at(1))
                self.store(sp, self.d["p_gla"], st[:, NC - 1])
                sp.wait_ge(self.pool_out.sem, self.pool_out.at(3))
                self.store(sp, self.d["s_gla"], ss)
                sp.wait_ge(self.stored.sem, self.stored.count)

            @block.scalar
            def _(act):
                self.act.tell(nc.scalar.activation(ex, b, ACT.Exp), self.scalar_out)
                self.act.tell(nc.scalar.activation(last_rows, rows_r[:, :, T - 1:N], ACT.Copy), self.squares_ready)
                act.wait_ge(self.vector_out.sem, self.vector_out.at(1))
                self.act.tell(nc.scalar.activation(diff, diff, ACT.Exp), self.scalar_out)
                last = b.rearrange("p j (c w) -> p j c w", c=NC)[:, :, :, P - 1]
                self.act.tell(nc.scalar.activation(dlast, last, ACT.Exp), self.scalar_out)
                act.wait_ge(self.tensor_out.sem, self.tensor_out.at(1))
                self.act.tell(nc.scalar.activation(vs[0:B].rearrange("p a b -> p (a b)"), self.ps[0:B, 4, :], ACT.Copy),
                              self.scalar_out)
                act.wait_ge(self.tensor_out.sem, self.tensor_out.at(2))
                self.act.tell(nc.scalar.activation(kt.rearrange("p a b -> p (a b)"), self.banks(2, 2), ACT.Copy),
                              self.scalar_out)
                act.wait_ge(self.tensor_out.sem, self.tensor_out.at(5))
                self.act.step(nc.scalar.activation(self.o[:, 0:4, 0:T], self.ps[:, 0:4, :], ACT.Copy))
                act.wait_ge(self.tensor_out.sem, self.tensor_out.at(6))
                for par in range(2):
                    self.act.step(nc.scalar.activation(self.o[:, par:4:2, T:N],
                                  self.ps[:, 4 + par, 0:2 * B].rearrange("p (j b) -> p j b", b=B), ACT.Copy))

            @block.vector
            def _(dve):
                for j in range(2):
                    bj = b[:, j].rearrange("p (c w) -> p c w", c=NC)
                    ref = bj[:, :, P - 1:P].to_broadcast([P, NC, P])
                    ins = nc.vector.tensor_tensor(diff[:, j].rearrange("p (c w) -> p c w", c=NC), ref, bj, ALU.subtract)
                    self.dve.step(ins) if j == 0 else self.dve.tell(ins, self.vector_out)
                shift_first(dve)
                dve.wait_ge(self.scalar_out.sem, self.scalar_out.at(2))
                self.dve.tell(nc.vector.tensor_tensor(ke, c[:, GK:GK + 2, 0:T], diff, ALU.mult), self.vector_out)
                self.dve.tell(nc.vector.tensor_tensor(qe, c[:, GQ:GQ + 2, 0:T], ex, ALU.mult), self.vector_out)
                shift_tiles(0, 3)
                dve.wait_ge(self.tensor_out.sem, self.tensor_out.at(3))
                for t in range(NC):
                    for j in range(2):
                        out, new = st[:, t, j * P:(j + 1) * P], self.ps[:, 2 + t // 2, (t % 2) * 256 + j * P:(t % 2) * 256 + (j + 1) * P]
                        if t == 0:
                            ins = nc.vector.tensor_copy(out, new)
                        else:
                            ins = nc.vector.scalar_tensor_tensor(out, st[:, t - 1, j * P:(j + 1) * P], dlast[:, j, t:t + 1],
                                                                 new, ALU.mult, ALU.add)
                        if t == NC - 1 and j == 1:
                            self.dve.tell(ins, self.vector_out2)
                        else:
                            self.dve.step(ins)
                dve.wait_ge(self.tensor_out.sem, self.tensor_out.at(4))
                for b0 in range(0, B, 2):
                    k2 = c[:, GK:GK + 2, T + b0:T + b0 + 2].rearrange("p j b -> p b j").unsqueeze(3)
                    self.dve.tell(nc.vector.tensor_tensor(
                        kv[:, b0:b0 + 2], self.ps[:, 4 + b0 // 2, :].rearrange("p (b j e) -> p b j e", b=2, j=2),
                        k2.to_broadcast([P, 2, 2, P]), ALU.mult), self.vector_out)
                shift_tiles(3, R_TILES)

            @block.gpsimd
            def _(pool):
                pool.wait_ge(self.inputs_loaded[1].sem, self.inputs_loaded[1].at(16))
                self.inputs_loaded[1].count += 16
                for j in range(2):
                    f = fs[:, j].unsqueeze(2).to_broadcast([P, B, P])
                    self.pool.tell(nc.gpsimd.tensor_tensor(ss[:, :, j], ss[:, :, j], f, ALU.mult), self.pool_out)
                pool.wait_ge(self.vector_out.sem, self.vector_out.at(7))
                self.pool.tell(nc.gpsimd.tensor_tensor(ss, ss, kv, ALU.add), self.pool_out)

            @block.tensor
            def _(pe):
                for h in range(4):
                    ins = nc.tensor.transpose(self.ps[0:B, 4, h * P:(h + 1) * P], c[:, GV + h, T:N], self.const("ident"))
                ins.then_inc(self.tensor_out.sem, 1)
                pe.wait_ge(self.vector_out.sem, self.vector_out.at(2))
                for t in range(NC):
                    for j in range(2):
                        ins = nc.tensor.transpose(self.ps[:, 2 + t // 2, (t % 2) * 256 + j * P:(t % 2) * 256 + (j + 1) * P],
                                                  ke[:, j, t * P:(t + 1) * P], self.const("ident"))
                ins.then_inc(self.tensor_out.sem, 1)
                pe.wait_ge(self.scalar_out.sem, self.scalar_out.at(5))
                for t in range(NC):
                    for h in range(4):
                        rows = slice(64 * (h % 2), 64 * (h % 2) + 64)
                        at = (t % 2) * 256 + (h // 2) * P
                        ins = nc.tensor.matmul(self.ps[rows, 2 + t // 2, at:at + P],
                                               kt[:, t, (h // 2) * P + rows.start:(h // 2) * P + rows.stop],
                                               vt[:, t, h], start=True, stop=True)
                ins.then_inc(self.tensor_out.sem, 1)
                pe.wait_ge(self.scalar_out.sem, self.scalar_out.at(4))
                for b0 in range(B):
                    for par in range(2):
                        ins = nc.tensor.matmul(self.ps[64 * par:64 * par + 64, 4 + b0 // 2, (b0 % 2) * 256:(b0 % 2) * 256 + 256],
                                               self.cst[0:B, SEL_AT + b0 * P:SEL_AT + b0 * P + 64],
                                               vs[0:B, par:4:2, :], start=True, stop=True)
                ins.then_inc(self.tensor_out.sem, 1)
                pe.wait_ge(self.vector_out.sem, self.vector_out.at(3))
                pe.wait_ge(self.vector_out2.sem, self.vector_out2.at(1))
                for h in range(4):
                    rows = slice(64 * (h % 2), 64 * (h % 2) + 64)
                    for t in range(NC):
                        cols = slice(t * P, (t + 1) * P)
                        out = self.ps[:, h, cols]
                        if t:
                            nc.tensor.matmul(out, st[rows, t - 1, (h // 2) * P:(h // 2 + 1) * P], qe[rows, h // 2, cols],
                                             start=True, stop=False)
                        ins = nc.tensor.matmul(out, vt[:, t, h], pt[:, 2 * (h % 2) + h // 2, cols], start=t == 0, stop=True)
                ins.then_inc(self.tensor_out.sem, 1)
                pe.wait_ge(self.pool_out.sem, self.pool_out.at(3))
                for par in range(2):
                    rows = slice(64 * par, 64 * par + 64)
                    for j in range(2):
                        for b0 in range(B):
                            at = j * B + b0
                            ins = nc.tensor.matmul(self.ps[:, 4 + par, at:at + 1], ss[rows, b0, j],
                                                   c[rows, GQ + j, T + b0:T + b0 + 1], start=True, stop=True)
                ins.then_inc(self.tensor_out.sem, 1)
                self.tensor_out.count += 6

    def gated_norm(self, n, gate, gain):
        nc, c = self.nc, self.c
        o = self.o[:, n:n + 4, :]
        sq, sg = self.cut(0, 4, N), self.cut(4 * N, 4, N)
        r = self.cut(8 * N, 4, N)
        with self.stage() as block:
            @block.scalar
            def _(act):
                for h in range(4):
                    self.act.tell(nc.scalar.activation(sq[:, h], o[:, h], ACT.Square), self.squares_ready)
                self.act.tell(nc.scalar.activation(sg, c[:, gate:gate + 4, :], ACT.Sigmoid), self.scalar_out)
                self.ln_exp()
                act.wait_ge(self.tensor_out.sem, self.tensor_out.at(1))
                self.act.step(nc.scalar.activation(r.rearrange("p h (s n) -> p (h s) n", s=2), self.ps[:, 0:8, 0:HALF],
                                                   ACT.Ln, bias=self.eps, scale=1.0 / P))
                self.act.tell(nc.scalar.activation(r, r, ACT.Exp, scale=-0.5), self.scalar_out)

            @block.tensor
            def _(pe):
                for h in range(4):
                    pe.wait_ge(self.squares_ready.sem, self.squares_ready.at(h + 1))
                    for s, (lo, hi) in enumerate(self.SPANS):
                        ins = nc.tensor.matmul(self.ps[:, 2 * h + s, 0:HALF], self.const("ones"), sq[:, h, lo:hi],
                                               start=True, stop=True)
                ins.then_inc(self.tensor_out.sem, 1)
                self.tensor_out.count += 1

            @block.vector
            def _(dve):
                dve.wait_ge(self.scalar_out.sem, self.scalar_out.at(1))
                self.dve.step(nc.vector.tensor_tensor(sg, sg, c[:, gate:gate + 4, :], ALU.mult))
                self.dve.step(nc.vector.scalar_tensor_tensor(sg, sg, self.param(gain)[:, 0:1], o, ALU.mult, ALU.mult))
                dve.wait_ge(self.scalar_out.sem, self.scalar_out.at(2))
                self.dve.step(nc.vector.tensor_tensor(o, sg, r, ALU.mult))

    W_KK, W_A, W_B, W_C, W_BON, W_DL, W_DS, W_1KA, W_FREE = 0, 2080, 4160, 6240, 8320, 10400, 10432, 10464, 10468
    C_G, C_A, C_W = 0, 4, 8
    OUT = 4

    def rwkv_low_rank(self):
        nc, c = self.nc, self.c
        wa2, g2 = self.param("wa2"), self.param("g2")
        with self.stage() as block:
            @block.sync
            def _(sp):
                states = self.h[:].rearrange("p a b -> p (a b)")[:, 0:2048].rearrange("p (b j i) -> p b j i", b=B, j=4)
                sp.dma_start(states, self.d["state_rwkv"]).then_inc(self.inputs_loaded[1].sem, 16)

            @block.scalar
            def _(act):
                self.act.step(nc.scalar.activation(c[0:64, RWA], c[0:64, RWA], ACT.Tanh))
                self.act.tell(nc.scalar.activation(c[:, RG], c[:, RG], ACT.Sigmoid), self.scalar_out)
                for n in range(8):
                    act.wait_ge(self.tensor_out.sem, self.tensor_out.at(n + 1))
                    at, bias = (self.C_W, "w0") if n < 4 else (self.C_A, "a0")
                    j = n % 4
                    nc.scalar.activation(self.tile_pair(c, at + j), self.pair(2 * (n % 4)), ACT.Sigmoid,
                                         bias=self.param(bias)[:, j:j + 1]).then_inc(self.scalar_out.sem, 1)
                self.scalar_out.count += 8

            @block.vector
            def _(dve):
                for j in range(4):
                    dve.wait_ge(self.scalar_out.sem, self.scalar_out.at(2 + j))
                    nc.vector.tensor_scalar(c[:, self.C_W + j], c[:, self.C_W + j], -float(np.exp(-0.5)), None, ALU.mult)
                for j in range(4):
                    dve.wait_ge(self.tensor_out.sem, self.tensor_out.at(9 + j))
                    self.dve.step(nc.vector.tensor_copy(self.tile_pair(c, self.C_G + j), self.pair(2 * j)))

            @block.tensor
            def _(pe):
                pe.wait_ge(self.scalar_out.sem, self.scalar_out.at(1))
                for n in range(12):
                    if n >= 4:
                        pe.wait_ge(self.scalar_out.sem, self.scalar_out.at(n - 2))
                    rows = (slice(0, 64), slice(64, P), slice(0, P))[n // 4]
                    w, src = (g2, RG) if n >= 8 else (wa2, RWA)
                    for s, (lo, hi) in enumerate(self.SPANS):
                        ins = nc.tensor.matmul(self.ps[:, 2 * (n % 4) + s, 0:HALF], w[rows, (n % 4) * P:(n % 4 + 1) * P],
                                               c[rows, src, lo:hi], start=True, stop=True)
                    ins.then_inc(self.tensor_out.sem, 1)
                self.tensor_out.count += 12

    def eight(self, t):
        return t.rearrange("p a (s n) -> p (a s) n", s=2)

    def head_sums(self, pe, src, ready, k):
        nc = self.nc
        pe.wait_ge(ready.sem, ready.at(k))
        for j in range(4):
            for s, (lo, hi) in enumerate(self.SPANS):
                ins = nc.tensor.matmul(self.ps[:, 2 * j + s, 0:HALF], self.const("head_ones"), src[:, j, lo:hi],
                                       start=True, stop=True)
        ins.then_inc(self.tensor_out.sem, 1)
        self.tensor_out.count += 1

    def rwkv_vectors(self):
        nc, c = self.nc, self.c
        kk, wa, wb, wc, bon = (self.cut(x, 4, N) for x in (self.W_KK, self.W_A, self.W_B, self.W_C, self.W_BON))
        one_ka = self.cut(self.W_1KA, 4)
        dl, ds = self.cut(self.W_DL, 4, 8), self.cut(self.W_DS, 4, B)
        r, k, v = c[:, RR:RR + 4], c[:, RK:RK + 4], c[:, RV:RV + 4]
        a, lw = c[:, self.C_A:self.C_A + 4], c[:, self.C_W:self.C_W + 4]
        banks = self.ps[:, :, 0:HALF]
        with self.stage() as block:
            @block.vector
            def _(dve):
                for j in range(4):
                    ins = nc.vector.tensor_scalar(kk[:, j], k[:, j], self.param("k_k")[:, j:j + 1], None, ALU.mult)
                    self.dve.step(ins) if j < 3 else self.dve.tell(ins, self.vector_out)
                self.dve.step(nc.vector.tensor_scalar(one_ka, self.param("k_a"), -1.0, 1.0, ALU.mult, ALU.add))
                for j in range(4):
                    self.dve.step(nc.vector.tensor_scalar(wb[:, j], a[:, j], self.param("k_a")[:, j:j + 1],
                                                          one_ka[:, j:j + 1], ALU.mult, ALU.add))
                self.dve.step(nc.vector.tensor_tensor(k, k, wb, ALU.mult))
                for j in range(4):
                    ins = nc.vector.scalar_tensor_tensor(wc[:, j], r[:, j], self.param("r_k")[:, j:j + 1], k[:, j],
                                                         ALU.mult, ALU.mult)
                    self.dve.step(ins) if j < 3 else self.dve.tell(ins, self.vector_out)
                dve.wait_ge(self.scalar_out.sem, self.scalar_out.at(2))
                self.dve.step(nc.vector.tensor_tensor(kk, kk, wa, ALU.mult))
                self.dve.step(nc.vector.tensor_tensor(a, a, kk, ALU.mult))
                cw = wa[:, :, 0:T]
                scan = self.cst[:, SCAN64_AT:SCAN64_AT + T]
                for j in range(4):
                    self.dve.step(nc.vector.tensor_tensor_scan(cw[:, j], scan, lw[:, j, 0:T], 0.0, ALU.mult, ALU.add))
                self.dve.tell(nc.vector.tensor_tensor(lw[:, :, 0:T], cw, lw[:, :, 0:T], ALU.subtract), self.vector_out)
                dve.wait_ge(self.tensor_out.sem, self.tensor_out.at(2))
                self.dve.step(nc.vector.tensor_tensor(self.eight(bon), banks, self.eight(v), ALU.mult))
                p = slice(0, T)
                dve.wait_ge(self.scalar_out.sem, self.scalar_out.at(3))
                self.dve.step(nc.vector.tensor_tensor(r[:, :, p], r[:, :, p], wb[:, :, p], ALU.mult))
                dve.wait_ge(self.scalar_out.sem, self.scalar_out.at(4))
                self.dve.step(nc.vector.tensor_tensor(a[:, :, p], a[:, :, p], wc[:, :, p], ALU.mult))
                self.dve.step(nc.vector.tensor_tensor(k[:, :, p], k[:, :, p], wc[:, :, p], ALU.mult))
                dve.wait_ge(self.scalar_out.sem, self.scalar_out.at(5))
                self.dve.step(nc.vector.scalar_tensor_tensor(kk[:, :, p], kk[:, :, p], -1.0, lw[:, :, p],
                                                             ALU.mult, ALU.mult))

            @block.scalar
            def _(act):
                act.wait_ge(self.vector_out.sem, self.vector_out.at(1))
                self.act.tell(nc.scalar.activation(wa, kk, ACT.Square), self.scalar_out)
                act.wait_ge(self.tensor_out.sem, self.tensor_out.at(1))
                self.act.step(nc.scalar.activation(self.eight(wa), banks, ACT.Ln, bias=self.eps))
                self.act.tell(nc.scalar.activation(wa, wa, ACT.Exp, scale=-0.5), self.scalar_out)
                act.wait_ge(self.vector_out.sem, self.vector_out.at(3))
                self.act.tell(nc.scalar.activation(wb[:, :, 0:T], wa[:, :, 0:T], ACT.Exp), self.scalar_out)
                act.wait_ge(self.tensor_out.sem, self.tensor_out.at(2))
                self.act.tell(nc.scalar.activation(wc[:, :, 0:T], wa[:, :, 0:T], ACT.Exp, scale=-1.0), self.scalar_out)
                self.act.tell(nc.scalar.activation(lw, lw, ACT.Exp), self.scalar_out)
                last = wa[:, :, 0:T].rearrange("p j (c w) -> p j c w", w=64)[:, :, :, 63]
                self.act.step(nc.scalar.activation(dl, last, ACT.Exp))

            @block.tensor
            def _(pe):
                self.head_sums(pe, wa, self.scalar_out, 1)
                pe.wait_ge(self.scalar_out.sem, self.scalar_out.at(2))
                self.head_sums(pe, wc, self.vector_out, 2)

    def rwkv_sample(self):
        nc, c = self.nc, self.c
        kk = self.cut(self.W_KK, 4, N)
        hf = self.h[:].rearrange("p a b -> p (a b)")
        ss, pr = (hf[:, x:x + 2048].rearrange("p (b j i) -> p b j i", b=B, j=4) for x in (0, 2048))
        t2 = self.cut(self.W_A, B, 4, 64)
        vs = self.cut(self.W_FREE, 4, P)

        def by_seq(t, lo=0):
            return t[:, :, T:N].rearrange("p j b -> p b j").unsqueeze(3).to_broadcast([P, B, 4, 64])

        with self.stage() as block:
            @block.sync
            def _(sp):
                sp.wait_ge(self.vector_out.sem, self.vector_out.at(4))
                self.store(sp, self.d["s_rwkv"], ss)
                sp.wait_ge(self.stored.sem, self.stored.count)

            @block.tensor
            def _(pe):
                for j in range(4):
                    ins = nc.tensor.transpose(self.ps[0:B, 4, j * P:(j + 1) * P], c[:, RV + j, T:N], self.const("ident"))
                ins.then_inc(self.tensor_out.sem, 1)
                pe.wait_ge(self.vector_out.sem, self.vector_out.at(1))
                flat = pr.rearrange("p b j i -> p (b j i)")
                for n in range(4):
                    ins = nc.tensor.matmul(self.ps[:, n, :], self.const("head_ones"), flat[:, n * 512:(n + 1) * 512],
                                           start=True, stop=True)
                ins.then_inc(self.tensor_out.sem, 1)
                pe.wait_ge(self.scalar_out.sem, self.scalar_out.at(1))
                vh = vs[0:B].rearrange("p j (q i) -> p j q i", q=2)
                for b0 in range(B):
                    for par in range(2):
                        ins = nc.tensor.matmul(self.ps[64 * par:64 * par + 64, 4 + b0 // 2, (b0 % 2) * 256:(b0 % 2) * 256 + 256],
                                               self.cst[0:B, SEL_AT + b0 * P:SEL_AT + b0 * P + 64], vh[:, :, par, :],
                                               start=True, stop=True)
                ins.then_inc(self.tensor_out.sem, 1)
                pe.wait_ge(self.vector_out.sem, self.vector_out.at(4))
                for par in range(2):
                    rows = slice(64 * par, 64 * par + 64)
                    for j in range(4):
                        for b0 in range(B):
                            at = j * B + b0
                            ins = nc.tensor.matmul(self.ps[rows, par, at:at + 1], ss[rows, b0, j], c[rows, RR + j, T + b0:T + b0 + 1],
                                                   start=True, stop=True)
                ins.then_inc(self.tensor_out.sem, 1)
                self.tensor_out.count += 4

            @block.scalar
            def _(act):
                act.wait_ge(self.tensor_out.sem, self.tensor_out.at(1))
                self.act.tell(nc.scalar.activation(vs[0:B].rearrange("p a b -> p (a b)"), self.ps[0:B, 4, :], ACT.Copy),
                              self.scalar_out)
                act.wait_ge(self.tensor_out.sem, self.tensor_out.at(4))
                for par in range(2):
                    rows = slice(64 * par, 64 * par + 64)
                    self.act.step(nc.scalar.activation(self.o[rows, self.OUT:self.OUT + 4, T:N],
                                  self.ps[rows, par, 0:4 * B].rearrange("p (j b) -> p j b", b=B), ACT.Copy))

            @block.gpsimd
            def _(pool):
                pool.wait_ge(self.vector_out.sem, self.vector_out.at(1))
                self.pool.tell(nc.gpsimd.tensor_tensor(ss, ss, by_seq(c[:, self.C_W:self.C_W + 4]), ALU.mult), self.pool_out)

            @block.vector
            def _(dve):
                dve.wait_ge(self.inputs_loaded[1].sem, self.inputs_loaded[1].at(16))
                self.inputs_loaded[1].count += 16
                self.dve.tell(nc.vector.tensor_tensor(pr, ss, by_seq(kk), ALU.mult), self.vector_out)
                dve.wait_ge(self.tensor_out.sem, self.tensor_out.at(2))
                self.dve.step(nc.vector.tensor_tensor(pr, self.banks(0, 4).rearrange("p (b j i) -> p b j i", b=B, j=4),
                                                      by_seq(c[:, self.C_A:self.C_A + 4]), ALU.mult))
                dve.wait_ge(self.pool_out.sem, self.pool_out.at(1))
                self.dve.tell(nc.vector.tensor_tensor(ss, ss, pr, ALU.subtract), self.vector_out)
                dve.wait_ge(self.tensor_out.sem, self.tensor_out.at(3))
                self.dve.tell(nc.vector.tensor_tensor(t2, self.banks(4, 4).rearrange("p (b j i) -> p b j i", b=B, j=4),
                                                      by_seq(c[:, RK:RK + 4]), ALU.mult), self.vector_out)
                self.dve.tell(nc.vector.tensor_tensor(ss, ss, t2, ALU.add), self.vector_out)

    def unit_inverses(self, groups, streams, masks, lt_at, t_at, x_at, inv, fill):
        nc = self.nc
        lt, tt, xx = ([self.cut(at + 1024 * i, 8, P) for i in range(streams)] for at in (lt_at, t_at, x_at))
        factor, levels = masks
        ident = self.const("ident").unsqueeze(1)

        def bank(i):
            return self.ps[:, 4 * i:4 * i + 2, :], self.ps[:, 4 * i + 2:4 * i + 4, :]

        def eight(a):
            return a.rearrange("p a (b t) -> p (a b) t", t=P)

        n_level = len(levels)
        with self.stage() as block:
            @block.tensor
            def _(pe):
                made = copied = masked = 0
                for g0 in range(0, groups, streams):
                    for i in range(streams):
                        if g0:
                            pe.wait_ge(self.vector_out.sem, self.vector_out.at((g0 // streams) * streams * (n_level + 1) - streams + i + 1))
                        fill(pe, g0 + i, 4 * i + 2)
                        self.tensor_out.count += 1
                    for n in range(n_level):
                        base_v = (g0 // streams) * streams * (n_level + 1)
                        base_s = (g0 // streams) * streams * (2 * n_level - 2)
                        if n:
                            for i in range(streams):
                                pe.wait_ge(self.scalar_out.sem, self.scalar_out.at(base_s + (2 * n - 2) * streams + i + 1))
                                for h in range(8):
                                    ins = nc.tensor.matmul(self.ps[:, 4 * i + h // 4, (h % 4) * P:(h % 4 + 1) * P], lt[i][:, h],
                                                           tt[i][:, h], start=True, stop=True)
                                ins.then_inc(self.tensor_out.sem, 1)
                                self.tensor_out.count += 1
                            for i in range(streams):
                                pe.wait_ge(self.scalar_out.sem, self.scalar_out.at(base_s + (2 * n - 1) * streams + i + 1))
                                for h in range(8):
                                    ins = nc.tensor.matmul(self.ps[:, 4 * i + 2 + h // 4, (h % 4) * P:(h % 4 + 1) * P], xx[i][:, h],
                                                           inv[g0 + i][:, h], start=True, stop=True)
                                ins.then_inc(self.tensor_out.sem, 1)
                                self.tensor_out.count += 1
                        if n < n_level - 1:
                            for i in range(streams):
                                pe.wait_ge(self.vector_out.sem, self.vector_out.at(base_v + (n + 1) * streams + i + 1))
                                for h in range(8):
                                    ins = nc.tensor.transpose(self.ps[:, 4 * i + h // 4, (h % 4) * P:(h % 4 + 1) * P],
                                                              inv[g0 + i][:, h], self.const("ident"))
                                ins.then_inc(self.tensor_out.sem, 1)
                                self.tensor_out.count += 1

            per = 3 * n_level - 2

            def product_at(g0, k, i):
                return self.tensor_out.at((g0 // streams) * streams * per + k * streams + i + 1)

            @block.scalar
            def _(act):
                for g0 in range(0, groups, streams):
                    for n in range(n_level):
                        if n:
                            for i in range(streams):
                                act.wait_ge(self.tensor_out.sem, product_at(g0, 3 * n - 1, i))
                                self.act.tell(nc.scalar.activation(xx[i], eight(bank(i)[0]), ACT.Copy), self.scalar_out)
                        if n < n_level - 1:
                            for i in range(streams):
                                act.wait_ge(self.tensor_out.sem, product_at(g0, 3 * n + 1, i))
                                self.act.tell(nc.scalar.activation(tt[i], eight(bank(i)[0]), ACT.Copy), self.scalar_out)

            @block.vector
            def _(dve):
                for g0 in range(0, groups, streams):
                    for i in range(streams):
                        dve.wait_ge(self.tensor_out.sem, product_at(g0, 0, i))
                        self.dve.tell(nc.vector.tensor_tensor(lt[i], eight(bank(i)[1]), factor(g0 + i), ALU.mult),
                                      self.vector_out)
                    for n, level in enumerate(levels):
                        m = self.const(level).unsqueeze(1).to_broadcast([P, 8, P])
                        for i in range(streams):
                            if n == 0:
                                self.dve.step(nc.vector.tensor_tensor(inv[g0 + i], lt[i], m, ALU.mult))
                                self.dve.tell(nc.vector.tensor_tensor(inv[g0 + i], inv[g0 + i], ident.to_broadcast([P, 8, P]),
                                                                      ALU.add), self.vector_out)
                            else:
                                dve.wait_ge(self.tensor_out.sem, product_at(g0, 3 * n, i))
                                self.dve.tell(nc.vector.copy_predicated(
                                    inv[g0 + i], self.mask(level).unsqueeze(1).to_broadcast([P, 8, P]), eight(bank(i)[1])),
                                    self.vector_out)

    def head_slot(self, h):
        return slice(64 * (h // 4), 64 * (h // 4) + 64), h % 4

    def rwkv_inverses(self):
        nc, c = self.nc, self.c
        a, bb = self.cut(self.W_KK, 4, N), c[:, self.C_A:self.C_A + 4]

        def fill(pe, g, bank):
            cols = slice(g * P, (g + 1) * P)
            for h in range(8):
                rows, j = self.head_slot(h)
                ins = nc.tensor.matmul(self.ps[:, bank + h // 4, j * P:(j + 1) * P], bb[rows, j, cols], a[rows, j, cols],
                                       start=True, stop=True)
            ins.then_inc(self.tensor_out.sem, 1)

        hf = self.h[:].rearrange("p a b -> p (a b)")
        self.inv = [hf[:, g * 1024:(g + 1) * 1024].rearrange("p (h t) -> p h t", h=8) for g in range(NC)]
        before = self.const("before64").unsqueeze(1).to_broadcast([P, 8, P])
        self.unit_inverses(NC, 2, (lambda g: before, [f"level{m}" for m in LEVELS[:0:-1]]), self.W_A, self.W_A + 2048,
                           self.W_A + 4096, self.inv, fill)

    def rwkv_chain(self):
        nc, c = self.nc, self.c
        A = self.cut(self.W_KK, 4, N)
        Bv, K, R = c[:, self.C_A:self.C_A + 4], c[:, RK:RK + 4], c[:, RR:RR + 4]
        low, high = self.flat(self.C_W), self.flat(RWA)
        eight = lambda t: t.rearrange("p (h t) -> p h t", h=8)
        ak, rb, rk = ([self.cut(self.W_A + 1024 * i, 8, P), eight(odd)] for i, odd in enumerate(
            (low[:, 0:1024], low[:, 1024:2048], high[:, 0:1024])))
        tok = [self.cut(self.W_A + 3072, 1536), high[:, 1024:2560]]
        vt, bt, kt = ([t[:, 512 * i:512 * (i + 1)].rearrange("p (j q f) -> p j q f", j=4, q=2) for t in tok] for i in range(3))
        p1, sa = (self.cut(self.W_A + 4608 + 512 * i, 8, 64) for i in range(2))
        st = self.cut(self.W_FREE, 9, 4, 64)
        dl = self.cut(self.W_DL, 4, 8)
        with self.stage() as block:
            @block.sync
            def _(sp):
                sp.wait_ge(self.vector_out2.sem, self.vector_out2.at(8))
                self.store(sp, self.d["p_rwkv"], st[:, 8].rearrange("p a b -> p (a b)"))

            @block.tensor
            def _(pe):
                def transposes(t, n):
                    src, bank = (c[:, RV:RV + 4], Bv, K)[n], 6 + n % 2
                    if n == 2:
                        pe.wait_ge(self.scalar_out2.sem, self.scalar_out2.at(3 * t + 1))
                    elif t:
                        pe.wait_ge(self.vector_out.sem, self.vector_out.at(3 * t))
                    for j in range(4):
                        ins = nc.tensor.transpose(self.ps[:, bank, j * P:(j + 1) * P], src[:, j, t * P:(t + 1) * P],
                                                  self.const("ident"))
                    ins.then_inc(self.tensor_out2.sem, 1)

                def matrix(t, n):
                    cols = slice(t * P, (t + 1) * P)
                    left, right = ((K, A), (Bv, R), (K, R))[n]
                    if n == 0:
                        pe.wait_ge(self.scalar_out2.sem, self.scalar_out2.at(3 * t + 3))
                    else:
                        pe.wait_ge(self.vector_out.sem, self.vector_out.at(3 * t + n))
                    for h in range(8):
                        rows, j = self.head_slot(h)
                        ins = nc.tensor.matmul(self.ps[:, 6 + h // 4, j * P:(j + 1) * P], left[rows, j, cols],
                                               right[rows, j, cols], start=True, stop=True)
                    ins.then_inc(self.tensor_out2.sem, 1)

                def prepare(t, parts):
                    if t < NC:
                        for n in parts:
                            transposes(t, n) if n < 3 else matrix(t, n - 3)

                prepare(0, range(6))
                for t in range(NC):
                    x = t % 2
                    pe.wait_ge(self.vector_out.sem, self.vector_out.at(3 * t + 3))
                    for sub in range(2):
                        n = 2 * t + sub
                        own = slice(64 * sub, 64 * sub + 64)
                        sc = slice(t * P + 64 * sub, t * P + 64 * sub + 64)
                        if n:
                            pe.wait_ge(self.vector_out2.sem, self.vector_out2.at(n))
                        for h in range(8):
                            rows, j = self.head_slot(h)
                            out = self.ps[own, h // 4, j * 64:(j + 1) * 64]
                            nc.tensor.matmul(out, A[rows, j, sc], st[rows, n, j], start=True, stop=False)
                            ins = nc.tensor.matmul(out, ak[x][:, h, own], vt[x][:, j, h // 4], start=False, stop=True)
                        ins.then_inc(self.tensor_out.sem, 1)
                        prepare(t + 1, (4,) if sub else (0, 1))
                        pe.wait_ge(self.scalar_out.sem, self.scalar_out.at(5 * t + 1 + 2 * sub))
                        for h in range(8):
                            ins = nc.tensor.matmul(self.ps[own, 2, h * 64:(h + 1) * 64], self.inv[t][own, h, own], p1[own, h],
                                                   start=True, stop=True)
                        ins.then_inc(self.tensor_out.sem, 1)
                        prepare(t + 1, (5,) if sub else (2,))
                        pe.wait_ge(self.scalar_out.sem, self.scalar_out.at(5 * t + 2 + 2 * sub))
                        for h in range(8):
                            rows, j = self.head_slot(h)
                            out = self.ps[rows, 3, j * 64:(j + 1) * 64]
                            nc.tensor.matmul(out, bt[x][own, j, h // 4], sa[own, h], start=True, stop=False)
                            ins = nc.tensor.matmul(out, kt[x][own, j, h // 4], vt[x][own, j, h // 4], start=False, stop=True)
                        ins.then_inc(self.tensor_out.sem, 1)
                        if sub == 0:
                            prepare(t + 1, (3,))
                    if t:
                        pe.wait_ge(self.scalar_out.sem, self.scalar_out.at(5 * t))
                    for h in range(8):
                        rows, j = self.head_slot(h)
                        out = self.ps[rows, 4 + h // 4, j * P:(j + 1) * P]
                        nc.tensor.matmul(out, vt[x][:, j, h // 4], rk[x][:, h], start=True, stop=False)
                        nc.tensor.matmul(out, sa[:, h], rb[x][:, h], start=False, stop=False)
                        for sub in range(2):
                            half = slice(64 * sub, 64 * sub + 64)
                            sc = slice(t * P + 64 * sub, t * P + 64 * sub + 64)
                            ins = nc.tensor.matmul(out[:, half], st[rows, 2 * t + sub, j], R[rows, j, sc],
                                                   start=False, stop=sub == 1)
                    ins.then_inc(self.tensor_out.sem, 1)
                self.tensor_out.count += NC * 7
                self.tensor_out2.count += NC * 6

            @block.scalar
            def _(act):
                def copy(t, n):
                    if t < NC:
                        act.wait_ge(self.tensor_out2.sem, self.tensor_out2.at(6 * t + n + 1))
                        self.act.tell(nc.scalar.activation(tok[t % 2][:, 512 * n:512 * (n + 1)], self.ps[:, 6 + n % 2, :], ACT.Copy),
                                      self.scalar_out2)

                for n in range(3):
                    copy(0, n)
                for t in range(NC):
                    cols = slice(t * P, (t + 1) * P)
                    for sub in range(2):
                        own = slice(64 * sub, 64 * sub + 64)
                        act.wait_ge(self.tensor_out.sem, self.tensor_out.at(7 * t + 1 + 3 * sub))
                        self.act.tell(nc.scalar.activation(
                            p1[own].rearrange("p (q j) i -> p q (j i)", q=2), self.ps[own, 0:2, 0:256], ACT.Copy),
                            self.scalar_out)
                        if sub == 0:
                            copy(t + 1, 0)
                            copy(t + 1, 1)
                        act.wait_ge(self.tensor_out.sem, self.tensor_out.at(7 * t + 2 + 3 * sub))
                        self.act.tell(nc.scalar.activation(sa[own].rearrange("p h i -> p (h i)"), self.ps[own, 2, :], ACT.Copy),
                                      self.scalar_out)
                        if sub == 0:
                            copy(t + 1, 2)
                    act.wait_ge(self.tensor_out.sem, self.tensor_out.at(7 * t + 7))
                    for q in range(2):
                        rows = slice(64 * q, 64 * q + 64)
                        ins = nc.scalar.activation(self.o[rows, self.OUT:self.OUT + 4, cols],
                                                   self.ps[rows, 4 + q, :].rearrange("p (j t) -> p j t", j=4), ACT.Copy)
                    self.act.tell(ins, self.scalar_out)

            @block.vector
            def _(dve):
                def masked(t, n):
                    if t < NC:
                        out, m = ((ak, "before64"), (rb, "causal64"), (rk, "causal64"))[n]
                        dve.wait_ge(self.tensor_out2.sem, self.tensor_out2.at(6 * t + 4 + n))
                        self.dve.tell(nc.vector.tensor_tensor(
                            out[t % 2], self.ps[:, 6:8, :].rearrange("p a (b t) -> p (a b) t", t=P),
                            self.const(m).unsqueeze(1).to_broadcast([P, 8, P]), ALU.mult), self.vector_out)

                self.dve.step(nc.vector.memset(sa, 0.0))
                self.dve.step(nc.vector.memset(st[:, 0], 0.0))
                for n in range(3):
                    masked(0, n)
                for t in range(NC):
                    for sub in range(2):
                        n = 2 * t + sub
                        if sub:
                            masked(t + 1, 1)
                            masked(t + 1, 2)
                        dve.wait_ge(self.tensor_out.sem, self.tensor_out.at(7 * t + 3 + 3 * sub))
                        new = st[:, n + 1]
                        self.dve.step(nc.vector.tensor_tensor(new, self.ps[:, 3, 0:256].rearrange("p (j i) -> p j i", j=4),
                                                              st[:, n], ALU.add))
                        self.dve.tell(nc.vector.tensor_tensor(new, new, dl[:, :, n:n + 1].to_broadcast([P, 4, 64]), ALU.mult),
                                      self.vector_out2)
                        if sub == 0:
                            masked(t + 1, 0)

    def rwkv_output(self):
        nc, c = self.nc, self.c
        y = self.o[:, self.OUT:self.OUT + 4, :]
        sq, r, bon = self.cut(self.W_A, 4, N), self.cut(self.W_B, 4, N), self.cut(self.W_BON, 4, N)
        half = lambda t, x: t[:, 2 * x:2 * x + 2]
        banks = lambda x: self.ps[:, 4 * x:4 * x + 4, 0:HALF]
        with self.stage() as block:
            @block.sync
            def _(sp):
                sp.wait_ge(self.stored.sem, self.stored.count)

            @block.tensor
            def _(pe):
                def sums(t, x):
                    for j in (2 * x, 2 * x + 1):
                        for s, (lo, hi) in enumerate(self.SPANS):
                            ins = nc.tensor.matmul(self.ps[:, 2 * j + s, 0:HALF], self.const("head_ones"), t[:, j, lo:hi],
                                                   start=True, stop=True)
                    ins.then_inc(self.tensor_out.sem, 1)

                for x in range(2):
                    sums(y, x)
                for x in range(2):
                    pe.wait_ge(self.vector_out.sem, self.vector_out.at(x + 1))
                    pe.wait_ge(self.scalar_out.sem, self.scalar_out.at(2 * x + 1))
                    sums(sq, x)
                self.tensor_out.count += 4

            @block.scalar
            def _(act):
                def squares(x):
                    act.wait_ge(self.vector_out.sem, self.vector_out.at(x + 1))
                    self.act.tell(nc.scalar.activation(half(sq, x), half(y, x), ACT.Square), self.scalar_out)

                def scale(x):
                    act.wait_ge(self.tensor_out.sem, self.tensor_out.at(3 + x))
                    out = self.eight(half(r, x))
                    self.act.step(nc.scalar.activation(out, banks(x), ACT.Ln, bias=self.ln_eps, scale=1.0 / 64))
                    self.act.tell(nc.scalar.activation(out, out, ACT.Exp, scale=-0.5), self.scalar_out)

                squares(0)
                self.ln_exp()
                scale(0)
                squares(1)
                scale(1)

            @block.vector
            def _(dve):
                for x in range(2):
                    dve.wait_ge(self.tensor_out.sem, self.tensor_out.at(x + 1))
                    out = self.eight(half(y, x))
                    self.dve.tell(nc.vector.scalar_tensor_tensor(out, banks(x), -1.0 / 64, out, ALU.mult, ALU.add),
                                  self.vector_out)
                for j in range(4):
                    if j % 2 == 0:
                        dve.wait_ge(self.scalar_out.sem, self.scalar_out.at(j + 2))
                    self.dve.step(nc.vector.scalar_tensor_tensor(y[:, j], y[:, j], self.param("ln_w")[:, j:j + 1], r[:, j],
                                                                 ALU.mult, ALU.mult))
                    self.dve.step(nc.vector.scalar_tensor_tensor(y[:, j], y[:, j], self.param("ln_b")[:, j:j + 1], bon[:, j],
                                                                 ALU.add, ALU.add))
                    self.dve.step(nc.vector.tensor_tensor(y[:, j], y[:, j], c[:, self.C_G + j], ALU.mult))

    X_KV, X_VM, X_Q, X_A = 0, 8, 12, 20

    def flat(self, tile):
        return self.c[:].rearrange("p a b -> p (a b)")[:, tile * N:]

    def memory(self, i, following):
        nc = self.nc
        lin = self.lin[f"xkv{i}"]
        kv = self.flat(self.X_KV)[:, 0:16 * MEM].rearrange("p (a m) -> p a m", a=16)

        def read(o, bank):
            out = kv[:, o] if isinstance(o, int) else kv[:, bass.ds(o, 1), :].rearrange("p o n -> p (o n)")
            return nc.scalar.activation(out, self.ps[:, bank, 0:MEM], ACT.Copy)
        self.normed_product(lin, self.memory_rows(), self.param("g_mem"), MEM, [(0, MEM)], following, read, True)

    def query(self, i, following):
        self.normed_product(self.lin[f"xq{i}"], self.x, self.param("g_cross"), N, self.SPANS, following, lambda o, bank: (
            self.nc.scalar.activation(self.tile_pair(self.c[:, self.X_Q:self.X_Q + KT], o), self.pair(bank), ACT.Copy)), summed=4)

    def head_norms(self, i):
        nc = self.nc
        q = self.c[:, self.X_Q:self.X_Q + KT]
        kv = self.flat(self.X_KV)[:, 0:16 * MEM].rearrange("p (a m) -> p a m", a=16)
        vm = self.flat(self.X_VM)[:, 0:2 * D].rearrange("p (a b) -> p a b", a=2)
        free = self.flat(self.X_A)
        sq, r = self.h[:], free[:, 0:4 * N].rearrange("p (h n) -> p h n", h=4)
        sqk, rk = free[:, 4 * N:4 * N + KT * MEM].rearrange("p (k m) -> p k m", k=KT), self.cut(6 * 2048, 4, MEM)
        half = lambda t, x: t[:, (t.shape[1] // 2) * x:(t.shape[1] // 2) * (x + 1)]
        with self.stage() as block:
            @block.sync
            def _(sp):
                for b0 in range(6):
                    self.load_keys(sp, i, b0)
                self.store(sp, self.d[f"p_mv{i}"], kv[:, KT:])

            @block.scalar
            def _(act):
                self.act.tell(nc.scalar.activation(half(sq, 1), half(q, 1), ACT.Square), self.squares_ready)
                self.act.tell(nc.scalar.activation(sqk, kv[:, 0:KT], ACT.Square), self.squares_ready)
                for x in range(2):
                    act.wait_ge(self.tensor_out.sem, self.tensor_out.at(x + 1))
                    out = half(r, x).rearrange("p a (s n) -> p (a s) n", s=2)
                    self.act.tell(nc.scalar.activation(out, self.ps[:, 4 * x:4 * x + 4, 0:HALF], ACT.Ln, bias=self.eps,
                                                       scale=1.0 / 256), self.scalar_out)
                    self.act.tell(nc.scalar.activation(out, out, ACT.Exp, scale=-0.5), self.scalar_out)
                act.wait_ge(self.tensor_out.sem, self.tensor_out.at(3))
                self.act.step(nc.scalar.activation(rk.rearrange("p a b -> p (a b)"), self.banks(0, 2), ACT.Ln, bias=self.eps,
                                                   scale=1.0 / 256))
                self.act.tell(nc.scalar.activation(rk, rk, ACT.Exp, scale=-0.5), self.scalar_out)
                for m in range(2):
                    act.wait_ge(self.tensor_out.sem, self.tensor_out.at(4 + m))
                    self.act.step(nc.scalar.activation(vm[:, m], self.banks(2 + 2 * m, 2), ACT.Copy))

            @block.tensor
            def _(pe):
                for h in range(4):
                    if h == 0:
                        pe.wait_ge(self.vector_out.sem, self.vector_out.at(1))
                    if h == 2:
                        pe.wait_ge(self.squares_ready.sem, self.squares_ready.at(1))
                    for s, (lo, hi) in enumerate(self.SPANS):
                        for j in range(2):
                            ins = nc.tensor.matmul(self.ps[:, 2 * h + s, 0:HALF], self.const("ones"),
                                                   sq[:, 2 * h + j, lo:hi], start=j == 0, stop=j == 1)
                    if h % 2:
                        ins.then_inc(self.tensor_out.sem, 1)
                pe.wait_ge(self.squares_ready.sem, self.squares_ready.at(2))
                pe.wait_ge(self.scalar_out.sem, self.scalar_out.at(1))
                for h in range(4):
                    for j in range(2):
                        ins = nc.tensor.matmul(self.ps[:, h // 2, (h % 2) * MEM:(h % 2 + 1) * MEM], self.const("ones"),
                                               sqk[:, 2 * h + j], start=j == 0, stop=j == 1)
                ins.then_inc(self.tensor_out.sem, 1)
                for m in range(2):
                    if m:
                        pe.wait_ge(self.scalar_out.sem, self.scalar_out.at(3))
                    for j in range(KT):
                        ins = nc.tensor.transpose(self.ps[:, 2 + 2 * m + j // 4, (j % 4) * P:(j % 4 + 1) * P],
                                                  kv[:, KT + j, m * P:(m + 1) * P], self.const("ident"))
                    ins.then_inc(self.tensor_out.sem, 1)
                self.tensor_out.count += 5

            @block.vector
            def _(dve):
                def scaled(t, gain, by):
                    t4 = t.rearrange("p (h j) m -> p h j m", j=2)
                    for j in range(2):
                        self.dve.step(nc.vector.scalar_tensor_tensor(t4[:, :, j], t4[:, :, j], self.param(gain)[:, j:j + 1], by,
                                                                     ALU.mult, ALU.mult))

                self.dve.tell(nc.vector.tensor_tensor(half(sq, 0), half(q, 0), half(q, 0), ALU.mult), self.vector_out)
                for x in range(2):
                    dve.wait_ge(self.scalar_out.sem, self.scalar_out.at(2 * x + 2))
                    scaled(half(q, x), "xq", half(r, x))
                dve.wait_ge(self.scalar_out.sem, self.scalar_out.at(5))
                scaled(kv[:, 0:KT], "xk", rk)

    def cache_slot(self, b0):
        return self.cut(2048 * b0, 2048) if b0 < 6 else self.h[:].rearrange("p a b -> p (a b)")[:, 2048 * (b0 - 6):2048 * (b0 - 5)]

    def load_keys(self, sp, i, b0):
        sp.dma_start(self.cache_slot(b0).rearrange("p (a m) -> p a m", a=8), self.d[f"mem_k{i}"][b0]).then_inc(
            self.inputs_loaded[b0].sem, 16)

    def attention(self, i):
        nc = self.nc
        q = self.c[:, self.X_Q:self.X_Q + KT]
        kv = self.flat(self.X_KV)[:, 0:16 * MEM].rearrange("p (a m) -> p a m", a=16)
        vm = self.flat(self.X_VM)[:, 0:2 * D].rearrange("p (a b) -> p a b", a=2)
        buf = self.flat(self.X_A)
        pr = [buf[:, x * 1024:(x + 1) * 1024].rearrange("p (t m) -> p t m", t=NC) for x in range(2)]
        pt = [buf[:, (x + 2) * 1024:(x + 3) * 1024].rearrange("p (a t) -> p a t", a=2) for x in range(2)]
        small = self.flat(28)
        top, total = [small[:, 8 * x:8 * x + 4] for x in range(2)], [small[:, 8 * x + 4:8 * x + 8] for x in range(2)]
        weight, row = small[:, 80:144], small[:, 144:400]
        stop, stotal = small[:, 400:401], small[:, 401:402]
        pick = small[:, 402:402 + 63]
        kc = [self.cache_slot(b0).rearrange("p (a m) -> p a m", a=8) for b0 in range(B)]
        vc = [self.cache_slot(b0).rearrange("p (a m) -> p a m", a=2) for b0 in range(B)]
        scale = 1.0 / 16
        HP = 4
        score_bank = (0, 6)

        with self.stage() as block:
            @block.sync
            def _(sp):
                for b0 in (6, 7):
                    self.load_keys(sp, i, b0)
                self.store(sp, self.d[f"p_mk{i}"], kv[:, 0:KT])
                for b0 in range(B):
                    sp.wait_ge(self.keys_used.sem, self.keys_used.at(b0 + 1))
                    sp.dma_start(vc[b0], self.d[f"mem_v{i}"][b0]).then_inc(self.values_loaded[b0].sem, 16)

            @block.tensor
            def _(pe):
                def scores(h):
                    if h >= 2:
                        pe.wait_ge(self.exp_ready.sem, self.exp_ready.at(h - 1))
                    for t in range(NC):
                        for j in range(2):
                            ins = nc.tensor.matmul(self.ps[:, score_bank[h % 2] + t // 2, (t % 2) * MEM:(t % 2 + 1) * MEM],
                                                   q[:, 2 * h + j, t * P:(t + 1) * P], kv[:, 2 * h + j],
                                                   start=j == 0, stop=j == 1)
                    ins.then_inc(self.scores_ready.sem, 1)

                def sample_sums(b0, bank, terms, k, used):
                    pe.wait_ge(self.cache_summed.sem, self.cache_summed.at(k + 1))
                    for h in range(HP):
                        r = b0 * HP + h
                        ins = nc.tensor.matmul(self.ps[0:32, bank, 0:256], pick[:, 31 - r:63 - r], terms(b0, h),
                                               start=r == 0, stop=r == B * HP - 1)
                    ins.then_inc(used.sem, 1)

                def sample_scores(b0):
                    sample_sums(b0, 4, lambda b, h: kc[b][:, 2 * h], b0, self.keys_used)

                def transposes(h):
                    pe.wait_ge(self.vector_out.sem, self.vector_out.at(h + 1))
                    if h:
                        pe.wait_ge(self.scalar_out.sem, self.scalar_out.at(h))
                    for m in range(2):
                        for t in range(NC):
                            ins = nc.tensor.transpose(self.ps[:, 2 + m, t * P:(t + 1) * P], pr[h % 2][:, t, m * P:(m + 1) * P],
                                                      self.const("ident"))
                    ins.then_inc(self.tensor_out.sem, 1)

                def outputs(h):
                    pe.wait_ge(self.scalar_out.sem, self.scalar_out.at(h + 1))
                    if h:
                        pe.wait_ge(self.vector_out2.sem, self.vector_out2.at(h))
                    for e in range(2):
                        for m in range(2):
                            ins = nc.tensor.matmul(self.ps[:, 4 + e, :], vm[:, m, (2 * h + e) * P:(2 * h + e + 1) * P],
                                                   pt[h % 2][:, m], start=m == 0, stop=m == 1)
                    ins.then_inc(self.tensor_out2.sem, 1)

                scores(0)
                scores(1)
                pe.wait_ge(self.pool_out.sem, self.pool_out.at(1))
                sample_scores(0)
                sample_scores(1)
                transposes(0)
                for b0 in range(2, 5):
                    sample_scores(b0)
                scores(2)
                for b0 in range(5, B):
                    sample_scores(b0)
                transposes(1)
                scores(3)
                pe.wait_ge(self.sample_vector.sem, self.sample_vector.at(2))
                for m in range(2):
                    ins = nc.tensor.transpose(self.ps[:, 5, m * 32:(m + 1) * 32], row[0:32, m * P:(m + 1) * P],
                                              self.cst[0:32, CONST_AT["ident"]:CONST_AT["ident"] + 32])
                ins.then_inc(self.sample_tensor.sem, 1)
                pe.wait_ge(self.sample_scalar.sem, self.sample_scalar.at(2))
                outputs(0)
                transposes(2)
                outputs(1)
                pe.wait_ge(self.exp_ready.sem, self.exp_ready.at(3))
                for b0 in range(B):
                    if b0 == 2:
                        transposes(3)
                    if b0 == 4:
                        outputs(2)
                    if b0 == 6:
                        outputs(3)
                    sample_sums(b0, 0, lambda b, h: vc[b][:, 0, h * 256:(h + 1) * 256], B + b0, self.values_used)
                pe.wait_ge(self.sample_scalar.sem, self.sample_scalar.at(3))
                for j in range(2):
                    ins = nc.tensor.transpose(self.ps[:, 1, j * 32:(j + 1) * 32], row[0:32, j * P:(j + 1) * P],
                                              self.cst[0:32, CONST_AT["ident"]:CONST_AT["ident"] + 32])
                ins.then_inc(self.sample_tensor.sem, 1)
                self.scores_ready.count += HP
                self.keys_used.count += B
                self.values_used.count += B
                self.tensor_out.count += HP
                self.tensor_out2.count += HP
                self.sample_tensor.count += 2
                for b0 in range(B):
                    self.inputs_loaded[b0].count += 16
                    self.values_loaded[b0].count += 16

            @block.scalar
            def _(act):
                def exp(h):
                    p = h % 2
                    act.wait_ge(self.maxima_ready.sem, self.maxima_ready.at(h + 1))
                    if h >= 2:
                        act.wait_ge(self.tensor_out.sem, self.tensor_out.at(h - 1))
                    for t in range(NC):
                        ins = nc.scalar.activation(pr[p][:, t], self.ps[:, score_bank[p] + t // 2, (t % 2) * MEM:(t % 2 + 1) * MEM],
                                                   ACT.Exp, bias=top[p][:, t:t + 1], scale=scale, accum_out=total[p][:, t:t + 1])
                        self.act.step(ins) if t < NC - 1 else self.act.tell(ins, self.exp_ready)

                def transposed(h):
                    act.wait_ge(self.tensor_out.sem, self.tensor_out.at(h + 1))
                    if h >= 2:
                        act.wait_ge(self.tensor_out2.sem, self.tensor_out2.at(h - 1))
                    self.act.tell(nc.scalar.activation(pt[h % 2].rearrange("p a b -> p (a b)"), self.banks(2, 2), ACT.Copy),
                                  self.scalar_out)

                def first_terms(b0, values):
                    own = self.values_loaded[b0] if values else self.inputs_loaded[b0]
                    act.wait_ge(own.sem, own.at(16))
                    for h in range(HP):
                        if values:
                            t, by = vc[b0][:, 0, h * 256:(h + 1) * 256], weight[:, b0 * HP + h:b0 * HP + h + 1]
                        else:
                            t, by = kc[b0][:, 2 * h], q[:, 2 * h, T + b0:T + b0 + 1]
                        ins = nc.scalar.activation(t, t, ACT.Copy, scale=by)
                    ins.then_inc(self.cache_scaled.sem, 1)

                first_terms(0, False)
                first_terms(1, False)
                exp(0)
                first_terms(2, False)
                first_terms(3, False)
                exp(1)
                first_terms(4, False)
                transposed(0)
                for b0 in range(5, B):
                    first_terms(b0, False)
                exp(2)
                transposed(1)
                act.wait_ge(self.sample_vector.sem, self.sample_vector.at(1))
                self.act.tell(nc.scalar.activation(row[0:32], self.ps[0:32, 4, 0:256], ACT.Exp, bias=stop[0:32], scale=scale,
                                                   accum_out=stotal[0:32]), self.sample_scalar)
                act.wait_ge(self.sample_tensor.sem, self.sample_tensor.at(1))
                self.act.tell(nc.scalar.activation(weight, self.ps[:, 5, 0:64], ACT.Copy), self.sample_scalar)
                exp(3)
                first_terms(0, True)
                first_terms(1, True)
                transposed(2)
                first_terms(2, True)
                first_terms(3, True)
                transposed(3)
                for b0 in range(4, B):
                    first_terms(b0, True)
                self.cache_scaled.count += 2 * B
                act.wait_ge(self.values_used.sem, self.values_used.at(B))
                self.act.tell(nc.scalar.activation(row[0:32], self.ps[0:32, 0, 0:256], ACT.Copy), self.sample_scalar)
                act.wait_ge(self.sample_tensor.sem, self.sample_tensor.at(2))
                for j in range(2):
                    ins = nc.scalar.activation(self.o[:, :, T:N].rearrange("p (h j) b -> p j b h", j=2)[:, j],
                                               self.ps[:, 1, j * 32:(j + 1) * 32].rearrange("p (b h) -> p b h", b=B), ACT.Copy)
                self.act.step(ins)

            @block.gpsimd
            def _(pool):
                self.pool.step(nc.gpsimd.memset(pick, 0.0))
                self.pool.tell(nc.gpsimd.memset(pick[:, 31:32], 1.0), self.pool_out)

            @block.vector
            def _(dve):
                def maxima(h):
                    p = h % 2
                    dve.wait_ge(self.scores_ready.sem, self.scores_ready.at(h + 1))
                    self.dve.step(nc.vector.tensor_reduce(
                        top[p], self.banks(score_bank[p], 2).rearrange("p (t m) -> p t m", t=NC), AX.X, ALU.max))
                    self.dve.tell(nc.vector.tensor_scalar(top[p], top[p], -scale, None, ALU.mult), self.maxima_ready)

                def normalised(h):
                    p = h % 2
                    dve.wait_ge(self.exp_ready.sem, self.exp_ready.at(h + 1))
                    self.dve.step(nc.vector.reciprocal(total[p], total[p]))
                    self.dve.tell(nc.vector.tensor_tensor(pr[p], pr[p], total[p].unsqueeze(2).to_broadcast([P, NC, MEM]),
                                                          ALU.mult), self.vector_out)

                def kept(h):
                    dve.wait_ge(self.tensor_out2.sem, self.tensor_out2.at(h + 1))
                    self.dve.tell(nc.vector.tensor_copy(self.o[:, 2 * h:2 * h + 2, 0:T], self.ps[:, 4:6, :]), self.vector_out2)

                def all_terms(b0, values):
                    k = b0 + B * values
                    dve.wait_ge(self.cache_scaled.sem, self.cache_scaled.base + k + 1)
                    for h in range(HP):
                        if values:
                            at = 32 + b0 * HP + h
                            one, two = (vc[b0][:, m, h * 256:(h + 1) * 256] for m in range(2))
                            by = weight[:, at:at + 1]
                        else:
                            one, two, by = kc[b0][:, 2 * h], kc[b0][:, 2 * h + 1], q[:, 2 * h + 1, T + b0:T + b0 + 1]
                        ins = nc.vector.scalar_tensor_tensor(one, two, by, one, ALU.mult, ALU.add)
                    ins.then_inc(self.cache_summed.sem, 1)

                maxima(0)
                all_terms(0, False)
                all_terms(1, False)
                maxima(1)
                normalised(0)
                all_terms(2, False)
                all_terms(3, False)
                all_terms(4, False)
                normalised(1)
                for b0 in range(5, B):
                    all_terms(b0, False)
                maxima(2)
                dve.wait_ge(self.keys_used.sem, self.keys_used.at(B))
                self.dve.step(nc.vector.tensor_reduce(stop[0:32], self.ps[0:32, 4, 0:256], AX.X, ALU.max))
                self.dve.tell(nc.vector.tensor_scalar(stop[0:32], stop[0:32], -scale, None, ALU.mult), self.sample_vector)
                dve.wait_ge(self.sample_scalar.sem, self.sample_scalar.at(1))
                self.dve.step(nc.vector.reciprocal(stotal[0:32], stotal[0:32]))
                self.dve.tell(nc.vector.tensor_scalar(row[0:32], row[0:32], stotal[0:32], None, ALU.mult), self.sample_vector)
                maxima(3)
                normalised(2)
                kept(0)
                all_terms(0, True)
                all_terms(1, True)
                normalised(3)
                kept(1)
                all_terms(2, True)
                all_terms(3, True)
                all_terms(4, True)
                all_terms(5, True)
                kept(2)
                all_terms(6, True)
                all_terms(7, True)
                kept(3)
                self.cache_summed.count += 2 * B

    def gate_up(self, i, following):
        nc = self.nc
        lin, site = self.lin[f"gu{i}"], self.mlp
        silu, prod = self.mlp_tmp[0:2], self.mlp_tmp[2]
        with self.stage() as block:
            @block.sync
            def _(sp):
                self.stream(sp, lin)
                self.prefetch(sp, following)

            @block.tensor
            def _(pe):
                self.product(pe, lin, site, self.SPANS)

            @block.scalar
            def _(act):
                self.norm_act(act, self.x, site, self.mlp_norm, N, self.SPANS, 6)
                nc.scalar.preload_act_table(ACT.Silu)
                with act.Fori(0, FT // 2) as it:
                    for u in range(2):
                        act.wait_ge(self.unit_done.sem, it * 4 + (lin.at + 2 * u + 1))
                        act.wait_ge(self.product_read[1].sem, self.product_read[1].base + it * 2 + u - 1)
                        nc.scalar.activation(silu[u][:].rearrange("p (s n) -> p s n", s=2), self.pair(0),
                                             ACT.Silu).then_inc(self.product_read[0].sem, 1)

            @block.vector
            def _(dve):
                for u in range(2):
                    self.split_unit(dve, lin, site, u)
                self.norm_dve(dve, self.x, site, self.mlp_norm, self.param("g_ffn"), N)

                def read(u, i):
                    if u % 2 == 0:
                        return
                    tile, pairs = i * 2 + u // 2, self.product_read[1].base
                    part = [t[:, bass.ds(tile, 1), :].rearrange("p o n -> p (o n)") if not isinstance(tile, int)
                            else t[:, tile] for t in self.hid.x]
                    dve.wait_ge(self.unit_done.sem, i * SLOTS + (lin.at + u + 1))
                    dve.wait_ge(self.product_read[0].sem, self.product_read[0].base + i * 2 + (u // 2 + 1))
                    nc.vector.tensor_tensor(prod[:].rearrange("p (s n) -> p s n", s=2),
                                            silu[u // 2 % 2][:].rearrange("p (s n) -> p s n", s=2), self.pair(2),
                                            ALU.mult).then_inc(self.product_read[1].sem, 1)
                    dve.wait_ge(self.product_read[1].sem, pairs + i * 2 + (u // 2 + 1))
                    nc.vector.tensor_copy(part[0], prod[:]).then_inc(self.hidden_hi.sem, 1)
                    dve.wait_ge(self.hidden_hi.sem, self.hidden_hi.base + i * 2 + (u // 2 + 1))
                    nc.vector.tensor_tensor(part[1], prod[:], part[0].bitcast(F32), ALU.subtract).then_inc(
                        self.hidden_lo.sem, 1)

                self.each_unit(dve, lin, site, read)
                self.tiles_read(lin)
                self.hidden_hi.count += FT
                self.hidden_lo.count += FT

    S_V, S_NZ, S_L = 0, 2048, 4608
    WIDTH = [T - s * P for s in range(NC)]
    START = [sum([T - s * P for s in range(n)]) for n in range(NC)]
    TRI = sum([T - s * P for s in range(NC)])

    def stick_norms(self):
        nc, c = self.nc, self.c
        q, k, v = c[:, SQ:SQ + 4], c[:, SK:SK + 4], c[:, SV:SV + 4]
        sq, r = ([self.cut(2080 * (1 + x + y), 4, N) for x in range(2)] for y in (0, 2))
        vt = self.cut(self.S_V, NC, T)
        gain_q = self.cut(2080 * 5, 1)
        half = lambda t, x: t[:, 2 * x:2 * x + 2]
        with self.stage() as block:
            @block.scalar
            def _(act):
                for x in range(2):
                    self.act.tell(nc.scalar.activation(half(sq[0], x), half(q, x), ACT.Square), self.squares_ready)
                for n in range(4):
                    act.wait_ge(self.tensor_out.sem, self.tensor_out.at(n + 1))
                    out = self.eight(half(r[n // 2], n % 2))
                    self.act.tell(nc.scalar.activation(out, self.ps[:, 4 * (n % 2):4 * (n % 2) + 4, 0:HALF], ACT.Ln,
                                                       bias=self.eps, scale=1.0 / 64), self.scalar_out)
                    self.act.tell(nc.scalar.activation(out, out, ACT.Exp, scale=-0.5), self.scalar_out)
                act.wait_ge(self.tensor_out.sem, self.tensor_out.at(5))
                self.act.step(nc.scalar.activation(vt.rearrange("p a b -> p (a b)"), self.banks(0, 4), ACT.Copy))

            @block.gpsimd
            def _(pool):
                for x in range(2):
                    self.pool.tell(nc.gpsimd.tensor_tensor(half(sq[1], x), half(k, x), half(k, x), ALU.mult), self.pool_out)

            @block.tensor
            def _(pe):
                for n in range(4):
                    if n < 2:
                        pe.wait_ge(self.squares_ready.sem, self.squares_ready.at(n + 1))
                    else:
                        pe.wait_ge(self.pool_out.sem, self.pool_out.at(n - 1))
                        pe.wait_ge(self.scalar_out.sem, self.scalar_out.at(2 * n - 3))
                    for m, (j, (lo, hi)) in enumerate((j, span) for j in range(2) for span in self.SPANS):
                        ins = nc.tensor.matmul(self.ps[:, 4 * (n % 2) + m, 0:HALF], self.const("head_ones"),
                                               sq[n // 2][:, 2 * (n % 2) + j, lo:hi], start=True, stop=True)
                    ins.then_inc(self.tensor_out.sem, 1)
                pe.wait_ge(self.scalar_out.sem, self.scalar_out.at(5))
                for t in range(NC):
                    for j in range(4):
                        ins = nc.tensor.transpose(self.ps[:, t, j * P:(j + 1) * P], v[:, j, t * P:(t + 1) * P],
                                                  self.const("ident"))
                ins.then_inc(self.tensor_out.sem, 1)
                self.tensor_out.count += 5

            @block.vector
            def _(dve):
                self.dve.step(nc.vector.tensor_scalar(gain_q, self.param("sbq")[:, 0:1], 0.125, None, ALU.mult))
                for n in range(4):
                    dve.wait_ge(self.scalar_out.sem, self.scalar_out.at(2 * n + 2))
                    t, gain = half((q, k)[n // 2], n % 2), (gain_q, self.param("sbk")[:, 0:1])[n // 2]
                    self.dve.tell(nc.vector.scalar_tensor_tensor(t, t, gain, half(r[n // 2], n % 2), ALU.mult, ALU.mult),
                                  self.vector_out)

            @block.sync
            def _(sp):
                self.store(sp, self.d["p_sbv"], v)
                sp.wait_ge(self.stored.sem, self.stored.count)
                sp.wait_ge(self.vector_out.sem, self.vector_out.at(4))
                self.store(sp, self.d["p_sbk"], k)

    def log_stay(self, nz, out):
        nc = self.nc

        def first():
            return nc.vector.scalar_tensor_tensor(out, nz, -1.0, nz, ALU.mult, ALU.min)

        def middle():
            self.act.step(nc.scalar.activation(out, out, ACT.Exp))
            self.act.tell(nc.scalar.activation(out, out, ACT.Ln, bias=1.0), self.scalar_out)

        def last():
            return nc.vector.scalar_tensor_tensor(out, nz, 0.0, out, ALU.min, ALU.subtract)
        return first, middle, last

    S_CONV = 11520
    S_GATES = 12790

    def conv(self):
        nc, c = self.nc, self.c
        x = c[:, DQ:DQ + 12]
        y = self.cut(self.S_CONV, 2, N)
        pc, t = self.cut(self.S_CONV + 2 * N, 12, 3), self.cut(self.S_CONV + 2 * N + 36, 12, B)
        buf, sc = self.cut(13310, 12, 3, B), self.cut(13598, 12, 3, B)
        w = self.param("dn_conv").rearrange("p (i a) -> p i a", i=4)

        def rows_out(pool):
            self.pool.tell(nc.gpsimd.tensor_copy(pc, x[:, :, T - 3:T]), self.pool_out)
            self.pool.tell(nc.gpsimd.tensor_copy(sc[:, :, 2], x[:, :, T:N]), self.pool_out)
            pool.wait_ge(self.conv_loaded.sem, self.conv_loaded.at(16))
            self.pool.tell(nc.gpsimd.tensor_copy(sc[:, :, 0:2], buf[:, :, 1:3]), self.pool_out)
            for i in range(3):
                wi = w[:, i].unsqueeze(2).to_broadcast([P, 12, B])
                self.pool.step(nc.gpsimd.tensor_tensor(buf[:, :, i], buf[:, :, i], wi, ALU.mult))
            self.pool.step(nc.gpsimd.tensor_tensor(t, buf[:, :, 0], buf[:, :, 1], ALU.add))
            self.pool.tell(nc.gpsimd.tensor_tensor(t, t, buf[:, :, 2], ALU.add), self.pool_out)

        def on_act(act, g):
            if g > 6:
                return
            for a in range(2 * g - 2, 2 * g):
                if a >= 0:
                    if a == 0:
                        act.wait_ge(self.pool_out.sem, self.pool_out.at(3))
                    act.wait_ge(self.conv_summed.sem, self.conv_summed.at(a + 1))
                    self.act.step(nc.scalar.activation(x[:, a], y[:, a % 2], ACT.Silu))
            if g:
                self.ln_exp()
            for a in range(2 * g, 2 * g + 2):
                if a < 12:
                    self.act.tell(nc.scalar.activation(y[:, a % 2], x[:, a], ACT.Copy, scale=w[:, 3, a:a + 1]), self.conv_scaled)

        def on_dve(dve, g):
            if g > 5:
                return
            if g == 0:
                dve.wait_ge(self.pool_out.sem, self.pool_out.at(4))
            for a in (2 * g, 2 * g + 1):
                dve.wait_ge(self.conv_scaled.sem, self.conv_scaled.at(a + 1))
                for i in range(3):
                    lag = 3 - i
                    self.dve.step(nc.vector.scalar_tensor_tensor(
                        y[:, a % 2, lag:T], x[:, a, 0:T - lag], w[:, i, a:a + 1], y[:, a % 2, lag:T], ALU.mult, ALU.add))
                self.dve.tell(nc.vector.tensor_tensor(y[:, a % 2, T:N], y[:, a % 2, T:N], t[:, a], ALU.add), self.conv_summed)
        return buf, pc, sc, rows_out, on_act, on_dve

    def stick_prompt(self):
        nc, c = self.nc, self.c
        q, k = c[:, SQ:SQ + 4], c[:, SK:SK + 4]
        vt = self.cut(self.S_V, NC, 8, 64)
        nz = [self.cut(self.S_NZ + self.TRI * x, self.TRI) for x in range(2)]
        ls = [self.cut(self.S_L + self.TRI * x, self.TRI) for x in range(2)]
        wt = self.cut(self.S_L + self.TRI * 2, self.TRI)
        heads = 8
        blk = [slice(self.START[s], self.START[s] + self.WIDTH[s]) for s in range(NC)]

        def z(h, s, lo=None):
            return self.ps[:, 4 * (h % 2) + s, (s if lo is None else lo) * P:T]

        buf, pc, sc, rows_out, conv_act, conv_dve = self.conv()
        with self.stage() as block:
            @block.sync
            def _(sp):
                sp.dma_start(buf, self.d["state_conv"]).then_inc(self.conv_loaded.sem, 16)
                for b0 in range(B):
                    self.load_pages(sp, "cache_k", b0, self.inputs_loaded[b0])
                for b0 in range(self.EARLY_V):
                    self.load_pages(sp, "cache_v", b0, self.values_loaded[b0])
                sp.wait_ge(self.pool_out.sem, self.pool_out.at(3))
                self.store(sp, self.d["p_conv"], pc)
                self.store(sp, self.d["s_conv"], sc)
                sp.wait_ge(self.stored.sem, self.stored.count)

            @block.gpsimd
            def _(pool):
                rows_out(pool)
                self.conv_loaded.count += 16

            @block.tensor
            def _(pe):
                def logits(h):
                    rows, j = slice(64 * (h % 2), 64 * (h % 2) + 64), h // 2
                    for s in (1, 2, 3, 0):
                        if s == 0 and h >= 2:
                            pe.wait_ge(self.vector_out2.sem, self.vector_out2.at(h - 1))
                        ins = nc.tensor.matmul(z(h, s), k[rows, j, s * P:(s + 1) * P], q[rows, j, s * P:T],
                                               start=True, stop=True)
                    ins.then_inc(self.scores_ready.sem, 1)

                def sums(h):
                    pe.wait_ge(self.vector_out.sem, self.vector_out.at(h + 1))
                    for s in range(NC):
                        diagonal = self.ps[:, 4 * (h % 2) + s, s * P:(s + 1) * P]
                        nc.tensor.matmul(diagonal, self.const("ident"), self.const("forbid"), start=False, stop=False,
                                         skip_group_check=True)
                        for n in range(s, NC):
                            ins = nc.tensor.matmul(z(h, s, n), self.const("key_after" if n == s else "ones"), ls[h % 2][:, blk[n]],
                                                   start=False, stop=n == NC - 1, skip_group_check=True)
                        ins.then_inc(self.tensor_out.sem, 1)

                def output(h):
                    rows = slice(64 * (h % 2), 64 * (h % 2) + 64)
                    for s in range(NC):
                        pe.wait_ge(self.weights_ready.sem, self.weights_ready.at(NC * h + s + 1))
                        ins = nc.tensor.matmul(self.ps[rows, 4 * (h % 2), s * P:T], vt[:, s, h], wt[:, blk[s]],
                                               start=s == 0, stop=s == NC - 1)
                    ins.then_inc(self.tensor_out2.sem, 1)

                logits(0)
                for h in range(heads):
                    if h:
                        output(h - 1)
                    if h + 1 < heads:
                        logits(h + 1)
                    sums(h)
                output(heads - 1)
                self.scores_ready.count += heads
                self.tensor_out.count += NC * heads
                self.tensor_out2.count += heads

            @block.vector
            def _(dve):
                def first(h):
                    dve.wait_ge(self.scores_ready.sem, self.scores_ready.at(h + 1))
                    for s in range(NC):
                        ins = nc.vector.tensor_scalar(nz[h % 2][:, blk[s]], z(h, s), self.param("sb_bias")[:, h:h + 1],
                                                      -1.0, ALU.add, ALU.mult)
                    self.dve.step(ins)
                    self.dve.tell(self.log_stay(nz[h % 2], ls[h % 2])[0](), self.exponent_ready)

                def second(h):
                    dve.wait_ge(self.scalar_out.sem, self.scalar_out.at(h + 1))
                    self.dve.step(self.log_stay(nz[h % 2], ls[h % 2])[2]())
                    for s in range(NC):
                        d = ls[h % 2][:, self.START[s]:self.START[s] + P]
                        ins = nc.vector.tensor_tensor(d, d, self.const("before"), ALU.mult)
                    self.dve.tell(ins, self.vector_out)

                def keep(h):
                    dve.wait_ge(self.tensor_out2.sem, self.tensor_out2.at(h + 1))
                    rows = slice(64 * (h % 2), 64 * (h % 2) + 64)
                    self.dve.tell(nc.vector.tensor_copy(self.o[rows, h // 2, 0:T], self.ps[rows, 4 * (h % 2), :]),
                                  self.vector_out2)

                first(0)
                second(0)
                for h in range(heads):
                    if h + 1 < heads:
                        first(h + 1)
                    conv_dve(dve, h)
                    keep(h)
                    if h + 1 < heads:
                        second(h + 1)

            @block.scalar
            def _(act):
                def middle(h):
                    act.wait_ge(self.exponent_ready.sem, self.exponent_ready.at(h + 1))
                    self.log_stay(nz[h % 2], ls[h % 2])[1]()

                def weights(h):
                    if h:
                        act.wait_ge(self.tensor_out2.sem, self.tensor_out2.at(h))
                    for s in range(NC):
                        act.wait_ge(self.tensor_out.sem, self.tensor_out.at(NC * h + s + 1))
                        self.act.tell(nc.scalar.activation(wt[:, blk[s]], z(h, s), ACT.Exp, bias=self.param("sb_bias")[:, h:h + 1]),
                                      self.weights_ready)

                middle(0)
                for h in range(heads):
                    conv_act(act, h)
                    weights(h)
                    if h + 1 < heads:
                        middle(h + 1)

    def page_slot(self, n):
        o = self.o[:, 4:8].rearrange("p a b -> p (a b)")
        v = self.c[:, SV:SV + 4].rearrange("p a b -> p (a b)")
        h = self.h[:].rearrange("p a b -> p (a b)")
        spots = [self.cut(self.S_L + self.TRI * 3 + 1024 * x, 1024) for x in range(3)] + [h[:, 1024 * x:1024 * (x + 1)] for x in range(4)]
        spots += [t[:, 1024 * x:1024 * (x + 1)] for t in (o, v) for x in range(2)]
        spots += [self.cut(at, 1024) for at in (0, 1024, 2048, 7424, self.S_CONV)]
        return spots[n]

    def load_pages(self, sp, name, b0, signal):
        slot = self.page_slot(b0 + (B if name == "cache_v" else 0))
        for pg in range(PAGES):
            n = b0 * PAGES + pg
            page = sp.value_load(self.pages[0:1, n:n + 1], min_val=0, max_val=NPHYS - 1)
            sp.dma_start(slot[:, pg * 512:(pg + 1) * 512], self.d[name][bass.ds(page, 1)].rearrange("o p n -> p (o n)")).then_inc(
                signal.sem, 16)

    EARLY_V = 3

    def stick_sample(self):
        nc, c = self.nc, self.c
        q = c[:, SQ:SQ + 4]
        kp = [self.page_slot(b0).rearrange("p (g j t) -> p g j t", g=PAGES, j=4) for b0 in range(B)]
        vp = [self.page_slot(B + b0).rearrange("p (g n) -> p g n", g=PAGES) for b0 in range(B)]
        R = B * 8
        at = 3072
        nz, ls, w = (self.cut(at + 128 * x, 128) for x in range(3))
        qz, wz = self.cut(3584, B, 4, R), self.cut(5632, B, PAGES, R)
        row, out = self.cut(6656, 256), self.cut(6912, 512)
        ident = self.cst[0:R, CONST_AT["ident"]:CONST_AT["ident"] + R]
        g, e, a = c[0:4, DAB], self.cut(13310, N)[0:4], self.cut(13310 + N, 1)[0:4]
        gs = self.cut(self.S_GATES, N)
        with self.stage() as block:
            @block.sync
            def _(sp):
                for b0 in range(self.EARLY_V, B):
                    self.load_pages(sp, "cache_v", b0, self.values_loaded[b0])

                sp.wait_ge(self.values_used.sem, self.values_used.at(1))
                states = self.h[:].rearrange("p a b -> p (a b)")[:, 0:4096].rearrange("p (b h e) -> p b h e", b=B, h=4)
                sp.dma_start(states, self.d["state_delta"]).then_inc(self.delta_loaded.sem, 16)

            @block.gpsimd
            def _(pool):
                self.pool.tell(nc.gpsimd.memset(wz, 0.0), self.pool_out)

            @block.tensor
            def _(pe):
                pe.wait_ge(self.vector_out.sem, self.vector_out.at(1))
                for b0 in range(B):
                    pe.wait_ge(self.inputs_loaded[b0].sem, self.inputs_loaded[b0].at(16 * PAGES))
                    for j in range(4):
                        ins = nc.tensor.matmul(self.ps[0:R, 0, 0:256].rearrange("r (g t) -> r g t", g=PAGES), qz[:, b0, j],
                                               kp[b0][:, :, j], start=b0 + j == 0, stop=b0 == B - 1 and j == 3)
                ins.then_inc(self.keys_used.sem, 1)
                pe.wait_ge(self.scalar_out.sem, self.scalar_out.at(1))
                for pg in range(PAGES):
                    ins = nc.tensor.transpose(self.ps[:, 1, pg * R:(pg + 1) * R], row[0:R, pg * P:(pg + 1) * P], ident)
                ins.then_inc(self.tensor_out.sem, 1)
                pe.wait_ge(self.vector_out.sem, self.vector_out.at(3))
                nc.tensor.matmul(self.ps[:, 2, 64:128], self.const("key_after"), ls[:, 64:128], start=True, stop=True)
                nc.tensor.matmul(self.ps[:, 2, 0:64], self.const("key_after"), ls[:, 0:64], start=True, stop=False)
                nc.tensor.matmul(self.ps[:, 2, 0:64], self.const("ones"), ls[:, 64:128], start=False, stop=True).then_inc(
                    self.tensor_out.sem, 1)
                pe.wait_ge(self.vector_out.sem, self.vector_out.at(5))
                for b0 in range(B):
                    pe.wait_ge(self.values_loaded[b0].sem, self.values_loaded[b0].at(16 * PAGES))
                    for pg in range(PAGES):
                        ins = nc.tensor.matmul(self.ps[0:R, 3, :], wz[:, b0, pg], vp[b0][:, pg],
                                               start=b0 + pg == 0, stop=b0 == B - 1 and pg == PAGES - 1)
                ins.then_inc(self.values_used.sem, 1)
                pe.wait_ge(self.scalar_out.sem, self.scalar_out.at(4))
                for j in range(4):
                    ins = nc.tensor.transpose(self.ps[:, 4, j * R:(j + 1) * R], out[0:R, j * P:(j + 1) * P], ident)
                ins.then_inc(self.tensor_out.sem, 1)
                self.keys_used.count += 1
                self.values_used.count += 1
                self.tensor_out.count += 3
                for b0 in range(B):
                    self.inputs_loaded[b0].count += 16 * PAGES
                    self.values_loaded[b0].count += 16 * PAGES

            @block.vector
            def _(dve):
                first, _, last = self.log_stay(nz, ls)
                self.dve.step(nc.vector.memset(qz, 0.0))
                flat = qz.rearrange("p b j r -> p (b j r)")
                for par in range(2):
                    rows = slice(64 * par, 64 * par + 64)
                    ins = nc.vector.tensor_copy(flat[rows, par:32 * R:R + 2].rearrange("p (b j) -> p b j", b=B),
                                                q[rows, :, T:N].rearrange("p j b -> p b j"))
                self.dve.tell(ins, self.vector_out)
                self.dve.step(nc.vector.tensor_scalar(g, g, self.param("dn_dt")[0:4, 0:1], None, ALU.add))
                self.dve.tell(nc.vector.scalar_tensor_tensor(e, g, -1.0, g, ALU.mult, ALU.min), self.gate_vector)
                dve.wait_ge(self.gate_scalar.sem, self.gate_scalar.at(1))
                self.dve.step(nc.vector.scalar_tensor_tensor(g, g, 0.0, e, ALU.max, ALU.add))
                self.dve.step(nc.vector.tensor_scalar(g, g, a, -1.0, ALU.mult, ALU.mult))
                self.dve.step(nc.vector.tensor_copy(gs[0:4, T:N], g[:, T:N]))
                self.dve.step(nc.vector.tensor_tensor_scan(gs[0:4, 0:T], self.cst[0:4, SCAN128_AT:SCAN128_AT + T], g[:, 0:T],
                                                           0.0, ALU.mult, ALU.add))
                dve.wait_ge(self.tensor_out.sem, self.tensor_out.at(1))
                by_head = lambda t: t.rearrange("p (a h) -> p a h", h=8)
                self.dve.step(nc.vector.tensor_tensor(by_head(nz), by_head(self.ps[:, 1, 0:128]),
                                                      self.param("sb_bias").unsqueeze(1).to_broadcast([P, 16, 8]), ALU.add))
                self.dve.step(nc.vector.tensor_scalar(nz, nz, -1.0, None, ALU.mult))
                self.dve.tell(first(), self.vector_out)
                dve.wait_ge(self.scalar_out.sem, self.scalar_out.at(2))
                self.dve.tell(last(), self.vector_out)
                dve.wait_ge(self.tensor_out.sem, self.tensor_out.at(2))
                self.dve.tell(nc.vector.tensor_tensor(w, self.ps[:, 2, 0:128], nz, ALU.subtract), self.vector_out)
                dve.wait_ge(self.scalar_out.sem, self.scalar_out.at(3))
                dve.wait_ge(self.pool_out.sem, self.pool_out.at(1))
                for b0 in range(B):
                    ins = nc.vector.tensor_copy(wz[:, b0, :, 8 * b0:8 * b0 + 8],
                                                w.rearrange("p (g b h) -> p g b h", g=PAGES, b=B)[:, :, b0])
                self.dve.tell(ins, self.vector_out)

            @block.scalar
            def _(act):
                self.act.step(nc.scalar.activation(gs[32:36], c[32:36, DAB], ACT.Sigmoid))
                self.ln_exp()
                act.wait_ge(self.gate_vector.sem, self.gate_vector.at(1))
                self.act.step(nc.scalar.activation(e, e, ACT.Exp))
                self.act.step(nc.scalar.activation(a, self.param("dn_a")[0:4], ACT.Exp))
                self.act.tell(nc.scalar.activation(e, e, ACT.Ln, bias=1.0), self.gate_scalar)
                act.wait_ge(self.keys_used.sem, self.keys_used.at(1))
                self.act.tell(nc.scalar.activation(row[0:R], self.ps[0:R, 0, 0:256], ACT.Copy), self.scalar_out)
                act.wait_ge(self.vector_out.sem, self.vector_out.at(2))
                self.log_stay(nz, ls)[1]()
                act.wait_ge(self.vector_out.sem, self.vector_out.at(4))
                self.act.tell(nc.scalar.activation(w, w, ACT.Exp), self.scalar_out)
                act.wait_ge(self.values_used.sem, self.values_used.at(1))
                self.act.tell(nc.scalar.activation(out[0:R], self.ps[0:R, 3, :], ACT.Copy), self.scalar_out)
                act.wait_ge(self.tensor_out.sem, self.tensor_out.at(3))
                for par in range(2):
                    rows = slice(64 * par, 64 * par + 64)
                    for j in range(4):
                        own = self.ps[rows, 4, j * R:(j + 1) * R].rearrange("p (b h) -> p b h", h=8)[:, :, 2 * j + par]
                        ins = nc.scalar.activation(self.o[rows, j, T:N], own, ACT.Copy)
                self.act.step(ins)

    E_EG, E_DM, E_LD = 0, 4, 8
    E_INV, E_VT, E_KT, E_QK, E_U, E_S, E_R = 6144, 0, 2048, 4096, 8192, 10240, 12800
    E_COL = 13312

    def delta_vectors(self):
        nc, c = self.nc, self.c
        q, k = c[:, DQ:DQ + 4], c[:, DK:DK + 4]
        sq, r = ([self.cut(2080 * (x + y), 4, N) for x in range(2)] for y in (0, 2))
        gs = self.cut(self.S_GATES, N)
        eg = c[:, self.E_EG:self.E_EG + 4]
        dm = self.flat(self.E_DM)[:, 0:2048].rearrange("p (c h t) -> p c h t", c=NC, h=4)
        ld = self.flat(self.E_LD)[:, 0:2048].rearrange("p (c h t) -> p c h t", c=NC, h=4)
        col = self.cut(self.E_COL, 4, NC, 4)
        bs = self.cut(self.E_COL + 64, 4, B)
        row = lambda h, base: self.cst[base:base + 4, SEL_AT + h * P:SEL_AT + (h + 1) * P]
        heads4 = self.ps[:, :, 0:HALF].rearrange("p (h s) n -> p h s n", s=2)

        half = lambda t, x: t[:, 2 * x:2 * x + 2]
        pairs = lambda x: self.ps[:, 4 * (x % 2):4 * (x % 2) + 4, 0:HALF]

        def spread(x, base):
            for h in (2 * x, 2 * x + 1):
                for s, (lo, hi) in enumerate(self.SPANS):
                    ins = nc.tensor.matmul(self.ps[:, 2 * h + s, 0:HALF], row(h, base), gs[base:base + 4, lo:hi],
                                           start=True, stop=True)
            ins.then_inc(self.tensor_out.sem, 1)

        with self.stage() as block:
            @block.scalar
            def _(act):
                for x in range(2):
                    self.act.tell(nc.scalar.activation(half(sq[0], x), half(q, x), ACT.Square), self.squares_ready)
                for n in range(4):
                    act.wait_ge(self.tensor_out.sem, self.tensor_out.at(n + 1))
                    out = half(r[n // 2], n % 2)
                    self.act.tell(nc.scalar.activation(self.eight(out), pairs(n), ACT.Ln, bias=self.eps), self.scalar_out)
                    self.act.tell(nc.scalar.activation(out, out, ACT.Exp, scale=-0.5), self.scalar_out)
                for n in range(2):
                    act.wait_ge(self.tensor_out.sem, self.tensor_out.at(5 + n))
                    self.act.tell(nc.scalar.activation(self.eight(half(eg, n)), pairs(n), ACT.Exp), self.scalar_out)
                for n in range(2):
                    act.wait_ge(self.vector_out.sem, self.vector_out.at(2 + n))
                    self.act.tell(nc.scalar.activation(dm[:, :, 2 * n:2 * n + 2], dm[:, :, 2 * n:2 * n + 2], ACT.Exp),
                                  self.scalar_out)
                self.act.step(nc.scalar.activation(col[:, 2], col[:, 2], ACT.Exp))
                self.act.step(nc.scalar.activation(col[:, 3], col[:, 3], ACT.Exp))

            @block.gpsimd
            def _(pool):
                for x in range(2):
                    self.pool.tell(nc.gpsimd.tensor_tensor(half(sq[1], x), half(k, x), half(k, x), ALU.mult), self.pool_out)

            @block.tensor
            def _(pe):
                for n, base in enumerate((0, 32)):
                    for t in range(NC):
                        ins = nc.tensor.transpose(self.ps[:, 4 + n, t * 4:t * 4 + 4], gs[base:base + 4, t * P:(t + 1) * P],
                                                  self.cst[base:base + 4, CONST_AT["ident"] + base:CONST_AT["ident"] + base + 4])
                ins.then_inc(self.tensor_out2.sem, 1)
                for n in range(4):
                    if n == 1:
                        pe.wait_ge(self.vector_out.sem, self.vector_out.at(1))
                    if n < 2:
                        pe.wait_ge(self.squares_ready.sem, self.squares_ready.at(n + 1))
                    else:
                        pe.wait_ge(self.pool_out.sem, self.pool_out.at(n - 1))
                        pe.wait_ge(self.scalar_out.sem, self.scalar_out.at(2 * n - 3))
                    for m, (h, (lo, hi)) in enumerate((h, span) for h in range(2) for span in self.SPANS):
                        ins = nc.tensor.matmul(self.ps[:, 4 * (n % 2) + m, 0:HALF], self.const("ones"),
                                               sq[n // 2][:, 2 * (n % 2) + h, lo:hi], start=True, stop=True)
                    ins.then_inc(self.tensor_out.sem, 1)
                for n in range(4):
                    if n < 2:
                        pe.wait_ge(self.scalar_out.sem, self.scalar_out.at(2 * n + 5))
                    else:
                        pe.wait_ge(self.vector_out.sem, self.vector_out.at(n))
                    spread(n % 2, 32 * (n // 2))
                self.tensor_out.count += 8
                self.tensor_out2.count += 1

            @block.vector
            def _(dve):
                dve.wait_ge(self.tensor_out2.sem, self.tensor_out2.at(1))
                self.dve.tell(nc.vector.tensor_copy(col[:, 0:2].rearrange("p x c h -> p x (c h)"), self.ps[:, 4:6, 0:16]),
                              self.vector_out)
                for n in range(4):
                    dve.wait_ge(self.scalar_out.sem, self.scalar_out.at(2 * n + 2))
                    x = half((q, k)[n // 2], n % 2)
                    if n < 2:
                        self.dve.step(nc.vector.scalar_tensor_tensor(x, x, P ** -0.5, half(r[0], n), ALU.mult, ALU.mult))
                    else:
                        self.dve.step(nc.vector.tensor_tensor(x, x, half(r[1], n - 2), ALU.mult))
                for n in range(2):
                    dve.wait_ge(self.scalar_out.sem, self.scalar_out.at(9 + n))
                    for t in range(NC):
                        for h in (2 * n, 2 * n + 1):
                            for lo, hi, bank, at in self.pieces(t):
                                self.dve.step(nc.vector.tensor_scalar(
                                    dm[:, t, h, lo:hi], self.ps[:, 2 * h + bank, at:at + hi - lo], col[:, 0, t, h:h + 1], 0.0,
                                    ALU.subtract, ALU.min))
                        end, two = (t + 1) * P - 1, slice(2 * n, 2 * n + 2)
                        last = heads4[:, two, end // HALF, end % HALF]
                        self.dve.step(nc.vector.tensor_copy(col[:, 3, t, two], last))
                        ins = nc.vector.tensor_tensor(col[:, 2, t, two], col[:, 3, t, two], col[:, 0, t, two], ALU.subtract)
                        self.dve.step(ins) if t < NC - 1 else self.dve.tell(ins, self.vector_out)
                for n in range(2):
                    dve.wait_ge(self.tensor_out.sem, self.tensor_out.at(7 + n))
                    dve.wait_ge(self.scalar_out.sem, self.scalar_out.at(11 + n))
                    two = slice(2 * n, 2 * n + 2)
                    self.dve.step(nc.vector.tensor_copy(bs[:, two], heads4[:, two, 1, HALF - B:HALF]))
                    for t in range(NC):
                        for lo, hi, bank, at in self.pieces(t):
                            self.dve.step(nc.vector.scalar_tensor_tensor(
                                ld[:, t, two, lo:hi], dm[:, t, two, lo:hi], -1.0, heads4[:, two, bank, at:at + hi - lo],
                                ALU.mult, ALU.mult))
                flat = ld.rearrange("p c h t -> p (c h) t")
                self.dve.step(nc.vector.tensor_tensor(flat, flat, self.const("before").unsqueeze(1).to_broadcast([P, 16, P]),
                                                      ALU.mult))
                flat = dm.rearrange("p c h t -> p (c h) t")
                self.dve.step(nc.vector.tensor_tensor(flat, flat, self.const("causal").unsqueeze(1).to_broadcast([P, 16, P]),
                                                      ALU.mult))

    def pieces(self, t):
        out = []
        for s, (lo, hi) in enumerate(self.SPANS):
            a, b = max(lo, t * P), min(hi, (t + 1) * P)
            if a < b:
                out.append((a - t * P, b - t * P, s, a - lo))
        return out

    def delta_inverses(self):
        nc, c = self.nc, self.c
        k = c[:, DK:DK + 4]
        ld = self.flat(self.E_LD)[:, 0:2048].rearrange("p (g x t) -> p g x t", g=2, x=8)

        def fill(pe, g, bank):
            for x in range(8):
                t, h = 2 * g + x // 4, x % 4
                kc = k[:, h, t * P:(t + 1) * P]
                ins = nc.tensor.matmul(self.ps[:, bank + x // 4, h * P:(h + 1) * P], kc, kc, start=True, stop=True)
            ins.then_inc(self.tensor_out.sem, 1)

        self.inv = [self.cut(self.E_INV + 1024 * g, 8, P) for g in range(2)]
        self.unit_inverses(2, 2, (lambda g: ld[:, g], [f"level{m}" for m in LEVELS[::-1]]), 0, 2048, 4096, self.inv, fill)

    def delta_chain(self):
        nc, c = self.nc, self.c
        q, k, v = (c[:, x:x + 4] for x in (DQ, DK, DV))
        eg = c[:, self.E_EG:self.E_EG + 4]
        dm = self.flat(self.E_DM)[:, 0:2048].rearrange("p (c h t) -> p c h t", c=NC, h=4)
        col = self.cut(self.E_COL, 4, NC, 4)
        inv = self.cut(self.E_INV, NC, 4, P)
        vt, kt, qk, u = (self.cut(x, NC, 4, P) for x in (self.E_VT, self.E_KT, self.E_QK, self.E_U))
        st = self.cut(self.E_S, NC + 1, 4, P)
        rr = self.cut(self.E_R, 4, P)

        def wide(t):
            return t.rearrange("p c h t -> p (c h t)")

        with self.stage() as block:
            @block.tensor
            def _(pe):
                for n, src in enumerate((v, k)):
                    for t in range(NC):
                        for h in range(4):
                            ins = nc.tensor.transpose(self.ps[:, 4 * n + t, h * P:(h + 1) * P], src[:, h, t * P:(t + 1) * P],
                                                      self.const("ident"))
                    ins.then_inc(self.tensor_out.sem, 1)
                pe.wait_ge(self.scalar_out.sem, self.scalar_out.at(1))
                for t in range(NC):
                    for h in range(4):
                        cols = slice(t * P, (t + 1) * P)
                        ins = nc.tensor.matmul(self.ps[:, t, h * P:(h + 1) * P], k[:, h, cols], q[:, h, cols],
                                               start=True, stop=True)
                ins.then_inc(self.tensor_out.sem, 1)
                pe.wait_ge(self.vector_out.sem, self.vector_out.at(1))

                def output(t, heads):
                    if t == 0:
                        pe.wait_ge(self.vector_out.sem, self.vector_out.at(2))
                    if t == 1:
                        pe.wait_ge(self.pool_out.sem, self.pool_out.at(1))
                    cols = slice(t * P, (t + 1) * P)
                    for h in heads:
                        ins = nc.tensor.matmul(self.ps[:, h, cols], u[:, t, h], qk[:, t, h], start=True, stop=t == 0)
                        if t:
                            ins = nc.tensor.matmul(self.ps[:, h, cols], st[:, t, h], q[:, h, cols], start=False, stop=True)
                    return ins

                for t in range(NC):
                    cols = slice(t * P, (t + 1) * P)
                    if t:
                        pe.wait_ge(self.vector_out2.sem, self.vector_out2.at(2 * t))
                        for h in range(4):
                            ins = nc.tensor.matmul(self.ps[:, 4, h * P:(h + 1) * P], k[:, h, cols], st[:, t, h],
                                                   start=True, stop=True)
                        ins.then_inc(self.tensor_out2.sem, 1)
                        output(t - 1, (0, 1))
                    pe.wait_ge(self.vector_out2.sem, self.vector_out2.at(2 * t + 1))
                    for h in range(4):
                        ins = nc.tensor.matmul(self.ps[:, 5, h * P:(h + 1) * P], inv[:, t, h], rr[:, h], start=True, stop=True)
                    ins.then_inc(self.tensor_out2.sem, 1)
                    if t:
                        output(t - 1, (2, 3))
                    pe.wait_ge(self.scalar_out.sem, self.scalar_out.at(2 + t))
                    for h in range(4):
                        ins = nc.tensor.matmul(self.ps[:, 6, h * P:(h + 1) * P], kt[:, t, h], u[:, t, h], start=True, stop=True)
                    ins.then_inc(self.tensor_out2.sem, 1)
                output(NC - 1, range(4)).then_inc(self.tensor_out.sem, 1)
                self.tensor_out.count += 4
                self.tensor_out2.count += 3 * NC - 1

            @block.scalar
            def _(act):
                act.wait_ge(self.tensor_out.sem, self.tensor_out.at(1))
                self.act.tell(nc.scalar.activation(wide(vt), self.banks(0, 4), ACT.Copy), self.scalar_out)
                for t in range(NC):
                    act.wait_ge(self.tensor_out2.sem, self.tensor_out2.at(3 * t + 1))
                    self.act.tell(nc.scalar.activation(u[:, t].rearrange("p h e -> p (h e)"), self.ps[:, 5, :], ACT.Copy),
                                  self.scalar_out)
                act.wait_ge(self.tensor_out.sem, self.tensor_out.at(4))
                self.act.step(nc.scalar.activation(self.o[:, 4:8, 0:T], self.ps[:, 0:4, :], ACT.Copy))

            @block.gpsimd
            def _(pool):
                pool.wait_ge(self.tensor_out.sem, self.tensor_out.at(3))
                self.pool.tell(nc.gpsimd.tensor_tensor(q[:, :, 0:T], q[:, :, 0:T], eg[:, :, 0:T], ALU.mult), self.pool_out)

            @block.vector
            def _(dve):
                flat = inv.rearrange("p c h t -> p (c h) t")
                beta = col[:, 1].rearrange("p c h -> p (c h)").unsqueeze(2).to_broadcast([P, 16, P])
                self.dve.step(nc.vector.tensor_tensor(flat, flat, beta, ALU.mult))
                dve.wait_ge(self.tensor_out.sem, self.tensor_out.at(2))
                decay = col[:, 2].rearrange("p c h -> p (c h)").unsqueeze(2).to_broadcast([P, 16, P])
                self.dve.step(nc.vector.tensor_tensor(kt.rearrange("p c h t -> p (c h) t"),
                                                      self.banks(4, 4).rearrange("p (x t) -> p x t", t=P), decay, ALU.mult))
                dve.wait_ge(self.tensor_out.sem, self.tensor_out.at(3))
                self.dve.tell(nc.vector.tensor_tensor(k[:, :, 0:T], k[:, :, 0:T], eg[:, :, 0:T], ALU.mult), self.vector_out)
                dve.wait_ge(self.scalar_out.sem, self.scalar_out.at(1))
                self.dve.tell(nc.vector.tensor_copy(rr, vt[:, 0]), self.vector_out2)
                self.dve.tell(nc.vector.tensor_tensor(wide(qk), self.banks(0, 4), wide(dm), ALU.mult), self.vector_out)
                for t in range(NC):
                    if t:
                        dve.wait_ge(self.tensor_out2.sem, self.tensor_out2.at(3 * t))
                        self.dve.tell(nc.vector.tensor_tensor(rr.rearrange("p h e -> p (h e)"), vt[:, t].rearrange("p h e -> p (h e)"),
                                                              self.ps[:, 4, :], ALU.subtract), self.vector_out2)
                    dve.wait_ge(self.tensor_out2.sem, self.tensor_out2.at(3 * t + 2))
                    new = st[:, t + 1]
                    if t == 0:
                        ins = nc.vector.tensor_copy(new.rearrange("p h e -> p (h e)"), self.ps[:, 6, :])
                    else:
                        self.dve.step(nc.vector.tensor_tensor(new, st[:, t], col[:, 3, t].unsqueeze(2).to_broadcast([P, 4, P]),
                                                              ALU.mult))
                        ins = nc.vector.tensor_tensor(new.rearrange("p h e -> p (h e)"), new.rearrange("p h e -> p (h e)"),
                                                      self.ps[:, 6, :], ALU.add)
                    self.dve.tell(ins, self.vector_out2)

            @block.sync
            def _(sp):
                sp.wait_ge(self.vector_out2.sem, self.vector_out2.at(2 * NC))
                self.store(sp, self.d["p_delta"], st[:, NC].rearrange("p h e -> p (h e)"))

    def delta_sample(self):
        nc, c = self.nc, self.c
        s4 = lambda x: c[:, x:x + 4, T:N]
        ss = self.h[:].rearrange("p a b -> p (a b)")[:, 0:4096].rearrange("p (b h e) -> p b h e", b=B, h=4)
        pr = self.cut(0, B, 4, P)
        vs = self.cut(4096, 4, P)
        nk, kb = self.cut(4608, 4, B), self.cut(4640, 4, B)
        bs = self.cut(self.E_COL + 64, 4, B)

        with self.stage() as block:
            @block.sync
            def _(sp):
                sp.wait_ge(self.vector_out2.sem, self.vector_out2.at(B))
                self.store(sp, self.d["s_delta"], ss)
                sp.wait_ge(self.stored.sem, self.stored.count)

            @block.tensor
            def _(pe):
                for h in range(4):
                    ins = nc.tensor.transpose(self.ps[0:B, 7, h * P:(h + 1) * P], c[:, DV + h, T:N], self.const("ident"))
                ins.then_inc(self.tensor_out.sem, 1)
                pe.wait_ge(self.scalar_out.sem, self.scalar_out.at(1))
                for b0 in range(B):
                    pe.wait_ge(self.vector_out.sem, self.vector_out.at(b0 + 1))
                    nc.tensor.matmul(self.ps[:, b0, :], self.cst[0:B, SEL_AT + b0 * P:SEL_AT + (b0 + 1) * P],
                                     vs[0:B].rearrange("p h e -> p (h e)"), start=True, stop=False)
                    nc.tensor.matmul(self.ps[:, b0, :], self.const("ones"), pr[:, b0].rearrange("p h e -> p (h e)"),
                                     start=False, stop=True).then_inc(self.tensor_out2.sem, 1)
                for b0 in range(B):
                    pe.wait_ge(self.vector_out2.sem, self.vector_out2.at(b0 + 1))
                    for h in range(4):
                        at = h * B + b0
                        ins = nc.tensor.matmul(self.ps[:, 0, at:at + 1], ss[:, b0, h], c[:, DQ + h, T + b0:T + b0 + 1],
                                               start=True, stop=True)
                ins.then_inc(self.tensor_out.sem, 1)
                self.tensor_out.count += 2
                self.tensor_out2.count += B

            @block.scalar
            def _(act):
                act.wait_ge(self.tensor_out.sem, self.tensor_out.at(1))
                self.act.tell(nc.scalar.activation(vs[0:B].rearrange("p a b -> p (a b)"), self.ps[0:B, 7, :], ACT.Copy),
                              self.scalar_out)
                act.wait_ge(self.tensor_out.sem, self.tensor_out.at(2))
                self.act.step(nc.scalar.activation(self.o[:, 4:8, T:N], self.ps[:, 0, 0:32].rearrange("p (h b) -> p h b", b=B),
                                                   ACT.Copy))

            @block.vector
            def _(dve):
                def wide(t, b0):
                    return t[:, :, b0].unsqueeze(2).to_broadcast([P, 4, P])

                self.dve.step(nc.vector.tensor_scalar(nk, s4(DK), -1.0, None, ALU.mult))
                self.dve.step(nc.vector.tensor_tensor(kb, s4(DK), bs, ALU.mult))
                dve.wait_ge(self.delta_loaded.sem, self.delta_loaded.at(16))
                self.delta_loaded.count += 16
                decay = c[:, self.E_EG:self.E_EG + 4, T:N]
                for b0 in range(B):
                    self.dve.step(nc.vector.tensor_tensor(ss[:, b0], ss[:, b0], wide(decay, b0), ALU.mult))
                    self.dve.tell(nc.vector.tensor_tensor(pr[:, b0], ss[:, b0], wide(nk, b0), ALU.mult), self.vector_out)
                for b0 in range(B):
                    dve.wait_ge(self.tensor_out2.sem, self.tensor_out2.at(b0 + 1))
                    self.dve.step(nc.vector.tensor_tensor(pr[:, b0], self.ps[:, b0, :].rearrange("p (h e) -> p h e", h=4),
                                                          wide(kb, b0), ALU.mult))
                    self.dve.tell(nc.vector.tensor_tensor(ss[:, b0], ss[:, b0], pr[:, b0], ALU.add), self.vector_out2)


    def run(self):
        nc = self.nc
        L = self.lin
        self.start()
        self.params = EVEN_PARAMS, self.par0
        self.projection(L["in0"], "g_mix", L["out0"], first=True)
        self.gla_gates()
        self.gla_levels()
        self.gla_states()
        self.gated_norm(0, GG, "gla_norm")
        self.rwkv_low_rank()
        self.rwkv_vectors()
        self.rwkv_sample()
        self.rwkv_inverses()
        self.rwkv_chain()
        self.rwkv_output()
        self.residual(L["out0"], self.std, L["xkv0"], src=self.o, load_memory=True, summed=4)
        self.memory(0, L["xq0"])
        self.query(0, L["xo0"])
        self.head_norms(0)
        self.attention(0)
        self.residual(L["xo0"], self.std, L["gu0"], src=self.o)
        self.gate_up(0, L["down0"])
        self.residual(L["down0"], self.hid, L["in1"], per=2)
        self.params = ODD_PARAMS, self.par1
        self.projection(L["in1"], "g_mix", L["out1"])
        self.stick_norms()
        self.stick_prompt()
        self.stick_sample()
        self.delta_vectors()
        self.delta_inverses()
        self.delta_chain()
        self.delta_sample()
        self.gated_norm(4, DZ, "dn_norm")
        self.residual(L["out1"], self.std, L["xkv1"], src=self.o, load_memory=True, summed=4)
        self.memory(1, L["xq1"])
        self.query(1, L["xo1"])
        self.head_norms(1)
        self.attention(1)
        self.residual(L["xo1"], self.std, L["gu1"], src=self.o)
        self.gate_up(1, L["down1"])
        self.residual(L["down1"], self.hid, None, per=2, summed=None)
        self.finish()

    def finish(self):
        with self.stage() as block:
            @block.sync
            def _(sp):
                self.store(sp, self.d["y"], self.x[:])
                sp.wait_ge(self.stored.sem, self.stored.count)


def units(w, kt=KT):
    k, n = w.shape
    a = w.reshape(k // (kt * P), kt, P, n // P, P).transpose(3, 0, 2, 1, 4)
    return np.ascontiguousarray(a.reshape(-1, P, kt * P))


def feature_major(a):
    return np.ascontiguousarray(a.reshape(a.shape[0], -1, P).transpose(2, 1, 0))


def column(v):
    return v.reshape(-1, P).T


def rows(v, width=1):
    v = v.reshape(-1, width) if v.ndim == 1 else v
    out = np.zeros((P, v.shape[1]), v.dtype)
    out[:v.shape[0]] = v
    return out


def lay_out(I):
    a = {"cst": constants()}
    a["x"] = np.concatenate([feature_major(I["x_prompt"][0]), feature_major(I["x_sample"][:, 0])], axis=2)
    a["mem"] = feature_major(I["mem_prompt"][0])
    we, wo = I["w_in_even"][0], I["w_in_odd"][0]
    tail0, tail1 = np.zeros((D, P), we.dtype), np.zeros((D, P), wo.dtype)
    tail0[:, 0:16] = we[:, 1536:1552]
    tail1[:, 0:4], tail1[:, 32:36] = wo[:, 3584:3588], wo[:, 3588:3592]
    a["w_in0"] = units(np.concatenate([we[:, 0:1536], we[:, 1552:], tail0], axis=1))
    a["w_in1"] = units(np.concatenate([wo[:, :3584], tail1], axis=1))
    a["w_out0"], a["w_out1"] = units(I["w_out_even"][0]), units(I["w_out_odd"][0])
    for i in range(2):
        a[f"w_xq{i}"], a[f"w_xkv{i}"], a[f"w_xo{i}"] = (units(I[n][i]) for n in ("w_xq", "w_xkv", "w_xo"))
        gu = I["w_gu"][i].reshape(D, 2, FT, P).transpose(0, 2, 1, 3).reshape(D, -1)
        a[f"w_gu{i}"], a[f"w_down{i}"] = units(gu), units(I["w_down"][i], SLOT_K)

    def common(i):
        return [column(I[n][i]) for n in ("norm_mix", "norm_cross", "norm_ffn", "mem_norm", "xq_norm", "xk_norm")]

    a["par0"] = np.concatenate(common(0) + [
        column(I["gla_b_a"][0]), column(I["gla_norm"][0])] + [column(I["rwkv_" + n][0]) for n in
        ("mu", "w0", "a0", "k_k", "k_a", "r_k", "ln_w", "ln_b")] + [
        rows(I["gla_w_a2"][0]), np.concatenate([I["rwkv_w2"][0], I["rwkv_a2"][0]]), I["rwkv_g2"][0]], axis=1)
    a["par1"] = np.concatenate(common(1) + [
        np.tile(I["sb_q_norm"][0], 2)[:, None], np.tile(I["sb_k_norm"][0], 2)[:, None],
        np.tile(I["sb_bias"][0], (P, 1)), I["dn_conv"][0].reshape(4, 12, P).transpose(2, 0, 1).reshape(P, 48),
        rows(I["dn_a_log"][0]), rows(I["dn_dt_bias"][0]), column(I["dn_norm"][0])], axis=1)
    a["state_gla"] = I["state_gla"][0].reshape(B, 2, P, P).transpose(2, 0, 1, 3)
    a["state_rwkv"] = I["state_rwkv"][0].reshape(B, 4, 2, 64, 64).transpose(2, 4, 0, 1, 3).reshape(P, B, 4, 64)
    a["state_shift"] = feature_major(I["state_rwkv_shift"][0])
    a["state_delta"] = I["state_delta"][0].transpose(2, 0, 1, 3)
    a["state_conv"] = I["state_delta_conv"][0].reshape(B, 3, 12, P).transpose(3, 2, 1, 0)
    a["cache_k"] = I["cache_sb_k"][0].reshape(NPHYS, PAGE, 4, P).transpose(0, 3, 2, 1).reshape(NPHYS, P, 512)
    a["cache_v"] = I["cache_sb_v"][0].reshape(NPHYS, PAGE, 512)
    a["page_table"] = I["page_table"].reshape(1, B * PAGES)
    for i in range(2):
        a[f"mem_k{i}"] = I["cache_mem_k"][i].reshape(B, MEM, 8, P).transpose(0, 3, 2, 1)
        a[f"mem_v{i}"] = I["cache_mem_v"][i].reshape(B, 2, P, D).transpose(0, 2, 1, 3)
    return {k: np.ascontiguousarray(v) for k, v in a.items()}


OUTPUTS = {
    "y": (P, KT, N), "p_gla": (P, 2 * P), "s_gla": (P, B, 2, P), "shift": (P, R_TILES, B + 1),
    "p_rwkv": (P, 4 * 64), "s_rwkv": (P, B, 4, 64), "p_sbk": (P, 4, N), "p_sbv": (P, 4, N),
    "p_delta": (P, 4 * P), "s_delta": (P, B, 4, P), "p_conv": (P, 12, 3), "s_conv": (P, 12, 3, B),
    "p_mk0": (P, 8, MEM), "p_mk1": (P, 8, MEM), "p_mv0": (P, 8, MEM), "p_mv1": (P, 8, MEM),
}


def build(nc, arrays):
    with ExitStack() as ctx:
        dram = {}
        for n, a in arrays.items():
            dt = I32 if a.dtype.kind == "i" else F32
            dram[n] = nc.dram_tensor("in_" + n, list(a.shape), dt, kind="ExternalInput").ap()
        for n, shape in OUTPUTS.items():
            dram[n] = nc.dram_tensor("out_" + n, list(shape), F32, kind="ExternalOutput").ap()
        k = Kernel(nc, dram, ctx)
        k.lin = {}
        for i, n_in in enumerate((EVEN_TILES, ODD_TILES)):
            for n, count, kt in (("in", n_in, KT), ("out", 8, KT), ("xkv", 16, KT), ("xq", 8, KT), ("xo", 8, KT),
                                 ("gu", 2 * FT, KT), ("down", 16, SLOT_K)):
                k.lin[f"{n}{i}"] = Linear(dram[f"w_{n}{i}"], count, kt)
        k.run()


def kernel(**inputs):
    from concourse import bacc
    from concourse.bass_utils import run_bass_kernel_spmd

    arrays = lay_out({k: np.asarray(v) for k, v in inputs.items()})
    nc = bacc.Bacc("TRN2", target_bir_lowering=False, num_devices=1)
    build(nc, arrays)
    r = run_bass_kernel_spmd(nc, [{"in_" + n: a for n, a in arrays.items()}], core_ids=[0]).results[0]
    o = {n: np.asarray(r["out_" + n]) for n in OUTPUTS}

    def token_major(t):
        return np.ascontiguousarray(t.transpose(2, 1, 0).reshape(t.shape[2], -1))

    y, k, v = token_major(o["y"]), token_major(o["p_sbk"]), token_major(o["p_sbv"])
    rwkv = lambda t: t.reshape(2, 64, -1, 4, 64).transpose(2, 3, 0, 4, 1).reshape(-1, 8, 64, 64)
    out = (
        y[None, :T], y[T:, None],
        o["p_gla"].reshape(P, 2, P).transpose(1, 0, 2).reshape(1, 1, 4, 64, P), rwkv(o["p_rwkv"])[None],
        token_major(o["shift"])[None, :1],
        k[:T].reshape(1, 1, T, 8, 64), v[:T].reshape(1, 1, T, 8, 64),
        o["p_delta"].reshape(P, 4, P).transpose(1, 0, 2)[None, None],
        o["p_conv"].transpose(2, 1, 0).reshape(1, 1, 3, 1536),
        np.stack([token_major(o[f"p_mk{i}"]).reshape(1, MEM, 4, 256) for i in range(2)]),
        np.stack([token_major(o[f"p_mv{i}"]).reshape(1, MEM, 4, 256) for i in range(2)]),
        o["s_gla"].transpose(1, 2, 0, 3).reshape(1, B, 4, 64, P), rwkv(o["s_rwkv"])[None],
        token_major(o["shift"])[None, 1:],
        k[T:].reshape(1, B, 1, 8, 64), v[T:].reshape(1, B, 1, 8, 64),
        o["s_delta"].transpose(1, 2, 0, 3)[None],
        o["s_conv"].transpose(3, 2, 1, 0).reshape(1, B, 3, 1536),
    )
    return tuple(np.ascontiguousarray(a) for a in out)
```
